# Optimizing a Trainium2 kernel written in Bass

```python
import math
import jax, jax.numpy as jnp
from jax import lax
import numpy as np

D_MODEL = 1024
BATCH = 1
SEQ = 1024
DEPTH = 1

GLA_HEADS = 4
GLA_DV = D_MODEL // GLA_HEADS
GLA_DK = GLA_DV // 2
GLA_RANK = 16
GLA_TAU = 16.0
GLA_CHUNK = 64
SWA_HD = 64
SWA_HEADS = D_MODEL // SWA_HD
SWA_KV_HEADS = 2
SWA_WINDOW = 128
ROPE_DIM = SWA_HD // 4
ROPE_THETA = 500000.0
D_FF = 2816
CONV_W = 3
N_BRANCH = 2
LN_EPS = 1e-5
RMS_EPS = 1e-6
ALPHA = (2.0 * DEPTH) ** 0.25
BETA = (8.0 * DEPTH) ** -0.25
N_MOD = 6

SPLITS = (
    GLA_HEADS * GLA_DK,
    GLA_HEADS * GLA_DK,
    GLA_HEADS * GLA_DV,
    GLA_HEADS * GLA_DV,
    GLA_RANK,
    SWA_HEADS * SWA_HD,
    SWA_KV_HEADS * SWA_HD,
    SWA_KV_HEADS * SWA_HD,
    N_BRANCH * D_MODEL,
)
D_IN = sum(SPLITS)
SPLIT_POINTS = tuple(int(v) for v in np.cumsum(SPLITS)[:-1])


def layer_norm(x, eps=LN_EPS):
    xf = x.astype(jnp.float32)
    mu = jnp.mean(xf, -1, keepdims=True)
    var = jnp.mean(jnp.square(xf - mu), -1, keepdims=True)
    return ((xf - mu) * lax.rsqrt(var + eps)).astype(x.dtype)

def layer_norm_affine(x, g, b):
    return layer_norm(x) * g + b

def rms_norm(x, g, eps=RMS_EPS):
    xf = x.astype(jnp.float32)
    y = xf * lax.rsqrt(jnp.mean(jnp.square(xf), -1, keepdims=True) + eps)
    return y.astype(x.dtype) * g

def partial_rope(t, cos, sin):
    half = ROPE_DIM // 2
    t1, t2, rest = t[..., :half], t[..., half:ROPE_DIM], t[..., ROPE_DIM:]
    return jnp.concatenate([t1 * cos - t2 * sin, t2 * cos + t1 * sin, rest], axis=-1)

def gla_chunked(q, k, v, log_a):
    B, S, H, DK = q.shape
    DV = v.shape[-1]
    n = S // GLA_CHUNK

    def to_chunks(t):
        return t.reshape(B, n, GLA_CHUNK, H, t.shape[-1]).transpose(1, 0, 3, 2, 4)

    qc, kc, vc, gc = map(to_chunks, (q, k, v, log_a))
    gcum = jnp.cumsum(gc.astype(jnp.float32), axis=3)
    g_last = gcum[..., -1:, :]
    g_mid = gcum[..., GLA_CHUNK // 2 - 1:GLA_CHUNK // 2, :]
    q_mid = qc * jnp.exp(gcum - g_mid)
    k_mid = kc * jnp.exp(g_mid - gcum)
    a_intra = jnp.einsum('nbhik,nbhjk->nbhij', q_mid, k_mid)
    causal = jnp.tril(jnp.ones((GLA_CHUNK, GLA_CHUNK), dtype=bool))
    a_intra = jnp.where(causal, a_intra, 0.0)
    o_intra = jnp.einsum('nbhij,nbhjv->nbhiv', a_intra, vc.astype(jnp.float32))
    q_in = qc * jnp.exp(gcum)
    k_out = kc * jnp.exp(g_last - gcum)
    decay = jnp.exp(g_last)

    def step(state, inp):
        q_i, k_o, v_i, dec = inp
        o = jnp.einsum('bhik,bhkv->bhiv', q_i, state)
        state = state * dec[:, :, 0, :, None] + jnp.einsum('bhjk,bhjv->bhkv', k_o, v_i.astype(jnp.float32))
        return state, o

    state0 = jnp.zeros((B, H, DK, DV), jnp.float32)
    _, o_inter = lax.scan(step, state0, (q_in, k_out, vc, decay))
    o = (o_intra + o_inter).astype(v.dtype)
    return o.transpose(1, 0, 3, 2, 4).reshape(B, S, H, DV)

def swa_with_sinks(q, k, v, sinks):
    B, S, HQ, hd = q.shape
    HKV = k.shape[2]
    G = HQ // HKV
    W = SWA_WINDOW
    n = S // W
    qb = q.reshape(B, n, W, HKV, G, hd)

    def band(t):
        tb = t.reshape(B, n, W, HKV, hd)
        prev = jnp.pad(tb[:, :-1], ((0, 0), (1, 0), (0, 0), (0, 0), (0, 0)))
        return jnp.concatenate([prev, tb], axis=2)

    kb, vb = band(k), band(v)
    s = jnp.einsum('bnqkgd,bnjkd->bkgnqj', qb, kb).astype(jnp.float32) * (hd ** -0.5)
    qi = jnp.arange(W)[:, None]
    kj = jnp.arange(2 * W)[None, :]
    diff = W + qi - kj
    win = (diff >= 0) & (diff < W)
    blk = jnp.arange(n)[:, None, None]
    mask = win[None] & ((blk > 0) | (kj >= W)[None])
    s = jnp.where(mask[None, None, None], s, -jnp.inf)
    sink = sinks.astype(jnp.float32).reshape(HKV, G)[None, :, :, None, None, None]
    m = jnp.maximum(jnp.max(s, -1, keepdims=True), sink)
    p = jnp.exp(s - m)
    p = p / (jnp.sum(p, -1, keepdims=True) + jnp.exp(sink - m))
    o = jnp.einsum('bkgnqj,bnjkd->bnqkgd', p.astype(v.dtype), vb)
    return o.reshape(B, S, HQ, hd)

def first_inputs(seed: int = 0) -> dict:
    key = jax.random.key(seed)
    ks = jax.random.split(key, 20)
    f32 = jnp.float32
    L, D = DEPTH, D_MODEL
    nrm = lambda k, shape, s: jax.random.normal(k, shape, f32) * s
    return {
        "x": nrm(ks[0], (BATCH, SEQ, D), 1.0),
        "c": nrm(ks[1], (BATCH, D), 1.0),
        "positions": jnp.broadcast_to(jnp.arange(SEQ, dtype=jnp.int32), (BATCH, SEQ)),
        "w_ada": nrm(ks[2], (L, D, N_MOD * D), 0.5 * D ** -0.5),
        "b_ada": nrm(ks[3], (L, N_MOD * D), 0.01),
        "w_in": nrm(ks[4], (L, D, D_IN), D ** -0.5),
        "gla_w_lr": nrm(ks[5], (L, GLA_RANK, GLA_HEADS * GLA_DK), GLA_RANK ** -0.5),
        "gla_b_lr": nrm(ks[6], (L, GLA_HEADS * GLA_DK), 0.01),
        "gla_norm_g": 1.0 + nrm(ks[7], (L, GLA_DV), 0.01),
        "swa_sinks": nrm(ks[8], (L, SWA_HEADS), 1.0),
        "w_o": nrm(ks[9], (L, D, D), BETA * D ** -0.5),
        "ln1_g": 1.0 + nrm(ks[10], (L, D), 0.01),
        "ln1_b": nrm(ks[11], (L, D), 0.01),
        "w_up": nrm(ks[12], (L, D, 2 * D_FF), D ** -0.5),
        "conv_w": nrm(ks[13], (L, CONV_W, 2 * D_FF), CONV_W ** -0.5),
        "conv_b": nrm(ks[14], (L, 2 * D_FF), 0.01),
        "w_down": nrm(ks[15], (L, D_FF, D), BETA * D_FF ** -0.5),
        "ln2_g": 1.0 + nrm(ks[16], (L, D), 0.01),
        "ln2_b": nrm(ks[17], (L, D), 0.01),
    }

def first_block(x, c, positions, w_ada, b_ada, w_in, gla_w_lr, gla_b_lr, gla_norm_g, swa_sinks,
              w_o, ln1_g, ln1_b, w_up, conv_w, conv_b, w_down, ln2_g, ln2_b):
    B, S, D = x.shape
    inv_freq = ROPE_THETA ** (-(jnp.arange(0, ROPE_DIM, 2, dtype=jnp.float32) / ROPE_DIM))
    ang = positions.astype(jnp.float32)[..., None] * inv_freq
    cos = jnp.cos(ang)[:, :, None, :].astype(x.dtype)
    sin = jnp.sin(ang)[:, :, None, :].astype(x.dtype)
    c_act = jax.nn.silu(c)

    for l in range(DEPTH):
        mod = c_act @ w_ada[l] + b_ada[l]
        shift1, scale1, gate1, shift2, scale2, gate2 = [m[:, None, :] for m in jnp.split(mod, N_MOD, axis=-1)]

        h = layer_norm(x) * (1.0 + scale1) + shift1
        proj = h @ w_in[l]
        qa, ka, va, ra, lra, qb, kb, vb, gates = jnp.split(proj, SPLIT_POINTS, axis=-1)

        log_a = jax.nn.log_sigmoid((lra @ gla_w_lr[l] + gla_b_lr[l]).astype(jnp.float32)) / GLA_TAU
        qa = qa.reshape(B, S, GLA_HEADS, GLA_DK) * (GLA_DK ** -0.5)
        ka = ka.reshape(B, S, GLA_HEADS, GLA_DK)
        va = va.reshape(B, S, GLA_HEADS, GLA_DV)
        log_a = log_a.reshape(B, S, GLA_HEADS, GLA_DK)
        o_a = gla_chunked(qa, ka, va, log_a)
        y_a = (rms_norm(o_a, gla_norm_g[l]) * jax.nn.silu(ra.reshape(B, S, GLA_HEADS, GLA_DV))).reshape(B, S, D)

        qb = partial_rope(qb.reshape(B, S, SWA_HEADS, SWA_HD), cos, sin)
        kb = partial_rope(kb.reshape(B, S, SWA_KV_HEADS, SWA_HD), cos, sin)
        vb = vb.reshape(B, S, SWA_KV_HEADS, SWA_HD)
        y_b = swa_with_sinks(qb, kb, vb, swa_sinks[l]).reshape(B, S, D)

        g_a, g_b = jnp.split(gates, N_BRANCH, axis=-1)
        y = jax.nn.sigmoid(g_a) * y_a + jax.nn.sigmoid(g_b) * y_b
        x = layer_norm_affine(ALPHA * x + gate1 * (y @ w_o[l]), ln1_g[l], ln1_b[l])

        h2 = layer_norm(x) * (1.0 + scale2) + shift2
        u = h2 @ w_up[l]
        up = jnp.pad(u, ((0, 0), (CONV_W - 1, 0), (0, 0)))
        u = conv_b[l] + sum(conv_w[l, t] * up[:, t:t + S] for t in range(CONV_W))
        u_gate, u_val = jnp.split(u, 2, axis=-1)
        f = jax.nn.gelu(u_gate, approximate=False) * u_val
        x = layer_norm_affine(ALPHA * x + gate2 * (f @ w_down[l]), ln2_g[l], ln2_b[l])

    return x


_first_inputs = first_inputs


def first_inputs(seed=0):
    import zlib

    import numpy as np

    out = dict(_first_inputs(seed))
    spreads = {}
    factors = {'b_ada': 8.0,
     'gla_w_lr': 5.552,
     'gla_b_lr': 64.0,
     'gla_norm_g': 200.0,
     'swa_sinks': 200.0,
     'ln1_g': 188.679,
     'ln1_b': 190.937,
     'conv_b': 200.0,
     'ln2_g': 198.216,
     'ln2_b': 189.395,
     'w_up': 8.0,
     'conv_w': 8.0,
     'w_down': 8.0}
    for name, (base, spread) in spreads.items():
        noise = np.random.default_rng([zlib.crc32(name.encode()), seed]).standard_normal(out[name].shape)
        drawn = base * np.exp(spread * noise) if base else spread * noise
        out[name] = __import__('jax').numpy.asarray(drawn.astype(out[name].dtype))
    for name, factor in factors.items():
        out[name] = (out[name] * factor).astype(out[name].dtype)
    return out


_narrow_inputs = first_inputs


def first_inputs(seed=0):

    out = dict(_narrow_inputs(seed))
    wider = {'gla_norm_g': 4.78,
     'swa_sinks': 12.0,
     'ln1_g': 4.75,
     'ln1_b': 4.69,
     'ln2_g': 6.42,
     'ln2_b': 6.76}
    for name, times in wider.items():
        mean = out[name].mean()
        out[name] = (mean + times * (out[name] - mean)).astype(out[name].dtype)
    return out


DEPTH_2 = 2

GRID_W = 64
CTX_LEN = 256
N_EVEN = (DEPTH_2 + 1) // 2
N_ODD = DEPTH_2 // 2
NORM_EPS = 1e-6
ROPE_BASE = 10000.0

RET_HEADS = 8
RET_HD = 64
RET_W = RET_HEADS * RET_HD
RET_CHUNK = 128
RWKV_HEADS = 8
RWKV_HD = 64
RWKV_W = RWKV_HEADS * RWKV_HD
DECAY_LORA = 64
A_LORA = 64
RWKV_GN_EPS = 64e-5
HY_W = 512
HY_ORDER = 2
HY_BANDS = 16
HY_EMB = 1 + 2 * HY_BANDS
HY_FFN = 64
HY_SHORT = 3
HY_TARGET = 1e-2
HY_FAST_PCT = 0.3
HY_SLOW_PCT = 1.5
NA_HEADS = 8
NA_HD = 64
NA_W = NA_HEADS * NA_HD
NA_WIN_R = 8
NA_WIN_C = 16

E_RQ = 0
E_RK = RET_W
E_RV = 2 * RET_W
E_RZ = 3 * RET_W
E_WZ = 4 * RET_W
E_SHIFT = E_WZ + RWKV_W
SHIFT_W = 3 * RWKV_W + 2 * DECAY_LORA + 2 * A_LORA
EVEN_IN = E_SHIFT + SHIFT_W
S_K = RWKV_W
S_V = 2 * RWKV_W
S_WD = 3 * RWKV_W
S_AD = S_WD + 2 * DECAY_LORA
O_HZ = 3 * HY_W
O_NQ = 4 * HY_W
O_NK = O_NQ + NA_W
O_NV = O_NK + NA_W
O_NZ = O_NV + NA_W
ODD_IN = O_NZ + NA_W


F32 = jnp.float32

def rmsnorm(x, w):
    xf = x.astype(F32)
    y = xf * lax.rsqrt(jnp.mean(xf * xf, axis=-1, keepdims=True) + NORM_EPS)
    return (y * w.astype(F32)).astype(x.dtype)

def split_heads(t, n_heads):
    b, l, _ = t.shape
    return t.reshape(b, l, n_heads, -1).transpose(0, 2, 1, 3)

def merge_heads(t):
    b, h, l, d = t.shape
    return t.transpose(0, 2, 1, 3).reshape(b, l, h * d)

def axial_rope(length, dim):
    t = jnp.arange(length)
    row = (t // GRID_W).astype(F32)
    col = (t % GRID_W).astype(F32)
    nf = dim // 4
    inv = ROPE_BASE ** (-jnp.arange(nf, dtype=F32) / nf)
    ang = jnp.concatenate([row[:, None] * inv, col[:, None] * inv], axis=-1)
    return jnp.cos(ang), jnp.sin(ang)

def apply_rope(x, cos, sin):
    half = x.shape[-1] // 2
    x1, x2 = x[..., :half], x[..., half:]
    return jnp.concatenate([x1 * cos - x2 * sin, x1 * sin + x2 * cos], axis=-1)

def head_rms(y):
    return y * lax.rsqrt(jnp.mean(y * y, axis=-1, keepdims=True) + NORM_EPS)

def retention_scan(q, k, v, log_g, s0):
    b, h, l, dk = q.shape
    dv = v.shape[-1]
    n = l // RET_CHUNK
    qc = q.reshape(b, h, n, RET_CHUNK, dk)
    kc = k.reshape(b, h, n, RET_CHUNK, dk)
    vc = v.reshape(b, h, n, RET_CHUNK, dv)
    pos = jnp.arange(RET_CHUNK, dtype=F32)
    diff = pos[:, None] - pos[None, :]
    lower = diff >= 0
    dmat = jnp.where(lower, jnp.exp(jnp.where(lower, diff, 0.0)[None] * log_g[:, None, None]), 0.0)
    scores = jnp.einsum('bhncd,bhnsd->bhncs', qc, kc) * dmat[None, :, None]
    y_intra = jnp.einsum('bhncs,bhnse->bhnce', scores, vc)
    k_decay = jnp.exp((RET_CHUNK - 1 - pos)[None] * log_g[:, None])
    kv = jnp.einsum('bhnsd,bhnse->nbhde', kc * k_decay[None, :, None, :, None], vc)
    g_chunk = jnp.exp(RET_CHUNK * log_g)[None, :, None, None]

    def step(s, kv_n):
        return g_chunk * s + kv_n, s

    s_fin, s_prev = lax.scan(step, s0, kv)
    q_decay = jnp.exp((pos + 1.0)[None] * log_g[:, None])
    y_cross = jnp.einsum('bhncd,nbhde->bhnce', qc * q_decay[None, :, None, :, None], s_prev)
    return (y_intra + y_cross).reshape(b, h, l, dv), s_fin

def token_shift_mix(u, mu):
    prev = jnp.pad(u[:, :-1], ((0, 0), (1, 0), (0, 0)))
    nxt = jnp.pad(u[:, 1:], ((0, 0), (0, 1), (0, 0)))
    return u + mu * (0.5 * (prev + nxt) - u)

def rwkv_prep(s, kk_w, ka, w0, w2, a0, a2):
    s = s.astype(F32)
    b, l, _ = s.shape
    hd = lambda t: t.reshape(b, l, RWKV_HEADS, RWKV_HD)
    r = s[..., :S_K]
    k = s[..., S_K:S_V]
    v = s[..., S_V:S_WD]
    wd = s[..., S_WD:S_AD].reshape(b, l, 2, DECAY_LORA)
    ad = s[..., S_AD:].reshape(b, l, 2, A_LORA)
    kk = hd(k * kk_w)
    kk = kk / jnp.maximum(jnp.sqrt(jnp.sum(kk * kk, axis=-1, keepdims=True)), 1e-12)
    dirs = []
    for d in range(2):
        w_log = -jax.nn.softplus(-(w0[d] + jnp.tanh(wd[:, :, d]) @ w2[d])) - 0.5
        a = jax.nn.sigmoid(a0[d] + ad[:, :, d] @ a2[d])
        dirs.append((hd(jnp.exp(-jnp.exp(w_log))), hd(k * (1.0 + (a - 1.0) * ka)), hd(a)))
    return hd(r), hd(v), kk, dirs

def rwkv7_scan(r, w, k, v, kk, a, s0):
    def step(s, inp):
        r_t, w_t, k_t, v_t, kk_t, a_t = inp
        sa = jnp.einsum('bhvk,bhk->bhv', s, -kk_t)
        s = s * w_t[:, :, None, :] + sa[..., None] * (kk_t * a_t)[:, :, None, :] + v_t[..., None] * k_t[:, :, None, :]
        return s, jnp.einsum('bhvk,bhk->bhv', s, r_t)

    xs = tuple(jnp.swapaxes(t.astype(F32), 0, 1) for t in (r, w, k, v, kk, a))
    s_fin, ys = lax.scan(step, s0, xs)
    return jnp.swapaxes(ys, 0, 1), s_fin

def even_layer(h_l, h_c, w_in, w_out, ret_decay, rw_mu, rw_w0, rw_w2, rw_a0, rw_a2, rw_kk, rw_ka, rw_rk,
               rw_ln_w, rw_ln_b, cos, sin, with_ctx):
    b = h_l.shape[0]
    u_l = h_l @ w_in
    u_c = h_c @ w_in

    def ret_qkv(u, rotate):
        q = split_heads(u[..., E_RQ:E_RK], RET_HEADS).astype(F32)
        k = split_heads(u[..., E_RK:E_RV], RET_HEADS).astype(F32) * RET_HD ** -0.5
        v = split_heads(u[..., E_RV:E_RZ], RET_HEADS).astype(F32)
        if rotate:
            q, k = apply_rope(q, cos, sin), apply_rope(k, cos, sin)
        return q, k, v

    log_g = -jnp.exp(ret_decay.astype(F32))
    lat = ret_qkv(u_l, True)
    con = ret_qkv(u_c, False)
    s0 = jnp.zeros((b, RET_HEADS, RET_HD, RET_HD), F32)
    flip_h = lambda t: t[:, :, ::-1]
    ret_c_f, st_f = retention_scan(*con, log_g[0], s0)
    ret_l_f, _ = retention_scan(*lat, log_g[0], st_f)
    ret_c_b, st_b = retention_scan(*[flip_h(t) for t in con], log_g[1], s0)
    ret_l_b, _ = retention_scan(*[flip_h(t) for t in lat], log_g[1], st_b)
    ret_l = ret_l_f + flip_h(ret_l_b)
    ret_c = ret_c_f + flip_h(ret_c_b)

    prep_l = rwkv_prep(token_shift_mix(u_l[..., E_SHIFT:], rw_mu), rw_kk, rw_ka, rw_w0, rw_w2, rw_a0, rw_a2)
    prep_c = rwkv_prep(token_shift_mix(u_c[..., E_SHIFT:], rw_mu), rw_kk, rw_ka, rw_w0, rw_w2, rw_a0, rw_a2)

    def dir_inputs(p, d):
        r, v, kk, dirs = p
        decay, k_d, a = dirs[d]
        return (r, decay, k_d, v, kk, a)

    flip_t = lambda t: t[:, ::-1]
    sw = jnp.zeros((b, RWKV_HEADS, RWKV_HD, RWKV_HD), F32)
    rw_c_f, sf = rwkv7_scan(*dir_inputs(prep_c, 0), sw)
    rw_l_f, _ = rwkv7_scan(*dir_inputs(prep_l, 0), sf)
    rw_c_b, sb = rwkv7_scan(*[flip_t(t) for t in dir_inputs(prep_c, 1)], sw)
    rw_l_b, _ = rwkv7_scan(*[flip_t(t) for t in dir_inputs(prep_l, 1)], sb)
    rw_l = rw_l_f + flip_t(rw_l_b)
    rw_c = rw_c_f + flip_t(rw_c_b)

    def combine(u, ret_y, rw_y, prep):
        r, v, _, dirs = prep
        bl, l = u.shape[0], u.shape[1]
        ret_o = merge_heads(head_rms(ret_y)) * jax.nn.silu(u[..., E_RZ:E_WZ])
        mean = jnp.mean(rw_y, axis=-1, keepdims=True)
        var = jnp.mean(jnp.square(rw_y - mean), axis=-1, keepdims=True)
        gn = ((rw_y - mean) * lax.rsqrt(var + RWKV_GN_EPS)).reshape(bl, l, RWKV_W) * rw_ln_w + rw_ln_b
        bonus = sum(jnp.sum(r * dirs[d][1] * rw_rk, axis=-1, keepdims=True) * v for d in range(2))
        rw_o = (gn + bonus.reshape(bl, l, RWKV_W)) * jax.nn.silu(u[..., E_WZ:E_SHIFT])
        return jnp.concatenate([ret_o, rw_o], axis=-1) @ w_out

    y_l = combine(u_l, ret_l, rw_l, prep_l)
    y_c = combine(u_c, ret_c, rw_c, prep_c) if with_ctx else None
    return y_l, y_c

def short_conv(u, w, bias):
    l = u.shape[1]
    p = jnp.pad(u, ((0, 0), (1, 1), (0, 0)))
    return p[:, :l] * w[0] + p[:, 1:l + 1] * w[1] + p[:, 2:] * w[2] + bias

def hyena_filters(length, w1, b1, f1, w2, b2, f2, w3):
    t = jnp.linspace(0.0, 1.0, length)[:, None]
    bands = jnp.linspace(1e-4, HY_BANDS - 1, HY_BANDS)
    ang = (2.0 * math.pi / length) * jnp.arange(length, dtype=F32)[:, None] * bands[None]
    z = jnp.concatenate([t, jnp.cos(ang), -jnp.sin(ang)], axis=-1)
    hid = jnp.sin(f1 * (z @ w1 + b1))
    hid = jnp.sin(f2 * (hid @ w2 + b2))
    h = (hid @ w3).reshape(length, HY_ORDER, 2, HY_W)
    deltas = jnp.abs(jnp.linspace(math.log(HY_TARGET) / HY_SLOW_PCT, math.log(HY_TARGET) / HY_FAST_PCT, HY_W))
    return (h * jnp.exp(-t * deltas)[:, None, None, :]).astype(F32)

def two_sided_fftconv(u, h_f, h_b):
    l = u.shape[1]
    kern = jnp.concatenate([h_f, jnp.zeros_like(h_f[:1]), h_b[1:][::-1]], axis=0)
    uf = jnp.fft.rfft(u, n=2 * l, axis=1)
    kf = jnp.fft.rfft(kern, axis=0)
    return jnp.fft.irfft(uf * kf[None], n=2 * l, axis=1)[:, :l]

def neighbourhood_attention(q, k, v, k_ctx, v_ctx, rpb):
    b, h, l, d = q.shape
    rows = l // GRID_W
    wr = min(NA_WIN_R, rows)
    r = jnp.arange(rows)
    c = jnp.arange(GRID_W)
    row_idx = jnp.clip(r - NA_WIN_R // 2, 0, rows - wr)[:, None] + jnp.arange(wr)[None]
    col_idx = jnp.clip(c - NA_WIN_C // 2, 0, GRID_W - NA_WIN_C)[:, None] + jnp.arange(NA_WIN_C)[None]
    qi = c[:, None]
    qg = q.reshape(b, h, rows, GRID_W, d)
    k_rows = k.reshape(b, h, rows, GRID_W, d)[:, :, row_idx]
    v_rows = v.reshape(b, h, rows, GRID_W, d)[:, :, row_idx]
    s_rows = jnp.einsum('bhrqd,bhrwkd->bhrwqk', qg, k_rows)
    s_win = s_rows[..., qi, col_idx]
    bias = rpb[:, (row_idx - r[:, None] + NA_WIN_R - 1)[:, :, None, None],
               (col_idx - c[:, None] + NA_WIN_C - 1)[None, None]]
    s_win = (s_win + bias[None]).transpose(0, 1, 2, 4, 3, 5).reshape(b, h, rows, GRID_W, wr * NA_WIN_C)
    s_ctx = jnp.einsum('bhrqd,bhcd->bhrqc', qg, k_ctx)
    p = jax.nn.softmax(jnp.concatenate([s_win, s_ctx], axis=-1).astype(F32), axis=-1)
    p_win = p[..., :wr * NA_WIN_C].reshape(b, h, rows, GRID_W, wr, NA_WIN_C).transpose(0, 1, 2, 4, 3, 5)
    p_ctx = p[..., wr * NA_WIN_C:]
    p_rows = jnp.zeros(s_rows.shape, p.dtype).at[..., qi, col_idx].set(p_win)
    out = jnp.einsum('bhrwqk,bhrwkd->bhrqd', p_rows, v_rows) + jnp.einsum('bhrqc,bhcd->bhrqd', p_ctx, v_ctx)
    return out.reshape(b, h, l, d)

def dense_attention(q, k, v):
    p = jax.nn.softmax(jnp.einsum('bhqd,bhkd->bhqk', q, k).astype(F32), axis=-1)
    return jnp.einsum('bhqk,bhkd->bhqd', p, v)

def odd_layer(h_l, h_c, w_in, w_out, conv_w, conv_b, f_w1, f_b1, f_f1, f_w2, f_b2, f_f2, f_w3, hy_bias, rpb,
              with_ctx):
    u_l = h_l @ w_in
    u_c = h_c @ w_in if with_ctx else None
    kv_c = u_c[..., O_NK:O_NZ] if with_ctx else h_c @ w_in[:, O_NK:O_NZ]
    k_c = split_heads(kv_c[..., :NA_W], NA_HEADS)
    v_c = split_heads(kv_c[..., NA_W:], NA_HEADS)

    def hyena(u):
        p = short_conv(u[..., :O_HZ], conv_w, conv_b).astype(F32)
        v, x1, x2 = p[..., :HY_W], p[..., HY_W:2 * HY_W], p[..., 2 * HY_W:]
        filt = hyena_filters(u.shape[1], f_w1, f_b1, f_f1, f_w2, f_b2, f_f2, f_w3)
        z = v
        for o, g in enumerate((x1, x2)):
            z = g * (two_sided_fftconv(z, filt[:, o, 0], filt[:, o, 1]) + z * hy_bias[o])
        return z * jax.nn.silu(u[..., O_HZ:O_NQ])

    q_l = split_heads(u_l[..., O_NQ:O_NK], NA_HEADS) * NA_HD ** -0.5
    k_l = split_heads(u_l[..., O_NK:O_NV], NA_HEADS)
    v_l = split_heads(u_l[..., O_NV:O_NZ], NA_HEADS)
    na_l = merge_heads(neighbourhood_attention(q_l, k_l, v_l, k_c, v_c, rpb)) * jax.nn.silu(u_l[..., O_NZ:])
    y_l = jnp.concatenate([hyena(u_l), na_l], axis=-1) @ w_out
    y_c = None
    if with_ctx:
        q_c = split_heads(u_c[..., O_NQ:O_NK], NA_HEADS) * NA_HD ** -0.5
        na_c = merge_heads(dense_attention(q_c, k_c, v_c)) * jax.nn.silu(u_c[..., O_NZ:])
        y_c = jnp.concatenate([hyena(u_c), na_c], axis=-1) @ w_out
    return y_l, y_c

def second_inputs(seed: int = 0) -> dict:
    key = jax.random.key(seed)
    ks = iter(jax.random.split(key, 40))
    nrm = lambda shape, s: jax.random.normal(next(ks), shape, F32) * s
    ret_base = jnp.asarray(np.log(-np.log(1.0 - 2.0 ** (-5.0 - np.arange(RET_HEADS)))), F32)
    return {
        'x': nrm((BATCH, SEQ, D_MODEL), 1.0),
        'c': nrm((BATCH, D_MODEL), 1.0),
        'ctx': nrm((BATCH, CTX_LEN, D_MODEL), 1.0),
        'c_ctx': nrm((D_MODEL,), 1.0),
        'ada_w': nrm((DEPTH_2, D_MODEL, 3 * D_MODEL), 0.5 * D_MODEL ** -0.5),
        'ada_b': nrm((DEPTH_2, 3 * D_MODEL), 0.02),
        'norm_w': 1.0 + nrm((DEPTH_2, D_MODEL), 0.02),
        'final_norm_w': 1.0 + nrm((D_MODEL,), 0.02),
        'even_w_in': nrm((N_EVEN, D_MODEL, EVEN_IN), D_MODEL ** -0.5),
        'even_w_out': nrm((N_EVEN, RET_W + RWKV_W, D_MODEL), (RET_W + RWKV_W) ** -0.5),
        'ret_decay': ret_base + nrm((N_EVEN, 2, RET_HEADS), 0.05),
        'rw_mu': jax.random.uniform(next(ks), (N_EVEN, SHIFT_W), F32),
        'rw_w0': jnp.linspace(-6.0, 1.0, RWKV_W) + nrm((N_EVEN, 2, RWKV_W), 0.1),
        'rw_w2': nrm((N_EVEN, 2, DECAY_LORA, RWKV_W), 0.1),
        'rw_a0': nrm((N_EVEN, 2, RWKV_W), 0.1),
        'rw_a2': nrm((N_EVEN, 2, A_LORA, RWKV_W), 0.1),
        'rw_kk': 0.85 + nrm((N_EVEN, RWKV_W), 0.02),
        'rw_ka': 1.0 + nrm((N_EVEN, RWKV_W), 0.02),
        'rw_rk': nrm((N_EVEN, RWKV_HEADS, RWKV_HD), 0.1),
        'rw_ln_w': 1.0 + nrm((N_EVEN, RWKV_W), 0.02),
        'rw_ln_b': nrm((N_EVEN, RWKV_W), 0.02),
        'odd_w_in': nrm((N_ODD, D_MODEL, ODD_IN), D_MODEL ** -0.5),
        'odd_w_out': nrm((N_ODD, HY_W + NA_W, D_MODEL), (HY_W + NA_W) ** -0.5),
        'hy_conv_w': nrm((N_ODD, HY_SHORT, 3 * HY_W), 0.5),
        'hy_conv_b': nrm((N_ODD, 3 * HY_W), 0.02),
        'hy_w1': nrm((N_ODD, HY_EMB, HY_FFN), HY_EMB ** -0.5),
        'hy_b1': nrm((N_ODD, HY_FFN), 0.1),
        'hy_f1': 1.0 + nrm((N_ODD, HY_FFN), 0.05),
        'hy_w2': nrm((N_ODD, HY_FFN, HY_FFN), HY_FFN ** -0.5),
        'hy_b2': nrm((N_ODD, HY_FFN), 0.1),
        'hy_f2': 1.0 + nrm((N_ODD, HY_FFN), 0.05),
        'hy_w3': nrm((N_ODD, HY_FFN, HY_ORDER * 2 * HY_W), 0.01),
        'hy_bias': nrm((N_ODD, HY_ORDER, HY_W), 0.5),
        'na_rpb': nrm((N_ODD, NA_HEADS, 2 * NA_WIN_R - 1, 2 * NA_WIN_C - 1), 0.1),
    }

def second_block(x, c, ctx, c_ctx, ada_w, ada_b, norm_w, final_norm_w, even_w_in, even_w_out, ret_decay, rw_mu,
              rw_w0, rw_w2, rw_a0, rw_a2, rw_kk, rw_ka, rw_rk, rw_ln_w, rw_ln_b, odd_w_in, odd_w_out, hy_conv_w,
              hy_conv_b, hy_w1, hy_b1, hy_f1, hy_w2, hy_b2, hy_f2, hy_w3, hy_bias, na_rpb):
    cos, sin = axial_rope(x.shape[1], RET_HD)
    sc = jax.nn.silu(c)
    scc = jax.nn.silu(c_ctx)
    h = x
    hc = ctx
    for i in range(DEPTH_2):
        with_ctx = i < DEPTH_2 - 1
        shift, scale, gate = jnp.split(sc @ ada_w[i] + ada_b[i], 3, axis=-1)
        shift_c, scale_c, gate_c = jnp.split(scc @ ada_w[i] + ada_b[i], 3, axis=-1)
        n_l = rmsnorm(h, norm_w[i]) * (1.0 + scale[:, None]) + shift[:, None]
        n_c = rmsnorm(hc, norm_w[i]) * (1.0 + scale_c) + shift_c
        j = i // 2
        if i % 2 == 0:
            y_l, y_c = even_layer(n_l, n_c, even_w_in[j], even_w_out[j], ret_decay[j], rw_mu[j], rw_w0[j], rw_w2[j],
                                  rw_a0[j], rw_a2[j], rw_kk[j], rw_ka[j], rw_rk[j], rw_ln_w[j], rw_ln_b[j],
                                  cos, sin, with_ctx)
        else:
            y_l, y_c = odd_layer(n_l, n_c, odd_w_in[j], odd_w_out[j], hy_conv_w[j], hy_conv_b[j], hy_w1[j],
                                 hy_b1[j], hy_f1[j], hy_w2[j], hy_b2[j], hy_f2[j], hy_w3[j], hy_bias[j], na_rpb[j],
                                 with_ctx)
        h = h + (gate[:, None] * y_l).astype(h.dtype)
        if with_ctx:
            hc = hc + (gate_c * y_c).astype(hc.dtype)
    return rmsnorm(h, final_norm_w)


_first_inputs_2 = second_inputs


def second_inputs(seed=0):
    import zlib

    import numpy as np

    out = dict(_first_inputs_2(seed))
    spreads = {}
    factors = {'norm_w': 5.719,
     'final_norm_w': 8.541,
     'rw_w2': 25.303,
     'rw_a0': 8.0,
     'rw_kk': 64.0,
     'rw_ka': 8.0,
     'rw_ln_w': 64.0,
     'rw_ln_b': 64.0,
     'hy_conv_b': 25.326,
     'hy_f1': 8.0,
     'hy_f2': 5.885,
     'na_rpb': 64.0,
     'ctx': 4.123,
     'c_ctx': 4.081,
     'ret_decay': 8.0,
     'rw_w0': 4.924}
    for name, (base, spread) in spreads.items():
        noise = np.random.default_rng([zlib.crc32(name.encode()), seed]).standard_normal(out[name].shape)
        drawn = base * np.exp(spread * noise) if base else spread * noise
        out[name] = __import__('jax').numpy.asarray(drawn.astype(out[name].dtype))
    for name, factor in factors.items():
        out[name] = (out[name] * factor).astype(out[name].dtype)
    return out


_narrow_inputs_2 = second_inputs


def second_inputs(seed=0):
    out = dict(_narrow_inputs_2(seed))
    wider = {'final_norm_w': 3.35, 'rw_kk': 12.0, 'rw_ln_w': 12.0, 'rw_ln_b': 12.0, 'na_rpb': 12.0}
    for name, times in wider.items():
        mean = out[name].mean()
        out[name] = (mean + times * (out[name] - mean)).astype(out[name].dtype)
    return out


def setup_inputs(seed=0):
    out = dict(first_inputs(seed))
    for name, value in second_inputs(seed + 1).items():
        if name != "x":
            out[name + "_2"] = value
    return out


def reference(
    x, c, positions, w_ada, b_ada, w_in, gla_w_lr, gla_b_lr, gla_norm_g, swa_sinks, w_o, ln1_g,
    ln1_b, w_up, conv_w, conv_b, w_down, ln2_g, ln2_b, c_2, ctx_2, c_ctx_2, ada_w_2, ada_b_2,
    norm_w_2, final_norm_w_2, even_w_in_2, even_w_out_2, ret_decay_2, rw_mu_2, rw_w0_2, rw_w2_2,
    rw_a0_2, rw_a2_2, rw_kk_2, rw_ka_2, rw_rk_2, rw_ln_w_2, rw_ln_b_2, odd_w_in_2, odd_w_out_2,
    hy_conv_w_2, hy_conv_b_2, hy_w1_2, hy_b1_2, hy_f1_2, hy_w2_2, hy_b2_2, hy_f2_2, hy_w3_2,
    hy_bias_2, na_rpb_2,
):
    x = first_block(
        x, c, positions, w_ada, b_ada, w_in, gla_w_lr, gla_b_lr, gla_norm_g, swa_sinks, w_o,
        ln1_g, ln1_b, w_up, conv_w, conv_b, w_down, ln2_g, ln2_b,
    )
    return second_block(
        x, c_2, ctx_2, c_ctx_2, ada_w_2, ada_b_2, norm_w_2, final_norm_w_2, even_w_in_2,
        even_w_out_2, ret_decay_2, rw_mu_2, rw_w0_2, rw_w2_2, rw_a0_2, rw_a2_2, rw_kk_2,
        rw_ka_2, rw_rk_2, rw_ln_w_2, rw_ln_b_2, odd_w_in_2, odd_w_out_2, hy_conv_w_2,
        hy_conv_b_2, hy_w1_2, hy_b1_2, hy_f1_2, hy_w2_2, hy_b2_2, hy_f2_2, hy_w3_2, hy_bias_2,
        na_rpb_2,
    )


_drawn_inputs = setup_inputs


def setup_inputs(seed=0):
    import zlib

    import numpy as np

    out = dict(_drawn_inputs(seed))
    spreads = {}
    factors = {}
    for name, (base, spread) in spreads.items():
        noise = np.random.default_rng([zlib.crc32(name.encode()), seed]).standard_normal(out[name].shape)
        drawn = base * np.exp(spread * noise) if base else spread * noise
        out[name] = __import__('jax').numpy.asarray(drawn.astype(out[name].dtype))
    for name, factor in factors.items():
        out[name] = (out[name] * factor).astype(out[name].dtype)
    return out
```

```python
import math
from collections import namedtuple
from contextlib import ExitStack, contextmanager

import numpy as np

import concourse.bass as bass
from concourse import mybir

F32 = mybir.dt.float32
I32 = mybir.dt.int32
U32 = mybir.dt.uint32
F32R = mybir.dt.float32r
ALU = mybir.AluOpType
ACT = mybir.ActivationFunctionType
AX_X = mybir.AxisListType.X

P = 128
D = 1024
KC = D // P
SEQ = 1024
NT = SEQ // P
CTX = 256
NTC = CTX // P
ALL = CTX + SEQ
NTA = ALL // P
D_FF = 2816
FC = D_FF // P
ALPHA = 2.0 ** 0.25
DMA = 16


@contextmanager
def stage(nc, name, *signals):
    sems = {s: nc.alloc_semaphore(f"{name}_{s}") for s in signals}
    with ExitStack() as mem:
        def sb(label, shape, dt=F32):
            return mem.enter_context(nc.sbuf_tensor(f"{name}_{label}", shape, dt))

        def ps(label, shape=(P, 512), dt=F32):
            return mem.enter_context(nc.psum_tensor(f"{name}_{label}", list(shape), dt))

        with nc.Block() as block:
            yield block, namedtuple("Signals", signals)(**sems), sb, ps
    nc.clear_and_free_semaphores(list(sems.values()))
    nc.all_engine_barrier()


def rows(start, n=P):
    return bass.ds(start, n)


def col_view(vec):
    return vec.rearrange("(k p) -> p k", p=P)


def ada_stage(nc, jobs):
    W = 512
    for n, (cs, w, b, out) in enumerate(jobs):
        M, N = len(cs), w.shape[1]
        with stage(nc, f"ada{n}", "c_in", "b_in", "w_even", "w_odd", "silu", "w_free", "mm", "ps_free", "res", "out") as (block, s, sb, ps):
            c_raw = sb("c_raw", [P, KC, M])
            c_act = sb("c_act", [P, KC, M])
            w_buf = sb("w_buf", [P, 2, KC, W])
            bias = sb("bias", [M, N])
            res = sb("res", [M, N])
            acc = [ps(f"acc{i}") for i in range(2)]
            w_v = w.rearrange("(p k) n -> p k n", k=KC)

            @block.sync
            def _(sp):
                for m, c in enumerate(cs):
                    sp.dma_start(c_raw[:, :, m:m + 1], c.rearrange("(p k a) -> p k a", k=KC, a=1),
                                 allow_slow_non_contiguous=True).then_inc(s.c_in, DMA)
                    sp.dma_start(bias[m:m + 1, :], b.rearrange("(a n) -> a n", a=1)).then_inc(s.b_in, DMA)
                with sp.Fori(0, N // W // 2) as i:
                    for par in range(2):
                        sp.wait_ge(s.w_free, 2 * i + par + 1)
                        sp.dma_start(w_buf[:, par], w_v[:, :, bass.ds(i * (2 * W) + par * W, W)]).then_inc((s.w_even, s.w_odd)[par], DMA)
                sp.wait_ge(s.res, N // W)
                sp.dma_start(out, res[:]).then_inc(s.out, DMA)
                sp.wait_ge(s.out, DMA)

            @block.scalar
            def _(act):
                act.wait_ge(s.c_in, DMA * M)
                act.activation(c_act[:], c_raw[:], ACT.Silu).then_inc(s.silu, 1)

            @block.tensor
            def _(pe):
                pe.sem_inc(s.w_free, 2)
                pe.wait_ge(s.silu, 1)
                with pe.Fori(0, N // W // 2) as i:
                    for par in range(2):
                        pe.wait_ge(s.ps_free, 2 * i + par + 1)
                        pe.wait_ge((s.w_even, s.w_odd)[par], i * DMA + DMA)
                        for k in range(KC):
                            mm = pe.matmul(acc[par][:M, :], c_act[:, k, :], w_buf[:, par, k, :], start=k == 0, stop=k == KC - 1)
                        mm.then_inc(s.mm, 1)
                        pe.wait_ge(s.mm, 2 * i + par + 1)
                        pe.sem_inc(s.w_free, 1)

            @block.vector
            def _(dve):
                dve.sem_inc(s.ps_free, 2)
                dve.wait_ge(s.b_in, DMA * M)
                with dve.Fori(0, N // W // 2) as i:
                    for par in range(2):
                        dve.wait_ge(s.mm, 2 * i + par + 1)
                        cols = bass.ds(i * (2 * W) + par * W, W)
                        dve.tensor_tensor(res[:, cols], acc[par][:M, :], bias[:, cols], ALU.add).then_inc(s.res, 1)
                        dve.wait_ge(s.res, 2 * i + par + 1)
                        dve.sem_inc(s.ps_free, 1)


def split_stage(nc, name, hT, hi, lo, kc):
    with stage(nc, name, "hi_done", "lo_done") as (block, s, sb, ps):
        @block.scalar
        def _(act):
            for k in range(kc):
                act.activation(hi[:, k, :], hT[:, k, :], ACT.Copy).then_inc(s.hi_done, 1)

        @block.vector
        def _(dve):
            for k in range(kc):
                dve.wait_ge(s.hi_done, k + 1)
                dve.tensor_tensor(lo[:, k, :], hT[:, k, :], hi[:, k, :], ALU.subtract)
            dve.drain()


def gemm_stage(nc, name, hi, lo, kc, ntiles, w, out, width=512):
    N = w.shape[1]
    nb = 8 if ntiles == 8 else 4
    full = N // width
    tail = N - full * width
    pairs = full // 2
    left = [(2 * pairs, 2 * pairs * width, width)] if full % 2 else []
    if tail:
        left.append((full, full * width, tail))
    total = full + (tail > 0)
    half = ntiles // 2
    split = lo is not None
    with stage(nc, name, "w_even", "w_odd", "hi_done", "lo_done", "mm", "act_free", "dve_free", "out_even", "out_odd") as (block, s, sb, ps):
        w_buf = sb("w_buf", [P, 2, kc, width])
        w_hi = sb("w_hi", [P, 2, kc, width], F32R) if split else w_buf
        w_lo = sb("w_lo", [P, 2, kc, width], F32R) if split else None
        o_buf = sb("o_buf", [P, 2, ntiles, width])
        acc = [ps(f"acc{i}") for i in range(nb)]
        w_v = w.rearrange("(k p) n -> p k n", p=P)
        o_v = out.rearrange("(t p) n -> p t n", p=P)

        def strips(eng, body, behind=None):
            def last(st, col, wd):
                if behind:
                    behind(st, st % 2, col, wd)
            for st in range(2):
                body(st, st, st * width, width)
                if st:
                    last(0, 0, width)
            if pairs > 1:
                with eng.Fori(1, pairs) as i:
                    for par in range(2):
                        st, col = 2 * i + par, i * (2 * width) + par * width
                        body(st, par, col, width)
                        if behind:
                            behind(2 * i + (par - 1), 1 - par, i * (2 * width) + (par - 1) * width, width)
            at = (2 * pairs - 1, (2 * pairs - 1) * width, width)
            for st, col, wd in left:
                body(st, st % 2, col, wd)
                last(*at)
                at = (st, col, wd)
            last(*at)

        @block.sync
        def _(sp):
            def load(st, par, col, wd):
                if not isinstance(st, int) or st >= 2:
                    if split:
                        sp.wait_ge(s.lo_done, st - 1)
                    else:
                        sp.wait_ge(s.mm, (st - 1) * ntiles)
                sp.dma_start(w_buf[:, par, :, :wd], w_v[:, :, bass.ds(col, wd)]).then_inc((s.w_even, s.w_odd)[par], DMA)
            strips(sp, load)

        @block.tensor
        def _(pe):
            def multiply(st, par, col, wd):
                if split:
                    pe.wait_ge(s.lo_done, st + 1)
                else:
                    pe.wait_ge((s.w_even, s.w_odd)[par], (st - par) * (DMA // 2) + DMA)
                for t in range(ntiles):
                    bank = (par * ntiles + t) % nb
                    pe.wait_ge(s.act_free if t % 2 == 0 else s.dve_free, st * half + t // 2 + 1)
                    for k in range(kc):
                        o, tt = acc[bank][:, :wd], slice(t * P, (t + 1) * P)
                        mm = pe.matmul(o, hi[:, k, tt], w_hi[:, par, k, :wd], start=k == 0, stop=not split and k == kc - 1)
                        if split:
                            pe.matmul(o, hi[:, k, tt], w_lo[:, par, k, :wd], start=False, stop=False)
                            mm = pe.matmul(o, lo[:, k, tt], w_hi[:, par, k, :wd], start=False, stop=k == kc - 1)
                    mm.then_inc(s.mm, 1)
            strips(pe, multiply)

        def evacuate(eng, which, free):
            def body(st, par, col, wd):
                if not isinstance(st, int) or st >= 2:
                    eng.wait_ge(s.out_even if par == 0 else s.out_odd, (st - par) * (DMA // 2))
                for t in range(which, ntiles, 2):
                    bank = (par * ntiles + t) % nb
                    eng.wait_ge(s.mm, st * ntiles + t + 1)
                    if which == 0:
                        op = eng.activation(o_buf[:, par, t, :wd], acc[bank][:, :wd], ACT.Copy)
                    else:
                        op = eng.tensor_copy(o_buf[:, par, t, :wd], acc[bank][:, :wd])
                    op.then_inc(free, 1)
            return body

        @block.scalar
        def _(act):
            act.sem_inc(s.act_free, nb // 2)

            def split_hi(st, par, col, wd):
                if split:
                    act.wait_ge((s.w_even, s.w_odd)[par], (st - par) * (DMA // 2) + DMA)
                    if not isinstance(st, int) or st >= 2:
                        act.wait_ge(s.mm, (st - 1) * ntiles)
                    act.activation(w_hi[:, par, :, :wd], w_buf[:, par, :, :wd], ACT.Copy).then_inc(s.hi_done, 1)
            strips(act, split_hi, evacuate(act, 0, s.act_free))

        @block.vector
        def _(dve):
            dve.sem_inc(s.dve_free, nb // 2)

            def split_lo(st, par, col, wd):
                if split:
                    dve.wait_ge(s.hi_done, st + 1)
                    dve.tensor_tensor(w_lo[:, par, :, :wd], w_buf[:, par, :, :wd], w_hi[:, par, :, :wd], ALU.subtract).then_inc(s.lo_done, 1)
            strips(dve, split_lo, evacuate(dve, 1, s.dve_free))

        @block.gpsimd
        def _(pool):
            def store(st, par, col, wd):
                pool.wait_ge(s.act_free, (st + 1) * half + nb // 2)
                pool.wait_ge(s.dve_free, (st + 1) * half + nb // 2)
                pool.dma_start(o_v[:, :, bass.ds(col, wd)], o_buf[:, par, :, :wd]).then_inc(
                    s.out_even if par == 0 else s.out_odd, DMA)
            strips(pool, store)
            pool.wait_ge(s.out_even, DMA * ((total + 1) // 2))
            pool.wait_ge(s.out_odd, DMA * (total // 2))


def norm_stage(nc, name, ident, src, row0, ntiles, hT, tok0, norm=None, scale=None, shift=None, weight=None,
               res=None, gate=None, alpha=1.0, affine=None, keep=None, final=None, res_row0=0):
    eps2 = 1e-5 if norm == "ln" else 1e-6
    with stage(nc, name, "rows_in", "x_even", "x_odd", "x_free", "chain", "xn", "turned", "ps_free", "var", "std", "h_out", "kept", "cols") as (block, s, sb, ps):
        x = sb("x", [P, 2, D])
        r = sb("r", [P, 2, D]) if res is not None else None
        gate_row = sb("gate_row", [P, D]) if res is not None else None
        g_row = sb("g_row", [P, D]) if affine else None
        b_row = sb("b_row", [P, D]) if affine else None
        f_row = sb("f_row", [P, D]) if final is not None else None
        xn = sb("xn", [P, 2, D])
        stats = sb("stats", [P, 2, 6])
        mv = sb("mv", [P, 2])
        rstd = sb("rstd", [P, 2])
        cols = sb("cols", [P, 3, KC])
        acc = [ps(f"acc{i}") for i in range(4)]
        n_rows = (res is not None) + 2 * bool(affine) + (final is not None)
        n_cols = (scale is not None) + (shift is not None) + (weight is not None)
        keeps = keep is not None
        n_norms = bool(affine) + bool(norm)
        per_x = DMA * (2 if res is not None else 1)

        @block.scalar
        def _(act):
            if res is not None:
                act.dma_start(gate_row[:], gate.partition_broadcast(P)).then_inc(s.rows_in, DMA)
            if affine:
                act.dma_start(g_row[:], affine[0].partition_broadcast(P)).then_inc(s.rows_in, DMA)
                act.dma_start(b_row[:], affine[1].partition_broadcast(P)).then_inc(s.rows_in, DMA)
            if final is not None:
                act.dma_start(f_row[:], final.partition_broadcast(P)).then_inc(s.rows_in, DMA)
            for c, v in enumerate((scale, shift, weight)):
                if v is not None:
                    act.dma_start(cols[:, c, :], col_view(v), allow_slow_non_contiguous=True).then_inc(s.rows_in, DMA)
            if scale is not None:
                act.wait_ge(s.cols, 1)
            with act.Fori(0, ntiles // 2) as i:
                for par in range(2):
                    for q in range(n_norms):
                        act.wait_ge(s.var, (2 * i + par) * n_norms + q + 1)
                        act.activation(rstd[:, 0:1], rstd[:, 1:2], ACT.Sqrt).then_inc(s.std, 1)
                    if norm and final is None:
                        act.wait_ge(s.turned, 2 * i + par + 1)
                        for k in range(KC):
                            bank = 2 * par + k // 4
                            op = act.activation(hT[:, k, bass.ds(i * (2 * P) + (tok0 + par * P), P)],
                                                acc[bank][:, (k % 4) * P:(k % 4 + 1) * P], ACT.Identity,
                                                scale=cols[:, 0, k:k + 1], bias=cols[:, 1, k:k + 1])
                        op.then_inc(s.ps_free, 1)

        @block.sync
        def _(sp):
            with sp.Fori(0, ntiles // 2) as i:
                for par in range(2):
                    sp.wait_ge(s.x_free, 2 * i + par + 1)
                    sp.dma_start(x[:, par], src[bass.ds(i * (2 * P) + (row0 + par * P), P), :]).then_inc((s.x_even, s.x_odd)[par], DMA)
                    if res is not None:
                        sp.dma_start(r[:, par], res[bass.ds(i * (2 * P) + (res_row0 + par * P), P), :]).then_inc((s.x_even, s.x_odd)[par], DMA)

        @block.gpsimd
        def _(pool):
            if keeps:
                with pool.Fori(0, ntiles // 2) as i:
                    for par in range(2):
                        pool.wait_ge(s.chain, 2 * i + par + 1)
                        pool.dma_start(keep[bass.ds(i * (2 * P) + par * P, P), :],
                                       (xn if final is not None else x)[:, par]).then_inc(s.kept, DMA)
                        pool.wait_ge(s.kept, (2 * i + par + 1) * DMA)
                        pool.sem_inc(s.h_out, 1)

        @block.tensor
        def _(pe):
            if norm and final is None:
                pe.sem_inc(s.ps_free, 2)
                with pe.Fori(0, ntiles // 2) as i:
                    for par in range(2):
                        pe.wait_ge(s.xn, 2 * i + par + 1)
                        pe.wait_ge(s.ps_free, 2 * i + par + 1)
                        for k in range(KC):
                            bank = 2 * par + k // 4
                            op = pe.transpose(acc[bank][:, (k % 4) * P:(k % 4 + 1) * P], xn[:, par, k * P:(k + 1) * P], ident[:])
                        op.then_inc(s.turned, 1)

        @block.vector
        def _(dve):
            dve.sem_inc(s.x_free, 2)
            dve.wait_ge(s.rows_in, DMA * (n_rows + n_cols))
            if scale is not None:
                dve.tensor_scalar(cols[:, 0, :], cols[:, 0, :], 1.0, None, ALU.add)
                dve.drain()
                if weight is not None:
                    dve.tensor_tensor(cols[:, 0, :], cols[:, 0, :], cols[:, 2, :], ALU.mult)
                    dve.drain()
                dve.sem_inc(s.cols, 1)

            def norm_of(src_t, dst_t, kind, eps, nth):
                for hf in range(2):
                    dve.bn_stats(stats[:, hf, :], src_t[:, hf * 512:(hf + 1) * 512])
                dve.drain()
                dve.bn_aggr(mv[:], stats[:])
                dve.drain()
                if kind == "rms":
                    dve.scalar_tensor_tensor(rstd[:, 1:2], mv[:, 0:1], mv[:, 0:1], mv[:, 1:2], ALU.mult, ALU.add)
                    dve.drain()
                    dve.tensor_scalar(rstd[:, 1:2], rstd[:, 1:2], eps, None, ALU.add).then_inc(s.var, 1)
                else:
                    dve.tensor_scalar(rstd[:, 1:2], mv[:, 1:2], eps, None, ALU.add).then_inc(s.var, 1)
                dve.wait_ge(s.std, nth + 1)
                dve.reciprocal(rstd[:, 0:1], rstd[:, 0:1])
                dve.drain()
                if kind == "rms":
                    return dve.tensor_scalar(dst_t, src_t, rstd[:, 0:1], None, ALU.mult)
                return dve.tensor_scalar(dst_t, src_t, mv[:, 0:1], rstd[:, 0:1], ALU.subtract, ALU.mult)

            with dve.Fori(0, ntiles // 2) as i:
                for par in range(2):
                    xt = x[:, par]
                    dve.wait_ge((s.x_even, s.x_odd)[par], i * per_x + per_x)
                    if res is not None:
                        dve.tensor_tensor(r[:, par], r[:, par], gate_row[:], ALU.mult)
                        dve.drain()
                        dve.scalar_tensor_tensor(xt, xt, alpha, r[:, par], ALU.mult, ALU.add)
                        dve.drain()
                    if affine:
                        norm_of(xt, xt, "ln", 1e-5, (2 * i + par) * n_norms)
                        dve.drain()
                        dve.tensor_tensor(xt, xt, g_row[:], ALU.mult)
                        dve.drain()
                        dve.tensor_tensor(xt, xt, b_row[:], ALU.add)
                        dve.drain()
                    if keeps and final is None:
                        dve.sem_inc(s.chain, 1)
                    if norm:
                        if final is None:
                            dve.wait_ge(s.turned, 2 * i + par)
                        norm_of(xt, xn[:, par], norm, eps2, (2 * i + par) * n_norms + n_norms - 1)
                        dve.drain()
                        if final is not None:
                            if keeps:
                                dve.wait_ge(s.h_out, 2 * i + par)
                            dve.tensor_tensor(xn[:, par], xn[:, par], f_row[:], ALU.mult)
                            dve.drain()
                            dve.sem_inc(s.chain, 1)
                        else:
                            dve.sem_inc(s.xn, 1)
                    if keeps:
                        dve.wait_ge(s.h_out, 2 * i + par + 1)
                    dve.sem_inc(s.x_free, 1)
C_Q, C_K, C_V, C_R, C_LR, C_QB, C_GA, C_GB = 0, 512, 1024, 2048, 3072, 3088, 4368, 5392
GH, GDK, GDV, CH = 4, 128, 256, 64
LN_END = (D // P) * P


def gla_tables():
    j, i = np.arange(P)[:, None], np.arange(P)[None, :]
    same = (j // CH) == (i // CH)
    prefix = (same & (j <= i)).astype(np.float32) / 16.0
    suffix = (same & (j > i)).astype(np.float32) / 16.0
    causal = np.tile((same & (j <= i)).astype(np.uint32), (1, GH))
    return prefix, suffix, causal


def gla_stage(nc, ident, P1, w_lr, b_lr, norm_g, t_prefix, t_suffix, t_causal, YA):
    with stage(nc, "gla", "const", "init", "x_in", "x_free", "lrT", "lrT_c", "z", "abs", "ln1", "g", "turned", "gsum", "dmid",
               "e_cum", "e_mid", "gla_ops", "scoresT", "masked", "kv", "state", "o_done", "sq", "var", "std", "e_gate", "y", "stored") as (block, s, sb, ps):
        x = sb("x", [P, C_QB])
        ga = sb("ga", [P, D])
        wlr = sb("wlr", [16, 512])
        blr = sb("blr", [1, 512])
        ones = sb("ones", [1, P])
        g_row = sb("g_row", [P, GH, GDV])
        prefix = sb("prefix", [P, P])
        suffix = sb("suffix", [P, P])
        causal = sb("causal", [P, GH * P], U32)
        lrT = sb("lrT", [16, P])
        za = sb("za", [P, 512])
        g = sb("g", [P, 512])
        dmid = sb("dmid", [P, GH * 2, CH])
        mid = sb("mid", [P, GH * 2, 1])
        e_cum = sb("e_cum", [P, 512])
        e_suf = sb("e_suf", [P, 512])
        e_up = sb("e_up", [P, 512])
        e_dn = sb("e_dn", [P, 512])
        qmid = sb("qmid", [P, 512])
        kmid = sb("kmid", [P, 512])
        qz = sb("qz", [P, 2, GH, P])
        kout = sb("kout", [P, 512])
        am = sb("am", [P, 512])
        S0 = sb("S0", [P, GH, GDV])
        S1 = sb("S1", [P, GH, GDV])
        sq = sb("sq", [P, GDV])
        ss = sb("ss", [P, GH])
        rs = sb("rs", [P, GH])
        eg = sb("eg", [P, 2, D])
        y = sb("y", [P, GH, GDV])
        pz = ps("pz")
        pq = ps("pq")
        pk = ps("pk")
        pg = ps("pg", [P, 1024])
        po = ps("po", [P, GH, GDV])
        pl = ps("pl")

        @block.sync
        def _(sp):
            sp.dma_start(wlr[:], w_lr).then_inc(s.const, DMA)
            sp.dma_start(blr[:], b_lr.rearrange("(a n) -> a n", a=1)).then_inc(s.const, DMA)
            sp.dma_start(prefix[:], t_prefix).then_inc(s.const, DMA)
            sp.dma_start(suffix[:], t_suffix).then_inc(s.const, DMA)
            sp.dma_start(causal[:], t_causal).then_inc(s.const, DMA)
            for h in range(GH):
                sp.dma_start(g_row[:, h, :], norm_g.partition_broadcast(P)).then_inc(s.const, DMA)
            with sp.Fori(0, NT) as i:
                sp.wait_ge(s.x_free, i)
                sp.dma_start(x[:], P1[rows(i * P), 0:C_QB]).then_inc(s.x_in, DMA)
                sp.dma_start(ga[:], P1[rows(i * P), C_GA:C_GB]).then_inc(s.x_in, DMA)
                sp.wait_ge(s.y, i + 1)
                sp.dma_start(YA[rows(i * P), :], y[:].rearrange("p h v -> p (h v)")).then_inc(s.stored, DMA)
            sp.wait_ge(s.stored, NT * DMA)

        @block.tensor
        def _(pe):
            pe.wait_ge(s.const, 9 * DMA)
            pe.wait_ge(s.init, 1)
            with pe.Fori(0, NT) as i:
                pe.wait_ge(s.x_in, (i + 1) * (2 * DMA))
                pe.transpose(pl[:16, :P], x[:, C_LR:C_LR + 16], ident[:]).then_inc(s.lrT, 1)
                for h in range(GH):
                    pe.transpose(pq[:, h * P:(h + 1) * P], x[:, C_Q + h * P:C_Q + (h + 1) * P], ident[:])
                for h in range(GH):
                    op = pe.transpose(pk[:, h * P:(h + 1) * P], x[:, C_K + h * P:C_K + (h + 1) * P], ident[:])
                op.then_inc(s.turned, 1)
                pe.wait_ge(s.lrT_c, i + 1)
                pe.matmul(pz[:], lrT[:], wlr[:], start=True, stop=False)
                pe.matmul(pz[:], ones[:], blr[:], start=False, stop=True).then_inc(s.z, 1)
                pe.wait_ge(s.g, i + 1)
                for h in range(GH):
                    pe.matmul(pg[:, h * P:(h + 1) * P], g[:, h * P:(h + 1) * P], prefix[:], start=True, stop=True)
                pe.matmul(pg[:, 512:], suffix[:], g[:], start=True, stop=True).then_inc(s.gsum, 1)
                pe.wait_ge(s.gla_ops, i + 1)
                for h in range(GH):
                    op = pe.matmul(pz[:, h * P:(h + 1) * P], kmid[:, h * P:(h + 1) * P], qmid[:, h * P:(h + 1) * P], start=True, stop=True)
                op.then_inc(s.scoresT, 1)
                for h in range(GH):
                    op = pe.matmul(pg[:, h * GDV:(h + 1) * GDV], kout[:CH, h * P:(h + 1) * P], x[:CH, C_V + h * GDV:C_V + (h + 1) * GDV], start=True, stop=True)
                op.then_inc(s.kv, 1)
                pe.wait_ge(s.masked, i + 1)
                pe.wait_ge(s.state, 2 * i + 1)
                for h in range(GH):
                    pe.matmul(po[:, h, :], am[:, h * P:(h + 1) * P], x[:, C_V + h * GDV:C_V + (h + 1) * GDV], start=True, stop=False)
                    pe.matmul(po[:, h, :], qz[:, 0, h, :], S0[:, h, :], start=False, stop=False)
                    op = pe.matmul(po[:, h, :], qz[:, 1, h, :], S1[:, h, :], start=False, stop=True)
                op.then_inc(s.o_done, 1)
                for h in range(GH):
                    op = pe.matmul(pg[:, h * GDV:(h + 1) * GDV], kout[CH:, h * P:(h + 1) * P], x[CH:, C_V + h * GDV:C_V + (h + 1) * GDV], start=True, stop=True)
                op.then_inc(s.kv, 1)

        @block.scalar
        def _(act):
            with act.Fori(0, NT) as i:
                act.wait_ge(s.lrT, i + 1)
                act.activation(lrT[:], pl[:16, :P], ACT.Copy).then_inc(s.lrT_c, 1)
                act.wait_ge(s.z, i + 1)
                act.activation(za[:], pz[:], ACT.Abs)
                act.drain()
                act.activation(za[:], za[:], ACT.Exp, scale=-1.0)
                act.drain()
                act.activation(za[:], za[:], ACT.Ln, bias=1.0).then_inc(s.ln1, 1)
                act.wait_ge(s.gsum, i + 1)
                act.activation(e_cum[:], pg[:, :512], ACT.Exp)
                act.activation(e_suf[:], pg[:, 512:], ACT.Exp).then_inc(s.e_cum, 1)
                act.wait_ge(s.dmid, i + 1)
                act.activation(e_up[:], dmid[:], ACT.Exp)
                act.activation(e_dn[:], dmid[:], ACT.Exp, scale=-1.0).then_inc(s.e_mid, 1)
                act.activation(eg[:, 0], x[:, C_R:C_R + D], ACT.Exp, scale=-1.0)
                act.activation(eg[:, 1], ga[:], ACT.Exp, scale=-1.0).then_inc(s.e_gate, 1)
                act.wait_ge(s.o_done, i + 1)
                for h in range(GH):
                    act.activation(sq[:], po[:, h, :], ACT.Square, accum_out=ss[:, h:h + 1])
                    act.drain()
                act.sem_inc(s.sq, 1)
                act.wait_ge(s.var, i + 1)
                act.activation(rs[:], ss[:], ACT.Sqrt).then_inc(s.std, 1)

        @block.vector
        def _(dve):
            dve.memset(ones[:], 1.0)
            dve.memset(S0[:], 0.0)
            dve.memset(qz[:], 0.0)
            dve.memset(am[:], 0.0)
            dve.drain()
            dve.sem_inc(s.init, 1)
            dve.wait_ge(s.const, 9 * DMA)
            with dve.Fori(0, NT) as i:
                dve.wait_ge(s.ln1, i + 1)
                dve.scalar_tensor_tensor(g[:], pz[:], 0.0, za[:], ALU.min, ALU.subtract).then_inc(s.g, 1)
                dve.wait_ge(s.e_cum, i + 1)
                cum = pg[:, :512].rearrange("p (c j) -> p c j", j=CH)
                dve.tensor_copy(mid[:], cum[:, :, CH // 2 - 1:CH // 2])
                dve.drain()
                dve.tensor_tensor(dmid[:], cum, mid[:].broadcast_to([P, 2 * GH, CH]), ALU.subtract).then_inc(s.dmid, 1)
                dve.wait_ge(s.turned, i + 1)
                scale = float(GDK) ** -0.5
                q4 = pq[:].rearrange("p (h c j) -> p h c j", h=GH, c=2)
                e4 = e_cum[:].rearrange("p (h c j) -> p h c j", h=GH, c=2)
                for c in range(2):
                    dve.scalar_tensor_tensor(qz[:, c, :, c * CH:(c + 1) * CH], q4[:, :, c, :], scale, e4[:, :, c, :], ALU.mult, ALU.mult)
                dve.tensor_tensor(kout[:], x[:, C_K:C_K + 512], e_suf[:], ALU.mult)
                dve.wait_ge(s.e_mid, i + 1)
                dve.scalar_tensor_tensor(qmid[:], pq[:], scale, e_up[:], ALU.mult, ALU.mult)
                dve.tensor_tensor(kmid[:], pk[:], e_dn[:], ALU.mult)
                dve.drain()
                dve.sem_inc(s.gla_ops, 1)
                dve.wait_ge(s.init, 1)
                dve.wait_ge(s.scoresT, i + 1)
                dve.copy_predicated(am[:], causal[:], pz[:])
                dve.drain()
                dve.sem_inc(s.masked, 1)
                for c, (old, new) in enumerate(((S0, S1), (S1, S0))):
                    dve.wait_ge(s.kv, 2 * i + c + 1)
                    for h in range(GH):
                        last = h * P + c * CH + CH - 1
                        dve.scalar_tensor_tensor(new[:, h, :], old[:, h, :], e_cum[:, last:last + 1], pg[:, h * GDV:(h + 1) * GDV], ALU.mult, ALU.add)
                    dve.drain()
                    dve.sem_inc(s.state, 1)
                dve.wait_ge(s.e_gate, i + 1)
                dve.tensor_scalar(eg[:, 0], eg[:, 0], 1.0, None, ALU.add)
                dve.drain()
                dve.scalar_tensor_tensor(eg[:, 0], eg[:, 1], 1.0, eg[:, 0], ALU.add, ALU.mult)
                dve.drain()
                dve.reciprocal(eg[:, 0], eg[:, 0])
                dve.tensor_tensor(eg[:, 1], x[:, C_R:C_R + D], g_row[:].rearrange("p h v -> p (h v)"), ALU.mult)
                dve.drain()
                dve.tensor_tensor(eg[:, 0], eg[:, 0], eg[:, 1], ALU.mult)
                dve.wait_ge(s.sq, i + 1)
                dve.tensor_scalar(ss[:], ss[:], 1.0 / GDV, 1e-6, ALU.mult, ALU.add).then_inc(s.var, 1)
                dve.wait_ge(s.std, i + 1)
                dve.reciprocal(rs[:], rs[:])
                dve.drain()
                dve.wait_ge(s.stored, i * DMA)
                for h in range(GH):
                    dve.scalar_tensor_tensor(y[:, h, :], po[:, h, :], rs[:, h:h + 1], eg[:, 0, h * GDV:(h + 1) * GDV], ALU.mult, ALU.mult)
                dve.drain()
                dve.sem_inc(s.y, 1)
                dve.sem_inc(s.x_free, 1)


SH, SHD, SKV = 16, 64, 2
NEG = -1.0e30
ROPE_F = 8
TWO_PI = 2.0 * math.pi
PI_1 = 6.28125
PI_2 = float(np.float32(TWO_PI - PI_1))
PI_3 = float(np.float32(TWO_PI - PI_1 - float(np.float32(TWO_PI - PI_1))))
ROUND = 12582912.0
PI_LIM = 3.1415925


def swa_tables():
    q, k = np.arange(P)[:, None], np.arange(P)[None, :]
    prev = np.where(k > q, 0.0, NEG)
    cur = np.where(k <= q, 0.0, NEG)
    mask = np.concatenate([prev, cur], 1).astype(np.float32)
    first = np.concatenate([np.full((P, P), NEG), cur], 1).astype(np.float32)
    freq = (500000.0 ** (-(np.arange(0, 16, 2, dtype=np.float32) / 16))).astype(np.float32)
    return mask, first, np.tile(freq, NT)[None, :]


def reduced_sine(dve, out, ang, turns, quarter):
    dve.tensor_scalar(turns, ang, 1.0 / TWO_PI, quarter, ALU.mult, ALU.add)
    dve.drain()
    dve.tensor_scalar(turns, turns, ROUND, None, ALU.add)
    dve.drain()
    dve.tensor_scalar(turns, turns, ROUND, None, ALU.subtract)
    dve.drain()
    dve.scalar_tensor_tensor(out, turns, -PI_1, ang, ALU.mult, ALU.add)
    dve.drain()
    dve.scalar_tensor_tensor(out, turns, -PI_2, out, ALU.mult, ALU.add)
    dve.drain()
    dve.scalar_tensor_tensor(out, turns, -PI_3, out, ALU.mult, ALU.add)
    dve.drain()
    if quarter:
        dve.tensor_scalar(out, out, quarter * TWO_PI, None, ALU.add)
        dve.drain()
    dve.tensor_scalar(out, out, PI_LIM, -PI_LIM, ALU.min, ALU.max)
    dve.drain()


def swa_stage(nc, ident, P1, pos, sinks, t_mask, t_first, t_freq, YA, Y1):
    with stage(nc, "swa", "const", "init", "arg", "table", "x_even", "x_odd", "x_free", "roped", "turned", "qkT", "scores", "s_done", "s_free",
               "neg_max", "probs", "p_turned", "p_copied", "p_free", "pv", "e_gate", "y", "stored") as (block, s, sb, ps):
        x = sb("x", [P, 2, 1280])
        gb = sb("gb", [P, 2, D])
        ya = sb("ya", [P, 2, D])
        pos_i = sb("pos_i", [P, NT], I32)
        pos_f = sb("pos_f", [P, NT, 1])
        freq = sb("freq", [P, NT, ROPE_F])
        ang = sb("ang", [P, NT, ROPE_F])
        turns = sb("turns", [P, NT, ROPE_F])
        arg = sb("arg", [P, 2, NT, 1, ROPE_F])
        cs = sb("cs", [P, 2, NT, 1, ROPE_F])
        mask = sb("mask", [P, 1, 256])
        mask_even = sb("mask_even", [P, 1, 256])
        sink = sb("sink", [P, SH])
        rope = sb("rope", [P, 4, 18, ROPE_F])
        kdup = sb("kdup", [P, 2, 2, SHD])
        qT = sb("qT", [P, 8, P])
        kT = sb("kT", [P, 2, 2, P])
        vv = sb("vv", [P, 2, P])
        sc = sb("sc", [P, 2, 4, 256])
        mx = sb("mx", [P, SH])
        nm = sb("nm", [P, SH])
        dsink = sb("dsink", [P, SH])
        esink = sb("esink", [P, SH])
        sums = sb("sums", [P, SH])
        rden = sb("rden", [P, SH, 1])
        pT = sb("pT", [P, 2, 8, P])
        eg = sb("eg", [P, D])
        y = sb("y", [P, SH, SHD])
        pt = ps("pt", [P, 8, P])
        pS = [ps(f"pS{i}", [P, 4, 256]) for i in range(2)]
        po = ps("po", [P, SH, SHD])
        G = 4

        @block.sync
        def _(sp):
            sp.dma_start(pos_i[:], pos.rearrange("(t p) -> p t", p=P), allow_slow_non_contiguous=True).then_inc(s.const, DMA)
            sp.dma_start(freq[:], t_freq[0].partition_broadcast(P).rearrange("p (t f) -> p t f", f=ROPE_F)).then_inc(s.const, DMA)
            sp.dma_start(mask[:, 0], t_mask).then_inc(s.const, DMA)
            sp.dma_start(mask_even[:, 0], t_first).then_inc(s.const, DMA)
            sp.dma_start(sink[:], sinks.partition_broadcast(P)).then_inc(s.const, DMA)
            with sp.Fori(0, NT // 2) as i:
                for par in range(2):
                    sp.wait_ge(s.x_free, 2 * i + par)
                    tile = rows(i * (2 * P) + par * P)
                    done = (s.x_even, s.x_odd)[par]
                    sp.dma_start(x[:, par], P1[tile, C_QB:C_GA]).then_inc(done, DMA)
                    sp.dma_start(gb[:, par], P1[tile, C_GB:C_GB + D]).then_inc(done, DMA)
                    sp.dma_start(ya[:, par], YA[tile, :]).then_inc(done, DMA)

        @block.gpsimd
        def _(pool):
            with pool.Fori(0, NT) as i:
                pool.wait_ge(s.y, i + 1)
                pool.dma_start(Y1[rows(i * P), :], y[:].rearrange("p h d -> p (h d)")).then_inc(s.stored, DMA)
            pool.wait_ge(s.stored, NT * DMA)

        @block.tensor
        def _(pe):
            pe.wait_ge(s.init, 1)
            with pe.Fori(0, NT // 2) as i:
                for par in range(2):
                    t = 2 * i + par
                    pe.wait_ge(s.roped, t + 1)
                    pe.wait_ge(s.p_copied, t * G)
                    for c in range(8):
                        pe.transpose(pt[:, c, :], x[:, par, c * P:(c + 1) * P], ident[:])
                    for c in range(2):
                        op = pe.transpose(pS[1][:, c, :P], kdup[:, c].rearrange("p a d -> p (a d)"), ident[:])
                    op.then_inc(s.turned, 1)
                    pe.wait_ge(s.qkT, t + 1)
                    for g in range(G + 1):
                        if g < G:
                            pe.wait_ge(s.s_free, t * G + g + 1)
                            for h in range(4):
                                hd, base, slot = 4 * g + h, (h % 2) * SHD, (h % 2) * 2 + h // 2
                                for side, kp in ((0, 1 - par), (1, par)):
                                    op = pe.matmul(pS[g % 2][:, slot, side * P:(side + 1) * P], qT[base:base + SHD, hd // 2, :],
                                                   kT[base:base + SHD, kp, hd // 8, :], start=True, stop=True)
                            op.then_inc(s.scores, 1)
                        if g:
                            q = g - 1
                            pe.wait_ge(s.probs, t * G + q + 1)
                            if q:
                                pe.wait_ge(s.p_copied, t * G + q)
                            for c in range(8):
                                op = pe.transpose(pt[:, c, :], sc[:, q % 2, c // 2, (c % 2) * P:(c % 2 + 1) * P], ident[:])
                            op.then_inc(s.p_turned, 1)
                            pe.wait_ge(s.p_copied, t * G + q + 1)
                            if q == 0:
                                pe.wait_ge(s.y, t)
                            for h in range(4):
                                hd = 4 * q + h
                                kv = hd // 8
                                slot = (h % 2) * 2 + h // 2
                                pe.matmul(po[:, hd, :], pT[:, q % 2, 2 * slot, :], vv[:, 1 - par, kv * SHD:(kv + 1) * SHD], start=True, stop=False)
                                op = pe.matmul(po[:, hd, :], pT[:, q % 2, 2 * slot + 1, :], vv[:, par, kv * SHD:(kv + 1) * SHD], start=False, stop=True)
                            op.then_inc(s.pv, 1)

        @block.scalar
        def _(act):
            act.wait_ge(s.arg, 1)
            act.activation(cs[:], arg[:], ACT.Sin).then_inc(s.table, 1)
            with act.Fori(0, NT // 2) as i:
                for par in range(2):
                    t = 2 * i + par
                    act.wait_ge(s.turned, t + 1)
                    act.activation(qT[:], pt[:], ACT.Copy)
                    act.activation(kT[:, par], pS[1][:, 0:2, :P], ACT.Copy).then_inc(s.qkT, 1)
                    for g in range(G + 1):
                        if g < G:
                            act.wait_ge(s.neg_max, t * G + g + 1)
                            for h in range(4):
                                hd, slot = 4 * g + h, (h % 2) * 2 + h // 2
                                act.activation(sc[:, g % 2, slot, :], sc[:, g % 2, slot, :], ACT.Exp, bias=nm[:, hd:hd + 1], accum_out=sums[:, hd:hd + 1])
                            act.activation(esink[:, 4 * g:4 * g + 4], dsink[:, 4 * g:4 * g + 4], ACT.Exp)
                            act.drain()
                            act.sem_inc(s.probs, 1)
                        if g:
                            q = g - 1
                            act.wait_ge(s.p_turned, t * G + q + 1)
                            if q >= 2:
                                act.wait_ge(s.pv, t * G + q - 1)
                            act.activation(pT[:, q % 2], pt[:], ACT.Copy).then_inc(s.p_copied, 1)
                    act.wait_ge(s.y, t)
                    act.activation(eg[:], gb[:, par], ACT.Exp, scale=-1.0).then_inc(s.e_gate, 1)

        @block.vector
        def _(dve):
            dve.memset(kT[:], 0.0)
            dve.memset(vv[:], 0.0)
            dve.drain()
            dve.sem_inc(s.init, 1)
            dve.sem_inc(s.s_free, 2)
            dve.wait_ge(s.const, 5 * DMA)
            dve.tensor_copy(pos_f[:, :, 0], pos_i[:])
            dve.drain()
            dve.tensor_tensor(ang[:], freq[:], pos_f[:].broadcast_to([P, NT, ROPE_F]), ALU.mult)
            dve.drain()
            reduced_sine(dve, arg[:, 0, :, 0, :], ang[:], turns[:], 0.25)
            reduced_sine(dve, arg[:, 1, :, 0, :], ang[:], turns[:], 0.0)
            dve.sem_inc(s.arg, 1)
            dve.wait_ge(s.table, 1)
            with dve.Fori(0, NT // 2) as i:
                for par in range(2):
                    t = 2 * i + par
                    dve.wait_ge((s.x_even, s.x_odd)[par], (i + 1) * (3 * DMA))
                    heads = x[:, par, :18 * SHD].rearrange("p (h d) -> p h d", d=SHD)
                    a, b = heads[:, :, 0:ROPE_F], heads[:, :, ROPE_F:2 * ROPE_F]
                    cos, sin = (cs[:, c, bass.ds(t, 1), 0, :].broadcast_to([P, 18, ROPE_F]) for c in range(2))
                    for n, (u, w) in enumerate(((a, cos), (b, sin), (b, cos), (a, sin))):
                        dve.tensor_tensor(rope[:, n], u, w, ALU.mult)
                    dve.drain()
                    dve.tensor_tensor(a, rope[:, 0], rope[:, 1], ALU.subtract)
                    dve.tensor_tensor(b, rope[:, 2], rope[:, 3], ALU.add)
                    dve.drain()
                    dve.wait_ge(s.pv, t * G)
                    for c in range(2):
                        for r in range(2):
                            dve.tensor_copy(kdup[:, c, r, :], x[:, par, D + c * SHD:D + (c + 1) * SHD])
                    dve.tensor_copy(vv[:, par, :], x[:, par, D + P:D + 2 * P])
                    dve.drain()
                    dve.sem_inc(s.roped, 1)
                    for g in range(G):
                        dve.wait_ge(s.scores, t * G + g + 1)
                        if g >= 2:
                            dve.wait_ge(s.p_turned, t * G + g - 1)
                        mk = (mask_even if par == 0 else mask)[:].broadcast_to([P, 4, 256])
                        dve.scalar_tensor_tensor(sc[:, g % 2], pS[g % 2][:], SHD ** -0.5, mk, ALU.mult, ALU.add)
                        dve.drain()
                        dve.sem_inc(s.s_free, 1)
                        hs = slice(4 * g, 4 * g + 4)
                        dve.tensor_reduce(mx[:, hs].rearrange("p (b a) -> p a b", a=2), sc[:, g % 2].rearrange("p (a b) k -> p a b k", a=2), AX_X, ALU.max)
                        dve.drain()
                        dve.tensor_tensor(mx[:, hs], mx[:, hs], sink[:, hs], ALU.max)
                        dve.drain()
                        dve.tensor_scalar(nm[:, hs], mx[:, hs], -1.0, None, ALU.mult)
                        dve.tensor_tensor(dsink[:, hs], sink[:, hs], mx[:, hs], ALU.subtract)
                        dve.drain()
                        dve.sem_inc(s.neg_max, 1)
                    if par == 0:
                        dve.tensor_copy(mask_even[:], mask[:])
                    dve.wait_ge(s.e_gate, t + 1)
                    dve.tensor_tensor(rden[:, :, 0], sums[:], esink[:], ALU.add)
                    dve.tensor_scalar(eg[:], eg[:], 1.0, None, ALU.add)
                    dve.drain()
                    dve.reciprocal(rden[:], rden[:])
                    dve.reciprocal(eg[:], eg[:])
                    dve.drain()
                    dve.wait_ge(s.pv, (t + 1) * G)
                    dve.wait_ge(s.stored, t * DMA)
                    dve.tensor_tensor(y[:], po[:], rden[:].broadcast_to([P, SH, SHD]), ALU.mult)
                    dve.drain()
                    yf = y[:].rearrange("p h d -> p (h d)")
                    dve.tensor_tensor(yf, yf, eg[:], ALU.mult)
                    dve.drain()
                    dve.tensor_tensor(yf, yf, ya[:, par], ALU.add)
                    dve.drain()
                    dve.sem_inc(s.y, 1)
                    dve.sem_inc(s.x_free, 1)


def ffn_up_stage(nc, ident, hi, lo, w_up, conv_w, conv_b, fT):
    with stage(nc, "up", "taps_in", "taps_T", "taps", "w_in", "hi_done", "lo_done", "mm", "act_c", "conv", "gelu", "ps_free") as (block, s, sb, ps):
        raw = sb("raw", [2 * FC, 4, P])
        taps = sb("taps", [P, 4, 2 * FC])
        w_buf = sb("w_buf", [P, 2, KC, P])
        w_hi = sb("w_hi", [P, 2, 2, KC, P], F32R)
        w_lo = sb("w_lo", [P, 2, 2, KC, P], F32R)
        cv = sb("cv", [P, 2, SEQ])
        acc = [[ps(f"acc{i}{j}", [P, SEQ]) for j in range(2)] for i in range(2)]
        w_v = w_up.rearrange("(k p) n -> p k n", p=P)

        def strips(eng, body, behind):
            for j in range(2):
                body(j, j)
                if j:
                    behind(0, 0)
            with eng.Fori(1, FC // 2) as i:
                for par in range(2):
                    body(2 * i + par, par)
                    behind(2 * i + (par - 1), 1 - par)
            behind(FC - 1, 1)

        @block.sync
        def _(sp):
            for tap in range(3):
                sp.dma_start(raw[:, tap, :], conv_w[tap].rearrange("(j p) -> j p", p=P)).then_inc(s.taps_in, DMA)
            sp.dma_start(raw[:, 3, :], conv_b.rearrange("(j p) -> j p", p=P)).then_inc(s.taps_in, DMA)
            with sp.Fori(0, FC) as j:
                sp.wait_ge(s.lo_done, j)
                for side in range(2):
                    sp.dma_start(w_buf[:, side], w_v[:, :, bass.ds(j * P + side * D_FF, P)]).then_inc(s.w_in, DMA)

        @block.tensor
        def _(pe):
            pe.wait_ge(s.taps_in, 4 * DMA)
            for c in range(4):
                op = pe.transpose(acc[0][0][:, c * P:c * P + 2 * FC], raw[:, c, :], ident[:2 * FC, :2 * FC])
            op.then_inc(s.taps_T, 1)
            with pe.Fori(0, FC // 2) as i:
                for par in range(2):
                    pe.wait_ge(s.ps_free, 2 * i + par + 1)
                    pe.wait_ge(s.lo_done, 2 * i + par + 1)
                    for side in range(2):
                        for k in range(KC):
                            for wt, ht in ((w_hi, hi), (w_hi, lo), (w_lo, hi)):
                                for hf in range(2):
                                    cols = slice(hf * 512, (hf + 1) * 512)
                                    op = pe.matmul(acc[par][side][:, cols], wt[:, par, side, k, :], ht[:, k, cols],
                                                   start=k == 0 and wt is w_hi and ht is hi, stop=k == KC - 1 and wt is w_lo)
                        op.then_inc(s.mm, 1)

        @block.scalar
        def _(act):
            act.wait_ge(s.taps, 1)

            def split_hi(j, par):
                act.wait_ge(s.w_in, j * (2 * DMA) + 2 * DMA)
                if not isinstance(j, int):
                    act.wait_ge(s.mm, (j - 1) * 2)
                act.activation(w_hi[:, par], w_buf[:], ACT.Copy).then_inc(s.hi_done, 1)

            def convolve(j, par):
                for side in range(2):
                    act.wait_ge(s.mm, j * 2 + side + 1)
                    act.wait_ge(s.conv, j * 3)
                    col = bass.ds(j + side * FC, 1)
                    act.activation(cv[:, side], acc[par][side][:], ACT.Identity, scale=taps[:, 2, col], bias=taps[:, 3, col]).then_inc(s.act_c, 1)
                    if side == 1:
                        act.wait_ge(s.conv, j * 3 + 1)
                        act.activation(cv[:, 0], cv[:, 0], ACT.Gelu).then_inc(s.gelu, 1)
            strips(act, split_hi, convolve)

        @block.vector
        def _(dve):
            dve.wait_ge(s.taps_T, 1)
            for c in range(4):
                dve.tensor_copy(taps[:, c, :], acc[0][0][:, c * P:c * P + 2 * FC])
            dve.drain()
            dve.sem_inc(s.taps, 1)
            dve.sem_inc(s.ps_free, 2)

            def split_lo(j, par):
                dve.wait_ge(s.hi_done, j + 1)
                dve.tensor_tensor(w_lo[:, par], w_buf[:], w_hi[:, par], ALU.subtract).then_inc(s.lo_done, 1)

            def convolve(j, par):
                for side in range(2):
                    col = bass.ds(j + side * FC, 1)
                    dve.wait_ge(s.act_c, j * 2 + side + 1)
                    for lag, tap in ((1, 1), (2, 0)):
                        dve.scalar_tensor_tensor(cv[:, side, lag:], acc[par][side][:, :SEQ - lag], taps[:, tap, col], cv[:, side, lag:], ALU.mult, ALU.add)
                        dve.drain()
                    dve.sem_inc(s.conv, 1)
                dve.sem_inc(s.ps_free, 1)
                dve.wait_ge(s.gelu, j + 1)
                dve.tensor_tensor(fT[:, bass.ds(j, 1), :].rearrange("p a t -> p (a t)"), cv[:, 0], cv[:, 1], ALU.mult)
                dve.drain()
                dve.sem_inc(s.conv, 1)
            strips(dve, split_lo, convolve)
def turn_stage(nc, name, ident, src, ntiles, hT):
    with stage(nc, name, "x_even", "x_odd", "x_free", "turned", "act_out", "dve_out") as (block, s, sb, ps):
        x = sb("x", [P, 2, D])
        acc = [ps(f"acc{i}") for i in range(4)]

        @block.sync
        def _(sp):
            with sp.Fori(0, ntiles // 2) as i:
                for par in range(2):
                    sp.wait_ge(s.x_free, 2 * i + par + 1)
                    sp.dma_start(x[:, par], src[rows(i * (2 * P) + par * P), :]).then_inc((s.x_even, s.x_odd)[par], DMA)

        @block.tensor
        def _(pe):
            pe.sem_inc(s.x_free, 2)
            pe.sem_inc(s.act_out, 2)
            pe.sem_inc(s.dve_out, 2)
            with pe.Fori(0, ntiles // 2) as i:
                for par in range(2):
                    pe.wait_ge((s.x_even, s.x_odd)[par], i * DMA + DMA)
                    for hf, free in enumerate((s.act_out, s.dve_out)):
                        pe.wait_ge(free, 2 * i + par + 1)
                        for k in range(4):
                            c = hf * 4 + k
                            op = pe.transpose(acc[2 * par + hf][:, k * P:(k + 1) * P], x[:, par, c * P:(c + 1) * P], ident[:])
                        op.then_inc(s.turned, 1)
                    pe.wait_ge(s.turned, (2 * i + par + 1) * 2)
                    pe.sem_inc(s.x_free, 1)

        @block.scalar
        def _(act):
            with act.Fori(0, ntiles // 2) as i:
                for par in range(2):
                    act.wait_ge(s.turned, (2 * i + par) * 2 + 1)
                    act.activation(hT[:, 0:4, rows(i * (2 * P) + par * P)], acc[2 * par][:].rearrange("p (k t) -> p k t", k=4), ACT.Copy).then_inc(s.act_out, 1)

        @block.vector
        def _(dve):
            with dve.Fori(0, ntiles // 2) as i:
                for par in range(2):
                    dve.wait_ge(s.turned, (2 * i + par) * 2 + 2)
                    dve.tensor_copy(hT[:, 4:8, rows(i * (2 * P) + par * P)], acc[2 * par + 1][:].rearrange("p (k t) -> p k t", k=4)).then_inc(s.dve_out, 1)


U_RQ, U_RV, U_RZ, U_WZ, U_SHIFT, SHIFT_W, EVEN_IN = 0, 1024, 1536, 2048, 2560, 1792, 4352
HN, HD = 8, 64
BWD_ORDER = [1, 0] + list(range(NTA - 1, NTC - 1, -1))


def retention_tables():
    nf = 16
    t = np.arange(SEQ)
    inv = (10000.0 ** (-np.arange(nf, dtype=np.float32) / nf)).astype(np.float32)
    ang = np.concatenate([(t // 64).astype(np.float32)[:, None] * inv, (t % 64).astype(np.float32)[:, None] * inv], -1).astype(np.float32)
    rope = np.zeros((ALL, 2, 32), np.float32)
    rope[:CTX, 0] = 1.0
    rope[CTX:, 0], rope[CTX:, 1] = np.cos(ang), np.sin(ang)
    sk, tq = np.arange(P)[:, None], np.arange(P)[None, :]
    dist = np.stack([np.maximum(tq - sk, 0), tq >= sk, np.maximum(sk - tq, 0), sk >= tq], 1).astype(np.float32)
    pos = np.arange(P, dtype=np.float32)
    q_pos = np.stack([pos + 1, P - pos])
    k_pos = np.stack([P - 1 - pos, pos], 1)
    return rope.reshape(ALL, 64), dist, q_pos, k_pos


def retention_stage(nc, ident, U2, decay, t_rope, t_dist, t_qpos, t_kpos, YB2):
    with stage(nc, "ret", "const", "init", "dec", "exps", "dmat", "in0", "in1", "in2", "in3", "in4", "ropes_even", "ropes_odd", "rope_free", "k_dec", "kv",
               "kv_out", "kv_cur", "states", "turned", "qk", "q_dec", "scores", "am", "y_done", "sq", "var", "std", "z_in", "silu", "y", "stored") as (block, s, sb, ps):
        qkv = sb("qkv", [P, NTA, 1536])
        rp = sb("rp", [P, 2, 2, 32])
        dist = sb("dist", [P, 4, P])
        qpos = sb("qpos", [P, 2, P])
        kpos = sb("kpos", [P, 2])
        lg_all = sb("lg_all", [P, 2, HN])
        lg_half = sb("lg_half", [P, 2, 4])
        kdec = sb("kdec", [P, 2, HN, 1])
        gch = sb("gch", [P, 2, 4, 1])
        dm = sb("dm", [P, HN, P])
        dtmp = sb("dtmp", [P, 2, HN, P])
        qdec = sb("qdec", [P, 2, 4, P])
        tmp = sb("tmp", [P, 4, 16, 32])
        kd = sb("kd", [P, 2, 512])
        kv = sb("kv", [P, NTA, 2, 4, P])
        run = sb("run", [P, 2, 4, P])
        qT = sb("qT", [P, 4, P])
        kT = sb("kT", [P, 4, P])
        qd = sb("qd", [P, 2, 4, P])
        am = sb("am", [P, 2, 4, P])
        sq = sb("sq", [P, HN, HD])
        ss = sb("ss", [P, HN])
        rs = sb("rs", [P, HN, 1])
        z = sb("z", [P, 512])
        y = sb("y", [P, HN, HD])
        pkv = [ps(f"pkv{i}", [P, 4, P]) for i in range(2)]
        pq = ps("pq", [P, 4, P])
        pk = ps("pk", [P, 4, P])
        pa = [ps(f"pa{i}", [P, 4, P]) for i in range(2)]
        po = ps("po", [P, HN, HD])
        vcur = sb("vcur", [P, 512])
        cur = sb("cur", [P, 1536])
        st = sb("st", [P, 2, 4, P])
        loaded = (s.in0, s.in1, s.in2, s.in3, s.in4)
        u_v = U2.rearrange("(t p) n -> p t n", p=P)

        @block.sync
        def _(sp):
            for a in range(2):
                half = decay.rearrange("d (b a) -> a d b", a=2)[a]
                sp.dma_start(lg_half[a * HD:(a + 1) * HD], half.partition_broadcast(HD), allow_slow_non_contiguous=True).then_inc(s.const, DMA)
            sp.dma_start(lg_all[:], decay.partition_broadcast(P)).then_inc(s.const, DMA)
            sp.dma_start(dist[:], t_dist).then_inc(s.const, DMA)
            sp.dma_start(qpos[:], t_qpos.partition_broadcast(P)).then_inc(s.const, DMA)
            sp.dma_start(kpos[:], t_kpos).then_inc(s.const, DMA)
            for t in range(5):
                sp.dma_start(qkv[:, 2 * t:2 * t + 2], u_v[:, 2 * t:2 * t + 2, 0:1536]).then_inc(loaded[t], DMA)
            with sp.Fori(0, NTA // 2) as i:
                for par in range(2):
                    sp.wait_ge(s.rope_free, 2 * i + par + 1)
                    sp.dma_start(rp[:, par], t_rope[rows(i * (2 * P) + par * P), :].rearrange("p (c f) -> p c f", c=2)).then_inc((s.ropes_even, s.ropes_odd)[par], DMA)
            with sp.Fori(0, NTA) as i:
                sp.wait_ge(s.y, i)
                sp.dma_start(z[:], U2[rows(i * P), U_RZ:U_WZ]).then_inc(s.z_in, DMA)
                sp.wait_ge(s.y, i + 1)
                sp.dma_start(YB2[rows(i * P), 0:512], y[:].rearrange("p h d -> p (h d)")).then_inc(s.stored, DMA)
            sp.wait_ge(s.stored, NTA * DMA)

        @block.tensor
        def _(pe):
            pe.wait_ge(s.init, 1)
            with pe.Fori(0, NTA) as i:
                pe.wait_ge(s.k_dec, i + 1)
                pe.wait_ge(s.kv_out, i)
                for d in range(2):
                    for b in range(4):
                        op = pe.matmul(pkv[d][:, b, :], kd[:, d, b * P:(b + 1) * P], vcur[:, b * P:(b + 1) * P], start=True, stop=True)
                op.then_inc(s.kv, 1)
            pe.wait_ge(s.states, 1)
            with pe.Fori(0, NTA) as i:
                pe.wait_ge(s.kv_cur, i + 1)
                for b in range(4):
                    pe.transpose(pq[:, b, :], cur[:, b * P:(b + 1) * P], ident[:])
                for b in range(4):
                    op = pe.transpose(pk[:, b, :], cur[:, 512 + b * P:512 + (b + 1) * P], ident[:])
                op.then_inc(s.turned, 1)
                pe.wait_ge(s.qk, i + 1)
                for h in range(HN):
                    base = (h % 2) * HD
                    op = pe.matmul(pa[h % 2][:, h // 2, :], kT[base:base + HD, h // 2, :], qT[base:base + HD, h // 2, :], start=True, stop=True)
                op.then_inc(s.scores, 1)
                pe.wait_ge(s.q_dec, i + 1)
                pe.wait_ge(s.am, i + 1)
                for b in range(4):
                    pair = po[:, 2 * b:2 * b + 2, :].rearrange("p h d -> p (h d)")
                    pe.matmul(pair, qd[:, 0, b, :], st[:, 0, b, :], start=True, stop=False)
                    pe.matmul(pair, qd[:, 1, b, :], st[:, 1, b, :], start=False, stop=False)
                    for a in range(2):
                        h = 2 * b + a
                        op = pe.matmul(po[:, h, :], am[:, a, b, :], cur[:, 1024 + h * HD:1024 + (h + 1) * HD], start=False, stop=a == 1)
                op.then_inc(s.y_done, 1)

        @block.scalar
        def _(act):
            act.wait_ge(s.const, 6 * DMA)
            act.activation(lg_all[:], lg_all[:], ACT.Exp)
            act.activation(lg_half[:], lg_half[:], ACT.Exp).then_inc(s.exps, 1)
            act.wait_ge(s.dec, 1)
            act.activation(kdec[:], kdec[:], ACT.Exp)
            act.activation(gch[:, :, :, 0], lg_half[:], ACT.Exp, scale=float(P))
            for d in range(2):
                for b in range(4):
                    act.activation(qdec[:, d, b, :], qpos[:, d, :], ACT.Exp, scale=lg_half[:, d, b:b + 1])
                for h in range(HN):
                    act.activation(dtmp[:, d, h, :], dist[:, 2 * d, :], ACT.Exp, scale=lg_all[:, d, h:h + 1])
            act.drain()
            act.sem_inc(s.dmat, 1)
            with act.Fori(0, NTA) as i:
                act.wait_ge(s.turned, i + 1)
                act.activation(qT[:], pq[:], ACT.Copy)
                act.activation(kT[:], pk[:], ACT.Copy).then_inc(s.qk, 1)
                act.wait_ge(s.z_in, (i + 1) * DMA)
                act.activation(z[:], z[:], ACT.Silu)
                act.wait_ge(s.y_done, i + 1)
                act.activation(sq[:], po[:], ACT.Square)
                act.drain()
                act.sem_inc(s.sq, 1)
                act.wait_ge(s.var, i + 1)
                act.activation(rs[:, :, 0], ss[:], ACT.Sqrt).then_inc(s.std, 1)

        @block.vector
        def _(dve):
            dve.memset(kv[:], 0.0)
            dve.memset(run[:], 0.0)
            dve.sem_inc(s.rope_free, 2)
            dve.wait_ge(s.exps, 1)
            dve.tensor_scalar(lg_all[:], lg_all[:], -1.0, None, ALU.mult)
            dve.tensor_scalar(lg_half[:], lg_half[:], -1.0, None, ALU.mult)
            dve.drain()
            for d in range(2):
                dve.tensor_scalar(kdec[:, d, :, 0], lg_all[:, d, :], kpos[:, d:d + 1], None, ALU.mult)
            dve.drain()
            dve.sem_inc(s.dec, 1)
            dve.sem_inc(s.init, 1)
            dve.wait_ge(s.dmat, 1)
            dve.tensor_scalar(kdec[:], kdec[:], HD ** -0.5, None, ALU.mult)
            for d in range(2):
                m = dist[:, 2 * d + 1:2 * d + 2, :].broadcast_to([P, HN, P])
                dve.scalar_tensor_tensor(dtmp[:, d], dtmp[:, d], HD ** -0.5, m, ALU.mult, ALU.mult)
            dve.drain()
            for a in range(2):
                dve.tensor_tensor(dm[:, 4 * a:4 * a + 4, :], dtmp[:, 0, a:HN:2, :], dtmp[:, 1, a:HN:2, :], ALU.add)
            for t in range(5):
                dve.wait_ge(loaded[t], DMA)
            with dve.Fori(0, NTA // 2) as i:
                for par in range(2):
                    t = 2 * i + par
                    dve.wait_ge((s.ropes_even, s.ropes_odd)[par], i * DMA + DMA)
                    src = qkv[:, bass.ds(t, 1), :].rearrange("p a n -> p (a n)")
                    heads = src[:, 0:1024].rearrange("p (h d) -> p h d", d=HD)
                    a, b = heads[:, :, 0:32], heads[:, :, 32:64]
                    cos, sin = (rp[:, par, c:c + 1, :].broadcast_to([P, 16, 32]) for c in range(2))
                    for n, (u, w) in enumerate(((a, cos), (b, sin), (a, sin), (b, cos))):
                        dve.tensor_tensor(tmp[:, n], u, w, ALU.mult)
                    dve.drain()
                    dve.sem_inc(s.rope_free, 1)
                    dve.tensor_tensor(a, tmp[:, 0], tmp[:, 1], ALU.subtract)
                    dve.tensor_tensor(b, tmp[:, 2], tmp[:, 3], ALU.add)
                    dve.drain()
                    dve.wait_ge(s.kv, t)
                    for d in range(2):
                        dve.tensor_tensor(kd[:, d].rearrange("p (h d) -> p h d", d=HD), heads[:, 8:16, :], kdec[:, d].broadcast_to([P, HN, HD]), ALU.mult)
                    dve.tensor_copy(vcur[:], src[:, 1024:1536])
                    dve.drain()
                    dve.sem_inc(s.k_dec, 1)
                    dve.wait_ge(s.kv, t + 1)
                    for d in range(2):
                        for q in range(2):
                            e = slice(q * HD, (q + 1) * HD)
                            dve.tensor_copy(kv[e, bass.ds(t, 1), d, :, e].rearrange("p a b e -> p (a b) e"), pkv[d][e, :, e])
                    dve.drain()
                    dve.sem_inc(s.kv_out, 1)
            for d, order in enumerate((range(NTA), BWD_ORDER)):
                for t in order:
                    dve.tensor_tensor(dtmp[:, 0, 0:4, :], run[:, d], gch[:, d].broadcast_to([P, 4, P]), ALU.mult)
                    dve.drain()
                    dve.tensor_tensor(dtmp[:, 0, 0:4, :], dtmp[:, 0, 0:4, :], kv[:, t, d], ALU.add)
                    dve.drain()
                    dve.tensor_copy(kv[:, t, d], run[:, d])
                    dve.drain()
                    dve.tensor_copy(run[:, d], dtmp[:, 0, 0:4, :])
                    dve.drain()
            dve.sem_inc(s.states, 1)
            with dve.Fori(0, NTA) as i:
                dve.wait_ge(s.y_done, i)
                dve.tensor_copy(cur[:], qkv[:, bass.ds(i, 1), :].rearrange("p a n -> p (a n)"))
                dve.tensor_copy(st[:], kv[:, bass.ds(i, 1)].rearrange("p t a b e -> p (t a) b e"))
                dve.drain()
                dve.sem_inc(s.kv_cur, 1)
                dve.wait_ge(s.qk, i + 1)
                for d in range(2):
                    dve.tensor_tensor(qd[:, d], qT[:], qdec[:, d], ALU.mult)
                dve.drain()
                dve.sem_inc(s.q_dec, 1)
                dve.wait_ge(s.scores, i + 1)
                for a in range(2):
                    dve.tensor_tensor(am[:, a], pa[a][:], dm[:, 4 * a:4 * a + 4, :], ALU.mult)
                dve.drain()
                dve.sem_inc(s.am, 1)
                dve.wait_ge(s.sq, i + 1)
                dve.tensor_reduce(ss[:], sq[:], AX_X, ALU.add)
                dve.drain()
                dve.tensor_scalar(ss[:], ss[:], 1.0 / HD, 1e-6, ALU.mult, ALU.add).then_inc(s.var, 1)
                dve.wait_ge(s.std, i + 1)
                dve.reciprocal(rs[:], rs[:])
                dve.drain()
                dve.wait_ge(s.stored, i * DMA)
                dve.tensor_tensor(y[:], po[:], rs[:].broadcast_to([P, HN, HD]), ALU.mult)
                dve.drain()
                dve.tensor_tensor(y[:], y[:], z[:].rearrange("p (h d) -> p h d", d=HD), ALU.mult)
                dve.drain()
                dve.sem_inc(s.y, 1)


def rwkv_edges():
    before, behind = np.ones((P, NTA), np.float32), np.ones((P, NTA), np.float32)
    before[0, 0] = before[0, NTC] = 0.0
    behind[P - 1, NTC - 1] = behind[P - 1, NTA - 1] = 0.0
    return np.stack([before, behind], 1)


def rwkv_prep_stage(nc, ident, U2p, mu, w0, w2, a0, a2, kk_w, ka, rk, t_edges, PC, PD):
    with stage(nc, "prep", "const", "x_in", "x_free", "scaled", "mixed", "norm_sq", "root", "tanh", "turned", "tT", "lora", "lora_b", "sig", "k_done", "stored") as (block, s, sb, ps):
        x = sb("x", [P, 3, SHIFT_W])
        mu_r = sb("mu_r", [P, SHIFT_W])
        rowsb = {n: sb(n, [P, 512]) for n in ("kkr", "kar", "rkr")}
        b_rows = sb("b_rows", [P, 2, 2, 512])
        lw = sb("lw", [P, 2, 512])
        edges = sb("edges", [P, 2, NTA])
        kk = sb("kk", [P, HN, HD])
        sq = sb("sq", [P, HN, HD])
        ss = sb("ss", [P, HN, 1])
        td = sb("td", [P, 2, P])
        tT = sb("tT", [P, 2, P])
        sg = sb("sg", [P, 2, 2, 512])
        oc = sb("oc", [P, 3 * 512 + HN])
        od = sb("od", [P, 2, 3, 512])
        dots = sb("dots", [P, 2, HN])
        pt = ps("pt", [P, 2, P])
        pl = [[ps(f"pl{i}{d}") for d in range(2)] for i in range(2)]

        @block.sync
        def _(sp):
            for dst, src in ((mu_r, mu), (rowsb["kkr"], kk_w), (rowsb["kar"], ka), (rowsb["rkr"], rk)):
                sp.dma_start(dst[:], src.partition_broadcast(P)).then_inc(s.const, DMA)
            for d in range(2):
                sp.dma_start(b_rows[:, 0, d], w0[d].partition_broadcast(P)).then_inc(s.const, DMA)
                sp.dma_start(b_rows[:, 1, d], a0[d].partition_broadcast(P)).then_inc(s.const, DMA)
            sp.dma_start(lw[:, 0], w2.rearrange("d r n -> (d r) n")).then_inc(s.const, DMA)
            sp.dma_start(lw[:, 1], a2.rearrange("d r n -> (d r) n")).then_inc(s.const, DMA)
            sp.dma_start(edges[:], t_edges).then_inc(s.const, DMA)
            with sp.Fori(0, NTA) as i:
                sp.wait_ge(s.x_free, i)
                for n, off in enumerate((1, 0, 2)):
                    sp.dma_start(x[:, n], U2p[rows(i * P + off), U_SHIFT:EVEN_IN]).then_inc(s.x_in, DMA)
                sp.wait_ge(s.k_done, i + 1)
                sp.dma_start(PC[rows(i * P), :], oc[:]).then_inc(s.stored, DMA)
                for d in range(2):
                    sp.dma_start(PD[d, rows(i * P), :], od[:, d].rearrange("p a n -> p (a n)")).then_inc(s.stored, DMA)
            sp.wait_ge(s.stored, NTA * 3 * DMA)

        @block.tensor
        def _(pe):
            pe.wait_ge(s.const, 11 * DMA)
            with pe.Fori(0, NTA) as i:
                pe.wait_ge(s.tanh, i + 1)
                for n in range(2):
                    op = pe.transpose(pt[:, n, :], td[:, n, :], ident[:])
                op.then_inc(s.turned, 1)
                pe.wait_ge(s.tT, i + 1)
                pe.wait_ge(s.lora_b, i)
                for d in range(2):
                    base = d * 64
                    for n in range(2):
                        op = pe.matmul(pl[n][d][:], tT[base:base + 64, n, :], lw[base:base + 64, n, :], start=True, stop=True)
                op.then_inc(s.lora, 1)

        @block.scalar
        def _(act):
            with act.Fori(0, NTA) as i:
                act.wait_ge(s.mixed, i + 1)
                act.activation(td[:, 0, :], x[:, 0, 1536:1664], ACT.Tanh)
                act.activation(td[:, 1, :], x[:, 0, 1664:1792], ACT.Copy)
                act.drain()
                act.sem_inc(s.tanh, 1)
                act.wait_ge(s.turned, i + 1)
                act.activation(tT[:], pt[:], ACT.Copy).then_inc(s.tT, 1)
                act.wait_ge(s.norm_sq, i + 1)
                act.activation(ss[:], ss[:], ACT.Sqrt).then_inc(s.root, 1)
                act.wait_ge(s.lora_b, i + 1)
                act.activation(sg[:], sg[:], ACT.Sigmoid).then_inc(s.sig, 1)

        @block.vector
        def _(dve):
            dve.wait_ge(s.const, 11 * DMA)
            with dve.Fori(0, NTA) as i:
                dve.wait_ge(s.x_in, (i + 1) * (3 * DMA))
                dve.tensor_scalar(x[:, 1], x[:, 1], edges[:, 0, bass.ds(i, 1)], None, ALU.mult)
                dve.drain()
                dve.scalar_tensor_tensor(x[:, 1], x[:, 2], edges[:, 1, bass.ds(i, 1)], x[:, 1], ALU.mult, ALU.add)
                dve.drain()
                dve.scalar_tensor_tensor(x[:, 1], x[:, 1], 0.5, x[:, 0], ALU.mult, ALU.subtract)
                dve.drain()
                dve.tensor_tensor(x[:, 1], x[:, 1], mu_r[:], ALU.mult)
                dve.drain()
                dve.tensor_tensor(x[:, 0], x[:, 0], x[:, 1], ALU.add)
                dve.drain()
                dve.sem_inc(s.mixed, 1)
                r, k, v = (x[:, 0, n * 512:(n + 1) * 512] for n in range(3))
                kf = kk[:].rearrange("p h d -> p (h d)")
                dve.tensor_tensor(kf, k, rowsb["kkr"][:], ALU.mult)
                dve.drain()
                dve.tensor_tensor(sq[:], kk[:], kk[:], ALU.mult)
                dve.drain()
                dve.tensor_reduce(ss[:, :, 0], sq[:], AX_X, ALU.add).then_inc(s.norm_sq, 1)
                dve.wait_ge(s.root, i + 1)
                dve.tensor_scalar(ss[:], ss[:], 1e-12, None, ALU.max)
                dve.drain()
                dve.reciprocal(ss[:], ss[:])
                dve.drain()
                dve.wait_ge(s.stored, i * (3 * DMA))
                okk = oc[:, 1024:1536]
                dve.tensor_tensor(okk.rearrange("p (h d) -> p h d", d=HD), kk[:], ss[:].broadcast_to([P, HN, HD]), ALU.mult)
                dve.tensor_copy(oc[:, 0:512], r)
                dve.tensor_copy(oc[:, 512:1024], v)
                dve.wait_ge(s.lora, i + 1)
                for n in range(2):
                    for d in range(2):
                        dve.tensor_tensor(sg[:, n, d], pl[n][d][:], b_rows[:, n, d], ALU.add)
                dve.drain()
                dve.sem_inc(s.lora_b, 1)
                dve.wait_ge(s.sig, i + 1)
                for d in range(2):
                    dve.tensor_scalar(od[:, d, 0], sg[:, 0, d], -math.exp(-0.5), None, ALU.mult)
                    dve.tensor_tensor(od[:, d, 2], okk, sg[:, 1, d], ALU.mult)
                    dve.drain()
                    dve.scalar_tensor_tensor(sg[:, 1, d], sg[:, 1, d], 1.0, rowsb["kar"][:], ALU.subtract, ALU.mult)
                    dve.drain()
                    dve.scalar_tensor_tensor(od[:, d, 1], sg[:, 1, d], 1.0, k, ALU.add, ALU.mult)
                    dve.drain()
                    dve.tensor_tensor(kf, od[:, d, 1], r, ALU.mult)
                    dve.drain()
                    dve.tensor_tensor(kf, kf, rowsb["rkr"][:], ALU.mult)
                    dve.drain()
                    dve.tensor_reduce(dots[:, d], kk[:], AX_X, ALU.add)
                    dve.drain()
                dve.tensor_tensor(oc[:, 1536:], dots[:, 0], dots[:, 1], ALU.add)
                dve.drain()
                dve.sem_inc(s.k_done, 1)
                dve.sem_inc(s.x_free, 1)


def rwkv_tables():
    j, t = np.arange(P)[:, None], np.arange(P)[None, :]
    sums = np.zeros((2, P, 3, P), np.float32)
    ends = np.zeros((2, P, 2), np.float32)
    pairs = np.zeros((2, P, 4, P), np.uint32)
    level = np.zeros((2, P, 8, P), np.float32)
    for d in range(2):
        upto = (j <= t) if d == 0 else (j >= t)
        before = (j < t) if d == 0 else (j > t)
        mid = (j < 64) if d == 0 else (j >= 64)
        sums[d, :, 0] = upto.astype(np.float32) - mid
        sums[d, :, 1] = before.astype(np.float32) - mid
        sums[d, :, 2] = 1.0 - upto
        ends[d, :, 0], ends[d, :, 1] = 1.0, mid[:, 0]
        for n, m in enumerate((before, upto, before, upto)):
            pairs[d, :, n] = m
        for lv in range(7):
            b = 1 << lv
            same = (j // (2 * b)) == (t // (2 * b))
            late = ((j // b) % 2) == (1 - d)
            early = ((t // b) % 2) == d
            level[d, :, lv] = same & late & early
        level[d, :, 7] = level[d, :, 0].T
    return sums, ends, pairs, level


def rwkv_stage(nc, ident, PC, PD, t_sums, t_ends, t_pairs, t_level, RW):
    LV = 7
    with stage(nc, "rwkv", "const", "init", "in_f", "in_b", "in_free", "gsum", "exps", "late", "ew", "turned", "t_act", "t_dve", "amat", "a_out",
               "x_mm", "x_out", "t_mm", "t_out", "r_mm", "r_out", "u_mm", "u_out", "o_mm", "o_out", "m_mm", "m_out", "stored_f", "stored_b") as (block, s, sb, ps):
        xc = sb("xc", [P, 2, 1536])
        xd = sb("xd", [P, 2, 3, 512])
        sums = sb("sums", [P, 2, 3, P])
        ends = sb("ends", [P, 2, 2])
        pairs = sb("pairs", [P, 2, 512], U32)
        level = sb("level", [P, 2, 8, P])
        ex = sb("ex", [P, 4, 512])
        ecol = sb("ecol", [P, 2, 4, 2])
        ew = sb("ew", [P, 4, 512])
        lat = sb("lat", [P, 2, 512])
        arT = sb("arT", [P, 4, 2, P])
        bT = sb("bT", [P, 4, P])
        kT = sb("kT", [P, 4, P])
        A = sb("A", [P, 2, HN, 4, P])
        T = sb("T", [P, HN, P])
        TT = sb("TT", [P, HN, P])
        X = sb("X", [P, HN, P])
        M = sb("M", [P, 2, 4, P])
        Mc = sb("Mc", [P, 4, P])
        R = sb("R", [P, 512])
        U = sb("U", [P, 512])
        O = sb("O", [P, 2, 512])
        idle = sb("idle", [P, HN])
        w = [ps(f"w{i}") for i in range(6)]
        ru = ps("ru")
        om = ps("om")
        C = lambda bank, h: bank[:, (h % 4) * P:(h % 4 + 1) * P]

        @block.sync
        def _(sp):
            sp.dma_start(sums[:], t_sums.rearrange("d p n t -> p d n t")).then_inc(s.const, DMA)
            sp.dma_start(ends[:], t_ends.rearrange("d p n -> p d n")).then_inc(s.const, DMA)
            sp.dma_start(pairs[:], t_pairs.rearrange("d p n t -> p d (n t)")).then_inc(s.const, DMA)
            sp.dma_start(level[:], t_level.rearrange("d p n t -> p d n t")).then_inc(s.const, DMA)
            with sp.Fori(0, NTA) as i:
                for d in range(2):
                    u = 2 * i + d
                    tile = rows(i * P) if d == 0 else rows(((i * (NTA - 1) + (NTC - 1)) % NTA) * P)
                    sp.wait_ge(s.const, 4 * DMA)
                    sp.wait_ge(s.in_free, u)
                    done = (s.in_f, s.in_b)[d]
                    sp.dma_start(xc[:, d], PC[tile, 0:1536]).then_inc(done, DMA)
                    sp.dma_start(xd[:, d].rearrange("p a n -> p (a n)"), PD[d, tile, :]).then_inc(done, DMA)

        @block.gpsimd
        def _(pool):
            with pool.Fori(0, NTA) as i:
                for d in range(2):
                    u = 2 * i + d
                    tile = rows(i * P) if d == 0 else rows(((i * (NTA - 1) + (NTC - 1)) % NTA) * P)
                    pool.wait_ge(s.const, 4 * DMA)
                    pool.wait_ge(s.o_out, u + 1)
                    pool.dma_start(RW[d, tile, :], O[:, d]).then_inc((s.stored_f, s.stored_b)[d], DMA)
            pool.wait_ge(s.stored_f, NTA * DMA)
            pool.wait_ge(s.stored_b, NTA * DMA)

        @block.tensor
        def _(pe):
            pe.wait_ge(s.const, 4 * DMA)
            pe.wait_ge(s.init, 1)
            with pe.Fori(0, NTA) as i:
                for d in range(2):
                    u = 2 * i + d
                    pe.wait_ge((s.in_f, s.in_b)[d], (i + 1) * (2 * DMA))
                    for n in range(3):
                        pe.matmul(w[n][:], sums[:, d, n, :], xd[:, d, 0, :], start=True, stop=True)
                    pe.wait_ge(s.m_out, 2 * u)
                    for b in range(4):
                        op = pe.matmul(om[:, 2 * b:2 * b + 2], xd[:, d, 0, b * P:(b + 1) * P], ends[:, d, :], start=True, stop=True)
                    op.then_inc(s.gsum, 1)
                    pe.wait_ge(s.ew, u + 1)
                    for n in range(4):
                        for b in range(4):
                            op = pe.transpose(w[n][:, b * P:(b + 1) * P], ew[:, n, b * P:(b + 1) * P], ident[:])
                        op.then_inc(s.turned, 1)
                    pe.wait_ge(s.t_act, 2 * u + 2)
                    pe.wait_ge(s.t_dve, 2 * u + 2)
                    for h in range(HN):
                        if h >= 4:
                            pe.wait_ge(s.a_out, u * HN + h - 3)
                        base = (h % 2) * HD
                        rhs = arT[base:base + HD, h // 2].rearrange("p a t -> p (a t)")
                        pe.matmul(w[h % 4][:, 0:256], bT[base:base + HD, h // 2, :], rhs, start=True, stop=True)
                        pe.matmul(w[h % 4][:, 256:512], kT[base:base + HD, h // 2, :], rhs, start=True, stop=True).then_inc(s.amat, 1)
                    pe.wait_ge(s.a_out, (u + 1) * HN)
                    for q in range(2):
                        for h in range(4 * q, 4 * q + 4):
                            op = pe.matmul(C(w[q], h), A[:, d, h, 0, :], ident[:], start=True, stop=True)
                        op.then_inc(s.x_mm, 1)
                    for lv in range(1, LV):
                        for q in range(2):
                            pe.wait_ge(s.t_out, u * (2 * LV) + 2 * lv - 1 + q)
                            for h in range(4 * q, 4 * q + 4):
                                op = pe.matmul(C(w[q], h), A[:, d, h, 0, :], T[:, h, :], start=True, stop=True)
                            op.then_inc(s.x_mm, 1)
                        for q in range(2):
                            pe.wait_ge(s.x_out, u * (2 * LV) + 2 * lv + 1 + q)
                            for h in range(4 * q, 4 * q + 4):
                                if lv < LV - 1:
                                    pe.matmul(C(w[2 + q], h), TT[:, h, :], X[:, h, :], start=True, stop=True)
                                op = pe.matmul(C(w[4 + q], h), X[:, h, :], TT[:, h, :], start=True, stop=True)
                            op.then_inc(s.t_mm, 1)
                    pe.wait_ge(s.m_out, 2 * u + 1)
                    for b in range(4):
                        pe.matmul(ru[:, b * P:(b + 1) * P], arT[:, b, 0, :], Mc[:, b, :], start=True, stop=False)
                        for h in (2 * b, 2 * b + 1):
                            op = pe.matmul(ru[:, h * HD:(h + 1) * HD], A[:, d, h, 2, :], xc[:, d, 512 + h * HD:512 + (h + 1) * HD], start=False, stop=h % 2 == 1)
                    op.then_inc(s.r_mm, 1)
                    pe.wait_ge(s.t_out, (u + 1) * (2 * LV))
                    pe.wait_ge(s.r_out, u + 1)
                    for h in range(HN):
                        op = pe.matmul(ru[:, h * HD:(h + 1) * HD], TT[:, h, :], R[:, h * HD:(h + 1) * HD], start=True, stop=True)
                    op.then_inc(s.u_mm, 1)
                    pe.wait_ge(s.u_out, u + 1)
                    for b in range(4):
                        pe.matmul(om[:, b * P:(b + 1) * P], lat[:, 0, b * P:(b + 1) * P], U[:, b * P:(b + 1) * P], start=True, stop=False)
                        op = pe.matmul(om[:, b * P:(b + 1) * P], lat[:, 1, b * P:(b + 1) * P], xc[:, d, 512 + b * P:512 + (b + 1) * P], start=False, stop=True)
                    op.then_inc(s.m_mm, 1)
                    for b in range(4):
                        pe.matmul(ru[:, b * P:(b + 1) * P], arT[:, b, 1, :], Mc[:, b, :], start=True, stop=False)
                        for h in (2 * b, 2 * b + 1):
                            pe.matmul(ru[:, h * HD:(h + 1) * HD], A[:, d, h, 1, :], U[:, h * HD:(h + 1) * HD], start=False, stop=False)
                            op = pe.matmul(ru[:, h * HD:(h + 1) * HD], A[:, d, h, 3, :], xc[:, d, 512 + h * HD:512 + (h + 1) * HD], start=False, stop=h % 2 == 1)
                    op.then_inc(s.o_mm, 1)
                    pe.wait_ge(s.o_out, u + 1)
                    pe.sem_inc(s.in_free, 1)

        @block.scalar
        def _(act):
            with act.Fori(0, NTA) as i:
                for d in range(2):
                    u = 2 * i + d
                    act.wait_ge(s.gsum, u + 1)
                    act.activation(ex[:, 0], w[0][:], ACT.Exp)
                    act.activation(ex[:, 1], w[0][:], ACT.Exp, scale=-1.0)
                    act.activation(ex[:, 2], w[1][:], ACT.Exp)
                    act.activation(ex[:, 3], w[2][:], ACT.Exp)
                    act.activation(ecol[:, d], om[:, 0:8].rearrange("p (b n) -> p b n", n=2), ACT.Exp)
                    act.drain()
                    act.sem_inc(s.exps, 1)
                    act.wait_ge(s.turned, 4 * u + 1)
                    act.activation(arT[:, :, 0, :], w[0][:].rearrange("p (b t) -> p b t", b=4), ACT.Copy).then_inc(s.t_act, 1)
                    act.wait_ge(s.turned, 4 * u + 3)
                    act.activation(bT[:], w[2][:].rearrange("p (b t) -> p b t", b=4), ACT.Copy).then_inc(s.t_act, 1)
                    act.wait_ge(s.r_mm, u + 1)
                    act.activation(R[:], ru[:], ACT.Copy).then_inc(s.r_out, 1)
                    act.wait_ge(s.u_mm, u + 1)
                    act.activation(U[:], ru[:], ACT.Copy).then_inc(s.u_out, 1)
                    act.wait_ge(s.o_mm, u + 1)
                    act.wait_ge((s.stored_f, s.stored_b)[d], i * DMA)
                    act.activation(O[:, d], ru[:], ACT.Copy).then_inc(s.o_out, 1)

        @block.vector
        def _(dve):
            dve.memset(A[:], 0.0)
            dve.memset(M[:], 0.0)
            dve.drain()
            dve.sem_inc(s.init, 1)
            dve.wait_ge(s.const, 4 * DMA)
            with dve.Fori(0, NTA) as i:
                for d in range(2):
                    u = 2 * i + d
                    r, kk = xc[:, d, 0:512], xc[:, d, 1024:1536]
                    dve.wait_ge(s.exps, u + 1)
                    dve.scalar_tensor_tensor(ew[:, 0], kk, -1.0, ex[:, 2], ALU.mult, ALU.mult)
                    dve.tensor_tensor(ew[:, 1], r, ex[:, 0], ALU.mult)
                    dve.tensor_tensor(ew[:, 2], xd[:, d, 2], ex[:, 1], ALU.mult)
                    dve.tensor_tensor(ew[:, 3], xd[:, d, 1], ex[:, 1], ALU.mult)
                    dve.drain()
                    dve.sem_inc(s.ew, 1)
                    dve.tensor_tensor(Mc[:], M[:, d], ecol[:, d, :, 1:2].broadcast_to([P, 4, P]), ALU.mult)
                    dve.tensor_tensor(lat[:, 0], xd[:, d, 2], ex[:, 3], ALU.mult)
                    dve.tensor_tensor(lat[:, 1], xd[:, d, 1], ex[:, 3], ALU.mult)
                    dve.drain()
                    dve.sem_inc(s.m_out, 1)
                    dve.wait_ge(s.turned, 4 * u + 2)
                    dve.tensor_copy(arT[:, :, 1, :], w[1][:].rearrange("p (b t) -> p b t", b=4)).then_inc(s.t_dve, 1)
                    dve.wait_ge(s.turned, 4 * u + 4)
                    dve.tensor_copy(kT[:], w[3][:].rearrange("p (b t) -> p b t", b=4)).then_inc(s.t_dve, 1)
                    for h in range(HN):
                        dve.wait_ge(s.amat, u * HN + h + 1)
                        dve.memset(idle[:, h:h + 1], 0.0)
                        dve.copy_predicated(A[:, d, h].rearrange("p a t -> p (a t)"), pairs[:, d], w[h % 4][:]).then_inc(s.a_out, 1)
                    idb = ident[:].rearrange("p (a t) -> p a t", a=1).broadcast_to([P, 4, P])
                    for q in range(2):
                        hs = slice(4 * q, 4 * q + 4)
                        m0 = level[:, d, 0:1, :].broadcast_to([P, 4, P])
                        m7 = level[:, d, 7:8, :].broadcast_to([P, 4, P])
                        dve.wait_ge(s.x_mm, u * (2 * LV) + q + 1)
                        dve.tensor_tensor(T[:, hs, :], w[q][:].rearrange("p (h t) -> p h t", h=4), m0, ALU.mult)
                        dve.tensor_tensor(TT[:, hs, :], A[:, d, hs, 0, :], m7, ALU.mult)
                        dve.drain()
                        dve.tensor_tensor(T[:, hs, :], T[:, hs, :], idb, ALU.add)
                        dve.tensor_tensor(TT[:, hs, :], TT[:, hs, :], idb, ALU.add)
                        dve.drain()
                        dve.sem_inc(s.x_out, 1)
                        dve.sem_inc(s.t_out, 1)
                    for lv in range(1, LV):
                        for q in range(2):
                            hs = slice(4 * q, 4 * q + 4)
                            dve.wait_ge(s.x_mm, u * (2 * LV) + 2 * lv + q + 1)
                            ml = level[:, d, lv:lv + 1, :].broadcast_to([P, 4, P])
                            dve.tensor_tensor(X[:, hs, :], w[q][:].rearrange("p (h t) -> p h t", h=4), ml, ALU.mult).then_inc(s.x_out, 1)
                        for q in range(2):
                            hs = slice(4 * q, 4 * q + 4)
                            dve.wait_ge(s.t_mm, u * (2 * LV - 2) + 2 * (lv - 1) + q + 1)
                            if lv < LV - 1:
                                dve.tensor_tensor(T[:, hs, :], w[2 + q][:].rearrange("p (h t) -> p h t", h=4), T[:, hs, :], ALU.add)
                            dve.tensor_tensor(TT[:, hs, :], w[4 + q][:].rearrange("p (h t) -> p h t", h=4), TT[:, hs, :], ALU.add)
                            dve.drain()
                            dve.sem_inc(s.t_out, 1)
                    dve.wait_ge(s.m_mm, u + 1)
                    for a in range(2):
                        e = slice(a * HD, (a + 1) * HD)
                        dve.tensor_tensor(M[e, d, :, e], M[e, d, :, e], ecol[e, d, :, 0:1].broadcast_to([HD, 4, HD]), ALU.mult)
                    dve.drain()
                    for a in range(2):
                        e = slice(a * HD, (a + 1) * HD)
                        dve.tensor_tensor(M[e, d, :, e], M[e, d, :, e], om[e, :].rearrange("p (b v) -> p b v", b=4)[:, :, e], ALU.add)
                    dve.drain()
                    dve.sem_inc(s.m_out, 1)


def rwkv_out_stage(nc, RW, PC, U2, ln_w, ln_b, YB2):
    with stage(nc, "rwo", "const", "x_in", "y_done", "var", "std", "silu", "stored") as (block, s, sb, ps):
        x = sb("x", [P, 2, 512])
        v = sb("v", [P, HN, HD])
        dot = sb("dot", [P, HN, 1])
        z = sb("z", [P, 512])
        w_r = sb("w_r", [P, 512])
        b_r = sb("b_r", [P, 512])
        sq = sb("sq", [P, HN, HD])
        mean = sb("mean", [P, HN, 1])
        var = sb("var", [P, HN, 1])
        y = sb("y", [P, 512])

        @block.sync
        def _(sp):
            sp.dma_start(w_r[:], ln_w.partition_broadcast(P)).then_inc(s.const, DMA)
            sp.dma_start(b_r[:], ln_b.partition_broadcast(P)).then_inc(s.const, DMA)
            with sp.Fori(0, NTA) as i:
                t = rows(i * P)
                sp.wait_ge(s.y_done, i)
                for d in range(2):
                    sp.dma_start(x[:, d], RW[d, t, :]).then_inc(s.x_in, DMA)
                sp.dma_start(v[:].rearrange("p h d -> p (h d)"), PC[t, 512:1024]).then_inc(s.x_in, DMA)
                sp.dma_start(dot[:, :, 0], PC[t, 1536:1536 + HN]).then_inc(s.x_in, DMA)
                sp.dma_start(z[:], U2[t, U_WZ:U_SHIFT]).then_inc(s.x_in, DMA)
                sp.wait_ge(s.y_done, i + 1)
                sp.dma_start(YB2[t, 512:1024], y[:]).then_inc(s.stored, DMA)
            sp.wait_ge(s.stored, NTA * DMA)

        @block.scalar
        def _(act):
            with act.Fori(0, NTA) as i:
                act.wait_ge(s.x_in, (i + 1) * (5 * DMA))
                act.activation(z[:], z[:], ACT.Silu).then_inc(s.silu, 1)
                act.wait_ge(s.var, i + 1)
                act.activation(var[:], var[:], ACT.Sqrt).then_inc(s.std, 1)

        @block.vector
        def _(dve):
            dve.wait_ge(s.const, 2 * DMA)
            with dve.Fori(0, NTA) as i:
                dve.wait_ge(s.x_in, (i + 1) * (5 * DMA))
                h0 = x[:, 0].rearrange("p (h d) -> p h d", d=HD)
                dve.tensor_tensor(x[:, 0], x[:, 0], x[:, 1], ALU.add)
                dve.tensor_tensor(v[:], v[:], dot[:].broadcast_to([P, HN, HD]), ALU.mult)
                dve.drain()
                dve.tensor_reduce(mean[:, :, 0], h0, AX_X, ALU.add)
                dve.drain()
                dve.tensor_scalar(mean[:], mean[:], 1.0 / HD, None, ALU.mult)
                dve.drain()
                dve.tensor_tensor(h0, h0, mean[:].broadcast_to([P, HN, HD]), ALU.subtract)
                dve.drain()
                dve.tensor_tensor(sq[:], h0, h0, ALU.mult)
                dve.drain()
                dve.tensor_reduce(var[:, :, 0], sq[:], AX_X, ALU.add)
                dve.drain()
                dve.tensor_scalar(var[:], var[:], 1.0 / HD, 64e-5, ALU.mult, ALU.add).then_inc(s.var, 1)
                dve.wait_ge(s.std, i + 1)
                dve.reciprocal(var[:], var[:])
                dve.drain()
                dve.tensor_tensor(h0, h0, var[:].broadcast_to([P, HN, HD]), ALU.mult)
                dve.drain()
                dve.tensor_tensor(x[:, 0], x[:, 0], w_r[:], ALU.mult)
                dve.drain()
                dve.tensor_tensor(x[:, 0], x[:, 0], b_r[:], ALU.add)
                dve.drain()
                dve.tensor_tensor(x[:, 0], x[:, 0], v[:].rearrange("p h d -> p (h d)"), ALU.add)
                dve.drain()
                dve.wait_ge(s.silu, i + 1)
                dve.wait_ge(s.stored, i * DMA)
                dve.tensor_tensor(y[:], x[:, 0], z[:], ALU.mult).then_inc(s.y_done, 1)
O_HY, O_HZ, O_NQ, O_NK, O_NV, O_NZ, ODD_IN = 0, 1536, 2048, 2560, 3072, 3584, 4096
HYW = 512
NFREQ = SEQ
FCH = NFREQ // P
GRID_C, GRID_R = 64, 16
WIN_R, WIN_C = 8, 16


def hyena_tables():
    n = np.arange(SEQ, dtype=np.float64)
    t = np.linspace(0.0, 1.0, SEQ, dtype=np.float32)[:, None]
    bands = np.linspace(1e-4, 15, 16, dtype=np.float32)
    ang = (np.float32(2.0 * math.pi / SEQ) * np.arange(SEQ, dtype=np.float32)[:, None] * bands[None]).astype(np.float32)
    feats = np.concatenate([t, np.cos(ang), -np.sin(ang)], -1).astype(np.float32).T.copy()
    deltas = np.abs(np.linspace(math.log(1e-2) / 1.5, math.log(1e-2) / 0.3, HYW, dtype=np.float32))
    decay = np.exp(-t * deltas).astype(np.float32)
    th = math.pi * ((np.outer(n, 2 * np.arange(NFREQ) + 1)) % 4096) / 2048
    c, sn = np.cos(th).astype(np.float32), np.sin(th).astype(np.float32)
    fwd = np.stack([c, sn], 1)
    inv = np.stack([c.T, sn.T], 1)
    return feats, decay, np.ascontiguousarray(fwd), np.ascontiguousarray(inv)


def edges_of_sequence():
    before, behind = np.ones((P, NT), np.float32), np.ones((P, NT), np.float32)
    before[0, 0] = 0.0
    behind[P - 1, NT - 1] = 0.0
    return np.stack([before, behind], 1)


def short_conv_stage(nc, U3p, cw, cb, t_edges, VX):
    with stage(nc, "sc", "const", "x_even", "x_odd", "x_free", "y_done", "out_even", "out_odd") as (block, s, sb, ps):
        W = 3 * HYW
        x = sb("x", [P, 2, 3, W])
        w = sb("w", [P, 4, W])
        edges = sb("edges", [P, 2, NT])

        @block.sync
        def _(sp):
            for n in range(3):
                sp.dma_start(w[:, n], cw[n].partition_broadcast(P)).then_inc(s.const, DMA)
            sp.dma_start(w[:, 3], cb.partition_broadcast(P)).then_inc(s.const, DMA)
            sp.dma_start(edges[:], t_edges).then_inc(s.const, DMA)
            with sp.Fori(0, NT // 2) as i:
                for par in range(2):
                    sp.wait_ge((s.out_even, s.out_odd)[par], i * DMA)
                    for n in range(3):
                        sp.dma_start(x[:, par, n], U3p[rows(i * (2 * P) + (par * P + n)), 0:W]).then_inc((s.x_even, s.x_odd)[par], DMA)

        @block.scalar
        def _(act):
            with act.Fori(0, NT // 2) as i:
                for par in range(2):
                    act.wait_ge(s.y_done, 2 * i + par + 1)
                    act.dma_start(VX[rows(i * (2 * P) + par * P), :], x[:, par, 1]).then_inc((s.out_even, s.out_odd)[par], DMA)
            act.wait_ge(s.out_even, NT // 2 * DMA)
            act.wait_ge(s.out_odd, NT // 2 * DMA)

        @block.vector
        def _(dve):
            dve.wait_ge(s.const, 5 * DMA)
            with dve.Fori(0, NT // 2) as i:
                for par in range(2):
                    dve.wait_ge((s.x_even, s.x_odd)[par], (i + 1) * (3 * DMA))
                    a, b, c = (x[:, par, n] for n in range(3))
                    e0, e1 = (edges[:, n, bass.ds(i * 2 + par, 1)] for n in range(2))
                    dve.scalar_tensor_tensor(a, a, e0, w[:, 0], ALU.mult, ALU.mult)
                    dve.scalar_tensor_tensor(c, c, e1, w[:, 2], ALU.mult, ALU.mult)
                    dve.tensor_tensor(b, b, w[:, 1], ALU.mult)
                    dve.drain()
                    dve.tensor_tensor(a, a, c, ALU.add)
                    dve.tensor_tensor(b, b, w[:, 3], ALU.add)
                    dve.drain()
                    dve.tensor_tensor(b, a, b, ALU.add).then_inc(s.y_done, 1)


def filter_stage(nc, t_feats, t_decay, w1, b1, f1, w2, b2, f2, w3, FS):
    with stage(nc, "filt", "const", "h_mm", "arg", "sine", "w3_mm", "f_done", "stored") as (block, s, sb, ps):
        feats = sb("feats", [33, SEQ])
        w1s = sb("w1s", [33, 64])
        w2s = sb("w2s", [64, 64])
        w3s = sb("w3s", [64, 2048])
        cols = sb("cols", [64, 4])
        dec = sb("dec", [P, NT, HYW])
        ang = sb("ang", [64, SEQ])
        turns = sb("turns", [64, SEQ])
        arg = sb("arg", [64, SEQ])
        hid = sb("hid", [64, SEQ])
        f = sb("f", [P, 4, HYW])
        o = sb("o", [P, 4, HYW])
        first = sb("first", [P, 1])
        ph = ps("ph", [64, SEQ])
        pw = [ps(f"pw{i}") for i in range(4)]

        @block.sync
        def _(sp):
            sp.dma_start(feats[:], t_feats).then_inc(s.const, DMA)
            sp.dma_start(w1s[:], w1).then_inc(s.const, DMA)
            sp.dma_start(w2s[:], w2).then_inc(s.const, DMA)
            sp.dma_start(w3s[:], w3).then_inc(s.const, DMA)
            for n, v in enumerate((b1, f1, b2, f2)):
                sp.dma_start(cols[:, n:n + 1], v.rearrange("(p a) -> p a", a=1), allow_slow_non_contiguous=True).then_inc(s.const, DMA)
            sp.dma_start(dec[:], t_decay.rearrange("(t p) c -> p t c", p=P)).then_inc(s.const, DMA)
            with sp.Fori(0, NT) as i:
                sp.wait_ge(s.f_done, i + 1)
                for n in range(2):
                    sp.dma_start(FS[n, rows(i * P), :], o[:, 2 * n:2 * n + 2].rearrange("p a c -> p (a c)")).then_inc(s.stored, DMA)
            sp.wait_ge(s.stored, 2 * NT * DMA)

        @block.tensor
        def _(pe):
            pe.wait_ge(s.const, 9 * DMA)
            for layer, (w, src) in enumerate(((w1s, feats), (w2s, hid))):
                if layer:
                    pe.wait_ge(s.sine, 1)
                for hf in range(2):
                    op = pe.matmul(ph[:, hf * 512:(hf + 1) * 512], w[:], src[:, hf * 512:(hf + 1) * 512], start=True, stop=True)
                op.then_inc(s.h_mm, 1)
            pe.wait_ge(s.sine, 2)
            with pe.Fori(0, NT) as i:
                pe.wait_ge(s.arg, 2 + i + 1)
                for n in range(4):
                    op = pe.matmul(pw[n][:], ang[:, 0:P], w3s[:, n * 512:(n + 1) * 512], start=True, stop=True)
                op.then_inc(s.w3_mm, 1)

        @block.scalar
        def _(act):
            for layer in range(2):
                act.wait_ge(s.arg, layer + 1)
                act.activation(hid[:], arg[:], ACT.Sin).then_inc(s.sine, 1)

        @block.vector
        def _(dve):
            dve.memset(first[:], 1.0)
            dve.drain()
            dve.memset(first[0:1, :], 0.0)
            dve.wait_ge(s.const, 9 * DMA)
            for layer in range(2):
                dve.wait_ge(s.h_mm, layer + 1)
                b, fr = cols[:, 2 * layer:2 * layer + 1], cols[:, 2 * layer + 1:2 * layer + 2]
                dve.tensor_scalar(ang[:], ph[:], b, fr, ALU.add, ALU.mult)
                dve.drain()
                reduced_sine(dve, arg[:], ang[:], turns[:], 0.0)
                dve.sem_inc(s.arg, 1)
            dve.wait_ge(s.sine, 2)
            with dve.Fori(0, NT) as i:
                dve.tensor_copy(ang[:, 0:P], hid[:, rows(i * P)])
                dve.drain()
                dve.sem_inc(s.arg, 1)
                dve.wait_ge(s.w3_mm, i + 1)
                for n in range(4):
                    dve.tensor_tensor(f[:, n], pw[n][:], dec[:, bass.ds(i, 1), :].rearrange("p a c -> p (a c)"), ALU.mult)
                dve.drain()
                for n in (1, 3):
                    dve.tensor_scalar(f[:, n], f[:, n], first[:, 0:1], None, ALU.mult)
                dve.drain()
                dve.memset(first[:], 1.0)
                dve.wait_ge(s.stored, i * (2 * DMA))
                for n in range(2):
                    dve.tensor_tensor(o[:, 2 * n], f[:, 2 * n], f[:, 2 * n + 1], ALU.add)
                    dve.tensor_tensor(o[:, 2 * n + 1], f[:, 2 * n], f[:, 2 * n + 1], ALU.subtract)
                dve.drain()
                dve.sem_inc(s.f_done, 1)


def spectrum_stage(nc, name, t_fwd, zin, same, out):
    with stage(nc, name, "z_in", "w_even", "w_odd", "w_free", "mm", "act_out", "dve_out", "stored_even", "stored_odd") as (block, s, sb, ps):
        nz = 1 if same else 2
        z = sb("z", [P, NT, nz, HYW])
        w = sb("w", [P, 2, NT, 2, P])
        o = sb("o", [P, 2, 2, HYW])
        acc = [[ps(f"acc{i}{j}") for j in range(2)] for i in range(2)]

        @block.sync
        def _(sp):
            sp.dma_start(z[:], zin.rearrange("(t p) (a c) -> p t a c", p=P, a=nz)).then_inc(s.z_in, DMA)
            with sp.Fori(0, FCH // 2) as i:
                for par in range(2):
                    sp.wait_ge(s.w_free, 2 * i + par + 1)
                    for n in range(2):
                        sp.dma_start(w[:, par, :, n, :], t_fwd[:, n, rows(i * (2 * P) + par * P)].rearrange("(t p) f -> p t f", p=P)).then_inc(
                            (s.w_even, s.w_odd)[par], DMA)

        @block.tensor
        def _(pe):
            pe.sem_inc(s.w_free, 2)
            pe.sem_inc(s.act_out, 2)
            pe.sem_inc(s.dve_out, 2)
            pe.wait_ge(s.z_in, DMA)
            with pe.Fori(0, FCH // 2) as i:
                for par in range(2):
                    pe.wait_ge((s.w_even, s.w_odd)[par], (i + 1) * (2 * DMA))
                    for n, free in enumerate((s.act_out, s.dve_out)):
                        pe.wait_ge(free, 2 * i + par + 1)
                        for t in range(NT):
                            op = pe.matmul(acc[par][n][:], w[:, par, t, n, :], z[:, t, n % nz, :], start=t == 0, stop=t == NT - 1)
                        op.then_inc(s.mm, 1)
                    pe.wait_ge(s.mm, (2 * i + par + 1) * 2)
                    pe.sem_inc(s.w_free, 1)

        @block.scalar
        def _(act):
            with act.Fori(0, FCH // 2) as i:
                for par in range(2):
                    act.wait_ge(s.mm, (2 * i + par) * 2 + 1)
                    act.wait_ge((s.stored_even, s.stored_odd)[par], i * DMA)
                    act.activation(o[:, par, 0], acc[par][0][:], ACT.Copy).then_inc(s.act_out, 1)

        @block.vector
        def _(dve):
            with dve.Fori(0, FCH // 2) as i:
                for par in range(2):
                    dve.wait_ge(s.mm, (2 * i + par) * 2 + 2)
                    dve.wait_ge((s.stored_even, s.stored_odd)[par], i * DMA)
                    dve.tensor_copy(o[:, par, 1], acc[par][1][:]).then_inc(s.dve_out, 1)

        @block.gpsimd
        def _(pool):
            with pool.Fori(0, FCH // 2) as i:
                for par in range(2):
                    pool.wait_ge(s.act_out, 2 * i + par + 3)
                    pool.wait_ge(s.dve_out, 2 * i + par + 3)
                    pool.dma_start(out[rows(i * (2 * P) + par * P), :], o[:, par].rearrange("p a c -> p (a c)")).then_inc((s.stored_even, s.stored_odd)[par], DMA)
            pool.wait_ge(s.stored_even, FCH // 2 * DMA)
            pool.wait_ge(s.stored_odd, FCH // 2 * DMA)


def conv_stage(nc, name, t_fwd, t_inv, zin, KS, gate, bias, ZO):
    with stage(nc, name, "z_in", "b_in", "f_even", "f_odd", "f_free", "k_even", "k_odd", "fwd_mm", "prod", "i_even", "i_odd", "i_free",
               "g_even", "g_odd", "inv_mm", "y_done", "stored") as (block, s, sb, ps):
        z = sb("z", [P, NT, HYW])
        Y = sb("Y", [P, FCH, 2, HYW])
        w = sb("w", [P, 2, NT, 2, P])
        ks = sb("ks", [P, 2, 2, HYW])
        g = sb("g", [P, 2, HYW])
        b_row = sb("b_row", [P, HYW])
        tmp = sb("tmp", [P, 4, HYW])
        o = sb("o", [P, HYW])
        acc = [[ps(f"acc{i}{j}") for j in range(2)] for i in range(2)]
        yac = [ps(f"yac{i}") for i in range(2)]

        @block.sync
        def _(sp):
            sp.dma_start(z[:], zin.rearrange("(t p) c -> p t c", p=P)).then_inc(s.z_in, DMA)
            sp.dma_start(b_row[:], bias.partition_broadcast(P)).then_inc(s.b_in, DMA)
            with sp.Fori(0, FCH // 2) as i:
                for par in range(2):
                    sp.wait_ge(s.f_free, 2 * i + par + 1)
                    for n in range(2):
                        sp.dma_start(w[:, par, :, n, :], t_fwd[:, n, rows(i * (2 * P) + par * P)].rearrange("(t p) f -> p t f", p=P)).then_inc(
                            (s.f_even, s.f_odd)[par], DMA)
                    sp.dma_start(ks[:, par].rearrange("p a c -> p (a c)"), KS[rows(i * (2 * P) + par * P), :]).then_inc((s.k_even, s.k_odd)[par], DMA)
            sp.wait_ge(s.f_free, FCH + 2)
            with sp.Fori(0, NT // 2) as i:
                for par in range(2):
                    sp.wait_ge(s.i_free, 2 * i + par + 1)
                    for n in range(2):
                        sp.dma_start(w[:, par, :, n, :], t_inv[:, n, rows(i * (2 * P) + par * P)].rearrange("(f p) t -> p f t", p=P)).then_inc(
                            (s.i_even, s.i_odd)[par], DMA)
                    sp.dma_start(g[:, par], gate[rows(i * (2 * P) + par * P), :]).then_inc((s.g_even, s.g_odd)[par], DMA)

        @block.gpsimd
        def _(pool):
            with pool.Fori(0, NT) as i:
                pool.wait_ge(s.y_done, i + 1)
                pool.dma_start(ZO[rows(i * P), :], o[:]).then_inc(s.stored, DMA)
            pool.wait_ge(s.stored, NT * DMA)

        @block.tensor
        def _(pe):
            pe.wait_ge(s.z_in, DMA)
            with pe.Fori(0, FCH // 2) as i:
                for par in range(2):
                    pe.wait_ge((s.f_even, s.f_odd)[par], (i + 1) * (2 * DMA))
                    pe.wait_ge(s.f_free, 2 * i + par + 1)
                    for n in range(2):
                        for t in range(NT):
                            op = pe.matmul(acc[par][n][:], w[:, par, t, n, :], z[:, t, :], start=t == 0, stop=t == NT - 1)
                    op.then_inc(s.fwd_mm, 1)
            pe.wait_ge(s.prod, FCH)
            with pe.Fori(0, NT // 2) as i:
                for par in range(2):
                    pe.wait_ge((s.i_even, s.i_odd)[par], (i + 1) * (2 * DMA))
                    pe.wait_ge(s.i_free, 2 * i + par + 1)
                    for n in range(2):
                        for f in range(FCH):
                            op = pe.matmul(yac[par][:], w[:, par, f, n, :], Y[:, f, n, :], start=n == 0 and f == 0, stop=n == 1 and f == FCH - 1)
                    op.then_inc(s.inv_mm, 1)

        @block.vector
        def _(dve):
            dve.sem_inc(s.f_free, 2)
            dve.sem_inc(s.i_free, 2)
            dve.wait_ge(s.b_in, DMA)
            with dve.Fori(0, FCH // 2) as i:
                for par in range(2):
                    dve.wait_ge((s.k_even, s.k_odd)[par], i * DMA + DMA)
                    dve.wait_ge(s.fwd_mm, 2 * i + par + 1)
                    zc, zs = acc[par][0][:], acc[par][1][:]
                    kc, kz = ks[:, par, 0], ks[:, par, 1]
                    yc, ys = (Y[:, bass.ds(i * 2 + par, 1), n, :].rearrange("p a c -> p (a c)") for n in range(2))
                    for n, (a, b) in enumerate(((zc, kc), (zs, kz), (zc, kz), (zs, kc))):
                        dve.tensor_tensor(tmp[:, n], a, b, ALU.mult)
                    dve.drain()
                    dve.sem_inc(s.f_free, 1)
                    dve.tensor_tensor(yc, tmp[:, 0], tmp[:, 1], ALU.subtract)
                    dve.tensor_tensor(ys, tmp[:, 2], tmp[:, 3], ALU.add)
                    dve.drain()
                    dve.sem_inc(s.prod, 1)
            with dve.Fori(0, NT // 2) as i:
                for par in range(2):
                    t = i * 2 + par
                    dve.wait_ge((s.g_even, s.g_odd)[par], i * DMA + DMA)
                    dve.tensor_tensor(tmp[:, 0], z[:, bass.ds(t, 1), :].rearrange("p a c -> p (a c)"), b_row[:], ALU.mult)
                    dve.drain()
                    dve.wait_ge(s.inv_mm, t + 1)
                    dve.scalar_tensor_tensor(tmp[:, 0], yac[par][:], 1.0 / NFREQ, tmp[:, 0], ALU.mult, ALU.add)
                    dve.drain()
                    dve.wait_ge(s.stored, t * DMA)
                    dve.tensor_tensor(o[:], tmp[:, 0], g[:, par], ALU.mult)
                    dve.drain()
                    dve.sem_inc(s.y_done, 1)
                    dve.sem_inc(s.i_free, 1)


def na_tables():
    q, k = np.arange(GRID_C)[:, None], np.arange(GRID_C)[None, :]
    lo = np.clip(q - WIN_C // 2, 0, GRID_C - WIN_C)
    inside = (k >= lo) & (k < lo + WIN_C)
    hot = np.zeros((2 * WIN_C, GRID_C, GRID_C), np.float32)
    for o in range(2 * WIN_C - 1):
        hot[o] = inside & (k - q + WIN_C - 1 == o)
    hot[2 * WIN_C - 1] = np.where(inside, 0.0, NEG)
    return hot.reshape(2 * WIN_C, GRID_C * GRID_C)


def na_bias_stage(nc, ident, rpb, t_hot, BIAS):
    HR = HN * (2 * WIN_R - 1)
    NC_ = 2 * WIN_C - 1
    with stage(nc, "nab", "const", "init", "turned", "tab", "mm", "b_out", "stored") as (block, s, sb, ps):
        tab = sb("tab", [HR, 2 * WIN_C])
        tabT = sb("tabT", [2 * WIN_C, HR])
        hot = sb("hot", [2 * WIN_C, GRID_C * GRID_C])
        o = sb("o", [HR, GRID_C * GRID_C])
        pt = ps("pt")
        acc = ps("acc")

        @block.sync
        def _(sp):
            sp.wait_ge(s.init, 1)
            sp.dma_start(tab[:, 0:NC_], rpb.rearrange("h r c -> (h r) c")).then_inc(s.const, DMA)
            sp.dma_start(hot[:], t_hot).then_inc(s.const, DMA)
            sp.wait_ge(s.b_out, GRID_C * GRID_C // 512)
            sp.dma_start(BIAS, o[:]).then_inc(s.stored, DMA)
            sp.wait_ge(s.stored, DMA)

        @block.tensor
        def _(pe):
            pe.wait_ge(s.const, 2 * DMA)
            pe.transpose(pt[:2 * WIN_C, :HR], tab[:], ident[:HR, :HR]).then_inc(s.turned, 1)
            pe.wait_ge(s.tab, 1)
            for n in range(GRID_C * GRID_C // 512):
                if n:
                    pe.wait_ge(s.b_out, n)
                pe.matmul(acc[:HR, :], tabT[:], hot[:, n * 512:(n + 1) * 512], start=True, stop=True).then_inc(s.mm, 1)

        @block.vector
        def _(dve):
            dve.memset(tab[:], 1.0)
            dve.drain()
            dve.sem_inc(s.init, 1)
            dve.wait_ge(s.turned, 1)
            dve.tensor_copy(tabT[:], pt[:2 * WIN_C, :HR]).then_inc(s.tab, 1)
            for n in range(GRID_C * GRID_C // 512):
                dve.wait_ge(s.mm, n + 1)
                dve.tensor_copy(o[:, n * 512:(n + 1) * 512], acc[:HR, :]).then_inc(s.b_out, 1)


def na_stage(nc, ident, U3, KV3, BIAS, NA):
    NR = 2 * WIN_R - 1
    WK = WIN_R * GRID_C
    NK = WK + CTX
    NP_ = NK // P
    HP = HN // 2
    NU = HP * GRID_R
    with stage(nc, "na", "init", "k_in", "q_in", "v_in", "b_in", "turned", "qk_out", "q_bd", "s_mm", "s_done", "neg_max", "probs",
               "p_turned", "p_out", "pv", "y", "stored") as (block, s, sb, ps):
        kin = sb("kin", [P, NTA, 512])
        qin = sb("qin", [P, NT, 512])
        kT = sb("kT", [P, HP * ALL])
        qT = sb("qT", [P, HP * SEQ + GRID_C])
        vc = sb("vc", [P, NTC, 512])
        vl = sb("vl", [P, 2 * NT, 512])
        bias = sb("bias", [P, HP * NR, GRID_C])
        qbd = sb("qbd", [P, 2, P])
        sc = sb("sc", [P, 2, NK])
        mx = sb("mx", [P, 2])
        sm = sb("sm", [P, 4])
        pT = sb("pT", [P, 2, NP_, P])
        y = sb("y", [P, NU, HD])
        pS = [ps(f"pS{i}", [P, 1024]) for i in range(2)]
        pP = ps("pP", [P, 8, P])
        pV = ps("pV")

        def place(u):
            r = u % GRID_R
            start = (r - 4) * (r >= 4) - (r - 12) * (r >= 12)
            off = start - r + (WIN_R - 1)
            if not isinstance(u, int):
                start, off = start.with_bounds(min_val=0, max_val=GRID_R - WIN_R), off.with_bounds(min_val=0, max_val=WIN_R - 1)
            return r, start, off

        def tile_of(start):
            tile = (start % 2) * NT + start // 2
            return tile if isinstance(start, int) else tile.with_bounds(min_val=0, max_val=2 * NT - 5)

        def steps(eng, body):
            for u in range(2):
                body(u, u % 2, u)
            with eng.Fori(1, NU // 2) as i:
                for par in range(2):
                    body(2 * i + par, par, None)
            for u in range(NU, NU + 2):
                body(u, u % 2, u)

        def active(at, lag):
            return at is None or 0 <= at - lag < NU

        @block.sync
        def _(sp):
            sp.dma_start(kin[:, 0:NTC], KV3[:, 0:512].rearrange("(t p) c -> p t c", p=P)).then_inc(s.k_in, DMA)
            sp.dma_start(kin[:, NTC:], U3[:, O_NK:O_NV].rearrange("(t p) c -> p t c", p=P)).then_inc(s.k_in, DMA)
            sp.dma_start(qin[:], U3[:, O_NQ:O_NK].rearrange("(t p) c -> p t c", p=P)).then_inc(s.q_in, DMA)
            for a in range(2):
                for hp in range(HP):
                    r0 = (2 * hp + a) * NR
                    sp.dma_start(bias[a * GRID_C:(a + 1) * GRID_C, hp * NR:(hp + 1) * NR], BIAS[r0:r0 + NR, :].rearrange("r (q c) -> q r c", q=GRID_C)).then_inc(s.b_in, DMA)
            sp.dma_start(vc[:], KV3[:, 512:1024].rearrange("(t p) c -> p t c", p=P)).then_inc(s.v_in, DMA)
            sp.dma_start(vl[:, 0:NT], U3[:, O_NV:O_NZ].rearrange("(t p) c -> p t c", p=P)).then_inc(s.v_in, DMA)
            sp.dma_start(vl[:, NT:2 * NT - 1], U3[GRID_C:SEQ - GRID_C, O_NV:O_NZ].rearrange("(t p) c -> p t c", p=P)).then_inc(s.v_in, DMA)
            na_v = NA.rearrange("(r q) c -> q r c", q=GRID_C)
            for hp in range(HP):
                sp.wait_ge(s.y, (hp + 1) * GRID_R)
                for a in range(2):
                    h = 2 * hp + a
                    sp.dma_start(na_v[:, :, h * HD:(h + 1) * HD], y[a * GRID_C:(a + 1) * GRID_C, hp * GRID_R:(hp + 1) * GRID_R]).then_inc(s.stored, DMA)
            sp.wait_ge(s.stored, 2 * HP * DMA)

        @block.tensor
        def _(pe):
            pe.wait_ge(s.init, 1)
            pe.wait_ge(s.k_in, 2 * DMA)
            pe.wait_ge(s.q_in, DMA)
            n = 0
            for hp in range(HP):
                for src, lo, hi in ((kin, 0, 5), (kin, 5, NTA), (qin, 0, NT)):
                    if n >= 2:
                        pe.wait_ge(s.qk_out, n - 1)
                    for t in range(lo, hi):
                        op = pe.transpose(pS[n % 2][:, (t - lo) * P:(t - lo + 1) * P], src[:, t, hp * P:(hp + 1) * P], ident[:])
                    op.then_inc(s.turned, 1)
                    n += 1
            pe.wait_ge(s.qk_out, n)
            pe.wait_ge(s.v_in, 3 * DMA)

            def step(u, par, at):
                if active(at, 0):
                    _, start, _ = place(u)
                    pe.wait_ge(s.q_bd, u + 1)
                    if at is None:
                        pe.wait_ge(s.s_done, u - 1)
                    col = (u // GRID_R) * ALL
                    pe.matmul(pS[par][:, 0:WK], qbd[:, par], kT[:, bass.ds(col + start * GRID_C + CTX, WK)], start=True, stop=True)
                    pe.matmul(pS[par][:, WK:NK], qbd[:, par], kT[:, bass.ds(col, CTX)], start=True, stop=True).then_inc(s.s_mm, 1)
                if active(at, 1):
                    pe.wait_ge(s.probs, u)
                    if active(at, 2):
                        pe.wait_ge(s.p_out, u - 1)
                    for c in range(NP_):
                        op = pe.transpose(pP[:, c, :], sc[:, 1 - par, c * P:(c + 1) * P], ident[:])
                    op.then_inc(s.p_turned, 1)
                if active(at, 2):
                    v = u - 2
                    _, start, _ = place(v)
                    pe.wait_ge(s.p_out, v + 1)
                    if at != 2:
                        pe.wait_ge(s.y, v)
                    hp = v // GRID_R
                    tile = tile_of(start)
                    for c in range(WK // P):
                        pe.matmul(pV[:, 0:P], pT[:, par, c, :], vl[:].rearrange("p t c -> p (t c)")[:, bass.ds((tile + c) * 512 + hp * P, P)], start=c == 0, stop=False)
                    for c in range(NTC):
                        op = pe.matmul(pV[:, 0:P], pT[:, par, WK // P + c, :], vc[:].rearrange("p t c -> p (t c)")[:, bass.ds(hp * P + c * 512, P)], start=False, stop=c == NTC - 1)
                    op.then_inc(s.pv, 1)
            steps(pe, step)

        @block.scalar
        def _(act):
            n = 0
            for hp in range(HP):
                for lo, hi in ((0, 5), (5, NTA), (NTA, NTA + NT)):
                    act.wait_ge(s.turned, n + 1)
                    src = pS[n % 2][:, 0:(hi - lo) * P]
                    if lo < NTA:
                        op = act.activation(kT[:, hp * ALL + lo * P:hp * ALL + hi * P], src, ACT.Copy)
                    else:
                        op = act.activation(qT[:, hp * SEQ:(hp + 1) * SEQ], src, ACT.Copy, scale=HD ** -0.5)
                    op.then_inc(s.qk_out, 1)
                    n += 1

            def step(u, par, at):
                if active(at, 0):
                    act.wait_ge(s.neg_max, u + 1)
                    act.activation(sc[:, par], sc[:, par], ACT.Exp, bias=mx[:, par:par + 1], accum_out=sm[:, 2 * par:2 * par + 1])
                    act.drain()
                    act.sem_inc(s.probs, 1)
                if active(at, 1):
                    act.wait_ge(s.p_turned, u)
                    if active(at, 3):
                        act.wait_ge(s.pv, u - 2)
                    act.activation(pT[:, 1 - par], pP[:, 0:NP_], ACT.Copy).then_inc(s.p_out, 1)
            steps(act, step)

        @block.vector
        def _(dve):
            def spread(v, par):
                for a in range(2):
                    e = slice(a * HD, (a + 1) * HD)
                    dve.tensor_copy(qbd[e, par, e], qT[e, bass.ds(v * GRID_C, GRID_C)])
                dve.drain()
                dve.sem_inc(s.q_bd, 1)

            dve.memset(qbd[:], 0.0)
            dve.memset(qT[:, HP * SEQ:], 0.0)
            dve.drain()
            dve.sem_inc(s.init, 1)
            dve.wait_ge(s.qk_out, 3 * HP)
            spread(0, 0)
            dve.wait_ge(s.b_in, 2 * HP * DMA)

            def step(u, par, at):
                if active(at, 0):
                    _, _, off = place(u)
                    if at is None or u + 1 < NU:
                        if at != 0:
                            dve.wait_ge(s.s_mm, u)
                        spread(u + 1, 1 - par)
                    dve.wait_ge(s.s_mm, u + 1)
                    if at is None:
                        dve.wait_ge(s.p_turned, u - 1)
                    b = bias[:, bass.ds((u // GRID_R) * NR + off, WIN_R), :].rearrange("p a c -> p (a c)")
                    dve.tensor_tensor(sc[:, par, 0:WK], pS[par][:, 0:WK], b, ALU.add)
                    dve.tensor_copy(sc[:, par, WK:], pS[par][:, WK:NK])
                    dve.drain()
                    dve.sem_inc(s.s_done, 1)
                    dve.tensor_reduce(mx[:, par:par + 1], sc[:, par], AX_X, ALU.max, negate=True)
                    dve.drain()
                    dve.sem_inc(s.neg_max, 1)
                if active(at, 2):
                    v = u - 2
                    dve.wait_ge(s.pv, v + 1)
                    for a in range(2):
                        e = slice(a * HD, (a + 1) * HD)
                        dve.tensor_scalar(y[e, bass.ds(v, 1), :].rearrange("p a c -> p (a c)"), pV[e, a * HD:(a + 1) * HD], sm[e, 2 * par + 1:2 * par + 2], None, ALU.mult)
                    dve.drain()
                    dve.sem_inc(s.y, 1)
                if active(at, 1):
                    dve.wait_ge(s.probs, u)
                    dve.reciprocal(sm[:, 3 - 2 * par:4 - 2 * par], sm[:, 2 - 2 * par:3 - 2 * par])
                    dve.drain()
            steps(dve, step)


def odd_out_stage(nc, Z, NA, U3, YB3):
    with stage(nc, "oo", "x_even", "x_odd", "silu", "y_done", "out_even", "out_odd") as (block, s, sb, ps):
        x = sb("x", [P, 2, 2, 512])
        z = sb("z", [P, 2, 2, 512])

        @block.sync
        def _(sp):
            with sp.Fori(0, NT // 2) as i:
                for par in range(2):
                    sp.wait_ge((s.out_even, s.out_odd)[par], i * DMA)
                    t = rows(i * (2 * P) + par * P)
                    done = (s.x_even, s.x_odd)[par]
                    sp.dma_start(x[:, par, 0], Z[t, :]).then_inc(done, DMA)
                    sp.dma_start(x[:, par, 1], NA[t, :]).then_inc(done, DMA)
                    sp.dma_start(z[:, par, 0], U3[t, O_HZ:O_NQ]).then_inc(done, DMA)
                    sp.dma_start(z[:, par, 1], U3[t, O_NZ:ODD_IN]).then_inc(done, DMA)

        @block.scalar
        def _(act):
            with act.Fori(0, NT // 2) as i:
                for par in range(2):
                    act.wait_ge((s.x_even, s.x_odd)[par], (i + 1) * (4 * DMA))
                    act.activation(z[:, par], z[:, par], ACT.Silu).then_inc(s.silu, 1)

        @block.vector
        def _(dve):
            with dve.Fori(0, NT // 2) as i:
                for par in range(2):
                    dve.wait_ge(s.silu, 2 * i + par + 1)
                    dve.tensor_tensor(x[:, par], x[:, par], z[:, par], ALU.mult).then_inc(s.y_done, 1)

        @block.gpsimd
        def _(pool):
            with pool.Fori(0, NT // 2) as i:
                for par in range(2):
                    pool.wait_ge(s.y_done, 2 * i + par + 1)
                    pool.dma_start(YB3[rows(i * (2 * P) + par * P), :], x[:, par].rearrange("p a c -> p (a c)")).then_inc((s.out_even, s.out_odd)[par], DMA)
            pool.wait_ge(s.out_even, NT // 2 * DMA)
            pool.wait_ge(s.out_odd, NT // 2 * DMA)
def tables():
    prefix, suffix, causal = gla_tables()
    mask, first, freq = swa_tables()
    rope, dist, q_pos, k_pos = retention_tables()
    sums, ends, pairs, level = rwkv_tables()
    feats, decay, fwd, inv = hyena_tables()
    return {
        "t_eye": np.eye(P, dtype=np.float32), "t_prefix": prefix, "t_suffix": suffix, "t_causal": causal,
        "t_mask": mask, "t_first": first, "t_freq": freq, "t_rope": rope, "t_dist": dist, "t_qpos": q_pos,
        "t_kpos": k_pos, "t_edges_all": rwkv_edges(), "t_sums": sums, "t_ends": ends, "t_pairs": pairs,
        "t_level": level, "t_edges_seq": edges_of_sequence(), "t_feats": feats, "t_decay": decay,
        "t_fwd": fwd, "t_inv": inv, "t_hot": na_tables(),
    }


def start_stage(nc, ident, t_eye, padded):
    with stage(nc, "start", "id_in", "zero", "pad_out") as (block, s, sb, ps):
        zero = sb("zero", [1, EVEN_IN])

        @block.vector
        def _(dve):
            dve.memset(zero[:], 0.0).then_inc(s.zero, 1)

        @block.sync
        def _(sp):
            sp.dma_start(ident[:], t_eye).then_inc(s.id_in, DMA)
            sp.wait_ge(s.zero, 1)
            for t in padded:
                for row in (0, t.shape[0] - 1):
                    sp.dma_start(t[row:row + 1, :], zero[:, :t.shape[1]]).then_inc(s.pad_out, DMA)
            sp.wait_ge(s.id_in, DMA)
            sp.wait_ge(s.pad_out, 2 * len(padded) * DMA)


@contextmanager
def split_pair(nc, name, tokens):
    with nc.sbuf_tensor(f"{name}_hi", [P, KC, tokens], F32R) as hi, nc.sbuf_tensor(f"{name}_lo", [P, KC, tokens], F32R) as lo:
        yield hi, lo


def program(nc, T):
    def scratch(name, *shape):
        return nc.dram_tensor(name, shape, F32, kind="Internal").ap()

    mod1 = scratch("mod1", 1, 6 * D)
    mod2 = scratch("mod2", 2, 2, 3 * D)
    P1 = scratch("P1", SEQ, T["w_in"].shape[2])
    YA, Y1, O1, X1, D1, X2 = (scratch(n, SEQ, D) for n in ("YA", "Y1", "O1", "X1", "D1", "X2"))
    U2p = scratch("U2p", ALL + 2, EVEN_IN)
    U2 = U2p[1:ALL + 1, :]
    YB2, O2 = scratch("YB2", ALL, D), scratch("O2", ALL, D)
    PC, PD = scratch("PC", ALL, 3 * 512 + HN), scratch("PD", 2, ALL, 3 * 512)
    RW = scratch("RW", 2, ALL, 512)
    H1 = scratch("H1", SEQ, D)
    U3p = scratch("U3p", SEQ + 2, ODD_IN)
    U3 = U3p[1:SEQ + 1, :]
    KV3 = scratch("KV3", CTX, 1024)
    VX = scratch("VX", SEQ, 3 * HYW)
    FS, KS = scratch("FS", 2, SEQ, 2 * HYW), scratch("KS", 2, NFREQ, 2 * HYW)
    Z1, Z2, NA = (scratch(n, SEQ, HYW) for n in ("Z1", "Z2", "NA"))
    BIAS = scratch("BIAS", HN * (2 * WIN_R - 1), GRID_C * GRID_C)
    YB3, O3 = scratch("YB3", SEQ, D), scratch("O3", SEQ, D)

    x, ctx = T["x"][0], T["ctx_2"][0]
    part1 = lambda n: mod1[0, n * D:(n + 1) * D]
    part2 = lambda layer, who, n: mod2[layer, who, n * D:(n + 1) * D]

    with nc.sbuf_tensor("ident", [P, P], F32) as ident:
        start_stage(nc, ident, T["t_eye"], (U2p, U3p))
        ada_stage(nc, [([T["c"][0]], T["w_ada"][0], T["b_ada"][0], mod1)]
                  + [([T["c_2"][0], T["c_ctx_2"]], T["ada_w_2"][n], T["ada_b_2"][n], mod2[n]) for n in range(2)])

        with split_pair(nc, "h1", SEQ) as (hi, lo):
            with nc.sbuf_tensor("h1T", [P, KC, SEQ], F32) as hT:
                norm_stage(nc, "n1", ident, x, 0, NT, hT, 0, norm="ln", scale=part1(1), shift=part1(0))
                split_stage(nc, "h1s", hT, hi, lo, KC)
            gemm_stage(nc, "g_in", hi, lo, KC, NT, T["w_in"][0], P1)
        gla_stage(nc, ident, P1, T["gla_w_lr"][0], T["gla_b_lr"][0], T["gla_norm_g"][0], T["t_prefix"], T["t_suffix"], T["t_causal"], YA)
        swa_stage(nc, ident, P1, T["positions"][0], T["swa_sinks"][0], T["t_mask"], T["t_first"], T["t_freq"], YA, Y1)
        with split_pair(nc, "y1", SEQ) as (hi, lo):
            with nc.sbuf_tensor("y1T", [P, KC, SEQ], F32) as yT:
                turn_stage(nc, "turn1", ident, Y1, NT, yT)
                split_stage(nc, "y1s", yT, hi, lo, KC)
            gemm_stage(nc, "g_o", hi, lo, KC, NT, T["w_o"][0], O1)
        with nc.sbuf_tensor("fT", [P, FC, SEQ], F32) as fT:
            with split_pair(nc, "h2", SEQ) as (hi, lo):
                hT = fT[:, 0:KC, :]
                norm_stage(nc, "n2", ident, x, 0, NT, hT, 0, norm="ln", scale=part1(4), shift=part1(3), res=O1, gate=part1(2),
                           alpha=ALPHA, affine=(T["ln1_g"][0], T["ln1_b"][0]), keep=X1)
                split_stage(nc, "h2s", hT, hi, lo, KC)
                ffn_up_stage(nc, ident, hi, lo, T["w_up"][0], T["conv_w"][0], T["conv_b"][0], fT)
            gemm_stage(nc, "g_down", fT, None, FC, NT, T["w_down"][0], D1, width=256)

        with split_pair(nc, "h3", ALL) as (hi, lo):
          with nc.sbuf_tensor("h3T", [P, KC, ALL], F32) as hT:
            norm_stage(nc, "n3", ident, X1, 0, NT, hT, CTX, norm="rms", scale=part2(0, 0, 1), shift=part2(0, 0, 0), weight=T["norm_w_2"][0],
                       res=D1, gate=part1(5), alpha=ALPHA, affine=(T["ln2_g"][0], T["ln2_b"][0]), keep=X2)
            norm_stage(nc, "n3c", ident, ctx, 0, NTC, hT, 0, norm="rms", scale=part2(0, 1, 1), shift=part2(0, 1, 0), weight=T["norm_w_2"][0])
            split_stage(nc, "h3s", hT, hi, lo, KC)
          gemm_stage(nc, "g_even", hi, lo, KC, NTA, T["even_w_in_2"][0], U2, width=384)
        retention_stage(nc, ident, U2, T["ret_decay_2"][0], T["t_rope"], T["t_dist"], T["t_qpos"], T["t_kpos"], YB2)
        rwkv_prep_stage(nc, ident, U2p, T["rw_mu_2"][0], T["rw_w0_2"][0], T["rw_w2_2"][0], T["rw_a0_2"][0], T["rw_a2_2"][0], T["rw_kk_2"][0],
                        T["rw_ka_2"][0], T["rw_rk_2"][0].rearrange("h d -> (h d)"), T["t_edges_all"], PC, PD)
        rwkv_stage(nc, ident, PC, PD, T["t_sums"], T["t_ends"], T["t_pairs"], T["t_level"], RW)
        rwkv_out_stage(nc, RW, PC, U2, T["rw_ln_w_2"][0], T["rw_ln_b_2"][0], YB2)
        with split_pair(nc, "y2", ALL) as (hi, lo):
            with nc.sbuf_tensor("y2T", [P, KC, ALL], F32) as yT:
                turn_stage(nc, "turn2", ident, YB2, NTA, yT)
                split_stage(nc, "y2s", yT, hi, lo, KC)
            gemm_stage(nc, "g_eout", hi, lo, KC, NTA, T["even_w_out_2"][0], O2, width=384)

        with split_pair(nc, "h4", ALL) as (hi, lo):
          with nc.sbuf_tensor("h4T", [P, KC, ALL], F32) as hT:
            norm_stage(nc, "n4", ident, X2, 0, NT, hT, CTX, norm="rms", scale=part2(1, 0, 1), shift=part2(1, 0, 0), weight=T["norm_w_2"][1],
                       res=O2, res_row0=CTX, gate=part2(0, 0, 2), keep=H1)
            norm_stage(nc, "n4c", ident, ctx, 0, NTC, hT, 0, norm="rms", scale=part2(1, 1, 1), shift=part2(1, 1, 0), weight=T["norm_w_2"][1],
                       res=O2, gate=part2(0, 1, 2))
            split_stage(nc, "h4s", hT, hi, lo, KC)
          gemm_stage(nc, "g_odd", hi[:, :, CTX:], lo[:, :, CTX:], KC, NT, T["odd_w_in_2"][0], U3, width=384)
          gemm_stage(nc, "g_ckv", hi[:, :, 0:CTX], lo[:, :, 0:CTX], KC, NTC, T["odd_w_in_2"][0][:, O_NK:O_NZ], KV3, width=384)
        short_conv_stage(nc, U3p, T["hy_conv_w_2"][0], T["hy_conv_b_2"][0], T["t_edges_seq"], VX)
        filter_stage(nc, T["t_feats"], T["t_decay"], T["hy_w1_2"][0], T["hy_b1_2"][0], T["hy_f1_2"][0], T["hy_w2_2"][0], T["hy_b2_2"][0],
                     T["hy_f2_2"][0], T["hy_w3_2"][0], FS)
        for order, (zin, zout) in enumerate(((VX[:, 0:HYW], Z1), (Z1, Z2))):
            spectrum_stage(nc, f"spec{order}", T["t_fwd"], FS[order], False, KS[order])
            conv_stage(nc, f"conv{order}", T["t_fwd"], T["t_inv"], zin, KS[order], VX[:, (order + 1) * HYW:(order + 2) * HYW], T["hy_bias_2"][0, order], zout)
        na_bias_stage(nc, ident, T["na_rpb_2"][0], T["t_hot"], BIAS)
        na_stage(nc, ident, U3, KV3, BIAS, NA)
        odd_out_stage(nc, Z2, NA, U3, YB3)
        with split_pair(nc, "y3", SEQ) as (hi, lo):
            with nc.sbuf_tensor("y3T", [P, KC, SEQ], F32) as yT:
                turn_stage(nc, "turn3", ident, YB3, NT, yT)
                split_stage(nc, "y3s", yT, hi, lo, KC)
            gemm_stage(nc, "g_oout", hi, lo, KC, NT, T["odd_w_out_2"][0], O3)
        norm_stage(nc, "n5", ident, H1, 0, NT, None, 0, norm="rms", res=O3, gate=part2(1, 0, 2), final=T["final_norm_w_2"], keep=T["out"][0])


def kernel(**inputs):
    import concourse.bacc as bacc
    from concourse.bass_utils import run_bass_kernel_spmd

    nc = bacc.Bacc("TRN2", target_bir_lowering=False, num_devices=1)
    arrays, T = {}, {}
    for name, a in list(inputs.items()) + list(tables().items()):
        a = np.ascontiguousarray(a)
        arrays[f"in_{name}"] = a
        T[name] = nc.dram_tensor(f"in_{name}", a.shape, mybir.dt.from_np(a.dtype), kind="ExternalInput").ap()
    T["out"] = nc.dram_tensor("out_y", (1, SEQ, D), F32, kind="ExternalOutput").ap()
    program(nc, T)
    r = run_bass_kernel_spmd(nc, [arrays], core_ids=[0])
    return r.results[0]["out_y"]
```

```python
import math
from collections import namedtuple
from contextlib import ExitStack, contextmanager

import numpy as np

import concourse.bass as bass
from concourse import mybir

F32 = mybir.dt.float32
I32 = mybir.dt.int32
U32 = mybir.dt.uint32
F32R = mybir.dt.float32r
ALU = mybir.AluOpType
ACT = mybir.ActivationFunctionType
AX_X = mybir.AxisListType.X

P = 128
D = 1024
KC = D // P
SEQ = 1024
NT = SEQ // P
CTX = 256
NTC = CTX // P
ALL = CTX + SEQ
NTA = ALL // P
D_FF = 2816
FC = D_FF // P
ALPHA = 2.0 ** 0.25
DMA = 16


@contextmanager
def stage(nc, name, *signals):
    sems = {s: nc.alloc_semaphore(f"{name}_{s}") for s in signals}
    with ExitStack() as mem:
        def sb(label, shape, dt=F32):
            return mem.enter_context(nc.sbuf_tensor(f"{name}_{label}", shape, dt))

        def ps(label, shape=(P, 512), dt=F32):
            return mem.enter_context(nc.psum_tensor(f"{name}_{label}", list(shape), dt))

        with nc.Block() as block:
            yield block, namedtuple("Signals", signals)(**sems), sb, ps
    nc.clear_and_free_semaphores(list(sems.values()))
    nc.all_engine_barrier()


def rows(start, n=P):
    return bass.ds(start, n)


def col_view(vec):
    return vec.rearrange("(k p) -> p k", p=P)


def ada_stage(nc, jobs):
    W = 512
    for n, (cs, w, b, out) in enumerate(jobs):
        M, N = len(cs), w.shape[1]
        with stage(nc, f"ada{n}", "c_in", "b_in", "w_even", "w_odd", "silu", "w_free", "mm", "ps_free", "res", "out") as (block, s, sb, ps):
            c_raw = sb("c_raw", [P, KC, M])
            c_act = sb("c_act", [P, KC, M])
            w_buf = sb("w_buf", [P, 2, KC, W])
            bias = sb("bias", [M, N])
            res = sb("res", [M, N])
            acc = [ps(f"acc{i}") for i in range(2)]
            w_v = w.rearrange("(p k) n -> p k n", k=KC)

            @block.sync
            def _(sp):
                for m, c in enumerate(cs):
                    sp.dma_start(c_raw[:, :, m:m + 1], c.rearrange("(p k a) -> p k a", k=KC, a=1),
                                 allow_slow_non_contiguous=True).then_inc(s.c_in, DMA)
                    sp.dma_start(bias[m:m + 1, :], b.rearrange("(a n) -> a n", a=1)).then_inc(s.b_in, DMA)
                with sp.Fori(0, N // W // 2) as i:
                    for par in range(2):
                        sp.wait_ge(s.w_free, 2 * i + par + 1)
                        sp.dma_start(w_buf[:, par], w_v[:, :, bass.ds(i * (2 * W) + par * W, W)]).then_inc((s.w_even, s.w_odd)[par], DMA)
                sp.wait_ge(s.res, N // W)
                sp.dma_start(out, res[:]).then_inc(s.out, DMA)
                sp.wait_ge(s.out, DMA)

            @block.scalar
            def _(act):
                act.wait_ge(s.c_in, DMA * M)
                act.activation(c_act[:], c_raw[:], ACT.Silu).then_inc(s.silu, 1)

            @block.tensor
            def _(pe):
                pe.sem_inc(s.w_free, 2)
                pe.wait_ge(s.silu, 1)
                with pe.Fori(0, N // W // 2) as i:
                    for par in range(2):
                        pe.wait_ge(s.ps_free, 2 * i + par + 1)
                        pe.wait_ge((s.w_even, s.w_odd)[par], i * DMA + DMA)
                        for k in range(KC):
                            mm = pe.matmul(acc[par][:M, :], c_act[:, k, :], w_buf[:, par, k, :], start=k == 0, stop=k == KC - 1)
                        mm.then_inc(s.mm, 1)
                        pe.wait_ge(s.mm, 2 * i + par + 1)
                        pe.sem_inc(s.w_free, 1)

            @block.vector
            def _(dve):
                dve.sem_inc(s.ps_free, 2)
                dve.wait_ge(s.b_in, DMA * M)
                with dve.Fori(0, N // W // 2) as i:
                    for par in range(2):
                        dve.wait_ge(s.mm, 2 * i + par + 1)
                        cols = bass.ds(i * (2 * W) + par * W, W)
                        dve.tensor_tensor(res[:, cols], acc[par][:M, :], bias[:, cols], ALU.add).then_inc(s.res, 1)
                        dve.wait_ge(s.res, 2 * i + par + 1)
                        dve.sem_inc(s.ps_free, 1)


def split_stage(nc, name, hT, hi, lo, kc):
    with stage(nc, name, "hi_done", "lo_done") as (block, s, sb, ps):
        @block.scalar
        def _(act):
            for k in range(kc):
                act.activation(hi[:, k, :], hT[:, k, :], ACT.Copy).then_inc(s.hi_done, 1)

        @block.vector
        def _(dve):
            for k in range(kc):
                dve.wait_ge(s.hi_done, k + 1)
                dve.tensor_tensor(lo[:, k, :], hT[:, k, :], hi[:, k, :], ALU.subtract)
            dve.drain()


def gemm_stage(nc, name, hi, lo, kc, ntiles, w, out, width=512):
    N = w.shape[1]
    nb = 8 if ntiles == 8 else 4
    full = N // width
    tail = N - full * width
    pairs = full // 2
    left = [(2 * pairs, 2 * pairs * width, width)] if full % 2 else []
    if tail:
        left.append((full, full * width, tail))
    total = full + (tail > 0)
    half = ntiles // 2
    split = lo is not None
    with stage(nc, name, "w_even", "w_odd", "hi_done", "lo_done", "mm", "act_free", "dve_free", "out_even", "out_odd") as (block, s, sb, ps):
        w_buf = sb("w_buf", [P, 2, kc, width])
        w_hi = sb("w_hi", [P, 2, kc, width], F32R) if split else w_buf
        w_lo = sb("w_lo", [P, 2, kc, width], F32R) if split else None
        o_buf = sb("o_buf", [P, 2, ntiles, width])
        acc = [ps(f"acc{i}") for i in range(nb)]
        w_v = w.rearrange("(k p) n -> p k n", p=P)
        o_v = out.rearrange("(t p) n -> p t n", p=P)

        def strips(eng, body, behind=None):
            def last(st, col, wd):
                if behind:
                    behind(st, st % 2, col, wd)
            for st in range(2):
                body(st, st, st * width, width)
                if st:
                    last(0, 0, width)
            if pairs > 1:
                with eng.Fori(1, pairs) as i:
                    for par in range(2):
                        st, col = 2 * i + par, i * (2 * width) + par * width
                        body(st, par, col, width)
                        if behind:
                            behind(2 * i + (par - 1), 1 - par, i * (2 * width) + (par - 1) * width, width)
            at = (2 * pairs - 1, (2 * pairs - 1) * width, width)
            for st, col, wd in left:
                body(st, st % 2, col, wd)
                last(*at)
                at = (st, col, wd)
            last(*at)

        @block.sync
        def _(sp):
            def load(st, par, col, wd):
                if not isinstance(st, int) or st >= 2:
                    if split:
                        sp.wait_ge(s.lo_done, st - 1)
                    else:
                        sp.wait_ge(s.mm, (st - 1) * ntiles)
                sp.dma_start(w_buf[:, par, :, :wd], w_v[:, :, bass.ds(col, wd)]).then_inc((s.w_even, s.w_odd)[par], DMA)
            strips(sp, load)

        @block.tensor
        def _(pe):
            def multiply(st, par, col, wd):
                if split:
                    pe.wait_ge(s.lo_done, st + 1)
                else:
                    pe.wait_ge((s.w_even, s.w_odd)[par], (st - par) * (DMA // 2) + DMA)
                for t in range(ntiles):
                    bank = (par * ntiles + t) % nb
                    pe.wait_ge(s.act_free if t % 2 == 0 else s.dve_free, st * half + t // 2 + 1)
                    for k in range(kc):
                        o, tt = acc[bank][:, :wd], slice(t * P, (t + 1) * P)
                        mm = pe.matmul(o, hi[:, k, tt], w_hi[:, par, k, :wd], start=k == 0, stop=not split and k == kc - 1)
                        if split:
                            pe.matmul(o, hi[:, k, tt], w_lo[:, par, k, :wd], start=False, stop=False)
                            mm = pe.matmul(o, lo[:, k, tt], w_hi[:, par, k, :wd], start=False, stop=k == kc - 1)
                    mm.then_inc(s.mm, 1)
            strips(pe, multiply)

        def evacuate(eng, which, free):
            def body(st, par, col, wd):
                if not isinstance(st, int) or st >= 2:
                    eng.wait_ge(s.out_even if par == 0 else s.out_odd, (st - par) * (DMA // 2))
                for t in range(which, ntiles, 2):
                    bank = (par * ntiles + t) % nb
                    eng.wait_ge(s.mm, st * ntiles + t + 1)
                    if which == 0:
                        op = eng.activation(o_buf[:, par, t, :wd], acc[bank][:, :wd], ACT.Copy)
                    else:
                        op = eng.tensor_copy(o_buf[:, par, t, :wd], acc[bank][:, :wd])
                    op.then_inc(free, 1)
            return body

        @block.scalar
        def _(act):
            act.sem_inc(s.act_free, nb // 2)

            def split_hi(st, par, col, wd):
                if split:
                    act.wait_ge((s.w_even, s.w_odd)[par], (st - par) * (DMA // 2) + DMA)
                    if not isinstance(st, int) or st >= 2:
                        act.wait_ge(s.mm, (st - 1) * ntiles)
                    act.activation(w_hi[:, par, :, :wd], w_buf[:, par, :, :wd], ACT.Copy).then_inc(s.hi_done, 1)
            strips(act, split_hi, evacuate(act, 0, s.act_free))

        @block.vector
        def _(dve):
            dve.sem_inc(s.dve_free, nb // 2)

            def split_lo(st, par, col, wd):
                if split:
                    dve.wait_ge(s.hi_done, st + 1)
                    dve.tensor_tensor(w_lo[:, par, :, :wd], w_buf[:, par, :, :wd], w_hi[:, par, :, :wd], ALU.subtract).then_inc(s.lo_done, 1)
            strips(dve, split_lo, evacuate(dve, 1, s.dve_free))

        @block.gpsimd
        def _(pool):
            def store(st, par, col, wd):
                pool.wait_ge(s.act_free, (st + 1) * half + nb // 2)
                pool.wait_ge(s.dve_free, (st + 1) * half + nb // 2)
                pool.dma_start(o_v[:, :, bass.ds(col, wd)], o_buf[:, par, :, :wd]).then_inc(
                    s.out_even if par == 0 else s.out_odd, DMA)
            strips(pool, store)
            pool.wait_ge(s.out_even, DMA * ((total + 1) // 2))
            pool.wait_ge(s.out_odd, DMA * (total // 2))


def norm_stage(nc, name, ident, src, row0, ntiles, hT, tok0, norm=None, scale=None, shift=None, weight=None,
               res=None, gate=None, alpha=1.0, affine=None, keep=None, final=None, res_row0=0):
    eps2 = 1e-5 if norm == "ln" else 1e-6
    with stage(nc, name, "rows_in", "x_even", "x_odd", "x_free", "chain", "xn", "turned", "ps_free", "var", "std", "h_out", "kept", "cols") as (block, s, sb, ps):
        x = sb("x", [P, 2, D])
        r = sb("r", [P, 2, D]) if res is not None else None
        gate_row = sb("gate_row", [P, D]) if res is not None else None
        g_row = sb("g_row", [P, D]) if affine else None
        b_row = sb("b_row", [P, D]) if affine else None
        f_row = sb("f_row", [P, D]) if final is not None else None
        xn = sb("xn", [P, 2, D])
        stats = sb("stats", [P, 2, 6])
        mv = sb("mv", [P, 2])
        rstd = sb("rstd", [P, 2])
        cols = sb("cols", [P, 3, KC])
        acc = [ps(f"acc{i}") for i in range(4)]
        n_rows = (res is not None) + 2 * bool(affine) + (final is not None)
        n_cols = (scale is not None) + (shift is not None) + (weight is not None)
        keeps = keep is not None
        n_norms = bool(affine) + bool(norm)
        per_x = DMA * (2 if res is not None else 1)

        @block.scalar
        def _(act):
            if res is not None:
                act.dma_start(gate_row[:], gate.partition_broadcast(P)).then_inc(s.rows_in, DMA)
            if affine:
                act.dma_start(g_row[:], affine[0].partition_broadcast(P)).then_inc(s.rows_in, DMA)
                act.dma_start(b_row[:], affine[1].partition_broadcast(P)).then_inc(s.rows_in, DMA)
            if final is not None:
                act.dma_start(f_row[:], final.partition_broadcast(P)).then_inc(s.rows_in, DMA)
            for c, v in enumerate((scale, shift, weight)):
                if v is not None:
                    act.dma_start(cols[:, c, :], col_view(v), allow_slow_non_contiguous=True).then_inc(s.rows_in, DMA)
            if scale is not None:
                act.wait_ge(s.cols, 1)
            with act.Fori(0, ntiles // 2) as i:
                for par in range(2):
                    for q in range(n_norms):
                        act.wait_ge(s.var, (2 * i + par) * n_norms + q + 1)
                        act.activation(rstd[:, 0:1], rstd[:, 1:2], ACT.Sqrt).then_inc(s.std, 1)
                    if norm and final is None:
                        act.wait_ge(s.turned, 2 * i + par + 1)
                        for k in range(KC):
                            bank = 2 * par + k // 4
                            op = act.activation(hT[:, k, bass.ds(i * (2 * P) + (tok0 + par * P), P)],
                                                acc[bank][:, (k % 4) * P:(k % 4 + 1) * P], ACT.Identity,
                                                scale=cols[:, 0, k:k + 1], bias=cols[:, 1, k:k + 1])
                        op.then_inc(s.ps_free, 1)

        @block.sync
        def _(sp):
            with sp.Fori(0, ntiles // 2) as i:
                for par in range(2):
                    sp.wait_ge(s.x_free, 2 * i + par + 1)
                    sp.dma_start(x[:, par], src[bass.ds(i * (2 * P) + (row0 + par * P), P), :]).then_inc((s.x_even, s.x_odd)[par], DMA)
                    if res is not None:
                        sp.dma_start(r[:, par], res[bass.ds(i * (2 * P) + (res_row0 + par * P), P), :]).then_inc((s.x_even, s.x_odd)[par], DMA)

        @block.gpsimd
        def _(pool):
            if keeps:
                with pool.Fori(0, ntiles // 2) as i:
                    for par in range(2):
                        pool.wait_ge(s.chain, 2 * i + par + 1)
                        pool.dma_start(keep[bass.ds(i * (2 * P) + par * P, P), :],
                                       (xn if final is not None else x)[:, par]).then_inc(s.kept, DMA)
                        pool.wait_ge(s.kept, (2 * i + par + 1) * DMA)
                        pool.sem_inc(s.h_out, 1)

        @block.tensor
        def _(pe):
            if norm and final is None:
                pe.sem_inc(s.ps_free, 2)
                with pe.Fori(0, ntiles // 2) as i:
                    for par in range(2):
                        pe.wait_ge(s.xn, 2 * i + par + 1)
                        pe.wait_ge(s.ps_free, 2 * i + par + 1)
                        for k in range(KC):
                            bank = 2 * par + k // 4
                            op = pe.transpose(acc[bank][:, (k % 4) * P:(k % 4 + 1) * P], xn[:, par, k * P:(k + 1) * P], ident[:])
                        op.then_inc(s.turned, 1)

        @block.vector
        def _(dve):
            dve.sem_inc(s.x_free, 2)
            dve.wait_ge(s.rows_in, DMA * (n_rows + n_cols))
            if scale is not None:
                dve.tensor_scalar(cols[:, 0, :], cols[:, 0, :], 1.0, None, ALU.add)
                dve.drain()
                if weight is not None:
                    dve.tensor_tensor(cols[:, 0, :], cols[:, 0, :], cols[:, 2, :], ALU.mult)
                    dve.drain()
                dve.sem_inc(s.cols, 1)

            def norm_of(src_t, dst_t, kind, eps, nth):
                for hf in range(2):
                    dve.bn_stats(stats[:, hf, :], src_t[:, hf * 512:(hf + 1) * 512])
                dve.drain()
                dve.bn_aggr(mv[:], stats[:])
                dve.drain()
                if kind == "rms":
                    dve.scalar_tensor_tensor(rstd[:, 1:2], mv[:, 0:1], mv[:, 0:1], mv[:, 1:2], ALU.mult, ALU.add)
                    dve.drain()
                    dve.tensor_scalar(rstd[:, 1:2], rstd[:, 1:2], eps, None, ALU.add).then_inc(s.var, 1)
                else:
                    dve.tensor_scalar(rstd[:, 1:2], mv[:, 1:2], eps, None, ALU.add).then_inc(s.var, 1)
                dve.wait_ge(s.std, nth + 1)
                dve.reciprocal(rstd[:, 0:1], rstd[:, 0:1])
                dve.drain()
                if kind == "rms":
                    return dve.tensor_scalar(dst_t, src_t, rstd[:, 0:1], None, ALU.mult)
                return dve.tensor_scalar(dst_t, src_t, mv[:, 0:1], rstd[:, 0:1], ALU.subtract, ALU.mult)

            with dve.Fori(0, ntiles // 2) as i:
                for par in range(2):
                    xt = x[:, par]
                    dve.wait_ge((s.x_even, s.x_odd)[par], i * per_x + per_x)
                    if res is not None:
                        dve.tensor_tensor(r[:, par], r[:, par], gate_row[:], ALU.mult)
                        dve.drain()
                        dve.scalar_tensor_tensor(xt, xt, alpha, r[:, par], ALU.mult, ALU.add)
                        dve.drain()
                    if affine:
                        norm_of(xt, xt, "ln", 1e-5, (2 * i + par) * n_norms)
                        dve.drain()
                        dve.tensor_tensor(xt, xt, g_row[:], ALU.mult)
                        dve.drain()
                        dve.tensor_tensor(xt, xt, b_row[:], ALU.add)
                        dve.drain()
                    if keeps and final is None:
                        dve.sem_inc(s.chain, 1)
                    if norm:
                        if final is None:
                            dve.wait_ge(s.turned, 2 * i + par)
                        norm_of(xt, xn[:, par], norm, eps2, (2 * i + par) * n_norms + n_norms - 1)
                        dve.drain()
                        if final is not None:
                            if keeps:
                                dve.wait_ge(s.h_out, 2 * i + par)
                            dve.tensor_tensor(xn[:, par], xn[:, par], f_row[:], ALU.mult)
                            dve.drain()
                            dve.sem_inc(s.chain, 1)
                        else:
                            dve.sem_inc(s.xn, 1)
                    if keeps:
                        dve.wait_ge(s.h_out, 2 * i + par + 1)
                    dve.sem_inc(s.x_free, 1)
C_Q, C_K, C_V, C_R, C_LR, C_QB, C_GA, C_GB = 0, 512, 1024, 2048, 3072, 3088, 4368, 5392
GH, GDK, GDV, CH = 4, 128, 256, 64
LN_END = (D // P) * P


def gla_tables():
    j, i = np.arange(P)[:, None], np.arange(P)[None, :]
    same = (j // CH) == (i // CH)
    prefix = (same & (j <= i)).astype(np.float32) / 16.0
    suffix = (same & (j > i)).astype(np.float32) / 16.0
    causal = np.tile((same & (j <= i)).astype(np.uint32), (1, GH))
    return prefix, suffix, causal


def gla_stage(nc, ident, P1, w_lr, b_lr, norm_g, t_prefix, t_suffix, t_causal, YA):
    with stage(nc, "gla", "const", "init", "x_even", "x_odd", "lrT", "lrT_c", "z", "abs", "ln1", "g", "turned", "gsum", "dmid",
               "e_cum", "e_mid", "gla_ops", "scoresT", "masked", "kv", "state", "o_done", "sq", "var", "std", "e_gate", "y", "stored") as (block, s, sb, ps):
        x_all = sb("x_all", [P, 2, C_QB])
        ga = sb("ga", [P, 2, D])
        wlr = sb("wlr", [16, 512])
        blr = sb("blr", [1, 512])
        ones = sb("ones", [1, P])
        g_row = sb("g_row", [P, GH, GDV])
        prefix = sb("prefix", [P, P])
        suffix = sb("suffix", [P, P])
        causal = sb("causal", [P, GH * P], U32)
        lrT = sb("lrT", [16, P])
        za = sb("za", [P, 512])
        g = sb("g", [P, 512])
        dmid = sb("dmid", [P, GH * 2, CH])
        mid = sb("mid", [P, GH * 2, 1])
        e_cum = sb("e_cum", [P, 512])
        e_suf = sb("e_suf", [P, 512])
        e_up = sb("e_up", [P, 512])
        e_dn = sb("e_dn", [P, 512])
        qmid = sb("qmid", [P, 512])
        kmid = sb("kmid", [P, 512])
        qz = sb("qz", [P, 2, GH, P])
        kout = sb("kout", [P, 512])
        am = sb("am", [P, 512])
        S0 = sb("S0", [P, GH, GDV])
        S1 = sb("S1", [P, GH, GDV])
        sq = sb("sq", [P, GDV])
        ss = sb("ss", [P, GH])
        rs = sb("rs", [P, GH])
        eg = sb("eg", [P, 2, D])
        y = sb("y", [P, GH, GDV])
        pz = ps("pz")
        pq = ps("pq")
        pk = ps("pk")
        pg = ps("pg", [P, 1024])
        po = ps("po", [P, GH, GDV])
        pl = ps("pl")

        @block.sync
        def _(sp):
            sp.dma_start(wlr[:], w_lr).then_inc(s.const, DMA)
            sp.dma_start(blr[:], b_lr.rearrange("(a n) -> a n", a=1)).then_inc(s.const, DMA)
            sp.dma_start(prefix[:], t_prefix).then_inc(s.const, DMA)
            sp.dma_start(suffix[:], t_suffix).then_inc(s.const, DMA)
            sp.dma_start(causal[:], t_causal).then_inc(s.const, DMA)
            for h in range(GH):
                sp.dma_start(g_row[:, h, :], norm_g.partition_broadcast(P)).then_inc(s.const, DMA)
            def load(i, par):
                if not isinstance(i, int):
                    sp.wait_ge(s.y, 2 * i + (par - 1))
                tile = rows(i * (2 * P) + par * P)
                sp.dma_start(x_all[:, par], P1[tile, 0:C_QB]).then_inc((s.x_even, s.x_odd)[par], DMA)
                sp.dma_start(ga[:, par], P1[tile, C_GA:C_GB]).then_inc((s.x_even, s.x_odd)[par], DMA)
            load(0, 0)
            load(0, 1)
            with sp.Fori(1, NT // 2) as i:
                load(i, 0)
                load(i, 1)

        @block.gpsimd
        def _(pool):
            with pool.Fori(0, NT) as i:
                pool.wait_ge(s.y, i + 1)
                pool.dma_start(YA[rows(i * P), :], y[:].rearrange("p h v -> p (h v)")).then_inc(s.stored, DMA)
            pool.wait_ge(s.stored, NT * DMA)

        def arrived(eng, t, par):
            eng.wait_ge((s.x_even, s.x_odd)[par], (t - par) * DMA + 2 * DMA)

        @block.tensor
        def _(pe):
            pe.wait_ge(s.const, 9 * DMA)
            pe.wait_ge(s.init, 1)
            def turn(t, par):
                x = x_all[:, par]
                arrived(pe, t, par)
                pe.transpose(pl[:16, :P], x[:, C_LR:C_LR + 16], ident[:]).then_inc(s.lrT, 1)
                for h in range(GH):
                    pe.transpose(pq[:, h * P:(h + 1) * P], x[:, C_Q + h * P:C_Q + (h + 1) * P], ident[:])
                for h in range(GH):
                    op = pe.transpose(pk[:, h * P:(h + 1) * P], x[:, C_K + h * P:C_K + (h + 1) * P], ident[:])
                op.then_inc(s.turned, 1)

            def gate(t):
                pe.wait_ge(s.lrT_c, t + 1)
                pe.matmul(pz[:], lrT[:], wlr[:], start=True, stop=False)
                pe.matmul(pz[:], ones[:], blr[:], start=False, stop=True).then_inc(s.z, 1)

            def attend(t, par, more):
                x = x_all[:, par]
                pe.wait_ge(s.g, t + 1)
                for h in range(GH):
                    pe.matmul(pg[:, h * P:(h + 1) * P], g[:, h * P:(h + 1) * P], prefix[:], start=True, stop=True)
                pe.matmul(pg[:, 512:], suffix[:], g[:], start=True, stop=True).then_inc(s.gsum, 1)
                pe.wait_ge(s.gla_ops, t + 1)
                for h in range(GH):
                    op = pe.matmul(pz[:, h * P:(h + 1) * P], kmid[:, h * P:(h + 1) * P], qmid[:, h * P:(h + 1) * P], start=True, stop=True)
                op.then_inc(s.scoresT, 1)
                for h in range(GH):
                    op = pe.matmul(pg[:, h * GDV:(h + 1) * GDV], kout[:CH, h * P:(h + 1) * P], x[:CH, C_V + h * GDV:C_V + (h + 1) * GDV], start=True, stop=True)
                op.then_inc(s.kv, 1)
                if more:
                    turn(t + 1, 1 - par)
                pe.wait_ge(s.masked, t + 1)
                pe.wait_ge(s.state, 2 * t + 1)
                if not isinstance(t, int) or t:
                    pe.wait_ge(s.y, t)
                for h in range(GH):
                    pe.matmul(po[:, h, :], am[:, h * P:(h + 1) * P], x[:, C_V + h * GDV:C_V + (h + 1) * GDV], start=True, stop=False)
                    pe.matmul(po[:, h, :], qz[:, 0, h, :], S0[:, h, :], start=False, stop=False)
                    op = pe.matmul(po[:, h, :], qz[:, 1, h, :], S1[:, h, :], start=False, stop=True)
                op.then_inc(s.o_done, 1)
                for h in range(GH):
                    op = pe.matmul(pg[:, h * GDV:(h + 1) * GDV], kout[CH:, h * P:(h + 1) * P], x[CH:, C_V + h * GDV:C_V + (h + 1) * GDV], start=True, stop=True)
                op.then_inc(s.kv, 1)
                if more:
                    gate(t + 1)
            turn(0, 0)
            gate(0)
            attend(0, 0, True)
            attend(1, 1, True)
            with pe.Fori(1, NT // 2 - 1) as i:
                for par in range(2):
                    attend(2 * i + par, par, True)
            attend(NT - 2, 0, True)
            attend(NT - 1, 1, False)

        @block.scalar
        def _(act):
            def low_rank(t):
                act.wait_ge(s.lrT, t + 1)
                act.activation(lrT[:], pl[:16, :P], ACT.Copy).then_inc(s.lrT_c, 1)

            def log_gate(t):
                act.wait_ge(s.z, t + 1)
                act.activation(za[:], pz[:], ACT.Abs)
                act.drain()
                act.activation(za[:], za[:], ACT.Exp, scale=-1.0)
                act.drain()
                act.activation(za[:], za[:], ACT.Ln, bias=1.0).then_inc(s.ln1, 1)

            def body(t, par, more):
                act.wait_ge(s.gsum, t + 1)
                act.activation(e_cum[:], pg[:, :512], ACT.Exp)
                act.activation(e_suf[:], pg[:, 512:], ACT.Exp).then_inc(s.e_cum, 1)
                act.wait_ge(s.dmid, t + 1)
                act.activation(e_up[:], dmid[:], ACT.Exp)
                act.activation(e_dn[:], dmid[:], ACT.Exp, scale=-1.0).then_inc(s.e_mid, 1)
                if more:
                    low_rank(t + 1)
                arrived(act, t, par)
                if not isinstance(t, int) or t:
                    act.wait_ge(s.y, t)
                act.activation(eg[:, 0], x_all[:, par, C_R:C_R + D], ACT.Sigmoid)
                act.activation(eg[:, 1], ga[:, par], ACT.Sigmoid).then_inc(s.e_gate, 1)
                act.wait_ge(s.o_done, t + 1)
                for h in range(GH):
                    act.activation(sq[:], po[:, h, :], ACT.Square, accum_out=ss[:, h:h + 1])
                    act.drain()
                act.sem_inc(s.sq, 1)
                act.wait_ge(s.var, t + 1)
                act.activation(rs[:], ss[:], ACT.Sqrt).then_inc(s.std, 1)
                if more:
                    log_gate(t + 1)
            low_rank(0)
            log_gate(0)
            body(0, 0, True)
            body(1, 1, True)
            with act.Fori(1, NT // 2 - 1) as i:
                for par in range(2):
                    body(2 * i + par, par, True)
            body(NT - 2, 0, True)
            body(NT - 1, 1, False)

        @block.vector
        def _(dve):
            dve.memset(ones[:], 1.0)
            dve.memset(S0[:], 0.0)
            dve.memset(qz[:], 0.0)
            dve.memset(am[:], 0.0)
            dve.drain()
            dve.sem_inc(s.init, 1)
            dve.wait_ge(s.const, 9 * DMA)
            def body(t, par):
                x = x_all[:, par]
                arrived(dve, t, par)
                dve.wait_ge(s.ln1, t + 1)
                dve.scalar_tensor_tensor(g[:], pz[:], 0.0, za[:], ALU.min, ALU.subtract).then_inc(s.g, 1)
                dve.wait_ge(s.e_cum, t + 1)
                cum = pg[:, :512].rearrange("p (c j) -> p c j", j=CH)
                dve.tensor_copy(mid[:], cum[:, :, CH // 2 - 1:CH // 2])
                dve.drain()
                dve.tensor_tensor(dmid[:], cum, mid[:].broadcast_to([P, 2 * GH, CH]), ALU.subtract).then_inc(s.dmid, 1)
                dve.wait_ge(s.turned, t + 1)
                scale = float(GDK) ** -0.5
                q4 = pq[:].rearrange("p (h c j) -> p h c j", h=GH, c=2)
                e4 = e_cum[:].rearrange("p (h c j) -> p h c j", h=GH, c=2)
                for c in range(2):
                    dve.scalar_tensor_tensor(qz[:, c, :, c * CH:(c + 1) * CH], q4[:, :, c, :], scale, e4[:, :, c, :], ALU.mult, ALU.mult)
                dve.tensor_tensor(kout[:], x[:, C_K:C_K + 512], e_suf[:], ALU.mult)
                dve.wait_ge(s.e_mid, t + 1)
                dve.scalar_tensor_tensor(qmid[:], pq[:], scale, e_up[:], ALU.mult, ALU.mult)
                dve.tensor_tensor(kmid[:], pk[:], e_dn[:], ALU.mult)
                dve.drain()
                dve.sem_inc(s.gla_ops, 1)
                dve.wait_ge(s.init, 1)
                dve.wait_ge(s.scoresT, t + 1)
                dve.copy_predicated(am[:], causal[:], pz[:])
                dve.drain()
                dve.sem_inc(s.masked, 1)
                for c, (old, new) in enumerate(((S0, S1), (S1, S0))):
                    dve.wait_ge(s.kv, 2 * t + c + 1)
                    for h in range(GH):
                        last = h * P + c * CH + CH - 1
                        dve.scalar_tensor_tensor(new[:, h, :], old[:, h, :], e_cum[:, last:last + 1], pg[:, h * GDV:(h + 1) * GDV], ALU.mult, ALU.add)
                    dve.drain()
                    dve.sem_inc(s.state, 1)
                dve.wait_ge(s.e_gate, t + 1)
                dve.tensor_tensor(eg[:, 0], eg[:, 0], x[:, C_R:C_R + D], ALU.mult)
                dve.tensor_tensor(eg[:, 1], eg[:, 1], g_row[:].rearrange("p h v -> p (h v)"), ALU.mult)
                dve.drain()
                dve.tensor_tensor(eg[:, 0], eg[:, 0], eg[:, 1], ALU.mult)
                dve.wait_ge(s.sq, t + 1)
                dve.tensor_scalar(ss[:], ss[:], 1.0 / GDV, 1e-6, ALU.mult, ALU.add).then_inc(s.var, 1)
                dve.wait_ge(s.std, t + 1)
                dve.reciprocal(rs[:], rs[:])
                dve.drain()
                if not isinstance(t, int) or t:
                    dve.wait_ge(s.stored, t * DMA)
                for h in range(GH):
                    dve.scalar_tensor_tensor(y[:, h, :], po[:, h, :], rs[:, h:h + 1], eg[:, 0, h * GDV:(h + 1) * GDV], ALU.mult, ALU.mult)
                dve.drain()
                dve.sem_inc(s.y, 1)
            body(0, 0)
            body(1, 1)
            with dve.Fori(1, NT // 2) as i:
                for par in range(2):
                    body(2 * i + par, par)


SH, SHD, SKV = 16, 64, 2
NEG = -1.0e30
ROPE_F = 8
TWO_PI = 2.0 * math.pi
PI_1 = 6.28125
PI_2 = float(np.float32(TWO_PI - PI_1))
PI_3 = float(np.float32(TWO_PI - PI_1 - float(np.float32(TWO_PI - PI_1))))
ROUND = 12582912.0
PI_LIM = 3.1415925


def swa_tables():
    q, k = np.arange(P)[:, None], np.arange(P)[None, :]
    prev = np.where(k > q, 0.0, NEG)
    cur = np.where(k <= q, 0.0, NEG)
    mask = np.concatenate([prev, cur], 1).astype(np.float32)
    first = np.concatenate([np.full((P, P), NEG), cur], 1).astype(np.float32)
    freq = (500000.0 ** (-(np.arange(0, 16, 2, dtype=np.float32) / 16))).astype(np.float32)
    return mask, first, np.tile(freq, NT)[None, :]


def reduced_sine(dve, out, ang, turns, quarter):
    dve.tensor_scalar(turns, ang, 1.0 / TWO_PI, quarter, ALU.mult, ALU.add)
    dve.drain()
    dve.tensor_scalar(turns, turns, ROUND, None, ALU.add)
    dve.drain()
    dve.tensor_scalar(turns, turns, ROUND, None, ALU.subtract)
    dve.drain()
    dve.scalar_tensor_tensor(out, turns, -PI_1, ang, ALU.mult, ALU.add)
    dve.drain()
    dve.scalar_tensor_tensor(out, turns, -PI_2, out, ALU.mult, ALU.add)
    dve.drain()
    dve.scalar_tensor_tensor(out, turns, -PI_3, out, ALU.mult, ALU.add)
    dve.drain()
    if quarter:
        dve.tensor_scalar(out, out, quarter * TWO_PI, None, ALU.add)
        dve.drain()
    dve.tensor_scalar(out, out, PI_LIM, -PI_LIM, ALU.min, ALU.max)
    dve.drain()


def swa_stage(nc, ident, P1, pos, sinks, t_mask, t_first, t_freq, YA, Y1):
    with stage(nc, "swa", "const", "init", "arg", "table", "x_even", "x_odd", "g_even", "g_odd", "roped", "turned", "qkT", "scores", "s_done", "s_free",
               "neg_max", "probs", "p_turned", "p_copied", "p_free", "pv", "e_gate", "y", "stored") as (block, s, sb, ps):
        x = sb("x", [P, 2, 1280])
        gb = sb("gb", [P, 2, D])
        ya = sb("ya", [P, 2, D])
        pos_i = sb("pos_i", [P, NT], I32)
        pos_f = sb("pos_f", [P, NT, 1])
        freq = sb("freq", [P, NT, ROPE_F])
        ang = sb("ang", [P, NT, ROPE_F])
        turns = sb("turns", [P, NT, ROPE_F])
        arg = sb("arg", [P, 2, NT, 1, ROPE_F])
        cs = sb("cs", [P, 2, NT, 1, ROPE_F])
        mask = sb("mask", [P, 1, 256])
        mask_even = sb("mask_even", [P, 1, 256])
        sink = sb("sink", [P, SH])
        rope = sb("rope", [P, 4, 18, ROPE_F])
        kdup = sb("kdup", [P, 2, 2, SHD])
        qT = sb("qT", [P, 8, P])
        kT = sb("kT", [P, 2, 2, P])
        vv = sb("vv", [P, 2, P])
        sc = sb("sc", [P, 2, 4, 256])
        mx = sb("mx", [P, SH])
        nm = sb("nm", [P, SH])
        dsink = sb("dsink", [P, SH])
        esink = sb("esink", [P, 2, SH])
        sums = sb("sums", [P, 2, SH])
        rden = sb("rden", [P, SH, 1])
        pT = sb("pT", [P, 2, 8, P])
        eg = sb("eg", [P, D])
        y = sb("y", [P, SH, SHD])
        pt = ps("pt", [P, 8, P])
        pS = [ps(f"pS{i}", [P, 4, 256]) for i in range(2)]
        po = ps("po", [P, SH, SHD])
        G = 4

        @block.sync
        def _(sp):
            sp.dma_start(pos_i[:], pos.rearrange("(t p) -> p t", p=P), allow_slow_non_contiguous=True).then_inc(s.const, DMA)
            sp.dma_start(freq[:], t_freq[0].partition_broadcast(P).rearrange("p (t f) -> p t f", f=ROPE_F)).then_inc(s.const, DMA)
            sp.dma_start(mask[:, 0], t_mask).then_inc(s.const, DMA)
            sp.dma_start(mask_even[:, 0], t_first).then_inc(s.const, DMA)
            sp.dma_start(sink[:], sinks.partition_broadcast(P)).then_inc(s.const, DMA)
            def load(i, par):
                tile = rows(i * (2 * P) + par * P)
                if not isinstance(i, int):
                    sp.wait_ge(s.qkT, 2 * i + (par - 1))
                sp.dma_start(x[:, par], P1[tile, C_QB:C_GA]).then_inc((s.x_even, s.x_odd)[par], DMA)
                if not isinstance(i, int):
                    sp.wait_ge(s.y, 2 * i + (par - 1))
                sp.dma_start(gb[:, par], P1[tile, C_GB:C_GB + D]).then_inc((s.g_even, s.g_odd)[par], DMA)
                sp.dma_start(ya[:, par], YA[tile, :]).then_inc((s.g_even, s.g_odd)[par], DMA)
            load(0, 0)
            load(0, 1)
            with sp.Fori(1, NT // 2) as i:
                load(i, 0)
                load(i, 1)

        @block.gpsimd
        def _(pool):
            with pool.Fori(0, NT) as i:
                pool.wait_ge(s.y, i + 1)
                pool.dma_start(Y1[rows(i * P), :], y[:].rearrange("p h d -> p (h d)")).then_inc(s.stored, DMA)
            pool.wait_ge(s.stored, NT * DMA)

        @block.tensor
        def _(pe):
            pe.wait_ge(s.init, 1)
            def turn(t, par):
                pe.wait_ge(s.roped, t + 1)
                if not isinstance(t, int) or t:
                    pe.wait_ge(s.p_copied, t * G)
                for c in range(8):
                    pe.transpose(pt[:, c, :], x[:, par, c * P:(c + 1) * P], ident[:])
                for c in range(2):
                    op = pe.transpose(pS[1][:, c, :P], kdup[:, c].rearrange("p a d -> p (a d)"), ident[:])
                op.then_inc(s.turned, 1)

            def attend(t, par):
                pe.wait_ge(s.qkT, t + 1)
                for g in range(G + 1):
                    if g < G:
                        pe.wait_ge(s.s_free, t * G + g + 1)
                        for h in range(4):
                            hd, base, slot = 4 * g + h, (h % 2) * SHD, (h % 2) * 2 + h // 2
                            for side, kp in ((0, 1 - par), (1, par)):
                                op = pe.matmul(pS[g % 2][:, slot, side * P:(side + 1) * P], qT[base:base + SHD, hd // 2, :],
                                               kT[base:base + SHD, kp, hd // 8, :], start=True, stop=True)
                        op.then_inc(s.scores, 1)
                    if g:
                        q = g - 1
                        pe.wait_ge(s.probs, t * G + q + 1)
                        if q:
                            pe.wait_ge(s.p_copied, t * G + q)
                        for c in range(8):
                            op = pe.transpose(pt[:, c, :], sc[:, q % 2, c // 2, (c % 2) * P:(c % 2 + 1) * P], ident[:])
                        op.then_inc(s.p_turned, 1)
                        pe.wait_ge(s.p_copied, t * G + q + 1)
                        if q == 0:
                            if not isinstance(t, int) or t:
                                pe.wait_ge(s.y, t)
                        for h in range(4):
                            hd = 4 * q + h
                            kv = hd // 8
                            slot = (h % 2) * 2 + h // 2
                            pe.matmul(po[:, hd, :], pT[:, q % 2, 2 * slot, :], vv[:, 1 - par, kv * SHD:(kv + 1) * SHD], start=True, stop=False)
                            op = pe.matmul(po[:, hd, :], pT[:, q % 2, 2 * slot + 1, :], vv[:, par, kv * SHD:(kv + 1) * SHD], start=False, stop=True)
                        op.then_inc(s.pv, 1)

            turn(0, 0)
            attend(0, 0)
            turn(1, 1)
            attend(1, 1)
            with pe.Fori(1, NT // 2) as i:
                for par in range(2):
                    turn(2 * i + par, par)
                    attend(2 * i + par, par)

        @block.scalar
        def _(act):
            act.wait_ge(s.arg, 1)
            act.activation(cs[:], arg[:], ACT.Sin).then_inc(s.table, 1)
            with act.Fori(0, NT // 2) as i:
                for par in range(2):
                    t = 2 * i + par
                    act.wait_ge(s.turned, t + 1)
                    act.activation(vv[:, par, :], x[:, par, D + P:D + 2 * P], ACT.Copy)
                    act.activation(qT[:], pt[:], ACT.Copy)
                    act.activation(kT[:, par], pS[1][:, 0:2, :P], ACT.Copy)
                    act.drain()
                    act.sem_inc(s.qkT, 1)
                    for g in range(G + 1):
                        if g:
                            q = g - 1
                            act.wait_ge(s.p_turned, t * G + q + 1)
                            if q >= 2:
                                act.wait_ge(s.pv, t * G + q - 1)
                            act.activation(pT[:, q % 2], pt[:], ACT.Copy).then_inc(s.p_copied, 1)
                        if g < G:
                            act.wait_ge(s.neg_max, t * G + g + 1)
                            for h in range(4):
                                hd, slot = 4 * g + h, (h % 2) * 2 + h // 2
                                act.activation(sc[:, g % 2, slot, :], sc[:, g % 2, slot, :], ACT.Exp, bias=nm[:, hd:hd + 1], accum_out=sums[:, par, hd:hd + 1])
                            act.activation(esink[:, par, 4 * g:4 * g + 4], dsink[:, 4 * g:4 * g + 4], ACT.Exp)
                            act.drain()
                            act.sem_inc(s.probs, 1)
                    act.wait_ge((s.g_even, s.g_odd)[par], (i + 1) * (2 * DMA))
                    act.wait_ge(s.y, t)
                    act.activation(eg[:], gb[:, par], ACT.Sigmoid).then_inc(s.e_gate, 1)

        @block.vector
        def _(dve):
            dve.memset(kT[:], 0.0)
            dve.memset(vv[:], 0.0)
            dve.drain()
            dve.sem_inc(s.init, 1)
            dve.sem_inc(s.s_free, 2)
            dve.wait_ge(s.const, 5 * DMA)
            dve.tensor_copy(pos_f[:, :, 0], pos_i[:])
            dve.drain()
            dve.tensor_tensor(ang[:], freq[:], pos_f[:].broadcast_to([P, NT, ROPE_F]), ALU.mult)
            dve.drain()
            reduced_sine(dve, arg[:, 0, :, 0, :], ang[:], turns[:], 0.25)
            reduced_sine(dve, arg[:, 1, :, 0, :], ang[:], turns[:], 0.0)
            dve.sem_inc(s.arg, 1)
            dve.wait_ge(s.table, 1)
            def rope_block(t, par):
                dve.wait_ge((s.x_even, s.x_odd)[par], (t - par) * (DMA // 2) + DMA)
                heads = x[:, par, :18 * SHD].rearrange("p (h d) -> p h d", d=SHD)
                a, b = heads[:, :, 0:ROPE_F], heads[:, :, ROPE_F:2 * ROPE_F]
                cos, sin = (cs[:, c, bass.ds(t, 1), 0, :].broadcast_to([P, 18, ROPE_F]) for c in range(2))
                for n, (u, w) in enumerate(((a, cos), (b, sin), (b, cos), (a, sin))):
                    dve.tensor_tensor(rope[:, n], u, w, ALU.mult)
                dve.drain()
                dve.tensor_tensor(a, rope[:, 0], rope[:, 1], ALU.subtract)
                dve.tensor_tensor(b, rope[:, 2], rope[:, 3], ALU.add)
                dve.drain()
                if not isinstance(t, int) or t:
                    dve.wait_ge(s.turned, t)
                for c in range(2):
                    for r in range(2):
                        dve.tensor_copy(kdup[:, c, r, :], x[:, par, D + c * SHD:D + (c + 1) * SHD])
                dve.drain()
                dve.sem_inc(s.roped, 1)

            def scores(t, par, g):
                dve.wait_ge(s.scores, t * G + g + 1)
                if g >= 2:
                    dve.wait_ge(s.p_turned, t * G + g - 1)
                elif not isinstance(t, int) or t:
                    dve.wait_ge(s.p_turned, t * G + g - 1)
                mk = (mask_even if par == 0 else mask)[:].broadcast_to([P, 4, 256])
                dve.scalar_tensor_tensor(sc[:, g % 2], pS[g % 2][:], SHD ** -0.5, mk, ALU.mult, ALU.add)
                dve.drain()
                dve.sem_inc(s.s_free, 1)
                hs = slice(4 * g, 4 * g + 4)
                dve.tensor_reduce(mx[:, hs].rearrange("p (b a) -> p a b", a=2), sc[:, g % 2].rearrange("p (a b) k -> p a b k", a=2), AX_X, ALU.max)
                dve.drain()
                dve.tensor_tensor(mx[:, hs], mx[:, hs], sink[:, hs], ALU.max)
                dve.drain()
                dve.tensor_scalar(nm[:, hs], mx[:, hs], -1.0, None, ALU.mult)
                dve.tensor_tensor(dsink[:, hs], sink[:, hs], mx[:, hs], ALU.subtract)
                dve.drain()
                dve.sem_inc(s.neg_max, 1)

            def output(t, par):
                dve.wait_ge(s.e_gate, t + 1)
                dve.tensor_tensor(rden[:, :, 0], sums[:, par], esink[:, par], ALU.add)
                dve.drain()
                dve.reciprocal(rden[:], rden[:])
                dve.drain()
                dve.wait_ge(s.pv, t * G + G)
                if not isinstance(t, int) or t:
                    dve.wait_ge(s.stored, t * DMA)
                dve.tensor_tensor(y[:], po[:], rden[:].broadcast_to([P, SH, SHD]), ALU.mult)
                dve.drain()
                yf = y[:].rearrange("p h d -> p (h d)")
                dve.tensor_tensor(yf, yf, eg[:], ALU.mult)
                dve.drain()
                dve.wait_ge((s.g_even, s.g_odd)[par], (t - par) * DMA + 2 * DMA)
                dve.tensor_tensor(yf, yf, ya[:, par], ALU.add)
                dve.drain()
                dve.sem_inc(s.y, 1)

            def block_step(t, par, before=True, behind=True):
                scores(t, par, 0)
                if before:
                    output(t - 1, 1 - par)
                scores(t, par, 1)
                scores(t, par, 2)
                scores(t, par, 3)
                if behind:
                    rope_block(t + 1, 1 - par)
            rope_block(0, 0)
            block_step(0, 0, before=False)
            dve.tensor_copy(mask_even[:], mask[:])
            dve.drain()
            block_step(1, 1)
            with dve.Fori(1, NT // 2 - 1) as i:
                for par in range(2):
                    block_step(2 * i + par, par)
            block_step(NT - 2, 0)
            block_step(NT - 1, 1, behind=False)
            output(NT - 1, 1)


def ffn_up_stage(nc, ident, hi, lo, w_up, conv_w, conv_b, fT):
    with stage(nc, "up", "taps_in", "taps_T", "taps", "w_in", "hi_done", "lo_done", "mm", "act_c", "conv", "gelu", "ps_free") as (block, s, sb, ps):
        raw = sb("raw", [2 * FC, 4, P])
        taps = sb("taps", [P, 4, 2 * FC])
        w_buf = sb("w_buf", [P, 2, KC, P])
        w_hi = sb("w_hi", [P, 2, 2, KC, P], F32R)
        w_lo = sb("w_lo", [P, 2, 2, KC, P], F32R)
        cv = sb("cv", [P, 2, SEQ])
        acc = [[ps(f"acc{i}{j}", [P, SEQ]) for j in range(2)] for i in range(2)]
        w_v = w_up.rearrange("(k p) n -> p k n", p=P)

        def strips(eng, body, behind):
            for j in range(2):
                body(j, j)
                if j:
                    behind(0, 0)
            with eng.Fori(1, FC // 2) as i:
                for par in range(2):
                    body(2 * i + par, par)
                    behind(2 * i + (par - 1), 1 - par)
            behind(FC - 1, 1)

        @block.sync
        def _(sp):
            for tap in range(3):
                sp.dma_start(raw[:, tap, :], conv_w[tap].rearrange("(j p) -> j p", p=P)).then_inc(s.taps_in, DMA)
            sp.dma_start(raw[:, 3, :], conv_b.rearrange("(j p) -> j p", p=P)).then_inc(s.taps_in, DMA)
            with sp.Fori(0, FC) as j:
                sp.wait_ge(s.lo_done, j)
                for side in range(2):
                    sp.dma_start(w_buf[:, side], w_v[:, :, bass.ds(j * P + side * D_FF, P)]).then_inc(s.w_in, DMA)

        @block.tensor
        def _(pe):
            pe.wait_ge(s.taps_in, 4 * DMA)
            for c in range(4):
                op = pe.transpose(acc[0][0][:, c * P:c * P + 2 * FC], raw[:, c, :], ident[:2 * FC, :2 * FC])
            op.then_inc(s.taps_T, 1)
            with pe.Fori(0, FC // 2) as i:
                for par in range(2):
                    pe.wait_ge(s.ps_free, 2 * i + par + 1)
                    pe.wait_ge(s.lo_done, 2 * i + par + 1)
                    for side in range(2):
                        for k in range(KC):
                            for wt, ht in ((w_hi, hi), (w_hi, lo), (w_lo, hi)):
                                for hf in range(2):
                                    cols = slice(hf * 512, (hf + 1) * 512)
                                    op = pe.matmul(acc[par][side][:, cols], wt[:, par, side, k, :], ht[:, k, cols],
                                                   start=k == 0 and wt is w_hi and ht is hi, stop=k == KC - 1 and wt is w_lo)
                        op.then_inc(s.mm, 1)

        @block.scalar
        def _(act):
            act.wait_ge(s.taps, 1)

            def split_hi(j, par):
                act.wait_ge(s.w_in, j * (2 * DMA) + 2 * DMA)
                if not isinstance(j, int):
                    act.wait_ge(s.mm, (j - 1) * 2)
                act.activation(w_hi[:, par], w_buf[:], ACT.Copy).then_inc(s.hi_done, 1)

            def convolve(j, par):
                for side in range(2):
                    act.wait_ge(s.mm, j * 2 + side + 1)
                    act.wait_ge(s.conv, j * 3)
                    col = bass.ds(j + side * FC, 1)
                    act.activation(cv[:, side], acc[par][side][:], ACT.Identity, scale=taps[:, 2, col], bias=taps[:, 3, col]).then_inc(s.act_c, 1)
                    if side == 1:
                        act.wait_ge(s.conv, j * 3 + 1)
                        act.activation(cv[:, 0], cv[:, 0], ACT.Gelu).then_inc(s.gelu, 1)
            strips(act, split_hi, convolve)

        @block.vector
        def _(dve):
            dve.wait_ge(s.taps_T, 1)
            for c in range(4):
                dve.tensor_copy(taps[:, c, :], acc[0][0][:, c * P:c * P + 2 * FC])
            dve.drain()
            dve.sem_inc(s.taps, 1)
            dve.sem_inc(s.ps_free, 2)

            def split_lo(j, par):
                dve.wait_ge(s.hi_done, j + 1)
                dve.tensor_tensor(w_lo[:, par], w_buf[:], w_hi[:, par], ALU.subtract).then_inc(s.lo_done, 1)

            def convolve(j, par):
                for side in range(2):
                    col = bass.ds(j + side * FC, 1)
                    dve.wait_ge(s.act_c, j * 2 + side + 1)
                    for lag, tap in ((1, 1), (2, 0)):
                        dve.scalar_tensor_tensor(cv[:, side, lag:], acc[par][side][:, :SEQ - lag], taps[:, tap, col], cv[:, side, lag:], ALU.mult, ALU.add)
                        dve.drain()
                    dve.sem_inc(s.conv, 1)
                dve.sem_inc(s.ps_free, 1)
                dve.wait_ge(s.gelu, j + 1)
                dve.tensor_tensor(fT[:, bass.ds(j, 1), :].rearrange("p a t -> p (a t)"), cv[:, 0], cv[:, 1], ALU.mult)
                dve.drain()
                dve.sem_inc(s.conv, 1)
            strips(dve, split_lo, convolve)
def turn_stage(nc, name, ident, src, ntiles, hT):
    with stage(nc, name, "x_even", "x_odd", "x_free", "turned", "act_out", "dve_out") as (block, s, sb, ps):
        x = sb("x", [P, 2, D])
        acc = [ps(f"acc{i}") for i in range(4)]

        @block.sync
        def _(sp):
            with sp.Fori(0, ntiles // 2) as i:
                for par in range(2):
                    sp.wait_ge(s.x_free, 2 * i + par + 1)
                    sp.dma_start(x[:, par], src[rows(i * (2 * P) + par * P), :]).then_inc((s.x_even, s.x_odd)[par], DMA)

        @block.tensor
        def _(pe):
            pe.sem_inc(s.x_free, 2)
            pe.sem_inc(s.act_out, 2)
            pe.sem_inc(s.dve_out, 2)
            with pe.Fori(0, ntiles // 2) as i:
                for par in range(2):
                    pe.wait_ge((s.x_even, s.x_odd)[par], i * DMA + DMA)
                    for hf, free in enumerate((s.act_out, s.dve_out)):
                        pe.wait_ge(free, 2 * i + par + 1)
                        for k in range(4):
                            c = hf * 4 + k
                            op = pe.transpose(acc[2 * par + hf][:, k * P:(k + 1) * P], x[:, par, c * P:(c + 1) * P], ident[:])
                        op.then_inc(s.turned, 1)
                    pe.wait_ge(s.turned, (2 * i + par + 1) * 2)
                    pe.sem_inc(s.x_free, 1)

        @block.scalar
        def _(act):
            with act.Fori(0, ntiles // 2) as i:
                for par in range(2):
                    act.wait_ge(s.turned, (2 * i + par) * 2 + 1)
                    act.activation(hT[:, 0:4, rows(i * (2 * P) + par * P)], acc[2 * par][:].rearrange("p (k t) -> p k t", k=4), ACT.Copy).then_inc(s.act_out, 1)

        @block.vector
        def _(dve):
            with dve.Fori(0, ntiles // 2) as i:
                for par in range(2):
                    dve.wait_ge(s.turned, (2 * i + par) * 2 + 2)
                    dve.tensor_copy(hT[:, 4:8, rows(i * (2 * P) + par * P)], acc[2 * par + 1][:].rearrange("p (k t) -> p k t", k=4)).then_inc(s.dve_out, 1)


U_RQ, U_RV, U_RZ, U_WZ, U_SHIFT, SHIFT_W, EVEN_IN = 0, 1024, 1536, 2048, 2560, 1792, 4352
HN, HD = 8, 64
BWD_ORDER = [1, 0] + list(range(NTA - 1, NTC - 1, -1))


def retention_tables():
    nf = 16
    t = np.arange(SEQ)
    inv = (10000.0 ** (-np.arange(nf, dtype=np.float32) / nf)).astype(np.float32)
    ang = np.concatenate([(t // 64).astype(np.float32)[:, None] * inv, (t % 64).astype(np.float32)[:, None] * inv], -1).astype(np.float32)
    rope = np.zeros((ALL, 2, 32), np.float32)
    rope[:CTX, 0] = 1.0
    rope[CTX:, 0], rope[CTX:, 1] = np.cos(ang), np.sin(ang)
    sk, tq = np.arange(P)[:, None], np.arange(P)[None, :]
    dist = np.stack([np.maximum(tq - sk, 0), tq >= sk, np.maximum(sk - tq, 0), sk >= tq], 1).astype(np.float32)
    pos = np.arange(P, dtype=np.float32)
    q_pos = np.stack([pos + 1, P - pos])
    k_pos = np.stack([P - 1 - pos, pos], 1)
    return rope.reshape(ALL, 64), dist, q_pos, k_pos


def retention_stage(nc, ident, U2, decay, t_rope, t_dist, t_qpos, t_kpos, YB2):
    with stage(nc, "ret", "const", "init", "dec", "exps", "dmat", "in0", "in1", "in2", "in3", "in4", "ropes_even", "ropes_odd", "rope_free", "k_dec", "kv",
               "kv_out", "kv_cur", "states", "turned", "qk", "q_dec", "scores", "am", "y_done", "sq", "var", "std", "z_in", "silu", "y", "stored") as (block, s, sb, ps):
        qkv = sb("qkv", [P, NTA, 1536])
        rp = sb("rp", [P, 2, 2, 32])
        dist = sb("dist", [P, 4, P])
        qpos = sb("qpos", [P, 2, P])
        kpos = sb("kpos", [P, 2])
        lg_all = sb("lg_all", [P, 2, HN])
        lg_half = sb("lg_half", [P, 2, 4])
        kdec = sb("kdec", [P, 2, HN, 1])
        gch = sb("gch", [P, 2, 4, 1])
        dm = sb("dm", [P, HN, P])
        dtmp = sb("dtmp", [P, 2, HN, P])
        qdec = sb("qdec", [P, 2, 4, P])
        tmp = sb("tmp", [P, 4, 16, 32])
        kd = sb("kd", [P, 2, 512])
        kv = sb("kv", [P, NTA, 2, 4, P])
        run = sb("run", [P, 2, 4, P])
        qT = sb("qT", [P, 4, P])
        kT = sb("kT", [P, 4, P])
        qd = sb("qd", [P, 2, 4, P])
        am = sb("am", [P, 2, 4, P])
        sq = sb("sq", [P, HN, HD])
        ss = sb("ss", [P, HN])
        rs = sb("rs", [P, HN, 1])
        z = sb("z", [P, 512])
        y = sb("y", [P, HN, HD])
        pkv = [ps(f"pkv{i}", [P, 4, P]) for i in range(2)]
        pq = ps("pq", [P, 4, P])
        pk = ps("pk", [P, 4, P])
        pa = [ps(f"pa{i}", [P, 4, P]) for i in range(2)]
        po = ps("po", [P, HN, HD])
        vcur = sb("vcur", [P, 512])
        cur = sb("cur", [P, 1536])
        st = sb("st", [P, 2, 4, P])
        loaded = (s.in0, s.in1, s.in2, s.in3, s.in4)
        u_v = U2.rearrange("(t p) n -> p t n", p=P)

        @block.sync
        def _(sp):
            for a in range(2):
                half = decay.rearrange("d (b a) -> a d b", a=2)[a]
                sp.dma_start(lg_half[a * HD:(a + 1) * HD], half.partition_broadcast(HD), allow_slow_non_contiguous=True).then_inc(s.const, DMA)
            sp.dma_start(lg_all[:], decay.partition_broadcast(P)).then_inc(s.const, DMA)
            sp.dma_start(dist[:], t_dist).then_inc(s.const, DMA)
            sp.dma_start(qpos[:], t_qpos.partition_broadcast(P)).then_inc(s.const, DMA)
            sp.dma_start(kpos[:], t_kpos).then_inc(s.const, DMA)
            for t in range(5):
                sp.dma_start(qkv[:, 2 * t:2 * t + 2], u_v[:, 2 * t:2 * t + 2, 0:1536]).then_inc(loaded[t], DMA)
            with sp.Fori(0, NTA // 2) as i:
                for par in range(2):
                    sp.wait_ge(s.rope_free, 2 * i + par + 1)
                    sp.dma_start(rp[:, par], t_rope[rows(i * (2 * P) + par * P), :].rearrange("p (c f) -> p c f", c=2)).then_inc((s.ropes_even, s.ropes_odd)[par], DMA)
            with sp.Fori(0, NTA) as i:
                sp.wait_ge(s.y, i)
                sp.dma_start(z[:], U2[rows(i * P), U_RZ:U_WZ]).then_inc(s.z_in, DMA)
                sp.wait_ge(s.y, i + 1)
                sp.dma_start(YB2[rows(i * P), 0:512], y[:].rearrange("p h d -> p (h d)")).then_inc(s.stored, DMA)
            sp.wait_ge(s.stored, NTA * DMA)

        @block.tensor
        def _(pe):
            pe.wait_ge(s.init, 1)
            with pe.Fori(0, NTA) as i:
                pe.wait_ge(s.k_dec, i + 1)
                pe.wait_ge(s.kv_out, i)
                for d in range(2):
                    for b in range(4):
                        op = pe.matmul(pkv[d][:, b, :], kd[:, d, b * P:(b + 1) * P], vcur[:, b * P:(b + 1) * P], start=True, stop=True)
                op.then_inc(s.kv, 1)
            pe.wait_ge(s.states, 1)
            with pe.Fori(0, NTA) as i:
                pe.wait_ge(s.kv_cur, i + 1)
                for b in range(4):
                    pe.transpose(pq[:, b, :], cur[:, b * P:(b + 1) * P], ident[:])
                for b in range(4):
                    op = pe.transpose(pk[:, b, :], cur[:, 512 + b * P:512 + (b + 1) * P], ident[:])
                op.then_inc(s.turned, 1)
                pe.wait_ge(s.qk, i + 1)
                for h in range(HN):
                    base = (h % 2) * HD
                    op = pe.matmul(pa[h % 2][:, h // 2, :], kT[base:base + HD, h // 2, :], qT[base:base + HD, h // 2, :], start=True, stop=True)
                op.then_inc(s.scores, 1)
                pe.wait_ge(s.q_dec, i + 1)
                pe.wait_ge(s.am, i + 1)
                for b in range(4):
                    pair = po[:, 2 * b:2 * b + 2, :].rearrange("p h d -> p (h d)")
                    pe.matmul(pair, qd[:, 0, b, :], st[:, 0, b, :], start=True, stop=False)
                    pe.matmul(pair, qd[:, 1, b, :], st[:, 1, b, :], start=False, stop=False)
                    for a in range(2):
                        h = 2 * b + a
                        op = pe.matmul(po[:, h, :], am[:, a, b, :], cur[:, 1024 + h * HD:1024 + (h + 1) * HD], start=False, stop=a == 1)
                op.then_inc(s.y_done, 1)

        @block.scalar
        def _(act):
            act.wait_ge(s.const, 6 * DMA)
            act.activation(lg_all[:], lg_all[:], ACT.Exp)
            act.activation(lg_half[:], lg_half[:], ACT.Exp).then_inc(s.exps, 1)
            act.wait_ge(s.dec, 1)
            act.activation(kdec[:], kdec[:], ACT.Exp)
            act.activation(gch[:, :, :, 0], lg_half[:], ACT.Exp, scale=float(P))
            for d in range(2):
                for b in range(4):
                    act.activation(qdec[:, d, b, :], qpos[:, d, :], ACT.Exp, scale=lg_half[:, d, b:b + 1])
                for h in range(HN):
                    act.activation(dtmp[:, d, h, :], dist[:, 2 * d, :], ACT.Exp, scale=lg_all[:, d, h:h + 1])
            act.drain()
            act.sem_inc(s.dmat, 1)
            with act.Fori(0, NTA) as i:
                act.wait_ge(s.turned, i + 1)
                act.activation(qT[:], pq[:], ACT.Copy)
                act.activation(kT[:], pk[:], ACT.Copy).then_inc(s.qk, 1)
                act.wait_ge(s.z_in, (i + 1) * DMA)
                act.activation(z[:], z[:], ACT.Silu)
                act.wait_ge(s.y_done, i + 1)
                act.activation(sq[:], po[:], ACT.Square)
                act.drain()
                act.sem_inc(s.sq, 1)
                act.wait_ge(s.var, i + 1)
                act.activation(rs[:, :, 0], ss[:], ACT.Sqrt).then_inc(s.std, 1)

        @block.vector
        def _(dve):
            dve.memset(kv[:], 0.0)
            dve.memset(run[:], 0.0)
            dve.sem_inc(s.rope_free, 2)
            dve.wait_ge(s.exps, 1)
            dve.tensor_scalar(lg_all[:], lg_all[:], -1.0, None, ALU.mult)
            dve.tensor_scalar(lg_half[:], lg_half[:], -1.0, None, ALU.mult)
            dve.drain()
            for d in range(2):
                dve.tensor_scalar(kdec[:, d, :, 0], lg_all[:, d, :], kpos[:, d:d + 1], None, ALU.mult)
            dve.drain()
            dve.sem_inc(s.dec, 1)
            dve.sem_inc(s.init, 1)
            dve.wait_ge(s.dmat, 1)
            dve.tensor_scalar(kdec[:], kdec[:], HD ** -0.5, None, ALU.mult)
            for d in range(2):
                m = dist[:, 2 * d + 1:2 * d + 2, :].broadcast_to([P, HN, P])
                dve.scalar_tensor_tensor(dtmp[:, d], dtmp[:, d], HD ** -0.5, m, ALU.mult, ALU.mult)
            dve.drain()
            for a in range(2):
                dve.tensor_tensor(dm[:, 4 * a:4 * a + 4, :], dtmp[:, 0, a:HN:2, :], dtmp[:, 1, a:HN:2, :], ALU.add)
            for t in range(5):
                dve.wait_ge(loaded[t], DMA)
            with dve.Fori(0, NTA // 2) as i:
                for par in range(2):
                    t = 2 * i + par
                    dve.wait_ge((s.ropes_even, s.ropes_odd)[par], i * DMA + DMA)
                    src = qkv[:, bass.ds(t, 1), :].rearrange("p a n -> p (a n)")
                    heads = src[:, 0:1024].rearrange("p (h d) -> p h d", d=HD)
                    a, b = heads[:, :, 0:32], heads[:, :, 32:64]
                    cos, sin = (rp[:, par, c:c + 1, :].broadcast_to([P, 16, 32]) for c in range(2))
                    for n, (u, w) in enumerate(((a, cos), (b, sin), (a, sin), (b, cos))):
                        dve.tensor_tensor(tmp[:, n], u, w, ALU.mult)
                    dve.drain()
                    dve.sem_inc(s.rope_free, 1)
                    dve.tensor_tensor(a, tmp[:, 0], tmp[:, 1], ALU.subtract)
                    dve.tensor_tensor(b, tmp[:, 2], tmp[:, 3], ALU.add)
                    dve.drain()
                    dve.wait_ge(s.kv, t)
                    for d in range(2):
                        dve.tensor_tensor(kd[:, d].rearrange("p (h d) -> p h d", d=HD), heads[:, 8:16, :], kdec[:, d].broadcast_to([P, HN, HD]), ALU.mult)
                    dve.tensor_copy(vcur[:], src[:, 1024:1536])
                    dve.drain()
                    dve.sem_inc(s.k_dec, 1)
                    dve.wait_ge(s.kv, t + 1)
                    for d in range(2):
                        for q in range(2):
                            e = slice(q * HD, (q + 1) * HD)
                            dve.tensor_copy(kv[e, bass.ds(t, 1), d, :, e].rearrange("p a b e -> p (a b) e"), pkv[d][e, :, e])
                    dve.drain()
                    dve.sem_inc(s.kv_out, 1)
            for d, order in enumerate((range(NTA), BWD_ORDER)):
                for t in order:
                    dve.tensor_tensor(dtmp[:, 0, 0:4, :], run[:, d], gch[:, d].broadcast_to([P, 4, P]), ALU.mult)
                    dve.drain()
                    dve.tensor_tensor(dtmp[:, 0, 0:4, :], dtmp[:, 0, 0:4, :], kv[:, t, d], ALU.add)
                    dve.drain()
                    dve.tensor_copy(kv[:, t, d], run[:, d])
                    dve.drain()
                    dve.tensor_copy(run[:, d], dtmp[:, 0, 0:4, :])
                    dve.drain()
            dve.sem_inc(s.states, 1)
            with dve.Fori(0, NTA) as i:
                dve.wait_ge(s.y_done, i)
                dve.tensor_copy(cur[:], qkv[:, bass.ds(i, 1), :].rearrange("p a n -> p (a n)"))
                dve.tensor_copy(st[:], kv[:, bass.ds(i, 1)].rearrange("p t a b e -> p (t a) b e"))
                dve.drain()
                dve.sem_inc(s.kv_cur, 1)
                dve.wait_ge(s.qk, i + 1)
                for d in range(2):
                    dve.tensor_tensor(qd[:, d], qT[:], qdec[:, d], ALU.mult)
                dve.drain()
                dve.sem_inc(s.q_dec, 1)
                dve.wait_ge(s.scores, i + 1)
                for a in range(2):
                    dve.tensor_tensor(am[:, a], pa[a][:], dm[:, 4 * a:4 * a + 4, :], ALU.mult)
                dve.drain()
                dve.sem_inc(s.am, 1)
                dve.wait_ge(s.sq, i + 1)
                dve.tensor_reduce(ss[:], sq[:], AX_X, ALU.add)
                dve.drain()
                dve.tensor_scalar(ss[:], ss[:], 1.0 / HD, 1e-6, ALU.mult, ALU.add).then_inc(s.var, 1)
                dve.wait_ge(s.std, i + 1)
                dve.reciprocal(rs[:], rs[:])
                dve.drain()
                dve.wait_ge(s.stored, i * DMA)
                dve.tensor_tensor(y[:], po[:], rs[:].broadcast_to([P, HN, HD]), ALU.mult)
                dve.drain()
                dve.tensor_tensor(y[:], y[:], z[:].rearrange("p (h d) -> p h d", d=HD), ALU.mult)
                dve.drain()
                dve.sem_inc(s.y, 1)


def rwkv_edges():
    before, behind = np.ones((P, NTA), np.float32), np.ones((P, NTA), np.float32)
    before[0, 0] = before[0, NTC] = 0.0
    behind[P - 1, NTC - 1] = behind[P - 1, NTA - 1] = 0.0
    return np.stack([before, behind], 1)


def rwkv_prep_stage(nc, ident, U2p, mu, w0, w2, a0, a2, kk_w, ka, rk, t_edges, PC, PD):
    STORES = 3 * DMA
    with stage(nc, "prep", "const", "u_even", "u_odd", "x_free", "edged", "own", "halves", "mixed", "norm_sq", "root", "tanh", "turned", "tT", "lora",
               "lora_b", "sig", "k_done", "rv_even", "rv_odd", "stored_even", "stored_odd") as (block, s, sb, ps):
        x = sb("x", [P, 2, 3, SHIFT_W])
        mu_h = sb("mu_h", [P, SHIFT_W])
        mu_n = sb("mu_n", [P, SHIFT_W])
        rowsb = {n: sb(n, [P, 512]) for n in ("kkr", "kar", "rkr")}
        b_rows = sb("b_rows", [P, 2, 2, 512])
        lw = sb("lw", [P, 2, 512])
        edges = sb("edges", [P, 2, NTA])
        kk = sb("kk", [P, HN, HD])
        sq = sb("sq", [P, HN, HD])
        ss = sb("ss", [P, HN, 1])
        td = sb("td", [P, 2, P])
        tT = sb("tT", [P, 2, P])
        sg = sb("sg", [P, 2, 2, 512])
        okk = sb("okk", [P, 2, 512])
        od = sb("od", [P, 2, 2, 3, 512])
        dots = sb("dots", [P, 2, HN])
        pt = ps("pt", [P, 2, P])
        pl = [[ps(f"pl{i}{d}") for d in range(2)] for i in range(2)]

        def tiles(eng, body, ahead=None):
            def one(t, par, more=True):
                body(t, par, (lambda: ahead(t + 1, 1 - par)) if ahead and more else lambda: None)
            if ahead:
                ahead(0, 0)
            with eng.Fori(0, NTA // 2 - 1) as i:
                for par in range(2):
                    one(2 * i + par, par)
            one(NTA - 2, 0)
            one(NTA - 1, 1, more=False)

        def arrived(eng, t, par):
            eng.wait_ge((s.u_even, s.u_odd)[par], (t - par) * (3 * DMA // 2) + 3 * DMA)

        @block.sync
        def _(sp):
            for dst, src in ((mu_h, mu), (rowsb["kkr"], kk_w), (rowsb["kar"], ka), (rowsb["rkr"], rk)):
                sp.dma_start(dst[:], src.partition_broadcast(P)).then_inc(s.const, DMA)
            for d in range(2):
                sp.dma_start(b_rows[:, 0, d], w0[d].partition_broadcast(P)).then_inc(s.const, DMA)
                sp.dma_start(b_rows[:, 1, d], a0[d].partition_broadcast(P)).then_inc(s.const, DMA)
            sp.dma_start(lw[:, 0], w2.rearrange("d r n -> (d r) n")).then_inc(s.const, DMA)
            sp.dma_start(lw[:, 1], a2.rearrange("d r n -> (d r) n")).then_inc(s.const, DMA)
            sp.dma_start(edges[:], t_edges).then_inc(s.const, DMA)

            def load(i, par, which):
                for n in which:
                    off = (1, 0, 2)[n]
                    sp.dma_start(x[:, par, n], U2p[rows(i * (2 * P) + (par * P + off)), U_SHIFT:EVEN_IN]).then_inc((s.u_even, s.u_odd)[par], DMA)

            def store_rv(i, par):
                tile = rows(i * (2 * P) + par * P)
                sp.wait_ge(s.mixed, 2 * i + par + 1)
                sp.dma_start(PC[tile, 0:512], x[:, par, 0, 0:512]).then_inc((s.rv_even, s.rv_odd)[par], DMA)
                sp.dma_start(PC[tile, 512:1024], x[:, par, 0, 1024:1536]).then_inc((s.rv_even, s.rv_odd)[par], DMA)
            load(0, 0, (0, 1, 2))
            load(0, 1, (0, 1, 2))
            store_rv(0, 0)
            with sp.Fori(1, NTA // 2) as i:
                for par in range(2):
                    store_rv(i - (1 - par), 1 - par)
                    sp.wait_ge((s.rv_even, s.rv_odd)[par], i * (2 * DMA))
                    load(i, par, (1, 2))
                    sp.wait_ge(s.k_done, 2 * i + (par - 1))
                    load(i, par, (0,))
            store_rv(NTA // 2 - 1, 1)
            sp.wait_ge(s.rv_even, NTA // 2 * 2 * DMA)
            sp.wait_ge(s.rv_odd, NTA // 2 * 2 * DMA)

        @block.gpsimd
        def _(pool):
            pool.wait_ge(s.const, 11 * DMA)
            pool.tensor_scalar(mu_n[:], mu_h[:], -1.0, 1.0, ALU.mult, ALU.add)
            pool.drain()
            pool.tensor_scalar(mu_h[:], mu_h[:], 0.5, None, ALU.mult)
            pool.drain()
            pool.sem_inc(s.halves, 1)

            def own(t, par):
                arrived(pool, t, par)
                pool.tensor_tensor(x[:, par, 0], x[:, par, 0], mu_n[:], ALU.mult).then_inc(s.own, 1)

            def store(t, par, ahead):
                ahead()
                pool.wait_ge(s.k_done, t + 1)
                done = (s.stored_even, s.stored_odd)[par]
                pool.dma_start(PC[rows(t * P), 1024:1536], okk[:, par]).then_inc(done, DMA)
                pool.dma_start(PC[rows(t * P), 1536:], dots[:, par]).then_inc(done, DMA)
                pool.dma_start(PD[:, rows(t * P), :].rearrange("d p n -> p d n"), od[:, par].rearrange("p d a n -> p d (a n)")).then_inc(done, DMA)
            tiles(pool, store, own)
            pool.wait_ge(s.stored_even, NTA // 2 * STORES)
            pool.wait_ge(s.stored_odd, NTA // 2 * STORES)

        @block.tensor
        def _(pe):
            pe.wait_ge(s.const, 11 * DMA)
            with pe.Fori(0, NTA) as i:
                pe.wait_ge(s.tanh, i + 1)
                for n in range(2):
                    op = pe.transpose(pt[:, n, :], td[:, n, :], ident[:])
                op.then_inc(s.turned, 1)
                pe.wait_ge(s.tT, i + 1)
                pe.wait_ge(s.lora_b, i)
                for d in range(2):
                    base = d * 64
                    for n in range(2):
                        op = pe.matmul(pl[n][d][:], tT[base:base + 64, n, :], lw[base:base + 64, n, :], start=True, stop=True)
                op.then_inc(s.lora, 1)

        @block.scalar
        def _(act):
            act.wait_ge(s.const, 11 * DMA)

            def edge(t, par):
                arrived(act, t, par)
                act.activation(x[:, par, 1], x[:, par, 1], ACT.Copy, scale=edges[:, 0, bass.ds(t, 1)]).then_inc(s.edged, 1)

            def body(t, par, ahead):
                act.wait_ge(s.mixed, t + 1)
                act.activation(td[:, 0, :], x[:, par, 0, 1536:1664], ACT.Tanh)
                act.activation(td[:, 1, :], x[:, par, 0, 1664:1792], ACT.Copy)
                act.drain()
                act.sem_inc(s.tanh, 1)
                act.wait_ge(s.turned, t + 1)
                act.activation(tT[:], pt[:], ACT.Copy).then_inc(s.tT, 1)
                ahead()
                act.wait_ge(s.norm_sq, t + 1)
                act.activation(ss[:], ss[:], ACT.Sqrt).then_inc(s.root, 1)
                act.wait_ge(s.lora_b, t + 1)
                act.activation(sg[:], sg[:], ACT.Sigmoid).then_inc(s.sig, 1)
            tiles(act, body, edge)

        @block.vector
        def _(dve):
            dve.wait_ge(s.const, 11 * DMA)
            dve.wait_ge(s.halves, 1)

            def mix(t, par):
                arrived(dve, t, par)
                dve.wait_ge(s.edged, t + 1)
                dve.scalar_tensor_tensor(x[:, par, 1], x[:, par, 2], edges[:, 1, bass.ds(t, 1)], x[:, par, 1], ALU.mult, ALU.add)
                dve.drain()
                dve.tensor_tensor(x[:, par, 1], x[:, par, 1], mu_h[:], ALU.mult)
                dve.drain()
                dve.wait_ge(s.own, t + 1)
                dve.tensor_tensor(x[:, par, 0], x[:, par, 0], x[:, par, 1], ALU.add).then_inc(s.mixed, 1)

            def body(t, par, ahead):
                r, k = x[:, par, 0, 0:512], x[:, par, 0, 512:1024]
                kf = kk[:].rearrange("p h d -> p (h d)")
                dve.wait_ge(s.mixed, t + 1)
                dve.tensor_tensor(kf, k, rowsb["kkr"][:], ALU.mult)
                dve.drain()
                dve.tensor_tensor(sq[:], kk[:], kk[:], ALU.mult)
                dve.drain()
                dve.tensor_reduce(ss[:, :, 0], sq[:], AX_X, ALU.add).then_inc(s.norm_sq, 1)
                ahead()
                dve.wait_ge(s.root, t + 1)
                dve.tensor_scalar(ss[:], ss[:], 1e-12, None, ALU.max)
                dve.drain()
                dve.reciprocal(ss[:], ss[:])
                dve.drain()
                if not isinstance(t, int) or t >= 2:
                    dve.wait_ge((s.stored_even, s.stored_odd)[par], (t - par) * (STORES // 2))
                dve.tensor_tensor(okk[:, par].rearrange("p (h d) -> p h d", d=HD), kk[:], ss[:].broadcast_to([P, HN, HD]), ALU.mult)
                dve.wait_ge(s.lora, t + 1)
                for n in range(2):
                    for d in range(2):
                        dve.tensor_tensor(sg[:, n, d], pl[n][d][:], b_rows[:, n, d], ALU.add)
                dve.drain()
                dve.sem_inc(s.lora_b, 1)
                dve.tensor_tensor(sq[:].rearrange("p h d -> p (h d)"), r, rowsb["rkr"][:], ALU.mult)
                dve.wait_ge(s.sig, t + 1)
                dve.tensor_scalar(od[:, par, :, 0], sg[:, 0], -math.exp(-0.5), None, ALU.mult)
                for d in range(2):
                    dve.tensor_tensor(od[:, par, d, 2], okk[:, par], sg[:, 1, d], ALU.mult)
                dve.drain()
                for d in range(2):
                    dve.scalar_tensor_tensor(sg[:, 1, d], sg[:, 1, d], 1.0, rowsb["kar"][:], ALU.subtract, ALU.mult)
                dve.drain()
                for d in range(2):
                    dve.scalar_tensor_tensor(od[:, par, d, 1], sg[:, 1, d], 1.0, k, ALU.add, ALU.mult)
                dve.drain()
                dve.tensor_tensor(kf, od[:, par, 0, 1], od[:, par, 1, 1], ALU.add)
                dve.drain()
                dve.tensor_tensor(kk[:], kk[:], sq[:], ALU.mult)
                dve.drain()
                dve.tensor_reduce(dots[:, par], kk[:], AX_X, ALU.add).then_inc(s.k_done, 1)
                dve.drain()
            tiles(dve, body, mix)


def rwkv_tables():
    j, t = np.arange(P)[:, None], np.arange(P)[None, :]
    sums = np.zeros((2, P, 3, P), np.float32)
    ends = np.zeros((2, P, 2), np.float32)
    pairs = np.zeros((2, P, 4, P), np.uint32)
    level = np.zeros((2, P, 8, P), np.float32)
    for d in range(2):
        upto = (j <= t) if d == 0 else (j >= t)
        before = (j < t) if d == 0 else (j > t)
        mid = (j < 64) if d == 0 else (j >= 64)
        sums[d, :, 0] = upto.astype(np.float32) - mid
        sums[d, :, 1] = before.astype(np.float32) - mid
        sums[d, :, 2] = 1.0 - upto
        ends[d, :, 0], ends[d, :, 1] = 1.0, mid[:, 0]
        for n, m in enumerate((before, upto, before, upto)):
            pairs[d, :, n] = m
        for lv in range(7):
            b = 1 << lv
            same = (j // (2 * b)) == (t // (2 * b))
            late = ((j // b) % 2) == (1 - d)
            early = ((t // b) % 2) == d
            level[d, :, lv] = same & late & early
        level[d, :, 7] = level[d, :, 0].T
    return sums, ends, pairs, level


def rwkv_stage(nc, ident, PC, PD, t_sums, t_ends, t_pairs, t_level, RW):
    LV = 7
    UNITS = 2 * NTA
    PLAN = {("X", 1): "front_sums", ("T", 1): "back_right", ("X", 2): "front_late", ("T", 2): "back_u", ("X", 3): "back_out",
            ("T", 3): "front_turn0", ("X", 4): "front_turn1", ("T", 4): "front_pairs0", ("X", 5): "front_pairs1",
            ("T", 5): "front_pairs2", ("X", 6): "front_pairs3"}

    def wait(eng, sem, count):
        if not isinstance(count, int) or count > 0:
            eng.wait_ge(sem, count)

    def in_order(eng, part):
        def step(i, d, front=True, back=True):
            n = 2 * i + d
            after = (n + 1, i + d, 1 - d)
            before = (n - 1, i + d - 1, 1 - d)
            part("level0", n, i, d)
            for lv in range(1, LV):
                for kind in "XT":
                    part(kind + str(lv), n, i, d)
                    what = PLAN.get((kind, lv), "none")
                    if front and what.startswith("front"):
                        part(what, *after)
                    if back and what.startswith("back"):
                        part(what, *before)
        for what in PLAN.values():
            if what.startswith("front"):
                part(what, 0, 0, 0)
        step(0, 0, back=False)
        step(0, 1)
        with eng.Fori(1, NTA - 1) as i:
            step(i, 0)
            step(i, 1)
        step(NTA - 1, 0)
        step(NTA - 1, 1, front=False)
        for what in PLAN.values():
            if what.startswith("back"):
                part(what, UNITS - 1, NTA - 1, 1)

    def tokens(i, d):
        return rows(i * P) if d == 0 else rows(((i * (NTA - 1) + (NTC - 1)) % NTA) * P)

    with stage(nc, "rwkv", "const", "init", "in_f", "in_b", "v_f", "v_b", "gsum", "exps", "late", "ew", "turned", "t_act", "amat", "a_out", "mc",
               "x_mm", "x_out", "t_mm", "t_out", "r_mm", "r_out", "u_mm", "u_out", "o_mm", "o_out", "m_mm", "m_out", "stored_f", "stored_b") as (block, s, sb, ps):
        xr = sb("xr", [P, 2, 512])
        xk = sb("xk", [P, 2, 512])
        v = sb("v", [P, 2, 512])
        xd = sb("xd", [P, 2, 3, 512])
        sums = sb("sums", [P, 2, 3, P])
        ends = sb("ends", [P, 2, 2])
        pairs = sb("pairs", [P, 2, 512], U32)
        level = sb("level", [P, 2, 8, P])
        ex = sb("ex", [P, 4, 512])
        ecol = sb("ecol", [P, 4, 2])
        ew = sb("ew", [P, 4, 512])
        lat = sb("lat", [P, 2, 2, 512])
        arT = sb("arT", [P, 2, 4, 2, P])
        bT = sb("bT", [P, 4, P])
        kT = sb("kT", [P, 4, P])
        A = sb("A", [P, 2, HN, 4, P])
        T = sb("T", [P, HN, P])
        TT = sb("TT", [P, 2, HN, P])
        X = sb("X", [P, HN, P])
        M = sb("M", [P, 2, 4, P])
        Mc = sb("Mc", [P, 2, 4, P])
        R = sb("R", [P, 512])
        U = sb("U", [P, 512])
        O = sb("O", [P, 2, 512])
        idle = sb("idle", [P, HN])
        w = [ps(f"w{i}") for i in range(4)]
        f = [ps(f"f{i}") for i in range(2)]
        ru = ps("ru")
        om = ps("om")
        C = lambda bank, h: bank[:, (h % 4) * P:(h % 4 + 1) * P]
        by_block = lambda bank: bank[:].rearrange("p (b t) -> p b t", b=4)

        @block.sync
        def _(sp):
            sp.dma_start(sums[:], t_sums.rearrange("d p n t -> p d n t")).then_inc(s.const, DMA)
            sp.dma_start(ends[:], t_ends.rearrange("d p n -> p d n")).then_inc(s.const, DMA)
            sp.dma_start(pairs[:], t_pairs.rearrange("d p n t -> p d (n t)")).then_inc(s.const, DMA)
            sp.dma_start(level[:], t_level.rearrange("d p n t -> p d n t")).then_inc(s.const, DMA)

            def load(i, d):
                n = 2 * i + d
                tile = tokens(i, d)
                wait(sp, s.gsum, (n - 1) * 2)
                wait(sp, s.ew, n - 1)
                wait(sp, s.late, n - 1)
                done = (s.in_f, s.in_b)[d]
                sp.dma_start(xr[:, d], PC[tile, 0:512]).then_inc(done, DMA)
                sp.dma_start(xk[:, d], PC[tile, 1024:1536]).then_inc(done, DMA)
                sp.dma_start(xd[:, d].rearrange("p a n -> p (a n)"), PD[d, tile, :]).then_inc(done, DMA)
                wait(sp, s.m_mm, n - 1)
                wait(sp, s.o_mm, n - 1)
                sp.dma_start(v[:, d], PC[tile, 512:1024]).then_inc((s.v_f, s.v_b)[d], DMA)
            load(0, 0)
            load(0, 1)
            with sp.Fori(1, NTA) as i:
                load(i, 0)
                load(i, 1)

        @block.gpsimd
        def _(pool):
            pool.wait_ge(s.const, 4 * DMA)

            def part(what, n, i, d):
                if what == "front_late":
                    pool.wait_ge((s.in_f, s.in_b)[d], (i + 1) * (3 * DMA))
                    pool.wait_ge(s.exps, 2 * n + 2)
                    wait(pool, s.m_mm, n - 1)
                    pool.tensor_tensor(lat[:, d, 0], xd[:, d, 2], ex[:, 3], ALU.mult)
                    pool.tensor_tensor(lat[:, d, 1], xd[:, d, 1], ex[:, 3], ALU.mult)
                    pool.drain()
                    pool.sem_inc(s.late, 1)
                if what == "back_out":
                    pool.wait_ge(s.o_out, n + 1)
                    pool.dma_start(RW[d, tokens(i, d), :], O[:, d]).then_inc((s.stored_f, s.stored_b)[d], DMA)
            in_order(pool, part)
            pool.wait_ge(s.stored_f, NTA * DMA)
            pool.wait_ge(s.stored_b, NTA * DMA)

        @block.tensor
        def _(pe):
            pe.wait_ge(s.const, 4 * DMA)
            pe.wait_ge(s.init, 1)

            def part(what, n, i, d):
                if what == "front_sums":
                    pe.wait_ge((s.in_f, s.in_b)[d], (i + 1) * (3 * DMA))
                    wait(pe, s.a_out, n * HN)
                    pe.matmul(f[0][:], sums[:, d, 0, :], xd[:, d, 0, :], start=True, stop=True)
                    pe.matmul(f[1][:], sums[:, d, 1, :], xd[:, d, 0, :], start=True, stop=True).then_inc(s.gsum, 1)
                if what == "front_late":
                    pe.wait_ge(s.exps, 2 * n + 1)
                    pe.matmul(f[0][:], sums[:, d, 2, :], xd[:, d, 0, :], start=True, stop=True)
                    for b in range(4):
                        op = pe.matmul(f[1][:, 2 * b:2 * b + 2], xd[:, d, 0, b * P:(b + 1) * P], ends[:, d, :], start=True, stop=True)
                    op.then_inc(s.gsum, 1)
                if what.startswith("front_turn"):
                    first = 2 * int(what[-1])
                    if first == 0:
                        pe.wait_ge(s.ew, n + 1)
                        pe.wait_ge(s.exps, 2 * n + 2)
                    for q in range(2):
                        if first:
                            pe.wait_ge(s.t_act, 4 * n + q + 1)
                        for b in range(4):
                            op = pe.transpose(f[q][:, b * P:(b + 1) * P], ew[:, first + q, b * P:(b + 1) * P], ident[:])
                        op.then_inc(s.turned, 1)
                if what.startswith("front_pairs"):
                    first = 2 * int(what[-1])
                    if first == 0:
                        pe.wait_ge(s.t_act, 4 * n + 4)
                    else:
                        pe.wait_ge(s.a_out, n * HN + first)
                    for h in (first, first + 1):
                        base = (h % 2) * HD
                        rhs = arT[base:base + HD, d, h // 2].rearrange("p a t -> p (a t)")
                        pe.matmul(f[h % 2][:, 0:256], bT[base:base + HD, h // 2, :], rhs, start=True, stop=True)
                        pe.matmul(f[h % 2][:, 256:512], kT[base:base + HD, h // 2, :], rhs, start=True, stop=True).then_inc(s.amat, 1)
                if what == "level0":
                    pe.wait_ge(s.a_out, n * HN + HN)
                    wait(pe, s.t_out, n * (2 * LV))
                    for q in range(2):
                        for h in range(4 * q, 4 * q + 4):
                            op = pe.matmul(C(w[q], h), A[:, d, h, 0, :], ident[:], start=True, stop=True)
                        op.then_inc(s.x_mm, 1)
                if what[0] == "X":
                    lv = int(what[1])
                    for q in range(2):
                        pe.wait_ge(s.t_out, n * (2 * LV) + 2 * lv - 1 + q)
                        for h in range(4 * q, 4 * q + 4):
                            op = pe.matmul(C(w[q], h), A[:, d, h, 0, :], T[:, h, :], start=True, stop=True)
                        op.then_inc(s.x_mm, 1)
                if what[0] == "T":
                    lv = int(what[1])
                    for q in range(2):
                        pe.wait_ge(s.x_out, n * (2 * LV) + 2 * lv + 1 + q)
                        for h in range(4 * q, 4 * q + 4):
                            if lv < LV - 1:
                                pe.matmul(C(w[q], h), TT[:, d, h, :], X[:, h, :], start=True, stop=True)
                            op = pe.matmul(C(w[2 + q], h), X[:, h, :], TT[:, d, h, :], start=True, stop=True)
                        op.then_inc(s.t_mm, 1)
                if what == "back_right":
                    pe.wait_ge(s.mc, n + 1)
                    pe.wait_ge((s.v_f, s.v_b)[d], (i + 1) * DMA)
                    wait(pe, s.o_out, n)
                    for b in range(4):
                        pe.matmul(ru[:, b * P:(b + 1) * P], arT[:, d, b, 0, :], Mc[:, d, b, :], start=True, stop=False)
                        for h in (2 * b, 2 * b + 1):
                            op = pe.matmul(ru[:, h * HD:(h + 1) * HD], A[:, d, h, 2, :], v[:, d, h * HD:(h + 1) * HD], start=False, stop=h % 2 == 1)
                    op.then_inc(s.r_mm, 1)
                if what == "back_u":
                    pe.wait_ge(s.t_out, n * (2 * LV) + 2 * LV)
                    pe.wait_ge(s.r_out, n + 1)
                    for h in range(HN):
                        op = pe.matmul(ru[:, h * HD:(h + 1) * HD], TT[:, d, h, :], R[:, h * HD:(h + 1) * HD], start=True, stop=True)
                    op.then_inc(s.u_mm, 1)
                if what == "back_out":
                    pe.wait_ge(s.u_out, n + 1)
                    pe.wait_ge(s.late, n + 1)
                    wait(pe, s.m_out, n)
                    for b in range(4):
                        pe.matmul(om[:, b * P:(b + 1) * P], lat[:, d, 0, b * P:(b + 1) * P], U[:, b * P:(b + 1) * P], start=True, stop=False)
                        op = pe.matmul(om[:, b * P:(b + 1) * P], lat[:, d, 1, b * P:(b + 1) * P], v[:, d, b * P:(b + 1) * P], start=False, stop=True)
                    op.then_inc(s.m_mm, 1)
                    for b in range(4):
                        pe.matmul(ru[:, b * P:(b + 1) * P], arT[:, d, b, 1, :], Mc[:, d, b, :], start=True, stop=False)
                        for h in (2 * b, 2 * b + 1):
                            pe.matmul(ru[:, h * HD:(h + 1) * HD], A[:, d, h, 1, :], U[:, h * HD:(h + 1) * HD], start=False, stop=False)
                            op = pe.matmul(ru[:, h * HD:(h + 1) * HD], A[:, d, h, 3, :], v[:, d, h * HD:(h + 1) * HD], start=False, stop=h % 2 == 1)
                    op.then_inc(s.o_mm, 1)
            in_order(pe, part)

        @block.scalar
        def _(act):
            def part(what, n, i, d):
                if what == "front_sums":
                    act.wait_ge(s.gsum, 2 * n + 1)
                    wait(act, s.ew, n)
                    wait(act, s.late, n)
                    act.activation(ex[:, 0], f[0][:], ACT.Exp)
                    act.activation(ex[:, 1], f[0][:], ACT.Exp, scale=-1.0)
                    act.activation(ex[:, 2], f[1][:], ACT.Exp)
                    act.drain()
                    act.sem_inc(s.exps, 1)
                if what == "front_late":
                    act.wait_ge(s.gsum, 2 * n + 2)
                    wait(act, s.mc, n)
                    act.activation(ex[:, 3], f[0][:], ACT.Exp)
                    act.activation(ecol[:], f[1][:, 0:8].rearrange("p (b n) -> p b n", n=2), ACT.Exp)
                    act.drain()
                    act.sem_inc(s.exps, 1)
                if what == "front_turn0":
                    wait(act, s.o_mm, n - 1)
                    for q in range(2):
                        act.wait_ge(s.turned, 4 * n + q + 1)
                        act.activation(arT[:, d, :, q, :], by_block(f[q]), ACT.Copy).then_inc(s.t_act, 1)
                if what == "front_turn1":
                    wait(act, s.amat, n * HN)
                    for q, dst in enumerate((bT, kT)):
                        act.wait_ge(s.turned, 4 * n + q + 3)
                        act.activation(dst[:], by_block(f[q]), ACT.Copy).then_inc(s.t_act, 1)
                if what == "back_right":
                    act.wait_ge(s.r_mm, n + 1)
                    act.activation(R[:], ru[:], ACT.Copy).then_inc(s.r_out, 1)
                if what == "back_u":
                    act.wait_ge(s.u_mm, n + 1)
                    act.activation(U[:], ru[:], ACT.Copy).then_inc(s.u_out, 1)
                if what == "back_out":
                    act.wait_ge(s.o_mm, n + 1)
                    wait(act, (s.stored_f, s.stored_b)[d], i * DMA)
                    act.activation(O[:, d], ru[:], ACT.Copy).then_inc(s.o_out, 1)
            in_order(act, part)

        @block.vector
        def _(dve):
            dve.memset(A[:], 0.0)
            dve.memset(M[:], 0.0)
            dve.drain()
            dve.sem_inc(s.init, 1)
            dve.wait_ge(s.const, 4 * DMA)
            by_head = lambda bank: bank[:].rearrange("p (h t) -> p h t", h=4)
            idb = ident[:].rearrange("p (a t) -> p a t", a=1).broadcast_to([P, 4, P])

            def part(what, n, i, d):
                if what == "front_late":
                    dve.wait_ge((s.in_f, s.in_b)[d], (i + 1) * (3 * DMA))
                    dve.wait_ge(s.exps, 2 * n + 2)
                    wait(dve, s.turned, 4 * n)
                    dve.scalar_tensor_tensor(ew[:, 0], xk[:, d], -1.0, ex[:, 2], ALU.mult, ALU.mult)
                    dve.tensor_tensor(ew[:, 1], xr[:, d], ex[:, 0], ALU.mult)
                    dve.tensor_tensor(ew[:, 2], xd[:, d, 2], ex[:, 1], ALU.mult)
                    dve.tensor_tensor(ew[:, 3], xd[:, d, 1], ex[:, 1], ALU.mult)
                    dve.drain()
                    dve.sem_inc(s.ew, 1)
                if what == "back_out":
                    dve.wait_ge(s.m_mm, n + 1)
                    for a in range(2):
                        e = slice(a * HD, (a + 1) * HD)
                        dve.tensor_tensor(M[e, d, :, e], M[e, d, :, e], by_block(om)[e, :, e], ALU.add)
                    dve.drain()
                    dve.sem_inc(s.m_out, 1)
                if what == "front_turn0":
                    wait(dve, s.o_mm, n - 1)
                    dve.tensor_tensor(Mc[:, d], M[:, d], ecol[:, :, 1:2].broadcast_to([P, 4, P]), ALU.mult)
                    dve.drain()
                    dve.tensor_tensor(M[:, d], M[:, d], ecol[:, :, 0:1].broadcast_to([P, 4, P]), ALU.mult)
                    dve.drain()
                    dve.sem_inc(s.mc, 1)
                if what.startswith("front_pairs"):
                    for h in range(2 * int(what[-1]), 2 * int(what[-1]) + 2):
                        dve.wait_ge(s.amat, n * HN + h + 1)
                        dve.memset(idle[:, h:h + 1], 0.0)
                        dve.copy_predicated(A[:, d, h].rearrange("p a t -> p (a t)"), pairs[:, d], f[h % 2][:]).then_inc(s.a_out, 1)
                if what == "level0":
                    wait(dve, s.u_mm, n - 1)
                    for q in range(2):
                        hs = slice(4 * q, 4 * q + 4)
                        m0 = level[:, d, 0:1, :].broadcast_to([P, 4, P])
                        m7 = level[:, d, 7:8, :].broadcast_to([P, 4, P])
                        dve.wait_ge(s.x_mm, n * (2 * LV) + q + 1)
                        dve.tensor_tensor(T[:, hs, :], by_head(w[q]), m0, ALU.mult)
                        dve.tensor_tensor(TT[:, d, hs, :], A[:, d, hs, 0, :], m7, ALU.mult)
                        dve.drain()
                        dve.tensor_tensor(T[:, hs, :], T[:, hs, :], idb, ALU.add)
                        dve.tensor_tensor(TT[:, d, hs, :], TT[:, d, hs, :], idb, ALU.add)
                        dve.drain()
                        dve.sem_inc(s.x_out, 1)
                        dve.sem_inc(s.t_out, 1)
                if what[0] == "X":
                    lv = int(what[1])
                    for q in range(2):
                        hs = slice(4 * q, 4 * q + 4)
                        dve.wait_ge(s.x_mm, n * (2 * LV) + 2 * lv + q + 1)
                        ml = level[:, d, lv:lv + 1, :].broadcast_to([P, 4, P])
                        dve.tensor_tensor(X[:, hs, :], by_head(w[q]), ml, ALU.mult).then_inc(s.x_out, 1)
                if what[0] == "T":
                    lv = int(what[1])
                    for q in range(2):
                        hs = slice(4 * q, 4 * q + 4)
                        dve.wait_ge(s.t_mm, n * (2 * LV - 2) + 2 * (lv - 1) + q + 1)
                        if lv < LV - 1:
                            dve.tensor_tensor(T[:, hs, :], by_head(w[q]), T[:, hs, :], ALU.add)
                        dve.tensor_tensor(TT[:, d, hs, :], by_head(w[2 + q]), TT[:, d, hs, :], ALU.add)
                        dve.drain()
                        dve.sem_inc(s.t_out, 1)
            in_order(dve, part)


def rwkv_out_stage(nc, RW, PC, U2, ln_w, ln_b, YB2):
    with stage(nc, "rwo", "const", "x_in", "y_done", "var", "std", "silu", "stored") as (block, s, sb, ps):
        x = sb("x", [P, 2, 512])
        v = sb("v", [P, HN, HD])
        dot = sb("dot", [P, HN, 1])
        z = sb("z", [P, 512])
        w_r = sb("w_r", [P, 512])
        b_r = sb("b_r", [P, 512])
        sq = sb("sq", [P, HN, HD])
        mean = sb("mean", [P, HN, 1])
        var = sb("var", [P, HN, 1])
        y = sb("y", [P, 512])

        @block.sync
        def _(sp):
            sp.dma_start(w_r[:], ln_w.partition_broadcast(P)).then_inc(s.const, DMA)
            sp.dma_start(b_r[:], ln_b.partition_broadcast(P)).then_inc(s.const, DMA)
            with sp.Fori(0, NTA) as i:
                t = rows(i * P)
                sp.wait_ge(s.y_done, i)
                for d in range(2):
                    sp.dma_start(x[:, d], RW[d, t, :]).then_inc(s.x_in, DMA)
                sp.dma_start(v[:].rearrange("p h d -> p (h d)"), PC[t, 512:1024]).then_inc(s.x_in, DMA)
                sp.dma_start(dot[:, :, 0], PC[t, 1536:1536 + HN]).then_inc(s.x_in, DMA)
                sp.dma_start(z[:], U2[t, U_WZ:U_SHIFT]).then_inc(s.x_in, DMA)
                sp.wait_ge(s.y_done, i + 1)
                sp.dma_start(YB2[t, 512:1024], y[:]).then_inc(s.stored, DMA)
            sp.wait_ge(s.stored, NTA * DMA)

        @block.scalar
        def _(act):
            with act.Fori(0, NTA) as i:
                act.wait_ge(s.x_in, (i + 1) * (5 * DMA))
                act.activation(z[:], z[:], ACT.Silu).then_inc(s.silu, 1)
                act.wait_ge(s.var, i + 1)
                act.activation(var[:], var[:], ACT.Sqrt).then_inc(s.std, 1)

        @block.vector
        def _(dve):
            dve.wait_ge(s.const, 2 * DMA)
            with dve.Fori(0, NTA) as i:
                dve.wait_ge(s.x_in, (i + 1) * (5 * DMA))
                h0 = x[:, 0].rearrange("p (h d) -> p h d", d=HD)
                dve.tensor_tensor(x[:, 0], x[:, 0], x[:, 1], ALU.add)
                dve.tensor_tensor(v[:], v[:], dot[:].broadcast_to([P, HN, HD]), ALU.mult)
                dve.drain()
                dve.tensor_reduce(mean[:, :, 0], h0, AX_X, ALU.add)
                dve.drain()
                dve.tensor_scalar(mean[:], mean[:], 1.0 / HD, None, ALU.mult)
                dve.drain()
                dve.tensor_tensor(h0, h0, mean[:].broadcast_to([P, HN, HD]), ALU.subtract)
                dve.drain()
                dve.tensor_tensor(sq[:], h0, h0, ALU.mult)
                dve.drain()
                dve.tensor_reduce(var[:, :, 0], sq[:], AX_X, ALU.add)
                dve.drain()
                dve.tensor_scalar(var[:], var[:], 1.0 / HD, 64e-5, ALU.mult, ALU.add).then_inc(s.var, 1)
                dve.wait_ge(s.std, i + 1)
                dve.reciprocal(var[:], var[:])
                dve.drain()
                dve.tensor_tensor(h0, h0, var[:].broadcast_to([P, HN, HD]), ALU.mult)
                dve.drain()
                dve.tensor_tensor(x[:, 0], x[:, 0], w_r[:], ALU.mult)
                dve.drain()
                dve.tensor_tensor(x[:, 0], x[:, 0], b_r[:], ALU.add)
                dve.drain()
                dve.tensor_tensor(x[:, 0], x[:, 0], v[:].rearrange("p h d -> p (h d)"), ALU.add)
                dve.drain()
                dve.wait_ge(s.silu, i + 1)
                dve.wait_ge(s.stored, i * DMA)
                dve.tensor_tensor(y[:], x[:, 0], z[:], ALU.mult).then_inc(s.y_done, 1)
O_HY, O_HZ, O_NQ, O_NK, O_NV, O_NZ, ODD_IN = 0, 1536, 2048, 2560, 3072, 3584, 4096
HYW = 512
NFREQ = SEQ
HALF = NFREQ // 2
FCH = HALF // P
GRID_C, GRID_R = 64, 16
WIN_R, WIN_C = 8, 16


def hyena_tables():
    n = np.arange(SEQ, dtype=np.float64)
    t = np.linspace(0.0, 1.0, SEQ, dtype=np.float32)[:, None]
    bands = np.linspace(1e-4, 15, 16, dtype=np.float32)
    ang = (np.float32(2.0 * math.pi / SEQ) * np.arange(SEQ, dtype=np.float32)[:, None] * bands[None]).astype(np.float32)
    feats = np.concatenate([t, np.cos(ang), -np.sin(ang)], -1).astype(np.float32).T.copy()
    deltas = np.abs(np.linspace(math.log(1e-2) / 1.5, math.log(1e-2) / 0.3, HYW, dtype=np.float32))
    decay = np.exp(-t * deltas).astype(np.float32)
    th = math.pi * ((np.outer(n, 2 * np.arange(HALF) + 1)) % 4096) / 2048
    both = np.stack([np.cos(th), np.sin(th)], 1).astype(np.float32)
    both = both.reshape(NT // 2, P, 2, 2, FCH, P)
    fwd = both.transpose(4, 1, 2, 0, 3, 5).reshape(FCH, P, NT, 2, P)
    inv = both.transpose(0, 5, 2, 4, 3, 1)
    return feats, decay, np.ascontiguousarray(fwd), np.ascontiguousarray(inv)


def edges_of_sequence():
    before, behind = np.ones((P, NT), np.float32), np.ones((P, NT), np.float32)
    before[0, 0] = 0.0
    behind[P - 1, NT - 1] = 0.0
    return np.stack([before, behind], 1)


def short_conv_stage(nc, U3p, cw, cb, t_edges, VX):
    with stage(nc, "sc", "const", "x_even", "x_odd", "x_free", "y_done", "out_even", "out_odd") as (block, s, sb, ps):
        W = 3 * HYW
        x = sb("x", [P, 2, 3, W])
        w = sb("w", [P, 4, W])
        edges = sb("edges", [P, 2, NT])

        @block.sync
        def _(sp):
            for n in range(3):
                sp.dma_start(w[:, n], cw[n].partition_broadcast(P)).then_inc(s.const, DMA)
            sp.dma_start(w[:, 3], cb.partition_broadcast(P)).then_inc(s.const, DMA)
            sp.dma_start(edges[:], t_edges).then_inc(s.const, DMA)
            with sp.Fori(0, NT // 2) as i:
                for par in range(2):
                    sp.wait_ge((s.out_even, s.out_odd)[par], i * DMA)
                    for n in range(3):
                        sp.dma_start(x[:, par, n], U3p[rows(i * (2 * P) + (par * P + n)), 0:W]).then_inc((s.x_even, s.x_odd)[par], DMA)

        @block.scalar
        def _(act):
            with act.Fori(0, NT // 2) as i:
                for par in range(2):
                    act.wait_ge(s.y_done, 2 * i + par + 1)
                    act.dma_start(VX[rows(i * (2 * P) + par * P), :], x[:, par, 1]).then_inc((s.out_even, s.out_odd)[par], DMA)
            act.wait_ge(s.out_even, NT // 2 * DMA)
            act.wait_ge(s.out_odd, NT // 2 * DMA)

        @block.vector
        def _(dve):
            dve.wait_ge(s.const, 5 * DMA)
            with dve.Fori(0, NT // 2) as i:
                for par in range(2):
                    dve.wait_ge((s.x_even, s.x_odd)[par], (i + 1) * (3 * DMA))
                    a, b, c = (x[:, par, n] for n in range(3))
                    e0, e1 = (edges[:, n, bass.ds(i * 2 + par, 1)] for n in range(2))
                    dve.scalar_tensor_tensor(a, a, e0, w[:, 0], ALU.mult, ALU.mult)
                    dve.scalar_tensor_tensor(c, c, e1, w[:, 2], ALU.mult, ALU.mult)
                    dve.tensor_tensor(b, b, w[:, 1], ALU.mult)
                    dve.drain()
                    dve.tensor_tensor(a, a, c, ALU.add)
                    dve.tensor_tensor(b, b, w[:, 3], ALU.add)
                    dve.drain()
                    dve.tensor_tensor(b, a, b, ALU.add).then_inc(s.y_done, 1)


def filter_stage(nc, t_feats, t_decay, w1, b1, f1, w2, b2, f2, w3, FS):
    with stage(nc, "filt", "const", "h_mm", "arg", "sine", "w3_mm", "f_done", "stored") as (block, s, sb, ps):
        feats = sb("feats", [33, SEQ])
        w1s = sb("w1s", [33, 64])
        w2s = sb("w2s", [64, 64])
        w3s = sb("w3s", [64, 2048])
        cols = sb("cols", [64, 4])
        dec = sb("dec", [P, NT, HYW])
        ang = sb("ang", [64, SEQ])
        turns = sb("turns", [64, SEQ])
        arg = sb("arg", [64, SEQ])
        hid = sb("hid", [64, SEQ])
        f = sb("f", [P, 4, HYW])
        o = sb("o", [P, 4, HYW])
        first = sb("first", [P, 1])
        ph = ps("ph", [64, SEQ])
        pw = [ps(f"pw{i}") for i in range(4)]

        @block.sync
        def _(sp):
            sp.dma_start(feats[:], t_feats).then_inc(s.const, DMA)
            sp.dma_start(w1s[:], w1).then_inc(s.const, DMA)
            sp.dma_start(w2s[:], w2).then_inc(s.const, DMA)
            sp.dma_start(w3s[:], w3).then_inc(s.const, DMA)
            for n, v in enumerate((b1, f1, b2, f2)):
                sp.dma_start(cols[:, n:n + 1], v.rearrange("(p a) -> p a", a=1), allow_slow_non_contiguous=True).then_inc(s.const, DMA)
            sp.dma_start(dec[:], t_decay.rearrange("(t p) c -> p t c", p=P)).then_inc(s.const, DMA)
            with sp.Fori(0, NT) as i:
                sp.wait_ge(s.f_done, i + 1)
                for n in range(2):
                    sp.dma_start(FS[n, rows(i * P), :], o[:, 2 * n:2 * n + 2].rearrange("p a c -> p (a c)")).then_inc(s.stored, DMA)
            sp.wait_ge(s.stored, 2 * NT * DMA)

        @block.tensor
        def _(pe):
            pe.wait_ge(s.const, 9 * DMA)
            for layer, (w, src) in enumerate(((w1s, feats), (w2s, hid))):
                if layer:
                    pe.wait_ge(s.sine, 1)
                for hf in range(2):
                    op = pe.matmul(ph[:, hf * 512:(hf + 1) * 512], w[:], src[:, hf * 512:(hf + 1) * 512], start=True, stop=True)
                op.then_inc(s.h_mm, 1)
            pe.wait_ge(s.sine, 2)
            with pe.Fori(0, NT) as i:
                pe.wait_ge(s.arg, 2 + i + 1)
                for n in range(4):
                    op = pe.matmul(pw[n][:], ang[:, 0:P], w3s[:, n * 512:(n + 1) * 512], start=True, stop=True)
                op.then_inc(s.w3_mm, 1)

        @block.scalar
        def _(act):
            for layer in range(2):
                act.wait_ge(s.arg, layer + 1)
                act.activation(hid[:], arg[:], ACT.Sin).then_inc(s.sine, 1)

        @block.vector
        def _(dve):
            dve.memset(first[:], 1.0)
            dve.drain()
            dve.memset(first[0:1, :], 0.0)
            dve.wait_ge(s.const, 9 * DMA)
            for layer in range(2):
                dve.wait_ge(s.h_mm, layer + 1)
                b, fr = cols[:, 2 * layer:2 * layer + 1], cols[:, 2 * layer + 1:2 * layer + 2]
                dve.tensor_scalar(ang[:], ph[:], b, fr, ALU.add, ALU.mult)
                dve.drain()
                reduced_sine(dve, arg[:], ang[:], turns[:], 0.0)
                dve.sem_inc(s.arg, 1)
            dve.wait_ge(s.sine, 2)
            with dve.Fori(0, NT) as i:
                dve.tensor_copy(ang[:, 0:P], hid[:, rows(i * P)])
                dve.drain()
                dve.sem_inc(s.arg, 1)
                dve.wait_ge(s.w3_mm, i + 1)
                for n in range(4):
                    dve.tensor_tensor(f[:, n], pw[n][:], dec[:, bass.ds(i, 1), :].rearrange("p a c -> p (a c)"), ALU.mult)
                dve.drain()
                for n in (1, 3):
                    dve.tensor_scalar(f[:, n], f[:, n], first[:, 0:1], None, ALU.mult)
                dve.drain()
                dve.memset(first[:], 1.0)
                dve.wait_ge(s.stored, i * (2 * DMA))
                for n in range(2):
                    dve.tensor_tensor(o[:, 2 * n], f[:, 2 * n], f[:, 2 * n + 1], ALU.add)
                    dve.tensor_tensor(o[:, 2 * n + 1], f[:, 2 * n], f[:, 2 * n + 1], ALU.subtract)
                dve.drain()
                dve.sem_inc(s.f_done, 1)


def spectrum_stage(nc, name, t_fwd, zin, out):
    with stage(nc, name, "z_in", "w_even", "w_odd", "mm", "odd_out", "sums_out", "stored_even", "stored_odd") as (block, s, sb, ps):
        z = sb("z", [P, 2, NT // 2, 2, HYW])
        w = sb("w", [P, 2, NT, 2, P])
        odd = sb("odd", [P, 2, 2, HYW])
        o = sb("o", [P, 2, 2, 2, HYW])
        acc = [[[ps(f"acc{i}{n}{r}") for r in range(2)] for n in range(2)] for i in range(2)]

        @block.sync
        def _(sp):
            for r in range(2):
                sp.dma_start(z[:, r], zin.rearrange("(t p r) (a c) -> r p t a c", p=P, r=2, a=2)[r]).then_inc(s.z_in, DMA)
            sp.dma_start(w[:, 0], t_fwd[0]).then_inc(s.w_even, DMA)
            sp.dma_start(w[:, 1], t_fwd[1]).then_inc(s.w_odd, DMA)
            for f in range(2, FCH):
                sp.wait_ge(s.mm, (f - 1) * 4)
                sp.dma_start(w[:, f % 2], t_fwd[f]).then_inc((s.w_even, s.w_odd)[f % 2], DMA)

        @block.tensor
        def _(pe):
            pe.wait_ge(s.z_in, 2 * DMA)
            with pe.Fori(0, FCH // 2) as i:
                for par in range(2):
                    pe.wait_ge((s.w_even, s.w_odd)[par], i * DMA + DMA)
                    pe.wait_ge(s.sums_out, 2 * i + par + 1)
                    for n in range(2):
                        for r in range(2):
                            for t in range(NT // 2):
                                op = pe.matmul(acc[par][n][r][:], w[:, par, r * (NT // 2) + t, n, :], z[:, r, t, n, :], start=t == 0, stop=t == NT // 2 - 1)
                            op.then_inc(s.mm, 1)

        @block.scalar
        def _(act):
            with act.Fori(0, FCH // 2) as i:
                for par in range(2):
                    for n in range(2):
                        act.wait_ge(s.mm, (2 * i + par) * 4 + (2 * n + 2))
                        act.wait_ge(s.sums_out, 2 * i + par + 1)
                        act.activation(odd[:, par, n], acc[par][n][1][:], ACT.Copy).then_inc(s.odd_out, 1)

        @block.vector
        def _(dve):
            dve.sem_inc(s.sums_out, 2)
            with dve.Fori(0, FCH // 2) as i:
                for par in range(2):
                    dve.wait_ge((s.stored_even, s.stored_odd)[par], i * DMA)
                    for n in range(2):
                        dve.wait_ge(s.odd_out, (2 * i + par) * 2 + (n + 1))
                        dve.tensor_tensor(o[:, par, n, 0], acc[par][n][0][:], odd[:, par, n], ALU.add)
                        dve.tensor_tensor(o[:, par, n, 1], acc[par][n][0][:], odd[:, par, n], ALU.subtract)
                    dve.drain()
                    dve.sem_inc(s.sums_out, 1)

        @block.gpsimd
        def _(pool):
            with pool.Fori(0, FCH // 2) as i:
                for par in range(2):
                    pool.wait_ge(s.sums_out, 2 * i + par + 3)
                    pool.dma_start(out[rows(i * (2 * P) + par * P), :], o[:, par].rearrange("p n a c -> p (n a c)")).then_inc((s.stored_even, s.stored_odd)[par], DMA)
            pool.wait_ge(s.stored_even, FCH // 2 * DMA)
            pool.wait_ge(s.stored_odd, FCH // 2 * DMA)


def conv_stage(nc, name, t_fwd, t_inv, zin, KS, gate, bias, ZO):
    with stage(nc, name, "z_in", "b_in", "f_even", "f_odd", "k_even", "k_odd", "fwd_mm", "odd_out", "read", "prod", "mixed", "i_even", "i_odd",
               "g_even", "g_odd", "inv_mm", "y_done", "stored_even", "stored_odd") as (block, s, sb, ps):
        z = sb("z", [P, 2, NT // 2, HYW])
        Y = sb("Y", [P, FCH, 2, 2, HYW])
        w = sb("w", [P, 2, NT, 2, P])
        ks = sb("ks", [P, 2, 2, 2, HYW])
        odd = sb("odd", [P, 2, HYW])
        zz = sb("zz", [P, 2, 2, HYW])
        prod = sb("prod", [P, 2, 2, 2, 2, HYW])
        g = sb("g", [P, 2, 2, HYW])
        b_row = sb("b_row", [P, HYW])
        tmp = sb("tmp", [P, 2, HYW])
        o = sb("o", [P, 2, 2, HYW])
        acc = [[[ps(f"acc{i}{n}{r}") for r in range(2)] for n in range(2)] for i in range(2)]
        yac = acc[0][0]

        @block.sync
        def _(sp):
            for r in range(2):
                sp.dma_start(z[:, r], zin.rearrange("(t p r) c -> r p t c", p=P, r=2)[r]).then_inc(s.z_in, DMA)
            sp.dma_start(b_row[:], bias.partition_broadcast(P)).then_inc(s.b_in, DMA)
            for f in range(FCH):
                if f >= 2:
                    sp.wait_ge(s.fwd_mm, (f - 1) * 2)
                sp.dma_start(w[:, f % 2], t_fwd[f]).then_inc((s.f_even, s.f_odd)[f % 2], DMA)
                if f >= 2:
                    sp.wait_ge(s.prod, f - 1)
                sp.dma_start(ks[:, f % 2].rearrange("p n a c -> p (n a c)"), KS[f * P:(f + 1) * P, :]).then_inc((s.k_even, s.k_odd)[f % 2], DMA)
            for t in range(NT // 2):
                if t < 2:
                    sp.wait_ge(s.fwd_mm, (FCH - 1 + t) * 2)
                else:
                    sp.wait_ge(s.inv_mm, (t - 1) * 2)
                    sp.wait_ge(s.y_done, (t - 1) * 2)
                sp.dma_start(w[:, t % 2].rearrange("p a b q -> p (a b q)"), t_inv[t].rearrange("p r f n t -> p (r f n t)")).then_inc((s.i_even, s.i_odd)[t % 2], DMA)
                sp.dma_start(g[:, t % 2], gate.rearrange("(t p r) c -> t p r c", p=P, r=2)[t]).then_inc((s.g_even, s.g_odd)[t % 2], DMA)

        @block.gpsimd
        def _(pool):
            for f in range(FCH):
                pool.wait_ge(s.prod, f + 1)
                a = prod[:, f % 2, 0]
                for n in range(2):
                    pool.tensor_tensor(Y[:, f, 0, n], a[:, 0, n], a[:, 1, n], ALU.add)
                    pool.tensor_tensor(Y[:, f, 1, n], a[:, 0, n], a[:, 1, n], ALU.subtract)
                pool.drain()
                pool.sem_inc(s.mixed, 1)
            for t in range(NT // 2):
                pool.wait_ge(s.y_done, 2 * t + 2)
                pool.dma_start(ZO.rearrange("(t p r) c -> t p r c", p=P, r=2)[t], o[:, t % 2]).then_inc((s.stored_even, s.stored_odd)[t % 2], DMA)
            pool.wait_ge(s.stored_even, NT // 4 * DMA)
            pool.wait_ge(s.stored_odd, NT // 4 * DMA)

        @block.tensor
        def _(pe):
            pe.wait_ge(s.z_in, 2 * DMA)
            for f in range(FCH):
                par = f % 2
                pe.wait_ge((s.f_even, s.f_odd)[par], (f // 2 + 1) * DMA)
                if f >= 2:
                    pe.wait_ge(s.read, f - 1)
                for n in range(2):
                    for r in range(2):
                        for t in range(NT // 2):
                            op = pe.matmul(acc[par][n][r][:], w[:, par, r * (NT // 2) + t, n, :], z[:, r, t, :], start=t == 0, stop=t == NT // 2 - 1)
                    op.then_inc(s.fwd_mm, 1)
            pe.wait_ge(s.read, FCH)
            for t in range(NT // 2):
                pe.wait_ge((s.i_even, s.i_odd)[t % 2], (t // 2 + 1) * DMA)
                for r in range(2):
                    if t:
                        pe.wait_ge(s.y_done, 2 * t - 1 + r)
                    for f in range(FCH):
                        if t == 0 and r == 0:
                            pe.wait_ge(s.mixed, f + 1)
                        for n in range(2):
                            op = pe.matmul(yac[r][:], w[:, t % 2, r * FCH + f, n, :], Y[:, f, r, n, :], start=n == 0 and f == 0, stop=n == 1 and f == FCH - 1)
                    op.then_inc(s.inv_mm, 1)

        @block.scalar
        def _(act):
            for f in range(FCH):
                for n in range(2):
                    act.wait_ge(s.fwd_mm, 2 * f + n + 1)
                    if f:
                        act.wait_ge(s.read, f)
                    act.activation(odd[:, n], acc[f % 2][n][1][:], ACT.Copy).then_inc(s.odd_out, 1)

        @block.vector
        def _(dve):
            for f in range(FCH):
                par = f % 2
                for n in range(2):
                    dve.wait_ge(s.odd_out, 2 * f + n + 1)
                    dve.tensor_tensor(zz[:, 0, n], acc[par][n][0][:], odd[:, n], ALU.add)
                    dve.tensor_tensor(zz[:, 1, n], acc[par][n][0][:], odd[:, n], ALU.subtract)
                dve.drain()
                dve.sem_inc(s.read, 1)
                dve.wait_ge((s.k_even, s.k_odd)[par], (f // 2 + 1) * DMA)
                if f >= 2:
                    dve.wait_ge(s.mixed, f - 1)
                for a in range(2):
                    (zc, zs), (kc, kz) = (zz[:, a, 0], zz[:, a, 1]), (ks[:, par, 0, a], ks[:, par, 1, a])
                    for q, n, u, v in ((0, 0, zc, kc), (1, 0, zs, kz), (0, 1, zc, kz), (1, 1, zs, kc)):
                        dve.tensor_tensor(prod[:, par, q, a, n], u, v, ALU.mult)
                dve.drain()
                first, second = prod[:, par, 0], prod[:, par, 1]
                dve.tensor_tensor(first[:, :, 0], first[:, :, 0], second[:, :, 0], ALU.subtract)
                dve.tensor_tensor(first[:, :, 1], first[:, :, 1], second[:, :, 1], ALU.add)
                dve.drain()
                dve.sem_inc(s.prod, 1)
            dve.wait_ge(s.b_in, DMA)
            for t in range(NT // 2):
                dve.wait_ge((s.g_even, s.g_odd)[t % 2], (t // 2 + 1) * DMA)
                if t >= 2:
                    dve.wait_ge((s.stored_even, s.stored_odd)[t % 2], DMA)
                for r in range(2):
                    dve.tensor_tensor(tmp[:, r], z[:, r, t, :], b_row[:], ALU.mult)
                dve.drain()
                for r in range(2):
                    dve.wait_ge(s.inv_mm, 2 * t + r + 1)
                    dve.scalar_tensor_tensor(tmp[:, r], yac[r][:], 1.0 / NFREQ, tmp[:, r], ALU.mult, ALU.add)
                    dve.drain()
                    dve.tensor_tensor(o[:, t % 2, r], tmp[:, r], g[:, t % 2, r], ALU.mult)
                    dve.drain()
                    dve.sem_inc(s.y_done, 1)


def na_tables():
    q, k = np.arange(GRID_C)[:, None], np.arange(GRID_C)[None, :]
    lo = np.clip(q - WIN_C // 2, 0, GRID_C - WIN_C)
    inside = (k >= lo) & (k < lo + WIN_C)
    hot = np.zeros((2 * WIN_C, GRID_C, GRID_C), np.float32)
    for o in range(2 * WIN_C - 1):
        hot[o] = inside & (k - q + WIN_C - 1 == o)
    hot[2 * WIN_C - 1] = np.where(inside, 0.0, NEG)
    return hot.reshape(2 * WIN_C, GRID_C * GRID_C)


def na_bias_stage(nc, ident, rpb, t_hot, BIAS):
    HR = HN * (2 * WIN_R - 1)
    NC_ = 2 * WIN_C - 1
    with stage(nc, "nab", "const", "init", "turned", "tab", "mm", "b_out", "stored") as (block, s, sb, ps):
        tab = sb("tab", [HR, 2 * WIN_C])
        tabT = sb("tabT", [2 * WIN_C, HR])
        hot = sb("hot", [2 * WIN_C, GRID_C * GRID_C])
        o = sb("o", [HR, GRID_C * GRID_C])
        pt = ps("pt")
        acc = ps("acc")

        @block.sync
        def _(sp):
            sp.wait_ge(s.init, 1)
            sp.dma_start(tab[:, 0:NC_], rpb.rearrange("h r c -> (h r) c")).then_inc(s.const, DMA)
            sp.dma_start(hot[:], t_hot).then_inc(s.const, DMA)
            sp.wait_ge(s.b_out, GRID_C * GRID_C // 512)
            sp.dma_start(BIAS, o[:]).then_inc(s.stored, DMA)
            sp.wait_ge(s.stored, DMA)

        @block.tensor
        def _(pe):
            pe.wait_ge(s.const, 2 * DMA)
            pe.transpose(pt[:2 * WIN_C, :HR], tab[:], ident[:HR, :HR]).then_inc(s.turned, 1)
            pe.wait_ge(s.tab, 1)
            for n in range(GRID_C * GRID_C // 512):
                if n:
                    pe.wait_ge(s.b_out, n)
                pe.matmul(acc[:HR, :], tabT[:], hot[:, n * 512:(n + 1) * 512], start=True, stop=True).then_inc(s.mm, 1)

        @block.vector
        def _(dve):
            dve.memset(tab[:], 1.0)
            dve.drain()
            dve.sem_inc(s.init, 1)
            dve.wait_ge(s.turned, 1)
            dve.tensor_copy(tabT[:], pt[:2 * WIN_C, :HR]).then_inc(s.tab, 1)
            for n in range(GRID_C * GRID_C // 512):
                dve.wait_ge(s.mm, n + 1)
                dve.tensor_copy(o[:, n * 512:(n + 1) * 512], acc[:HR, :]).then_inc(s.b_out, 1)


def na_stage(nc, ident, U3, KV3, BIAS, NA):
    NR = 2 * WIN_R - 1
    WK = WIN_R * GRID_C
    NK = WK + CTX
    NP_ = NK // P
    HP = HN // 2
    NU = HP * GRID_R
    with stage(nc, "na", "init", "k_in", "q_in", "v_in", "b_in", "turned", "qk_out", "q_bd", "s_mm", "s_done", "neg_max", "probs",
               "p_turned", "p_out", "pv", "y", "stored") as (block, s, sb, ps):
        kin = sb("kin", [P, NTA, 512])
        qin = sb("qin", [P, NT, 512])
        kT = sb("kT", [P, HP * ALL])
        qT = sb("qT", [P, HP * SEQ + GRID_C])
        vc = sb("vc", [P, NTC, 512])
        vl = sb("vl", [P, 2 * NT, 512])
        bias = sb("bias", [P, HP * NR, GRID_C])
        qbd = sb("qbd", [P, 2, P])
        sc = sb("sc", [P, 2, NK])
        mx = sb("mx", [P, 2])
        sm = sb("sm", [P, 4])
        pT = sb("pT", [P, 2, NP_, P])
        y = sb("y", [P, NU, HD])
        pS = [ps(f"pS{i}", [P, 1024]) for i in range(2)]
        pP = ps("pP", [P, 8, P])
        pV = ps("pV")

        def place(u):
            r = u % GRID_R
            start = (r - 4) * (r >= 4) - (r - 12) * (r >= 12)
            off = start - r + (WIN_R - 1)
            if not isinstance(u, int):
                start, off = start.with_bounds(min_val=0, max_val=GRID_R - WIN_R), off.with_bounds(min_val=0, max_val=WIN_R - 1)
            return r, start, off

        def tile_of(start):
            tile = (start % 2) * NT + start // 2
            return tile if isinstance(start, int) else tile.with_bounds(min_val=0, max_val=2 * NT - 5)

        def steps(eng, body):
            for u in range(2):
                body(u, u % 2, u)
            with eng.Fori(1, NU // 2) as i:
                for par in range(2):
                    body(2 * i + par, par, None)
            for u in range(NU, NU + 2):
                body(u, u % 2, u)

        def active(at, lag):
            return at is None or 0 <= at - lag < NU

        @block.sync
        def _(sp):
            sp.dma_start(kin[:, 0:NTC], KV3[:, 0:512].rearrange("(t p) c -> p t c", p=P)).then_inc(s.k_in, DMA)
            sp.dma_start(kin[:, NTC:], U3[:, O_NK:O_NV].rearrange("(t p) c -> p t c", p=P)).then_inc(s.k_in, DMA)
            sp.dma_start(qin[:], U3[:, O_NQ:O_NK].rearrange("(t p) c -> p t c", p=P)).then_inc(s.q_in, DMA)
            for a in range(2):
                for hp in range(HP):
                    r0 = (2 * hp + a) * NR
                    sp.dma_start(bias[a * GRID_C:(a + 1) * GRID_C, hp * NR:(hp + 1) * NR], BIAS[r0:r0 + NR, :].rearrange("r (q c) -> q r c", q=GRID_C)).then_inc(s.b_in, DMA)
            sp.dma_start(vc[:], KV3[:, 512:1024].rearrange("(t p) c -> p t c", p=P)).then_inc(s.v_in, DMA)
            sp.dma_start(vl[:, 0:NT], U3[:, O_NV:O_NZ].rearrange("(t p) c -> p t c", p=P)).then_inc(s.v_in, DMA)
            sp.dma_start(vl[:, NT:2 * NT - 1], U3[GRID_C:SEQ - GRID_C, O_NV:O_NZ].rearrange("(t p) c -> p t c", p=P)).then_inc(s.v_in, DMA)
            na_v = NA.rearrange("(r q) c -> q r c", q=GRID_C)
            for hp in range(HP):
                sp.wait_ge(s.y, (hp + 1) * GRID_R)
                for a in range(2):
                    h = 2 * hp + a
                    sp.dma_start(na_v[:, :, h * HD:(h + 1) * HD], y[a * GRID_C:(a + 1) * GRID_C, hp * GRID_R:(hp + 1) * GRID_R]).then_inc(s.stored, DMA)
            sp.wait_ge(s.stored, 2 * HP * DMA)

        @block.tensor
        def _(pe):
            pe.wait_ge(s.init, 1)
            pe.wait_ge(s.k_in, 2 * DMA)
            pe.wait_ge(s.q_in, DMA)
            n = 0
            for hp in range(HP):
                for src, lo, hi in ((kin, 0, 5), (kin, 5, NTA), (qin, 0, NT)):
                    if n >= 2:
                        pe.wait_ge(s.qk_out, n - 1)
                    for t in range(lo, hi):
                        op = pe.transpose(pS[n % 2][:, (t - lo) * P:(t - lo + 1) * P], src[:, t, hp * P:(hp + 1) * P], ident[:])
                    op.then_inc(s.turned, 1)
                    n += 1
            pe.wait_ge(s.qk_out, n)
            pe.wait_ge(s.v_in, 3 * DMA)

            def step(u, par, at):
                if active(at, 0):
                    _, start, _ = place(u)
                    pe.wait_ge(s.q_bd, u + 1)
                    if at is None:
                        pe.wait_ge(s.s_done, u - 1)
                    col = (u // GRID_R) * ALL
                    pe.matmul(pS[par][:, 0:WK], qbd[:, par], kT[:, bass.ds(col + start * GRID_C + CTX, WK)], start=True, stop=True)
                    pe.matmul(pS[par][:, WK:NK], qbd[:, par], kT[:, bass.ds(col, CTX)], start=True, stop=True).then_inc(s.s_mm, 1)
                if active(at, 1):
                    pe.wait_ge(s.probs, u)
                    if active(at, 2):
                        pe.wait_ge(s.p_out, u - 1)
                    for c in range(NP_):
                        op = pe.transpose(pP[:, c, :], sc[:, 1 - par, c * P:(c + 1) * P], ident[:])
                    op.then_inc(s.p_turned, 1)
                if active(at, 2):
                    v = u - 2
                    _, start, _ = place(v)
                    pe.wait_ge(s.p_out, v + 1)
                    if at != 2:
                        pe.wait_ge(s.y, v)
                    hp = v // GRID_R
                    tile = tile_of(start)
                    for c in range(WK // P):
                        pe.matmul(pV[:, 0:P], pT[:, par, c, :], vl[:].rearrange("p t c -> p (t c)")[:, bass.ds((tile + c) * 512 + hp * P, P)], start=c == 0, stop=False)
                    for c in range(NTC):
                        op = pe.matmul(pV[:, 0:P], pT[:, par, WK // P + c, :], vc[:].rearrange("p t c -> p (t c)")[:, bass.ds(hp * P + c * 512, P)], start=False, stop=c == NTC - 1)
                    op.then_inc(s.pv, 1)
            steps(pe, step)

        @block.scalar
        def _(act):
            n = 0
            for hp in range(HP):
                for lo, hi in ((0, 5), (5, NTA), (NTA, NTA + NT)):
                    act.wait_ge(s.turned, n + 1)
                    src = pS[n % 2][:, 0:(hi - lo) * P]
                    if lo < NTA:
                        op = act.activation(kT[:, hp * ALL + lo * P:hp * ALL + hi * P], src, ACT.Copy)
                    else:
                        op = act.activation(qT[:, hp * SEQ:(hp + 1) * SEQ], src, ACT.Copy, scale=HD ** -0.5)
                    op.then_inc(s.qk_out, 1)
                    n += 1

            def step(u, par, at):
                if active(at, 0):
                    act.wait_ge(s.neg_max, u + 1)
                    act.activation(sc[:, par], sc[:, par], ACT.Exp, bias=mx[:, par:par + 1], accum_out=sm[:, 2 * par:2 * par + 1])
                    act.drain()
                    act.sem_inc(s.probs, 1)
                if active(at, 1):
                    act.wait_ge(s.p_turned, u)
                    if active(at, 3):
                        act.wait_ge(s.pv, u - 2)
                    act.activation(pT[:, 1 - par], pP[:, 0:NP_], ACT.Copy).then_inc(s.p_out, 1)
            steps(act, step)

        @block.vector
        def _(dve):
            def spread(v, par):
                for a in range(2):
                    e = slice(a * HD, (a + 1) * HD)
                    dve.tensor_copy(qbd[e, par, e], qT[e, bass.ds(v * GRID_C, GRID_C)])
                dve.drain()
                dve.sem_inc(s.q_bd, 1)

            dve.memset(qbd[:], 0.0)
            dve.memset(qT[:, HP * SEQ:], 0.0)
            dve.drain()
            dve.sem_inc(s.init, 1)
            dve.wait_ge(s.qk_out, 3 * HP)
            spread(0, 0)
            dve.wait_ge(s.b_in, 2 * HP * DMA)

            def step(u, par, at):
                if active(at, 0):
                    _, _, off = place(u)
                    if at is None or u + 1 < NU:
                        if at != 0:
                            dve.wait_ge(s.s_mm, u)
                        spread(u + 1, 1 - par)
                    dve.wait_ge(s.s_mm, u + 1)
                    if at is None:
                        dve.wait_ge(s.p_turned, u - 1)
                    b = bias[:, bass.ds((u // GRID_R) * NR + off, WIN_R), :].rearrange("p a c -> p (a c)")
                    dve.tensor_tensor(sc[:, par, 0:WK], pS[par][:, 0:WK], b, ALU.add)
                    dve.tensor_copy(sc[:, par, WK:], pS[par][:, WK:NK])
                    dve.drain()
                    dve.sem_inc(s.s_done, 1)
                    dve.tensor_reduce(mx[:, par:par + 1], sc[:, par], AX_X, ALU.max, negate=True)
                    dve.drain()
                    dve.sem_inc(s.neg_max, 1)
                if active(at, 2):
                    v = u - 2
                    dve.wait_ge(s.pv, v + 1)
                    for a in range(2):
                        e = slice(a * HD, (a + 1) * HD)
                        dve.tensor_scalar(y[e, bass.ds(v, 1), :].rearrange("p a c -> p (a c)"), pV[e, a * HD:(a + 1) * HD], sm[e, 2 * par + 1:2 * par + 2], None, ALU.mult)
                    dve.drain()
                    dve.sem_inc(s.y, 1)
                if active(at, 1):
                    dve.wait_ge(s.probs, u)
                    dve.reciprocal(sm[:, 3 - 2 * par:4 - 2 * par], sm[:, 2 - 2 * par:3 - 2 * par])
                    dve.drain()
            steps(dve, step)


def odd_out_stage(nc, Z, NA, U3, YB3):
    with stage(nc, "oo", "x_even", "x_odd", "silu", "y_done", "out_even", "out_odd") as (block, s, sb, ps):
        x = sb("x", [P, 2, 2, 512])
        z = sb("z", [P, 2, 2, 512])

        @block.sync
        def _(sp):
            with sp.Fori(0, NT // 2) as i:
                for par in range(2):
                    sp.wait_ge((s.out_even, s.out_odd)[par], i * DMA)
                    t = rows(i * (2 * P) + par * P)
                    done = (s.x_even, s.x_odd)[par]
                    sp.dma_start(x[:, par, 0], Z[t, :]).then_inc(done, DMA)
                    sp.dma_start(x[:, par, 1], NA[t, :]).then_inc(done, DMA)
                    sp.dma_start(z[:, par, 0], U3[t, O_HZ:O_NQ]).then_inc(done, DMA)
                    sp.dma_start(z[:, par, 1], U3[t, O_NZ:ODD_IN]).then_inc(done, DMA)

        @block.scalar
        def _(act):
            with act.Fori(0, NT // 2) as i:
                for par in range(2):
                    act.wait_ge((s.x_even, s.x_odd)[par], (i + 1) * (4 * DMA))
                    act.activation(z[:, par], z[:, par], ACT.Silu).then_inc(s.silu, 1)

        @block.vector
        def _(dve):
            with dve.Fori(0, NT // 2) as i:
                for par in range(2):
                    dve.wait_ge(s.silu, 2 * i + par + 1)
                    dve.tensor_tensor(x[:, par], x[:, par], z[:, par], ALU.mult).then_inc(s.y_done, 1)

        @block.gpsimd
        def _(pool):
            with pool.Fori(0, NT // 2) as i:
                for par in range(2):
                    pool.wait_ge(s.y_done, 2 * i + par + 1)
                    pool.dma_start(YB3[rows(i * (2 * P) + par * P), :], x[:, par].rearrange("p a c -> p (a c)")).then_inc((s.out_even, s.out_odd)[par], DMA)
            pool.wait_ge(s.out_even, NT // 2 * DMA)
            pool.wait_ge(s.out_odd, NT // 2 * DMA)
def tables():
    prefix, suffix, causal = gla_tables()
    mask, first, freq = swa_tables()
    rope, dist, q_pos, k_pos = retention_tables()
    sums, ends, pairs, level = rwkv_tables()
    feats, decay, fwd, inv = hyena_tables()
    return {
        "t_eye": np.eye(P, dtype=np.float32), "t_prefix": prefix, "t_suffix": suffix, "t_causal": causal,
        "t_mask": mask, "t_first": first, "t_freq": freq, "t_rope": rope, "t_dist": dist, "t_qpos": q_pos,
        "t_kpos": k_pos, "t_edges_all": rwkv_edges(), "t_sums": sums, "t_ends": ends, "t_pairs": pairs,
        "t_level": level, "t_edges_seq": edges_of_sequence(), "t_feats": feats, "t_decay": decay,
        "t_fwd": fwd, "t_inv": inv, "t_hot": na_tables(),
    }


def start_stage(nc, ident, t_eye, padded):
    with stage(nc, "start", "id_in", "zero", "pad_out") as (block, s, sb, ps):
        zero = sb("zero", [1, EVEN_IN])

        @block.vector
        def _(dve):
            dve.memset(zero[:], 0.0).then_inc(s.zero, 1)

        @block.sync
        def _(sp):
            sp.dma_start(ident[:], t_eye).then_inc(s.id_in, DMA)
            sp.wait_ge(s.zero, 1)
            for t in padded:
                for row in (0, t.shape[0] - 1):
                    sp.dma_start(t[row:row + 1, :], zero[:, :t.shape[1]]).then_inc(s.pad_out, DMA)
            sp.wait_ge(s.id_in, DMA)
            sp.wait_ge(s.pad_out, 2 * len(padded) * DMA)


@contextmanager
def split_pair(nc, name, tokens):
    with nc.sbuf_tensor(f"{name}_hi", [P, KC, tokens], F32R) as hi, nc.sbuf_tensor(f"{name}_lo", [P, KC, tokens], F32R) as lo:
        yield hi, lo


def program(nc, T):
    def scratch(name, *shape):
        return nc.dram_tensor(name, shape, F32, kind="Internal").ap()

    mod1 = scratch("mod1", 1, 6 * D)
    mod2 = scratch("mod2", 2, 2, 3 * D)
    P1 = scratch("P1", SEQ, T["w_in"].shape[2])
    YA, Y1, O1, X1, D1, X2 = (scratch(n, SEQ, D) for n in ("YA", "Y1", "O1", "X1", "D1", "X2"))
    U2p = scratch("U2p", ALL + 2, EVEN_IN)
    U2 = U2p[1:ALL + 1, :]
    YB2, O2 = scratch("YB2", ALL, D), scratch("O2", ALL, D)
    PC, PD = scratch("PC", ALL, 3 * 512 + HN), scratch("PD", 2, ALL, 3 * 512)
    RW = scratch("RW", 2, ALL, 512)
    H1 = scratch("H1", SEQ, D)
    U3p = scratch("U3p", SEQ + 2, ODD_IN)
    U3 = U3p[1:SEQ + 1, :]
    KV3 = scratch("KV3", CTX, 1024)
    VX = scratch("VX", SEQ, 3 * HYW)
    FS, KS = scratch("FS", 2, SEQ, 2 * HYW), scratch("KS", 2, HALF, 4 * HYW)
    Z1, Z2, NA = (scratch(n, SEQ, HYW) for n in ("Z1", "Z2", "NA"))
    BIAS = scratch("BIAS", HN * (2 * WIN_R - 1), GRID_C * GRID_C)
    YB3, O3 = scratch("YB3", SEQ, D), scratch("O3", SEQ, D)

    x, ctx = T["x"][0], T["ctx_2"][0]
    part1 = lambda n: mod1[0, n * D:(n + 1) * D]
    part2 = lambda layer, who, n: mod2[layer, who, n * D:(n + 1) * D]

    with nc.sbuf_tensor("ident", [P, P], F32) as ident:
        start_stage(nc, ident, T["t_eye"], (U2p, U3p))
        ada_stage(nc, [([T["c"][0]], T["w_ada"][0], T["b_ada"][0], mod1)]
                  + [([T["c_2"][0], T["c_ctx_2"]], T["ada_w_2"][n], T["ada_b_2"][n], mod2[n]) for n in range(2)])

        with split_pair(nc, "h1", SEQ) as (hi, lo):
            with nc.sbuf_tensor("h1T", [P, KC, SEQ], F32) as hT:
                norm_stage(nc, "n1", ident, x, 0, NT, hT, 0, norm="ln", scale=part1(1), shift=part1(0))
                split_stage(nc, "h1s", hT, hi, lo, KC)
            gemm_stage(nc, "g_in", hi, lo, KC, NT, T["w_in"][0], P1)
        gla_stage(nc, ident, P1, T["gla_w_lr"][0], T["gla_b_lr"][0], T["gla_norm_g"][0], T["t_prefix"], T["t_suffix"], T["t_causal"], YA)
        swa_stage(nc, ident, P1, T["positions"][0], T["swa_sinks"][0], T["t_mask"], T["t_first"], T["t_freq"], YA, Y1)
        with split_pair(nc, "y1", SEQ) as (hi, lo):
            with nc.sbuf_tensor("y1T", [P, KC, SEQ], F32) as yT:
                turn_stage(nc, "turn1", ident, Y1, NT, yT)
                split_stage(nc, "y1s", yT, hi, lo, KC)
            gemm_stage(nc, "g_o", hi, lo, KC, NT, T["w_o"][0], O1)
        with nc.sbuf_tensor("fT", [P, FC, SEQ], F32) as fT:
            with split_pair(nc, "h2", SEQ) as (hi, lo):
                hT = fT[:, 0:KC, :]
                norm_stage(nc, "n2", ident, x, 0, NT, hT, 0, norm="ln", scale=part1(4), shift=part1(3), res=O1, gate=part1(2),
                           alpha=ALPHA, affine=(T["ln1_g"][0], T["ln1_b"][0]), keep=X1)
                split_stage(nc, "h2s", hT, hi, lo, KC)
                ffn_up_stage(nc, ident, hi, lo, T["w_up"][0], T["conv_w"][0], T["conv_b"][0], fT)
            gemm_stage(nc, "g_down", fT, None, FC, NT, T["w_down"][0], D1, width=256)

        with split_pair(nc, "h3", ALL) as (hi, lo):
          with nc.sbuf_tensor("h3T", [P, KC, ALL], F32) as hT:
            norm_stage(nc, "n3", ident, X1, 0, NT, hT, CTX, norm="rms", scale=part2(0, 0, 1), shift=part2(0, 0, 0), weight=T["norm_w_2"][0],
                       res=D1, gate=part1(5), alpha=ALPHA, affine=(T["ln2_g"][0], T["ln2_b"][0]), keep=X2)
            norm_stage(nc, "n3c", ident, ctx, 0, NTC, hT, 0, norm="rms", scale=part2(0, 1, 1), shift=part2(0, 1, 0), weight=T["norm_w_2"][0])
            split_stage(nc, "h3s", hT, hi, lo, KC)
          gemm_stage(nc, "g_even", hi, lo, KC, NTA, T["even_w_in_2"][0], U2, width=384)
        retention_stage(nc, ident, U2, T["ret_decay_2"][0], T["t_rope"], T["t_dist"], T["t_qpos"], T["t_kpos"], YB2)
        rwkv_prep_stage(nc, ident, U2p, T["rw_mu_2"][0], T["rw_w0_2"][0], T["rw_w2_2"][0], T["rw_a0_2"][0], T["rw_a2_2"][0], T["rw_kk_2"][0],
                        T["rw_ka_2"][0], T["rw_rk_2"][0].rearrange("h d -> (h d)"), T["t_edges_all"], PC, PD)
        rwkv_stage(nc, ident, PC, PD, T["t_sums"], T["t_ends"], T["t_pairs"], T["t_level"], RW)
        rwkv_out_stage(nc, RW, PC, U2, T["rw_ln_w_2"][0], T["rw_ln_b_2"][0], YB2)
        with split_pair(nc, "y2", ALL) as (hi, lo):
            with nc.sbuf_tensor("y2T", [P, KC, ALL], F32) as yT:
                turn_stage(nc, "turn2", ident, YB2, NTA, yT)
                split_stage(nc, "y2s", yT, hi, lo, KC)
            gemm_stage(nc, "g_eout", hi, lo, KC, NTA, T["even_w_out_2"][0], O2, width=384)

        with split_pair(nc, "h4", ALL) as (hi, lo):
          with nc.sbuf_tensor("h4T", [P, KC, ALL], F32) as hT:
            norm_stage(nc, "n4", ident, X2, 0, NT, hT, CTX, norm="rms", scale=part2(1, 0, 1), shift=part2(1, 0, 0), weight=T["norm_w_2"][1],
                       res=O2, res_row0=CTX, gate=part2(0, 0, 2), keep=H1)
            norm_stage(nc, "n4c", ident, ctx, 0, NTC, hT, 0, norm="rms", scale=part2(1, 1, 1), shift=part2(1, 1, 0), weight=T["norm_w_2"][1],
                       res=O2, gate=part2(0, 1, 2))
            split_stage(nc, "h4s", hT, hi, lo, KC)
          gemm_stage(nc, "g_odd", hi[:, :, CTX:], lo[:, :, CTX:], KC, NT, T["odd_w_in_2"][0], U3, width=384)
          gemm_stage(nc, "g_ckv", hi[:, :, 0:CTX], lo[:, :, 0:CTX], KC, NTC, T["odd_w_in_2"][0][:, O_NK:O_NZ], KV3, width=384)
        short_conv_stage(nc, U3p, T["hy_conv_w_2"][0], T["hy_conv_b_2"][0], T["t_edges_seq"], VX)
        filter_stage(nc, T["t_feats"], T["t_decay"], T["hy_w1_2"][0], T["hy_b1_2"][0], T["hy_f1_2"][0], T["hy_w2_2"][0], T["hy_b2_2"][0],
                     T["hy_f2_2"][0], T["hy_w3_2"][0], FS)
        for order, (zin, zout) in enumerate(((VX[:, 0:HYW], Z1), (Z1, Z2))):
            spectrum_stage(nc, f"spec{order}", T["t_fwd"], FS[order], KS[order])
            conv_stage(nc, f"conv{order}", T["t_fwd"], T["t_inv"], zin, KS[order], VX[:, (order + 1) * HYW:(order + 2) * HYW], T["hy_bias_2"][0, order], zout)
        na_bias_stage(nc, ident, T["na_rpb_2"][0], T["t_hot"], BIAS)
        na_stage(nc, ident, U3, KV3, BIAS, NA)
        odd_out_stage(nc, Z2, NA, U3, YB3)
        with split_pair(nc, "y3", SEQ) as (hi, lo):
            with nc.sbuf_tensor("y3T", [P, KC, SEQ], F32) as yT:
                turn_stage(nc, "turn3", ident, YB3, NT, yT)
                split_stage(nc, "y3s", yT, hi, lo, KC)
            gemm_stage(nc, "g_oout", hi, lo, KC, NT, T["odd_w_out_2"][0], O3)
        norm_stage(nc, "n5", ident, H1, 0, NT, None, 0, norm="rms", res=O3, gate=part2(1, 0, 2), final=T["final_norm_w_2"], keep=T["out"][0])


def kernel(**inputs):
    import concourse.bacc as bacc
    from concourse.bass_utils import run_bass_kernel_spmd

    nc = bacc.Bacc("TRN2", target_bir_lowering=False, num_devices=1)
    arrays, T = {}, {}
    for name, a in list(inputs.items()) + list(tables().items()):
        a = np.ascontiguousarray(a)
        arrays[f"in_{name}"] = a
        T[name] = nc.dram_tensor(f"in_{name}", a.shape, mybir.dt.from_np(a.dtype), kind="ExternalInput").ap()
    T["out"] = nc.dram_tensor("out_y", (1, SEQ, D), F32, kind="ExternalOutput").ap()
    program(nc, T)
    r = run_bass_kernel_spmd(nc, [arrays], core_ids=[0])
    return r.results[0]["out_y"]
```

```python
import math
from collections import namedtuple
from contextlib import ExitStack, contextmanager

import numpy as np

import concourse.bass as bass
from concourse import mybir

F32 = mybir.dt.float32
I32 = mybir.dt.int32
U32 = mybir.dt.uint32
F32R = mybir.dt.float32r
ALU = mybir.AluOpType
ACT = mybir.ActivationFunctionType
AX_X = mybir.AxisListType.X

P = 128
D = 1024
KC = D // P
SEQ = 1024
NT = SEQ // P
CTX = 256
NTC = CTX // P
ALL = CTX + SEQ
NTA = ALL // P
D_FF = 2816
FC = D_FF // P
ALPHA = 2.0 ** 0.25
DMA = 16


@contextmanager
def stage(nc, name, *signals):
    sems = {s: nc.alloc_semaphore(f"{name}_{s}") for s in signals}
    with ExitStack() as mem:
        def sb(label, shape, dt=F32):
            return mem.enter_context(nc.sbuf_tensor(f"{name}_{label}", shape, dt))

        def ps(label, shape=(P, 512), dt=F32):
            return mem.enter_context(nc.psum_tensor(f"{name}_{label}", list(shape), dt))

        with nc.Block() as block:
            yield block, namedtuple("Signals", signals)(**sems), sb, ps
    nc.clear_and_free_semaphores(list(sems.values()))
    nc.all_engine_barrier()


def rows(start, n=P):
    return bass.ds(start, n)


def col_view(vec):
    return vec.rearrange("(k p) -> p k", p=P)


def ada_stage(nc, jobs):
    W = 512
    for n, (cs, w, b, out) in enumerate(jobs):
        M, N = len(cs), w.shape[1]
        with stage(nc, f"ada{n}", "c_in", "b_in", "w_even", "w_odd", "silu", "w_free", "mm", "ps_free", "res", "out") as (block, s, sb, ps):
            c_raw = sb("c_raw", [P, KC, M])
            c_act = sb("c_act", [P, KC, M])
            w_buf = sb("w_buf", [P, 2, KC, W])
            bias = sb("bias", [M, N])
            res = sb("res", [M, N])
            acc = [ps(f"acc{i}") for i in range(2)]
            w_v = w.rearrange("(p k) n -> p k n", k=KC)

            @block.sync
            def _(sp):
                for m, c in enumerate(cs):
                    sp.dma_start(c_raw[:, :, m:m + 1], c.rearrange("(p k a) -> p k a", k=KC, a=1),
                                 allow_slow_non_contiguous=True).then_inc(s.c_in, DMA)
                    sp.dma_start(bias[m:m + 1, :], b.rearrange("(a n) -> a n", a=1)).then_inc(s.b_in, DMA)
                with sp.Fori(0, N // W // 2) as i:
                    for par in range(2):
                        sp.wait_ge(s.w_free, 2 * i + par + 1)
                        sp.dma_start(w_buf[:, par], w_v[:, :, bass.ds(i * (2 * W) + par * W, W)]).then_inc((s.w_even, s.w_odd)[par], DMA)
                sp.wait_ge(s.res, N // W)
                sp.dma_start(out, res[:]).then_inc(s.out, DMA)
                sp.wait_ge(s.out, DMA)

            @block.scalar
            def _(act):
                act.wait_ge(s.c_in, DMA * M)
                act.activation(c_act[:], c_raw[:], ACT.Silu).then_inc(s.silu, 1)

            @block.tensor
            def _(pe):
                pe.sem_inc(s.w_free, 2)
                pe.wait_ge(s.silu, 1)
                with pe.Fori(0, N // W // 2) as i:
                    for par in range(2):
                        pe.wait_ge(s.ps_free, 2 * i + par + 1)
                        pe.wait_ge((s.w_even, s.w_odd)[par], i * DMA + DMA)
                        for k in range(KC):
                            mm = pe.matmul(acc[par][:M, :], c_act[:, k, :], w_buf[:, par, k, :], start=k == 0, stop=k == KC - 1)
                        mm.then_inc(s.mm, 1)
                        pe.wait_ge(s.mm, 2 * i + par + 1)
                        pe.sem_inc(s.w_free, 1)

            @block.vector
            def _(dve):
                dve.sem_inc(s.ps_free, 2)
                dve.wait_ge(s.b_in, DMA * M)
                with dve.Fori(0, N // W // 2) as i:
                    for par in range(2):
                        dve.wait_ge(s.mm, 2 * i + par + 1)
                        cols = bass.ds(i * (2 * W) + par * W, W)
                        dve.tensor_tensor(res[:, cols], acc[par][:M, :], bias[:, cols], ALU.add).then_inc(s.res, 1)
                        dve.wait_ge(s.res, 2 * i + par + 1)
                        dve.sem_inc(s.ps_free, 1)


def split_stage(nc, name, hT, hi, lo, kc):
    with stage(nc, name, "hi_done", "lo_done") as (block, s, sb, ps):
        @block.scalar
        def _(act):
            for k in range(kc):
                act.activation(hi[:, k, :], hT[:, k, :], ACT.Copy).then_inc(s.hi_done, 1)

        @block.vector
        def _(dve):
            for k in range(kc):
                dve.wait_ge(s.hi_done, k + 1)
                dve.tensor_tensor(lo[:, k, :], hT[:, k, :], hi[:, k, :], ALU.subtract)
            dve.drain()


def gemm_stage(nc, name, hi, lo, kc, ntiles, w, out, width=512):
    N = w.shape[1]
    nb = 8 if ntiles == 8 else 4
    full = N // width
    tail = N - full * width
    pairs = full // 2
    left = [(2 * pairs, 2 * pairs * width, width)] if full % 2 else []
    if tail:
        left.append((full, full * width, tail))
    total = full + (tail > 0)
    half = ntiles // 2
    split = lo is not None
    with stage(nc, name, "w_even", "w_odd", "hi_done", "lo_done", "mm", "act_free", "dve_free", "out_even", "out_odd") as (block, s, sb, ps):
        w_buf = sb("w_buf", [P, 2, kc, width])
        w_hi = sb("w_hi", [P, 2, kc, width], F32R) if split else w_buf
        w_lo = sb("w_lo", [P, 2, kc, width], F32R) if split else None
        o_buf = sb("o_buf", [P, 2, ntiles, width])
        acc = [ps(f"acc{i}") for i in range(nb)]
        w_v = w.rearrange("(k p) n -> p k n", p=P)
        o_v = out.rearrange("(t p) n -> p t n", p=P)

        def strips(eng, body, behind=None):
            def last(st, col, wd):
                if behind:
                    behind(st, st % 2, col, wd)
            for st in range(2):
                body(st, st, st * width, width)
                if st:
                    last(0, 0, width)
            if pairs > 1:
                with eng.Fori(1, pairs) as i:
                    for par in range(2):
                        st, col = 2 * i + par, i * (2 * width) + par * width
                        body(st, par, col, width)
                        if behind:
                            behind(2 * i + (par - 1), 1 - par, i * (2 * width) + (par - 1) * width, width)
            at = (2 * pairs - 1, (2 * pairs - 1) * width, width)
            for st, col, wd in left:
                body(st, st % 2, col, wd)
                last(*at)
                at = (st, col, wd)
            last(*at)

        @block.sync
        def _(sp):
            def load(st, par, col, wd):
                if not isinstance(st, int) or st >= 2:
                    if split:
                        sp.wait_ge(s.lo_done, st - 1)
                    else:
                        sp.wait_ge(s.mm, (st - 1) * ntiles)
                sp.dma_start(w_buf[:, par, :, :wd], w_v[:, :, bass.ds(col, wd)]).then_inc((s.w_even, s.w_odd)[par], DMA)
            strips(sp, load)

        @block.tensor
        def _(pe):
            def multiply(st, par, col, wd):
                if split:
                    pe.wait_ge(s.lo_done, st + 1)
                else:
                    pe.wait_ge((s.w_even, s.w_odd)[par], (st - par) * (DMA // 2) + DMA)
                for t in range(ntiles):
                    bank = (par * ntiles + t) % nb
                    pe.wait_ge(s.act_free if t % 2 == 0 else s.dve_free, st * half + t // 2 + 1)
                    for k in range(kc):
                        o, tt = acc[bank][:, :wd], slice(t * P, (t + 1) * P)
                        mm = pe.matmul(o, hi[:, k, tt], w_hi[:, par, k, :wd], start=k == 0, stop=not split and k == kc - 1)
                        if split:
                            pe.matmul(o, hi[:, k, tt], w_lo[:, par, k, :wd], start=False, stop=False)
                            mm = pe.matmul(o, lo[:, k, tt], w_hi[:, par, k, :wd], start=False, stop=k == kc - 1)
                    mm.then_inc(s.mm, 1)
            strips(pe, multiply)

        def evacuate(eng, which, free):
            def body(st, par, col, wd):
                if not isinstance(st, int) or st >= 2:
                    eng.wait_ge(s.out_even if par == 0 else s.out_odd, (st - par) * (DMA // 2))
                for t in range(which, ntiles, 2):
                    bank = (par * ntiles + t) % nb
                    eng.wait_ge(s.mm, st * ntiles + t + 1)
                    if which == 0:
                        op = eng.activation(o_buf[:, par, t, :wd], acc[bank][:, :wd], ACT.Copy)
                    else:
                        op = eng.tensor_copy(o_buf[:, par, t, :wd], acc[bank][:, :wd])
                    op.then_inc(free, 1)
            return body

        @block.scalar
        def _(act):
            act.sem_inc(s.act_free, nb // 2)

            def split_hi(st, par, col, wd):
                if split:
                    act.wait_ge((s.w_even, s.w_odd)[par], (st - par) * (DMA // 2) + DMA)
                    if not isinstance(st, int) or st >= 2:
                        act.wait_ge(s.mm, (st - 1) * ntiles)
                    act.activation(w_hi[:, par, :, :wd], w_buf[:, par, :, :wd], ACT.Copy).then_inc(s.hi_done, 1)
            strips(act, split_hi, evacuate(act, 0, s.act_free))

        @block.vector
        def _(dve):
            dve.sem_inc(s.dve_free, nb // 2)

            def split_lo(st, par, col, wd):
                if split:
                    dve.wait_ge(s.hi_done, st + 1)
                    dve.tensor_tensor(w_lo[:, par, :, :wd], w_buf[:, par, :, :wd], w_hi[:, par, :, :wd], ALU.subtract).then_inc(s.lo_done, 1)
            strips(dve, split_lo, evacuate(dve, 1, s.dve_free))

        @block.gpsimd
        def _(pool):
            def store(st, par, col, wd):
                pool.wait_ge(s.act_free, (st + 1) * half + nb // 2)
                pool.wait_ge(s.dve_free, (st + 1) * half + nb // 2)
                pool.dma_start(o_v[:, :, bass.ds(col, wd)], o_buf[:, par, :, :wd]).then_inc(
                    s.out_even if par == 0 else s.out_odd, DMA)
            strips(pool, store)
            pool.wait_ge(s.out_even, DMA * ((total + 1) // 2))
            pool.wait_ge(s.out_odd, DMA * (total // 2))


def norm_stage(nc, name, ident, src, row0, ntiles, hT, tok0, norm=None, scale=None, shift=None, weight=None,
               res=None, gate=None, alpha=1.0, affine=None, keep=None, final=None, res_row0=0):
    eps2 = 1e-5 if norm == "ln" else 1e-6
    with stage(nc, name, "rows_in", "x_even", "x_odd", "r_even", "r_odd", "gated", "x_free", "chain", "xn", "turned", "ps_free", "var", "std", "kept_even", "kept_odd", "cols") as (block, s, sb, ps):
        x = sb("x", [P, 2, D])
        r = sb("r", [P, 2, D]) if res is not None else None
        gate_row = sb("gate_row", [P, D]) if res is not None else None
        g_row = sb("g_row", [P, D]) if affine else None
        b_row = sb("b_row", [P, D]) if affine else None
        f_row = sb("f_row", [P, D]) if final is not None else None
        xn = sb("xn", [P, 2, D])
        stats = sb("stats", [P, 2, 6])
        mv = sb("mv", [P, 2])
        rstd = sb("rstd", [P, 2])
        cols = sb("cols", [P, 3, KC])
        acc = [ps(f"acc{i}") for i in range(4)]
        n_rows = (res is not None) + 2 * bool(affine) + (final is not None)
        n_cols = (scale is not None) + (shift is not None) + (weight is not None)
        keeps = keep is not None
        n_norms = bool(affine) + bool(norm)

        @block.scalar
        def _(act):
            if res is not None:
                act.dma_start(gate_row[:], gate.partition_broadcast(P)).then_inc(s.rows_in, DMA)
            if affine:
                act.dma_start(g_row[:], affine[0].partition_broadcast(P)).then_inc(s.rows_in, DMA)
                act.dma_start(b_row[:], affine[1].partition_broadcast(P)).then_inc(s.rows_in, DMA)
            if final is not None:
                act.dma_start(f_row[:], final.partition_broadcast(P)).then_inc(s.rows_in, DMA)
            for c, v in enumerate((scale, shift, weight)):
                if v is not None:
                    act.dma_start(cols[:, c, :], col_view(v), allow_slow_non_contiguous=True).then_inc(s.rows_in, DMA)
            if scale is not None:
                act.wait_ge(s.cols, 1)
            with act.Fori(0, ntiles // 2) as i:
                for par in range(2):
                    for q in range(n_norms):
                        act.wait_ge(s.var, (2 * i + par) * n_norms + q + 1)
                        act.activation(rstd[:, 0:1], rstd[:, 1:2], ACT.Sqrt).then_inc(s.std, 1)
                    if norm and final is None:
                        act.wait_ge(s.turned, 2 * i + par + 1)
                        for k in range(KC):
                            bank = 2 * par + k // 4
                            op = act.activation(hT[:, k, bass.ds(i * (2 * P) + (tok0 + par * P), P)],
                                                acc[bank][:, (k % 4) * P:(k % 4 + 1) * P], ACT.Identity,
                                                scale=cols[:, 0, k:k + 1], bias=cols[:, 1, k:k + 1])
                        op.then_inc(s.ps_free, 1)

        @block.sync
        def _(sp):
            with sp.Fori(0, ntiles // 2) as i:
                for par in range(2):
                    sp.wait_ge(s.x_free, 2 * i + par + 1)
                    if res is not None:
                        sp.dma_start(r[:, par], res[bass.ds(i * (2 * P) + (res_row0 + par * P), P), :]).then_inc((s.r_even, s.r_odd)[par], DMA)
                    if keeps and final is None:
                        sp.wait_ge((s.kept_even, s.kept_odd)[par], i * DMA)
                    sp.dma_start(x[:, par], src[bass.ds(i * (2 * P) + (row0 + par * P), P), :]).then_inc((s.x_even, s.x_odd)[par], DMA)

        @block.gpsimd
        def _(pool):
            def gate_rows(t, par):
                if res is not None:
                    pool.wait_ge((s.r_even, s.r_odd)[par], (t - par) * (DMA // 2) + DMA)
                    pool.tensor_tensor(r[:, par], r[:, par], gate_row[:], ALU.mult).then_inc(s.gated, 1)

            def store(i, par):
                if keeps:
                    pool.wait_ge(s.chain, 2 * i + par + 1)
                    pool.dma_start(keep[bass.ds(i * (2 * P) + par * P, P), :],
                                   (xn if final is not None else x)[:, par]).then_inc((s.kept_even, s.kept_odd)[par], DMA)
            pool.wait_ge(s.rows_in, DMA * (n_rows + n_cols))
            gate_rows(0, 0)
            if ntiles > 2:
                with pool.Fori(0, ntiles // 2 - 1) as i:
                    gate_rows(2 * i + 1, 1)
                    store(i, 0)
                    gate_rows(2 * i + 2, 0)
                    store(i, 1)
            gate_rows(ntiles - 1, 1)
            store(ntiles // 2 - 1, 0)
            store(ntiles // 2 - 1, 1)
            if keeps:
                pool.wait_ge(s.kept_even, ntiles // 2 * DMA)
                pool.wait_ge(s.kept_odd, ntiles // 2 * DMA)

        @block.tensor
        def _(pe):
            if norm and final is None:
                pe.sem_inc(s.ps_free, 2)
                with pe.Fori(0, ntiles // 2) as i:
                    for par in range(2):
                        pe.wait_ge(s.xn, 2 * i + par + 1)
                        pe.wait_ge(s.ps_free, 2 * i + par + 1)
                        for k in range(KC):
                            bank = 2 * par + k // 4
                            op = pe.transpose(acc[bank][:, (k % 4) * P:(k % 4 + 1) * P], xn[:, par, k * P:(k + 1) * P], ident[:])
                        op.then_inc(s.turned, 1)

        @block.vector
        def _(dve):
            dve.sem_inc(s.x_free, 2)
            dve.wait_ge(s.rows_in, DMA * (n_rows + n_cols))
            if scale is not None:
                dve.tensor_scalar(cols[:, 0, :], cols[:, 0, :], 1.0, None, ALU.add)
                dve.drain()
                if weight is not None:
                    dve.tensor_tensor(cols[:, 0, :], cols[:, 0, :], cols[:, 2, :], ALU.mult)
                    dve.drain()
                dve.sem_inc(s.cols, 1)

            def norm_of(src_t, dst_t, kind, eps, nth):
                for hf in range(2):
                    dve.bn_stats(stats[:, hf, :], src_t[:, hf * 512:(hf + 1) * 512])
                dve.drain()
                dve.bn_aggr(mv[:], stats[:])
                dve.drain()
                if kind == "rms":
                    dve.scalar_tensor_tensor(rstd[:, 1:2], mv[:, 0:1], mv[:, 0:1], mv[:, 1:2], ALU.mult, ALU.add)
                    dve.drain()
                    dve.tensor_scalar(rstd[:, 1:2], rstd[:, 1:2], eps, None, ALU.add).then_inc(s.var, 1)
                else:
                    dve.tensor_scalar(rstd[:, 1:2], mv[:, 1:2], eps, None, ALU.add).then_inc(s.var, 1)
                dve.wait_ge(s.std, nth + 1)
                dve.reciprocal(rstd[:, 0:1], rstd[:, 0:1])
                dve.drain()
                if kind == "rms":
                    return dve.tensor_scalar(dst_t, src_t, rstd[:, 0:1], None, ALU.mult)
                return dve.tensor_scalar(dst_t, src_t, mv[:, 0:1], rstd[:, 0:1], ALU.subtract, ALU.mult)

            with dve.Fori(0, ntiles // 2) as i:
                for par in range(2):
                    xt = x[:, par]
                    dve.wait_ge((s.x_even, s.x_odd)[par], i * DMA + DMA)
                    if res is not None:
                        dve.wait_ge(s.gated, 2 * i + par + 1)
                        dve.scalar_tensor_tensor(xt, xt, alpha, r[:, par], ALU.mult, ALU.add)
                        dve.drain()
                    if affine:
                        norm_of(xt, xt, "ln", 1e-5, (2 * i + par) * n_norms)
                        dve.drain()
                        dve.tensor_tensor(xt, xt, g_row[:], ALU.mult)
                        dve.drain()
                        dve.tensor_tensor(xt, xt, b_row[:], ALU.add)
                        dve.drain()
                    if keeps and final is None:
                        dve.sem_inc(s.chain, 1)
                    if norm:
                        if final is not None:
                            dve.wait_ge((s.kept_even, s.kept_odd)[par], i * DMA)
                        else:
                            dve.wait_ge(s.turned, 2 * i + par)
                        norm_of(xt, xn[:, par], norm, eps2, (2 * i + par) * n_norms + n_norms - 1)
                        dve.drain()
                        if final is not None:
                            dve.tensor_tensor(xn[:, par], xn[:, par], f_row[:], ALU.mult)
                            dve.drain()
                            dve.sem_inc(s.chain, 1)
                        else:
                            dve.sem_inc(s.xn, 1)
                    dve.sem_inc(s.x_free, 1)
C_Q, C_K, C_V, C_R, C_LR, C_QB, C_GA, C_GB = 0, 512, 1024, 2048, 3072, 3088, 4368, 5392
GH, GDK, GDV, CH = 4, 128, 256, 64
LN_END = (D // P) * P


def gla_tables():
    j, i = np.arange(P)[:, None], np.arange(P)[None, :]
    same = (j // CH) == (i // CH)
    prefix = (same & (j <= i)).astype(np.float32) / 16.0
    suffix = (same & (j > i)).astype(np.float32) / 16.0
    causal = np.tile((same & (j <= i)).astype(np.uint32), (1, GH))
    return prefix, suffix, causal


def gla_stage(nc, ident, P1, w_lr, b_lr, norm_g, t_prefix, t_suffix, t_causal, YA):
    with stage(nc, "gla", "const", "init", "x_even", "x_odd", "lrT", "lrT_c", "z", "abs", "ln1", "g", "turned", "gsum", "dmid",
               "e_cum", "e_mid", "gla_ops", "scoresT", "masked", "kv", "state", "o_done", "sq", "var", "std", "e_gate", "y", "stored") as (block, s, sb, ps):
        x_all = sb("x_all", [P, 2, C_QB])
        ga = sb("ga", [P, 2, D])
        wlr = sb("wlr", [16, 512])
        blr = sb("blr", [1, 512])
        ones = sb("ones", [1, P])
        g_row = sb("g_row", [P, GH, GDV])
        prefix = sb("prefix", [P, P])
        suffix = sb("suffix", [P, P])
        causal = sb("causal", [P, GH * P], U32)
        lrT = sb("lrT", [16, P])
        za = sb("za", [P, 512])
        g = sb("g", [P, 512])
        dmid = sb("dmid", [P, GH * 2, CH])
        mid = sb("mid", [P, GH * 2, 1])
        e_cum = sb("e_cum", [P, 512])
        e_suf = sb("e_suf", [P, 512])
        e_up = sb("e_up", [P, 512])
        e_dn = sb("e_dn", [P, 512])
        qmid = sb("qmid", [P, 512])
        kmid = sb("kmid", [P, 512])
        qz = sb("qz", [P, 2, GH, P])
        kout = sb("kout", [P, 512])
        am = sb("am", [P, 512])
        S0 = sb("S0", [P, GH, GDV])
        S1 = sb("S1", [P, GH, GDV])
        sq = sb("sq", [P, GDV])
        ss = sb("ss", [P, GH])
        rs = sb("rs", [P, GH])
        eg = sb("eg", [P, 2, D])
        y = sb("y", [P, GH, GDV])
        pz = ps("pz")
        pq = ps("pq")
        pk = ps("pk")
        pg = ps("pg", [P, 1024])
        po = ps("po", [P, GH, GDV])
        pl = ps("pl")

        @block.sync
        def _(sp):
            sp.dma_start(wlr[:], w_lr).then_inc(s.const, DMA)
            sp.dma_start(blr[:], b_lr.rearrange("(a n) -> a n", a=1)).then_inc(s.const, DMA)
            sp.dma_start(prefix[:], t_prefix).then_inc(s.const, DMA)
            sp.dma_start(suffix[:], t_suffix).then_inc(s.const, DMA)
            sp.dma_start(causal[:], t_causal).then_inc(s.const, DMA)
            for h in range(GH):
                sp.dma_start(g_row[:, h, :], norm_g.partition_broadcast(P)).then_inc(s.const, DMA)
            def load(i, par):
                if not isinstance(i, int):
                    sp.wait_ge(s.y, 2 * i + (par - 1))
                tile = rows(i * (2 * P) + par * P)
                sp.dma_start(x_all[:, par], P1[tile, 0:C_QB]).then_inc((s.x_even, s.x_odd)[par], DMA)
                sp.dma_start(ga[:, par], P1[tile, C_GA:C_GB]).then_inc((s.x_even, s.x_odd)[par], DMA)
            load(0, 0)
            load(0, 1)
            with sp.Fori(1, NT // 2) as i:
                load(i, 0)
                load(i, 1)

        @block.gpsimd
        def _(pool):
            with pool.Fori(0, NT) as i:
                pool.wait_ge(s.y, i + 1)
                pool.dma_start(YA[rows(i * P), :], y[:].rearrange("p h v -> p (h v)")).then_inc(s.stored, DMA)
            pool.wait_ge(s.stored, NT * DMA)

        def arrived(eng, t, par):
            eng.wait_ge((s.x_even, s.x_odd)[par], (t - par) * DMA + 2 * DMA)

        @block.tensor
        def _(pe):
            pe.wait_ge(s.const, 9 * DMA)
            pe.wait_ge(s.init, 1)
            def turn(t, par):
                x = x_all[:, par]
                arrived(pe, t, par)
                pe.transpose(pl[:16, :P], x[:, C_LR:C_LR + 16], ident[:]).then_inc(s.lrT, 1)
                for h in range(GH):
                    pe.transpose(pq[:, h * P:(h + 1) * P], x[:, C_Q + h * P:C_Q + (h + 1) * P], ident[:])
                for h in range(GH):
                    op = pe.transpose(pk[:, h * P:(h + 1) * P], x[:, C_K + h * P:C_K + (h + 1) * P], ident[:])
                op.then_inc(s.turned, 1)

            def gate(t):
                pe.wait_ge(s.lrT_c, t + 1)
                pe.matmul(pz[:], lrT[:], wlr[:], start=True, stop=False)
                pe.matmul(pz[:], ones[:], blr[:], start=False, stop=True).then_inc(s.z, 1)

            def attend(t, par, more):
                x = x_all[:, par]
                pe.wait_ge(s.g, t + 1)
                for h in range(GH):
                    pe.matmul(pg[:, h * P:(h + 1) * P], g[:, h * P:(h + 1) * P], prefix[:], start=True, stop=True)
                pe.matmul(pg[:, 512:], suffix[:], g[:], start=True, stop=True).then_inc(s.gsum, 1)
                pe.wait_ge(s.gla_ops, t + 1)
                for h in range(GH):
                    op = pe.matmul(pz[:, h * P:(h + 1) * P], kmid[:, h * P:(h + 1) * P], qmid[:, h * P:(h + 1) * P], start=True, stop=True)
                op.then_inc(s.scoresT, 1)
                for h in range(GH):
                    op = pe.matmul(pg[:, h * GDV:(h + 1) * GDV], kout[:CH, h * P:(h + 1) * P], x[:CH, C_V + h * GDV:C_V + (h + 1) * GDV], start=True, stop=True)
                op.then_inc(s.kv, 1)
                if more:
                    turn(t + 1, 1 - par)
                pe.wait_ge(s.masked, t + 1)
                if more:
                    gate(t + 1)
                pe.wait_ge(s.state, 2 * t + 1)
                if not isinstance(t, int) or t:
                    pe.wait_ge(s.y, t)
                for h in range(GH):
                    pe.matmul(po[:, h, :], am[:, h * P:(h + 1) * P], x[:, C_V + h * GDV:C_V + (h + 1) * GDV], start=True, stop=False)
                    pe.matmul(po[:, h, :], qz[:, 0, h, :], S0[:, h, :], start=False, stop=False)
                    op = pe.matmul(po[:, h, :], qz[:, 1, h, :], S1[:, h, :], start=False, stop=True)
                op.then_inc(s.o_done, 1)
                for h in range(GH):
                    op = pe.matmul(pg[:, h * GDV:(h + 1) * GDV], kout[CH:, h * P:(h + 1) * P], x[CH:, C_V + h * GDV:C_V + (h + 1) * GDV], start=True, stop=True)
                op.then_inc(s.kv, 1)
            turn(0, 0)
            gate(0)
            attend(0, 0, True)
            attend(1, 1, True)
            with pe.Fori(1, NT // 2 - 1) as i:
                for par in range(2):
                    attend(2 * i + par, par, True)
            attend(NT - 2, 0, True)
            attend(NT - 1, 1, False)

        @block.scalar
        def _(act):
            def low_rank(t):
                act.wait_ge(s.lrT, t + 1)
                act.activation(lrT[:], pl[:16, :P], ACT.Copy).then_inc(s.lrT_c, 1)

            def log_gate(t):
                act.wait_ge(s.z, t + 1)
                act.activation(za[:], pz[:], ACT.Abs)
                act.drain()
                act.activation(za[:], za[:], ACT.Exp, scale=-1.0)
                act.drain()
                act.activation(za[:], za[:], ACT.Ln, bias=1.0).then_inc(s.ln1, 1)

            def body(t, par, more):
                act.wait_ge(s.gsum, t + 1)
                act.activation(e_cum[:], pg[:, :512], ACT.Exp)
                act.activation(e_suf[:], pg[:, 512:], ACT.Exp).then_inc(s.e_cum, 1)
                act.wait_ge(s.dmid, t + 1)
                act.activation(e_up[:], dmid[:], ACT.Exp)
                act.activation(e_dn[:], dmid[:], ACT.Exp, scale=-1.0).then_inc(s.e_mid, 1)
                if more:
                    low_rank(t + 1)
                arrived(act, t, par)
                if not isinstance(t, int) or t:
                    act.wait_ge(s.y, t)
                act.activation(eg[:, 0], x_all[:, par, C_R:C_R + D], ACT.Sigmoid)
                act.activation(eg[:, 1], ga[:, par], ACT.Sigmoid).then_inc(s.e_gate, 1)
                if more:
                    log_gate(t + 1)
                act.wait_ge(s.o_done, t + 1)
                for h in range(GH):
                    act.activation(sq[:], po[:, h, :], ACT.Square, accum_out=ss[:, h:h + 1])
                    act.drain()
                act.sem_inc(s.sq, 1)
                act.wait_ge(s.var, t + 1)
                act.activation(rs[:], ss[:], ACT.Sqrt).then_inc(s.std, 1)
            low_rank(0)
            log_gate(0)
            body(0, 0, True)
            body(1, 1, True)
            with act.Fori(1, NT // 2 - 1) as i:
                for par in range(2):
                    body(2 * i + par, par, True)
            body(NT - 2, 0, True)
            body(NT - 1, 1, False)

        @block.vector
        def _(dve):
            dve.memset(ones[:], 1.0)
            dve.memset(S0[:], 0.0)
            dve.memset(qz[:], 0.0)
            dve.memset(am[:], 0.0)
            dve.drain()
            dve.sem_inc(s.init, 1)
            dve.wait_ge(s.const, 9 * DMA)
            def decay(t):
                dve.wait_ge(s.ln1, t + 1)
                dve.scalar_tensor_tensor(g[:], pz[:], 0.0, za[:], ALU.min, ALU.subtract).then_inc(s.g, 1)

            def body(t, par, more=True):
                x = x_all[:, par]
                arrived(dve, t, par)
                dve.wait_ge(s.e_cum, t + 1)
                cum = pg[:, :512].rearrange("p (c j) -> p c j", j=CH)
                dve.tensor_copy(mid[:], cum[:, :, CH // 2 - 1:CH // 2])
                dve.drain()
                dve.tensor_tensor(dmid[:], cum, mid[:].broadcast_to([P, 2 * GH, CH]), ALU.subtract).then_inc(s.dmid, 1)
                dve.wait_ge(s.turned, t + 1)
                scale = float(GDK) ** -0.5
                q4 = pq[:].rearrange("p (h c j) -> p h c j", h=GH, c=2)
                e4 = e_cum[:].rearrange("p (h c j) -> p h c j", h=GH, c=2)
                for c in range(2):
                    dve.scalar_tensor_tensor(qz[:, c, :, c * CH:(c + 1) * CH], q4[:, :, c, :], scale, e4[:, :, c, :], ALU.mult, ALU.mult)
                dve.tensor_tensor(kout[:], x[:, C_K:C_K + 512], e_suf[:], ALU.mult)
                dve.wait_ge(s.e_mid, t + 1)
                dve.scalar_tensor_tensor(qmid[:], pq[:], scale, e_up[:], ALU.mult, ALU.mult)
                dve.tensor_tensor(kmid[:], pk[:], e_dn[:], ALU.mult)
                dve.drain()
                dve.sem_inc(s.gla_ops, 1)
                dve.wait_ge(s.init, 1)
                dve.wait_ge(s.scoresT, t + 1)
                dve.copy_predicated(am[:], causal[:], pz[:])
                dve.drain()
                dve.sem_inc(s.masked, 1)
                for c, (old, new) in enumerate(((S0, S1), (S1, S0))):
                    dve.wait_ge(s.kv, 2 * t + c + 1)
                    for h in range(GH):
                        last = h * P + c * CH + CH - 1
                        dve.scalar_tensor_tensor(new[:, h, :], old[:, h, :], e_cum[:, last:last + 1], pg[:, h * GDV:(h + 1) * GDV], ALU.mult, ALU.add)
                    dve.drain()
                    dve.sem_inc(s.state, 1)
                if more:
                    decay(t + 1)
                dve.wait_ge(s.e_gate, t + 1)
                dve.tensor_tensor(eg[:, 0], eg[:, 0], x[:, C_R:C_R + D], ALU.mult)
                dve.tensor_tensor(eg[:, 1], eg[:, 1], g_row[:].rearrange("p h v -> p (h v)"), ALU.mult)
                dve.drain()
                dve.tensor_tensor(eg[:, 0], eg[:, 0], eg[:, 1], ALU.mult)
                dve.wait_ge(s.sq, t + 1)
                dve.tensor_scalar(ss[:], ss[:], 1.0 / GDV, 1e-6, ALU.mult, ALU.add).then_inc(s.var, 1)
                dve.wait_ge(s.std, t + 1)
                dve.reciprocal(rs[:], rs[:])
                dve.drain()
                if not isinstance(t, int) or t:
                    dve.wait_ge(s.stored, t * DMA)
                for h in range(GH):
                    dve.scalar_tensor_tensor(y[:, h, :], po[:, h, :], rs[:, h:h + 1], eg[:, 0, h * GDV:(h + 1) * GDV], ALU.mult, ALU.mult)
                dve.drain()
                dve.sem_inc(s.y, 1)
            decay(0)
            body(0, 0)
            body(1, 1)
            with dve.Fori(1, NT // 2 - 1) as i:
                for par in range(2):
                    body(2 * i + par, par)
            body(NT - 2, 0)
            body(NT - 1, 1, more=False)


SH, SHD, SKV = 16, 64, 2
NEG = -1.0e30
ROPE_F = 8
TWO_PI = 2.0 * math.pi
PI_1 = 6.28125
PI_2 = float(np.float32(TWO_PI - PI_1))
PI_3 = float(np.float32(TWO_PI - PI_1 - float(np.float32(TWO_PI - PI_1))))
ROUND = 12582912.0
PI_LIM = 3.1415925


def swa_tables():
    q, k = np.arange(P)[:, None], np.arange(P)[None, :]
    prev = np.where(k > q, 0.0, NEG)
    cur = np.where(k <= q, 0.0, NEG)
    mask = np.concatenate([prev, cur], 1).astype(np.float32)
    first = np.concatenate([np.full((P, P), NEG), cur], 1).astype(np.float32)
    freq = (500000.0 ** (-(np.arange(0, 16, 2, dtype=np.float32) / 16))).astype(np.float32)
    return mask, first, np.tile(freq, NT)[None, :]


def reduced_sine(dve, out, ang, turns, quarter):
    dve.tensor_scalar(turns, ang, 1.0 / TWO_PI, quarter, ALU.mult, ALU.add)
    dve.drain()
    dve.tensor_scalar(turns, turns, ROUND, None, ALU.add)
    dve.drain()
    dve.tensor_scalar(turns, turns, ROUND, None, ALU.subtract)
    dve.drain()
    dve.scalar_tensor_tensor(out, turns, -PI_1, ang, ALU.mult, ALU.add)
    dve.drain()
    dve.scalar_tensor_tensor(out, turns, -PI_2, out, ALU.mult, ALU.add)
    dve.drain()
    dve.scalar_tensor_tensor(out, turns, -PI_3, out, ALU.mult, ALU.add)
    dve.drain()
    if quarter:
        dve.tensor_scalar(out, out, quarter * TWO_PI, None, ALU.add)
        dve.drain()
    dve.tensor_scalar(out, out, PI_LIM, -PI_LIM, ALU.min, ALU.max)
    dve.drain()


def swa_stage(nc, ident, P1, pos, sinks, t_mask, t_first, t_freq, YA, Y1):
    with stage(nc, "swa", "const", "init", "arg", "table", "x_even", "x_odd", "g_even", "g_odd", "roped", "turned", "qkT", "scores", "s_done", "s_free",
               "neg_max", "probs", "p_turned", "p_copied", "p_free", "pv", "e_gate", "y", "stored") as (block, s, sb, ps):
        x = sb("x", [P, 2, 1280])
        gb = sb("gb", [P, 2, D])
        ya = sb("ya", [P, 2, D])
        pos_i = sb("pos_i", [P, NT], I32)
        pos_f = sb("pos_f", [P, NT, 1])
        freq = sb("freq", [P, NT, ROPE_F])
        ang = sb("ang", [P, NT, ROPE_F])
        turns = sb("turns", [P, NT, ROPE_F])
        arg = sb("arg", [P, 2, NT, 1, ROPE_F])
        cs = sb("cs", [P, 2, NT, 1, ROPE_F])
        mask = sb("mask", [P, 1, 256])
        mask_even = sb("mask_even", [P, 1, 256])
        sink = sb("sink", [P, SH])
        rope = sb("rope", [P, 4, 18, ROPE_F])
        kdup = sb("kdup", [P, 2, 2, SHD])
        qT = sb("qT", [P, 8, P])
        kT = sb("kT", [P, 2, 2, P])
        vv = sb("vv", [P, 2, P])
        sc = sb("sc", [P, 2, 4, 256])
        mx = sb("mx", [P, SH])
        nm = sb("nm", [P, SH])
        dsink = sb("dsink", [P, SH])
        esink = sb("esink", [P, 2, SH])
        sums = sb("sums", [P, 2, SH])
        rden = sb("rden", [P, SH, 1])
        pT = sb("pT", [P, 2, 8, P])
        eg = sb("eg", [P, D])
        y = sb("y", [P, SH, SHD])
        pt = ps("pt", [P, 8, P])
        pS = [ps(f"pS{i}", [P, 4, 256]) for i in range(2)]
        po = ps("po", [P, SH, SHD])
        G = 4

        @block.sync
        def _(sp):
            sp.dma_start(pos_i[:], pos.rearrange("(t p) -> p t", p=P), allow_slow_non_contiguous=True).then_inc(s.const, DMA)
            sp.dma_start(freq[:], t_freq[0].partition_broadcast(P).rearrange("p (t f) -> p t f", f=ROPE_F)).then_inc(s.const, DMA)
            sp.dma_start(mask[:, 0], t_mask).then_inc(s.const, DMA)
            sp.dma_start(mask_even[:, 0], t_first).then_inc(s.const, DMA)
            sp.dma_start(sink[:], sinks.partition_broadcast(P)).then_inc(s.const, DMA)
            def load(i, par):
                tile = rows(i * (2 * P) + par * P)
                if not isinstance(i, int):
                    sp.wait_ge(s.qkT, 2 * i + (par - 1))
                sp.dma_start(x[:, par], P1[tile, C_QB:C_GA]).then_inc((s.x_even, s.x_odd)[par], DMA)
                if not isinstance(i, int):
                    sp.wait_ge(s.y, 2 * i + (par - 1))
                sp.dma_start(gb[:, par], P1[tile, C_GB:C_GB + D]).then_inc((s.g_even, s.g_odd)[par], DMA)
                sp.dma_start(ya[:, par], YA[tile, :]).then_inc((s.g_even, s.g_odd)[par], DMA)
            load(0, 0)
            load(0, 1)
            with sp.Fori(1, NT // 2) as i:
                load(i, 0)
                load(i, 1)

        @block.gpsimd
        def _(pool):
            with pool.Fori(0, NT) as i:
                pool.wait_ge(s.y, i + 1)
                pool.dma_start(Y1[rows(i * P), :], y[:].rearrange("p h d -> p (h d)")).then_inc(s.stored, DMA)
            pool.wait_ge(s.stored, NT * DMA)

        @block.tensor
        def _(pe):
            pe.wait_ge(s.init, 1)
            def turn(t, par):
                pe.wait_ge(s.roped, t + 1)
                if not isinstance(t, int) or t:
                    pe.wait_ge(s.p_copied, t * G)
                for c in range(8):
                    pe.transpose(pt[:, c, :], x[:, par, c * P:(c + 1) * P], ident[:])
                for c in range(2):
                    op = pe.transpose(pS[1][:, c, :P], kdup[:, c].rearrange("p a d -> p (a d)"), ident[:])
                op.then_inc(s.turned, 1)

            def score(t, par, g):
                pe.wait_ge(s.s_free, t * G + g + 1)
                for h in range(4):
                    hd, base, slot = 4 * g + h, (h % 2) * SHD, (h % 2) * 2 + h // 2
                    for side, kp in ((0, 1 - par), (1, par)):
                        op = pe.matmul(pS[g % 2][:, slot, side * P:(side + 1) * P], qT[base:base + SHD, hd // 2, :],
                                       kT[base:base + SHD, kp, hd // 8, :], start=True, stop=True)
                op.then_inc(s.scores, 1)

            def attend(t, par):
                pe.wait_ge(s.qkT, t + 1)
                score(t, par, 0)
                score(t, par, 1)
                for q in range(G):
                    pe.wait_ge(s.probs, t * G + q + 1)
                    if q:
                        pe.wait_ge(s.p_copied, t * G + q)
                    for c in range(8):
                        op = pe.transpose(pt[:, c, :], sc[:, q % 2, c // 2, (c % 2) * P:(c % 2 + 1) * P], ident[:])
                    op.then_inc(s.p_turned, 1)
                    if q + 2 < G:
                        score(t, par, q + 2)
                    pe.wait_ge(s.p_copied, t * G + q + 1)
                    if q == 0:
                        if not isinstance(t, int) or t:
                            pe.wait_ge(s.y, t)
                    for h in range(4):
                        hd = 4 * q + h
                        kv = hd // 8
                        slot = (h % 2) * 2 + h // 2
                        pe.matmul(po[:, hd, :], pT[:, q % 2, 2 * slot, :], vv[:, 1 - par, kv * SHD:(kv + 1) * SHD], start=True, stop=False)
                        op = pe.matmul(po[:, hd, :], pT[:, q % 2, 2 * slot + 1, :], vv[:, par, kv * SHD:(kv + 1) * SHD], start=False, stop=True)
                    op.then_inc(s.pv, 1)

            turn(0, 0)
            attend(0, 0)
            turn(1, 1)
            attend(1, 1)
            with pe.Fori(1, NT // 2) as i:
                for par in range(2):
                    turn(2 * i + par, par)
                    attend(2 * i + par, par)

        @block.scalar
        def _(act):
            act.wait_ge(s.arg, 1)
            act.activation(cs[:], arg[:], ACT.Sin).then_inc(s.table, 1)
            with act.Fori(0, NT // 2) as i:
                for par in range(2):
                    t = 2 * i + par
                    act.wait_ge(s.turned, t + 1)
                    act.activation(vv[:, par, :], x[:, par, D + P:D + 2 * P], ACT.Copy)
                    act.activation(qT[:], pt[:], ACT.Copy)
                    act.activation(kT[:, par], pS[1][:, 0:2, :P], ACT.Copy)
                    act.drain()
                    act.sem_inc(s.qkT, 1)
                    for g in range(G + 1):
                        if g:
                            q = g - 1
                            act.wait_ge(s.p_turned, t * G + q + 1)
                            if q >= 2:
                                act.wait_ge(s.pv, t * G + q - 1)
                            act.activation(pT[:, q % 2], pt[:], ACT.Copy).then_inc(s.p_copied, 1)
                        if g < G:
                            act.wait_ge(s.neg_max, t * G + g + 1)
                            for h in range(4):
                                hd, slot = 4 * g + h, (h % 2) * 2 + h // 2
                                act.activation(sc[:, g % 2, slot, :], sc[:, g % 2, slot, :], ACT.Exp, bias=nm[:, hd:hd + 1], accum_out=sums[:, par, hd:hd + 1])
                            act.activation(esink[:, par, 4 * g:4 * g + 4], dsink[:, 4 * g:4 * g + 4], ACT.Exp)
                            act.drain()
                            act.sem_inc(s.probs, 1)
                    act.wait_ge((s.g_even, s.g_odd)[par], (i + 1) * (2 * DMA))
                    act.wait_ge(s.y, t)
                    act.activation(eg[:], gb[:, par], ACT.Sigmoid).then_inc(s.e_gate, 1)

        @block.vector
        def _(dve):
            dve.memset(kT[:], 0.0)
            dve.memset(vv[:], 0.0)
            dve.drain()
            dve.sem_inc(s.init, 1)
            dve.sem_inc(s.s_free, 2)
            dve.wait_ge(s.const, 5 * DMA)
            dve.tensor_copy(pos_f[:, :, 0], pos_i[:])
            dve.drain()
            dve.tensor_tensor(ang[:], freq[:], pos_f[:].broadcast_to([P, NT, ROPE_F]), ALU.mult)
            dve.drain()
            reduced_sine(dve, arg[:, 0, :, 0, :], ang[:], turns[:], 0.25)
            reduced_sine(dve, arg[:, 1, :, 0, :], ang[:], turns[:], 0.0)
            dve.sem_inc(s.arg, 1)
            dve.wait_ge(s.table, 1)
            def rope_block(t, par):
                dve.wait_ge((s.x_even, s.x_odd)[par], (t - par) * (DMA // 2) + DMA)
                heads = x[:, par, :18 * SHD].rearrange("p (h d) -> p h d", d=SHD)
                a, b = heads[:, :, 0:ROPE_F], heads[:, :, ROPE_F:2 * ROPE_F]
                cos, sin = (cs[:, c, bass.ds(t, 1), 0, :].broadcast_to([P, 18, ROPE_F]) for c in range(2))
                for n, (u, w) in enumerate(((a, cos), (b, sin), (b, cos), (a, sin))):
                    dve.tensor_tensor(rope[:, n], u, w, ALU.mult)
                dve.drain()
                dve.tensor_tensor(a, rope[:, 0], rope[:, 1], ALU.subtract)
                dve.tensor_tensor(b, rope[:, 2], rope[:, 3], ALU.add)
                dve.drain()
                if not isinstance(t, int) or t:
                    dve.wait_ge(s.turned, t)
                for c in range(2):
                    for r in range(2):
                        dve.tensor_copy(kdup[:, c, r, :], x[:, par, D + c * SHD:D + (c + 1) * SHD])
                dve.drain()
                dve.sem_inc(s.roped, 1)

            def scores(t, par, g):
                dve.wait_ge(s.scores, t * G + g + 1)
                if g >= 2:
                    dve.wait_ge(s.p_turned, t * G + g - 1)
                elif not isinstance(t, int) or t:
                    dve.wait_ge(s.p_turned, t * G + g - 1)
                mk = (mask_even if par == 0 else mask)[:].broadcast_to([P, 4, 256])
                dve.scalar_tensor_tensor(sc[:, g % 2], pS[g % 2][:], SHD ** -0.5, mk, ALU.mult, ALU.add)
                dve.drain()
                dve.sem_inc(s.s_free, 1)
                hs = slice(4 * g, 4 * g + 4)
                dve.tensor_reduce(mx[:, hs].rearrange("p (b a) -> p a b", a=2), sc[:, g % 2].rearrange("p (a b) k -> p a b k", a=2), AX_X, ALU.max)
                dve.drain()
                dve.tensor_tensor(mx[:, hs], mx[:, hs], sink[:, hs], ALU.max)
                dve.drain()
                dve.tensor_scalar(nm[:, hs], mx[:, hs], -1.0, None, ALU.mult)
                dve.tensor_tensor(dsink[:, hs], sink[:, hs], mx[:, hs], ALU.subtract)
                dve.drain()
                dve.sem_inc(s.neg_max, 1)

            def output(t, par):
                dve.wait_ge(s.e_gate, t + 1)
                dve.tensor_tensor(rden[:, :, 0], sums[:, par], esink[:, par], ALU.add)
                dve.drain()
                dve.reciprocal(rden[:], rden[:])
                dve.drain()
                dve.wait_ge(s.pv, t * G + G)
                if not isinstance(t, int) or t:
                    dve.wait_ge(s.stored, t * DMA)
                dve.tensor_tensor(y[:], po[:], rden[:].broadcast_to([P, SH, SHD]), ALU.mult)
                dve.drain()
                yf = y[:].rearrange("p h d -> p (h d)")
                dve.tensor_tensor(yf, yf, eg[:], ALU.mult)
                dve.drain()
                dve.wait_ge((s.g_even, s.g_odd)[par], (t - par) * DMA + 2 * DMA)
                dve.tensor_tensor(yf, yf, ya[:, par], ALU.add)
                dve.drain()
                dve.sem_inc(s.y, 1)

            def block_step(t, par, before=True, behind=True):
                scores(t, par, 0)
                if before:
                    output(t - 1, 1 - par)
                scores(t, par, 1)
                scores(t, par, 2)
                scores(t, par, 3)
                if behind:
                    rope_block(t + 1, 1 - par)
            rope_block(0, 0)
            block_step(0, 0, before=False)
            dve.tensor_copy(mask_even[:], mask[:])
            dve.drain()
            block_step(1, 1)
            with dve.Fori(1, NT // 2 - 1) as i:
                for par in range(2):
                    block_step(2 * i + par, par)
            block_step(NT - 2, 0)
            block_step(NT - 1, 1, behind=False)
            output(NT - 1, 1)


def ffn_up_stage(nc, ident, hi, lo, w_up, conv_w, conv_b, fT):
    with stage(nc, "up", "taps_in", "taps_T", "taps", "w_in", "hi_done", "lo_done", "mm", "act_c", "conv", "gelu", "ps_free") as (block, s, sb, ps):
        raw = sb("raw", [2 * FC, 4, P])
        taps = sb("taps", [P, 4, 2 * FC])
        w_buf = sb("w_buf", [P, 2, KC, P])
        w_hi = sb("w_hi", [P, 2, 2, KC, P], F32R)
        w_lo = sb("w_lo", [P, 2, 2, KC, P], F32R)
        cv = sb("cv", [P, 2, SEQ])
        acc = [[ps(f"acc{i}{j}", [P, SEQ]) for j in range(2)] for i in range(2)]
        w_v = w_up.rearrange("(k p) n -> p k n", p=P)

        def strips(eng, body, behind):
            for j in range(2):
                body(j, j)
                if j:
                    behind(0, 0)
            with eng.Fori(1, FC // 2) as i:
                for par in range(2):
                    body(2 * i + par, par)
                    behind(2 * i + (par - 1), 1 - par)
            behind(FC - 1, 1)

        @block.sync
        def _(sp):
            for tap in range(3):
                sp.dma_start(raw[:, tap, :], conv_w[tap].rearrange("(j p) -> j p", p=P)).then_inc(s.taps_in, DMA)
            sp.dma_start(raw[:, 3, :], conv_b.rearrange("(j p) -> j p", p=P)).then_inc(s.taps_in, DMA)
            with sp.Fori(0, FC) as j:
                sp.wait_ge(s.lo_done, j)
                for side in range(2):
                    sp.dma_start(w_buf[:, side], w_v[:, :, bass.ds(j * P + side * D_FF, P)]).then_inc(s.w_in, DMA)

        @block.tensor
        def _(pe):
            pe.wait_ge(s.taps_in, 4 * DMA)
            for c in range(4):
                op = pe.transpose(acc[0][0][:, c * P:c * P + 2 * FC], raw[:, c, :], ident[:2 * FC, :2 * FC])
            op.then_inc(s.taps_T, 1)
            with pe.Fori(0, FC // 2) as i:
                for par in range(2):
                    pe.wait_ge(s.ps_free, 2 * i + par + 1)
                    pe.wait_ge(s.lo_done, 2 * i + par + 1)
                    for side in range(2):
                        for k in range(KC):
                            for wt, ht in ((w_hi, hi), (w_hi, lo), (w_lo, hi)):
                                for hf in range(2):
                                    cols = slice(hf * 512, (hf + 1) * 512)
                                    op = pe.matmul(acc[par][side][:, cols], wt[:, par, side, k, :], ht[:, k, cols],
                                                   start=k == 0 and wt is w_hi and ht is hi, stop=k == KC - 1 and wt is w_lo)
                        op.then_inc(s.mm, 1)

        @block.scalar
        def _(act):
            act.wait_ge(s.taps, 1)

            def split_hi(j, par):
                act.wait_ge(s.w_in, j * (2 * DMA) + 2 * DMA)
                if not isinstance(j, int):
                    act.wait_ge(s.mm, (j - 1) * 2)
                act.activation(w_hi[:, par], w_buf[:], ACT.Copy).then_inc(s.hi_done, 1)

            def convolve(j, par):
                for side in range(2):
                    act.wait_ge(s.mm, j * 2 + side + 1)
                    act.wait_ge(s.conv, j * 3)
                    col = bass.ds(j + side * FC, 1)
                    act.activation(cv[:, side], acc[par][side][:], ACT.Identity, scale=taps[:, 2, col], bias=taps[:, 3, col]).then_inc(s.act_c, 1)
                    if side == 1:
                        act.wait_ge(s.conv, j * 3 + 1)
                        act.activation(cv[:, 0], cv[:, 0], ACT.Gelu).then_inc(s.gelu, 1)
            strips(act, split_hi, convolve)

        @block.vector
        def _(dve):
            dve.wait_ge(s.taps_T, 1)
            for c in range(4):
                dve.tensor_copy(taps[:, c, :], acc[0][0][:, c * P:c * P + 2 * FC])
            dve.drain()
            dve.sem_inc(s.taps, 1)
            dve.sem_inc(s.ps_free, 2)

            def split_lo(j, par):
                dve.wait_ge(s.hi_done, j + 1)
                dve.tensor_tensor(w_lo[:, par], w_buf[:], w_hi[:, par], ALU.subtract).then_inc(s.lo_done, 1)

            def convolve(j, par):
                for side in range(2):
                    col = bass.ds(j + side * FC, 1)
                    dve.wait_ge(s.act_c, j * 2 + side + 1)
                    for lag, tap in ((1, 1), (2, 0)):
                        dve.scalar_tensor_tensor(cv[:, side, lag:], acc[par][side][:, :SEQ - lag], taps[:, tap, col], cv[:, side, lag:], ALU.mult, ALU.add)
                        dve.drain()
                    dve.sem_inc(s.conv, 1)
                dve.sem_inc(s.ps_free, 1)
                dve.wait_ge(s.gelu, j + 1)
                dve.tensor_tensor(fT[:, bass.ds(j, 1), :].rearrange("p a t -> p (a t)"), cv[:, 0], cv[:, 1], ALU.mult)
                dve.drain()
                dve.sem_inc(s.conv, 1)
            strips(dve, split_lo, convolve)
def turn_stage(nc, name, ident, parts, ntiles, hi, lo, gates=None):
    n_in = len(parts) * (2 if gates else 1)
    W = D // len(parts)
    with stage(nc, name, "x_even", "x_odd", "silu", "gated", "turned", "hi_done", "lo_done") as (block, s, sb, ps):
        x = sb("x", [P, 2, len(parts), W])
        z = sb("z", [P, 2, len(parts), W]) if gates else None
        acc = [ps(f"acc{i}") for i in range(4)]
        arrived = lambda eng, i, par: eng.wait_ge((s.x_even, s.x_odd)[par], i * (n_in * DMA) + n_in * DMA)

        @block.sync
        def _(sp):
            def load(i, par):
                if not isinstance(i, int):
                    sp.wait_ge(s.turned, 4 * i + (2 * par - 2))
                t = rows(i * (2 * P) + par * P)
                for n in range(len(parts)):
                    sp.dma_start(x[:, par, n], parts[n][t, :]).then_inc((s.x_even, s.x_odd)[par], DMA)
                    if gates:
                        sp.dma_start(z[:, par, n], gates[n][t, :]).then_inc((s.x_even, s.x_odd)[par], DMA)
            load(0, 0)
            load(0, 1)
            with sp.Fori(1, ntiles // 2) as i:
                load(i, 0)
                load(i, 1)

        @block.tensor
        def _(pe):
            pe.sem_inc(s.lo_done, 4)
            with pe.Fori(0, ntiles // 2) as i:
                for par in range(2):
                    t = 2 * i + par
                    arrived(pe, i, par)
                    if gates:
                        pe.wait_ge(s.gated, t + 1)
                    for hf in range(2):
                        pe.wait_ge(s.lo_done, 2 * t + (hf + 1))
                        for k in range(4):
                            c = hf * 4 + k
                            op = pe.transpose(acc[2 * par + hf][:, k * P:(k + 1) * P], x[:, par].rearrange("p n c -> p (n c)")[:, c * P:(c + 1) * P], ident[:])
                        op.then_inc(s.turned, 1)

        @block.scalar
        def _(act):
            def gate(i, par):
                if gates:
                    arrived(act, i, par)
                    act.activation(z[:, par], z[:, par], ACT.Silu).then_inc(s.silu, 1)

            def leading(i, par):
                for hf in range(2):
                    act.wait_ge(s.turned, (2 * i + par) * 2 + (hf + 1))
                    act.activation(hi[:, hf * 4:hf * 4 + 4, rows(i * (2 * P) + par * P)], acc[2 * par + hf][:].rearrange("p (k t) -> p k t", k=4), ACT.Copy).then_inc(s.hi_done, 1)
            gate(0, 0)
            with act.Fori(0, ntiles // 2 - 1) as i:
                gate(i, 1)
                leading(i, 0)
                gate(i + 1, 0)
                leading(i, 1)
            gate(ntiles // 2 - 1, 1)
            leading(ntiles // 2 - 1, 0)
            leading(ntiles // 2 - 1, 1)

        @block.vector
        def _(dve):
            def multiply(i, par):
                if gates:
                    dve.wait_ge(s.silu, 2 * i + par + 1)
                    dve.tensor_tensor(x[:, par], x[:, par], z[:, par], ALU.mult).then_inc(s.gated, 1)

            def rest(i, par):
                for hf in range(2):
                    dve.wait_ge(s.hi_done, (2 * i + par) * 2 + (hf + 1))
                    at = (slice(None), slice(hf * 4, hf * 4 + 4), rows(i * (2 * P) + par * P))
                    dve.tensor_tensor(lo[at], acc[2 * par + hf][:].rearrange("p (k t) -> p k t", k=4), hi[at], ALU.subtract).then_inc(s.lo_done, 1)
            multiply(0, 0)
            with dve.Fori(0, ntiles // 2 - 1) as i:
                multiply(i, 1)
                rest(i, 0)
                multiply(i + 1, 0)
                rest(i, 1)
            multiply(ntiles // 2 - 1, 1)
            rest(ntiles // 2 - 1, 0)
            rest(ntiles // 2 - 1, 1)


U_RQ, U_RV, U_RZ, U_WZ, U_SHIFT, SHIFT_W, EVEN_IN = 0, 1024, 1536, 2048, 2560, 1792, 4352
HN, HD = 8, 64
BWD_ORDER = [1, 0] + list(range(NTA - 1, NTC - 1, -1))


def retention_tables():
    nf = 16
    t = np.arange(SEQ)
    inv = (10000.0 ** (-np.arange(nf, dtype=np.float32) / nf)).astype(np.float32)
    ang = np.concatenate([(t // 64).astype(np.float32)[:, None] * inv, (t % 64).astype(np.float32)[:, None] * inv], -1).astype(np.float32)
    rope = np.zeros((ALL, 2, 32), np.float32)
    rope[:CTX, 0] = 1.0
    rope[CTX:, 0], rope[CTX:, 1] = np.cos(ang), np.sin(ang)
    sk, tq = np.arange(P)[:, None], np.arange(P)[None, :]
    dist = np.stack([np.maximum(tq - sk, 0), tq >= sk, np.maximum(sk - tq, 0), sk >= tq], 1).astype(np.float32)
    pos = np.arange(P, dtype=np.float32)
    q_pos = np.stack([pos + 1, P - pos])
    k_pos = np.stack([P - 1 - pos, pos], 1)
    return rope.reshape(ALL, 64), dist, q_pos, k_pos


def retention_stage(nc, ident, U2, decay, t_rope, t_dist, t_qpos, t_kpos, YB2):
    with stage(nc, "ret", "const", "init", "dec", "exps", "dmat", "in0", "in1", "in2", "in3", "in4", "ropes_even", "ropes_odd", "rope_free", "k_dec", "kv",
               "kv_out", "cur", "state", "states", "turned", "qk", "q_dec", "scores", "am", "y_done", "sq", "var", "std", "z_even", "z_odd", "silu", "y", "stored") as (block, s, sb, ps):
        qkv = sb("qkv", [P, NTA, 1536])
        rp = sb("rp", [P, 2, 2, 32])
        dist = sb("dist", [P, 4, P])
        qpos = sb("qpos", [P, 2, P])
        kpos = sb("kpos", [P, 2])
        lg_all = sb("lg_all", [P, 2, HN])
        lg_half = sb("lg_half", [P, 2, 4])
        kdec = sb("kdec", [P, 2, HN, 1])
        gch = sb("gch", [P, 2, 4, 1])
        dm = sb("dm", [P, HN, P])
        dtmp = sb("dtmp", [P, 2, HN, P])
        qdec = sb("qdec", [P, 2, 4, P])
        tmp = sb("tmp", [P, 4, 16, 32])
        kd = sb("kd", [P, 2, 2, 512])
        kv = sb("kv", [P, NTA, 2, 4, HD])
        run = sb("run", [P, 2, 2, 4, HD])
        qT = sb("qT", [P, 4, P])
        kT = sb("kT", [P, 4, P])
        qd = sb("qd", [P, 2, 2, 4, P])
        am = sb("am", [P, 2, 2, 4, P])
        sq = sb("sq", [P, HN, HD])
        ss = sb("ss", [P, HN])
        rs = sb("rs", [P, HN, 1])
        z = sb("z", [P, 2, 512])
        y = sb("y", [P, HN, HD])
        pkv = [ps(f"pkv{i}", [P, 4, P]) for i in range(2)]
        pq = ps("pq", [P, 4, P])
        pk = ps("pk", [P, 4, P])
        pa = [ps(f"pa{i}", [P, 4, P]) for i in range(2)]
        po = ps("po", [P, HN, HD])
        cur = sb("cur", [P, 2, 1024])
        st = sb("st", [P, 2, 2, 4, P])
        loaded = (s.in0, s.in1, s.in2, s.in3, s.in4)
        u_v = U2.rearrange("(t p) n -> p t n", p=P)

        def ahead(eng, front, back):
            front(0, 0)
            for t in range(2):
                front(t + 1, 1 - t % 2)
                back(t, t % 2)
            with eng.Fori(1, NTA // 2 - 1) as i:
                for par in range(2):
                    front(2 * i + par + 1, 1 - par)
                    back(2 * i + par, par)
            front(NTA - 1, 1)
            back(NTA - 2, 0)
            back(NTA - 1, 1)

        def later(t, least=1):
            return not isinstance(t, int) or t >= least

        @block.sync
        def _(sp):
            for a in range(2):
                half = decay.rearrange("d (b a) -> a d b", a=2)[a]
                sp.dma_start(lg_half[a * HD:(a + 1) * HD], half.partition_broadcast(HD), allow_slow_non_contiguous=True).then_inc(s.const, DMA)
            sp.dma_start(lg_all[:], decay.partition_broadcast(P)).then_inc(s.const, DMA)
            sp.dma_start(dist[:], t_dist).then_inc(s.const, DMA)
            sp.dma_start(qpos[:], t_qpos.partition_broadcast(P)).then_inc(s.const, DMA)
            sp.dma_start(kpos[:], t_kpos).then_inc(s.const, DMA)
            for t in range(5):
                sp.dma_start(qkv[:, 2 * t:2 * t + 2], u_v[:, 2 * t:2 * t + 2, 0:1536]).then_inc(loaded[t], DMA)
            with sp.Fori(0, NTA // 2) as i:
                for par in range(2):
                    sp.wait_ge(s.rope_free, 2 * i + par + 1)
                    sp.dma_start(rp[:, par], t_rope[rows(i * (2 * P) + par * P), :].rearrange("p (c f) -> p c f", c=2)).then_inc((s.ropes_even, s.ropes_odd)[par], DMA)
            def load_z(i, par):
                sp.dma_start(z[:, par], U2[rows(i * (2 * P) + par * P), U_RZ:U_WZ]).then_inc((s.z_even, s.z_odd)[par], DMA)

            def store(i, par):
                sp.wait_ge(s.y, 2 * i + par + 1)
                sp.dma_start(YB2[rows(i * (2 * P) + par * P), 0:512], y[:].rearrange("p h d -> p (h d)")).then_inc(s.stored, DMA)
            load_z(0, 0)
            load_z(0, 1)
            with sp.Fori(0, NTA // 2 - 1) as i:
                for par in range(2):
                    store(i, par)
                    load_z(i + 1, par)
            store(NTA // 2 - 1, 0)
            store(NTA // 2 - 1, 1)
            sp.wait_ge(s.stored, NTA * DMA)

        @block.gpsimd
        def _(pool):
            pool.memset(st[:], 0.0)
            pool.drain()
            pool.wait_ge(s.states, 1)

            def place(t, par):
                if later(t, 2):
                    pool.wait_ge(s.turned, t - 1)
                pool.tensor_copy(cur[:, par], qkv[:, bass.ds(t, 1), 0:1024].rearrange("p a n -> p (a n)"))
                pool.drain()
                pool.sem_inc(s.cur, 1)
                if later(t, 2):
                    pool.wait_ge(s.y_done, t - 1)
                for a in range(2):
                    e = slice(a * HD, (a + 1) * HD)
                    pool.tensor_copy(st[e, par, :, :, e], kv[e, bass.ds(t, 1)].rearrange("p t a b e -> p (t a) b e"))
                    pool.drain()
                pool.sem_inc(s.state, 1)
            place(0, 0)
            place(1, 1)
            with pool.Fori(1, NTA // 2) as i:
                place(2 * i, 0)
                place(2 * i + 1, 1)

        @block.tensor
        def _(pe):
            pe.wait_ge(s.init, 1)
            with pe.Fori(0, NTA // 2) as i:
                for par in range(2):
                    t = 2 * i + par
                    pe.wait_ge(s.k_dec, t + 1)
                    pe.wait_ge(s.kv_out, t)
                    for d in range(2):
                        for b in range(4):
                            op = pe.matmul(pkv[d][:, b, :], kd[:, par, d, b * P:(b + 1) * P],
                                           qkv[:, bass.ds(t, 1), 1024 + b * P:1024 + (b + 1) * P].rearrange("p a n -> p (a n)"), start=True, stop=True)
                    op.then_inc(s.kv, 1)

            def score(t, par):
                pe.wait_ge(s.cur, t + 1)
                if later(t):
                    pe.wait_ge(s.qk, t)
                for b in range(4):
                    pe.transpose(pq[:, b, :], cur[:, par, b * P:(b + 1) * P], ident[:])
                for b in range(4):
                    op = pe.transpose(pk[:, b, :], cur[:, par, 512 + b * P:512 + (b + 1) * P], ident[:])
                op.then_inc(s.turned, 1)
                pe.wait_ge(s.qk, t + 1)
                if later(t):
                    pe.wait_ge(s.am, t)
                for h in range(HN):
                    base = (h % 2) * HD
                    op = pe.matmul(pa[h % 2][:, h // 2, :], kT[base:base + HD, h // 2, :], qT[base:base + HD, h // 2, :], start=True, stop=True)
                op.then_inc(s.scores, 1)

            def output(t, par):
                pe.wait_ge(s.q_dec, t + 1)
                pe.wait_ge(s.am, t + 1)
                pe.wait_ge(s.state, t + 1)
                if later(t):
                    pe.wait_ge(s.y, t)
                for b in range(4):
                    pair = po[:, 2 * b:2 * b + 2, :].rearrange("p h d -> p (h d)")
                    pe.matmul(pair, qd[:, par, 0, b, :], st[:, par, 0, b, :], start=True, stop=False)
                    pe.matmul(pair, qd[:, par, 1, b, :], st[:, par, 1, b, :], start=False, stop=False)
                    for a in range(2):
                        h = 2 * b + a
                        op = pe.matmul(po[:, h, :], am[:, par, a, b, :], qkv[:, bass.ds(t, 1), 1024 + h * HD:1024 + (h + 1) * HD].rearrange("p a n -> p (a n)"),
                                       start=False, stop=a == 1)
                op.then_inc(s.y_done, 1)
            ahead(pe, score, output)

        @block.scalar
        def _(act):
            act.wait_ge(s.const, 6 * DMA)
            act.activation(lg_all[:], lg_all[:], ACT.Exp)
            act.activation(lg_half[:], lg_half[:], ACT.Exp).then_inc(s.exps, 1)
            act.wait_ge(s.dec, 1)
            act.activation(kdec[:], kdec[:], ACT.Exp)
            act.activation(gch[:, :, :, 0], lg_half[:], ACT.Exp, scale=float(P))
            for d in range(2):
                for b in range(4):
                    act.activation(qdec[:, d, b, :], qpos[:, d, :], ACT.Exp, scale=lg_half[:, d, b:b + 1])
                for h in range(HN):
                    act.activation(dtmp[:, d, h, :], dist[:, 2 * d, :], ACT.Exp, scale=lg_all[:, d, h:h + 1])
            act.drain()
            act.sem_inc(s.dmat, 1)
            def copy_out(t, par):
                act.wait_ge(s.turned, t + 1)
                if later(t):
                    act.wait_ge(s.scores, t)
                    act.wait_ge(s.q_dec, t)
                act.activation(qT[:], pq[:], ACT.Copy)
                act.activation(kT[:], pk[:], ACT.Copy).then_inc(s.qk, 1)

            def finish(t, par):
                act.wait_ge((s.z_even, s.z_odd)[par], (t - par) * (DMA // 2) + DMA)
                act.activation(z[:, par], z[:, par], ACT.Silu).then_inc(s.silu, 1)
                act.wait_ge(s.y_done, t + 1)
                act.activation(sq[:], po[:], ACT.Square)
                act.drain()
                act.sem_inc(s.sq, 1)
                act.wait_ge(s.var, t + 1)
                act.activation(rs[:, :, 0], ss[:], ACT.Sqrt).then_inc(s.std, 1)
            ahead(act, copy_out, finish)

        @block.vector
        def _(dve):
            dve.memset(run[:], 0.0)
            dve.sem_inc(s.rope_free, 2)
            dve.wait_ge(s.exps, 1)
            dve.tensor_scalar(lg_all[:], lg_all[:], -1.0, None, ALU.mult)
            dve.tensor_scalar(lg_half[:], lg_half[:], -1.0, None, ALU.mult)
            dve.drain()
            for d in range(2):
                dve.tensor_scalar(kdec[:, d, :, 0], lg_all[:, d, :], kpos[:, d:d + 1], None, ALU.mult)
            dve.drain()
            dve.sem_inc(s.dec, 1)
            dve.sem_inc(s.init, 1)
            dve.wait_ge(s.dmat, 1)
            dve.tensor_scalar(kdec[:], kdec[:], HD ** -0.5, None, ALU.mult)
            for d in range(2):
                m = dist[:, 2 * d + 1:2 * d + 2, :].broadcast_to([P, HN, P])
                dve.scalar_tensor_tensor(dtmp[:, d], dtmp[:, d], HD ** -0.5, m, ALU.mult, ALU.mult)
            dve.drain()
            for a in range(2):
                dve.tensor_tensor(dm[:, 4 * a:4 * a + 4, :], dtmp[:, 0, a:HN:2, :], dtmp[:, 1, a:HN:2, :], ALU.add)
            for t in range(5):
                dve.wait_ge(loaded[t], DMA)
            def rotate(t, par):
                dve.wait_ge((s.ropes_even, s.ropes_odd)[par], (t - par) * (DMA // 2) + DMA)
                src = qkv[:, bass.ds(t, 1), :].rearrange("p a n -> p (a n)")
                heads = src[:, 0:1024].rearrange("p (h d) -> p h d", d=HD)
                a, b = heads[:, :, 0:32], heads[:, :, 32:64]
                cos, sin = (rp[:, par, c:c + 1, :].broadcast_to([P, 16, 32]) for c in range(2))
                for n, (u, w) in enumerate(((a, cos), (b, sin), (a, sin), (b, cos))):
                    dve.tensor_tensor(tmp[:, n], u, w, ALU.mult)
                dve.drain()
                dve.sem_inc(s.rope_free, 1)
                dve.tensor_tensor(a, tmp[:, 0], tmp[:, 1], ALU.subtract)
                dve.tensor_tensor(b, tmp[:, 2], tmp[:, 3], ALU.add)
                dve.drain()
                if later(t, 2):
                    dve.wait_ge(s.kv, t - 1)
                for d in range(2):
                    dve.tensor_tensor(kd[:, par, d].rearrange("p (h d) -> p h d", d=HD), heads[:, 8:16, :], kdec[:, d].broadcast_to([P, HN, HD]), ALU.mult)
                dve.drain()
                dve.sem_inc(s.k_dec, 1)

            def keep_kv(t, par):
                dve.wait_ge(s.kv, t + 1)
                for d in range(2):
                    for q in range(2):
                        e = slice(q * HD, (q + 1) * HD)
                        dve.tensor_copy(kv[e, bass.ds(t, 1), d].rearrange("p a b e -> p (a b) e"), pkv[d][e, :, e])
                dve.drain()
                dve.sem_inc(s.kv_out, 1)
            ahead(dve, rotate, keep_kv)
            for n, at in enumerate(zip(range(NTA), BWD_ORDER)):
                old, new = run[:, n % 2], run[:, (n + 1) % 2]
                for d in range(2):
                    dve.tensor_tensor(new[:, d], old[:, d], gch[:, d].broadcast_to([P, 4, HD]), ALU.mult)
                dve.drain()
                for d in range(2):
                    dve.tensor_tensor(new[:, d], new[:, d], kv[:, at[d], d], ALU.add)
                dve.drain()
                for d in range(2):
                    dve.tensor_copy(kv[:, at[d], d], old[:, d])
                dve.drain()
            dve.sem_inc(s.states, 1)

            def decays(t, par):
                dve.wait_ge(s.qk, t + 1)
                if later(t, 2):
                    dve.wait_ge(s.y_done, t - 1)
                for d in range(2):
                    dve.tensor_tensor(qd[:, par, d], qT[:], qdec[:, d], ALU.mult)
                dve.drain()
                dve.sem_inc(s.q_dec, 1)
                dve.wait_ge(s.scores, t + 1)
                for a in range(2):
                    dve.tensor_tensor(am[:, par, a], pa[a][:], dm[:, 4 * a:4 * a + 4, :], ALU.mult)
                dve.drain()
                dve.sem_inc(s.am, 1)

            def norm_gate(t, par):
                dve.wait_ge(s.sq, t + 1)
                dve.tensor_reduce(ss[:], sq[:], AX_X, ALU.add)
                dve.drain()
                dve.tensor_scalar(ss[:], ss[:], 1.0 / HD, 1e-6, ALU.mult, ALU.add).then_inc(s.var, 1)
                dve.wait_ge(s.std, t + 1)
                dve.reciprocal(rs[:], rs[:])
                dve.drain()
                if later(t):
                    dve.wait_ge(s.stored, t * DMA)
                dve.tensor_tensor(y[:], po[:], rs[:].broadcast_to([P, HN, HD]), ALU.mult)
                dve.drain()
                dve.wait_ge(s.silu, t + 1)
                dve.tensor_tensor(y[:], y[:], z[:, par].rearrange("p (h d) -> p h d", d=HD), ALU.mult)
                dve.drain()
                dve.sem_inc(s.y, 1)
            ahead(dve, decays, norm_gate)


def rwkv_edges():
    before, behind = np.ones((P, NTA), np.float32), np.ones((P, NTA), np.float32)
    before[0, 0] = before[0, NTC] = 0.0
    behind[P - 1, NTC - 1] = behind[P - 1, NTA - 1] = 0.0
    return np.stack([before, behind], 1)


def rwkv_prep_stage(nc, ident, U2p, mu, w0, w2, a0, a2, kk_w, ka, rk, t_edges, PC, PD):
    STORES = 3 * DMA
    with stage(nc, "prep", "const", "side_even", "side_odd", "self_even", "self_odd", "edged", "own", "halves", "mixed", "norm_sq", "root", "tanh", "turned", "tT", "lora",
               "lora_b", "sig", "k_done", "rv_even", "rv_odd", "stored_even", "stored_odd") as (block, s, sb, ps):
        x = sb("x", [P, 2, 3, SHIFT_W])
        mu_h = sb("mu_h", [P, SHIFT_W])
        mu_n = sb("mu_n", [P, SHIFT_W])
        rowsb = {n: sb(n, [P, 512]) for n in ("kkr", "kar", "rkr")}
        b_rows = sb("b_rows", [P, 2, 2, 512])
        lw = sb("lw", [P, 2, 512])
        edges = sb("edges", [P, 2, NTA])
        kk = sb("kk", [P, HN, HD])
        sq = sb("sq", [P, HN, HD])
        ss = sb("ss", [P, HN, 1])
        td = sb("td", [P, 2, P])
        tT = sb("tT", [P, 2, P])
        sg = sb("sg", [P, 2, 2, 512])
        okk = sb("okk", [P, 2, 512])
        od = sb("od", [P, 2, 2, 3, 512])
        dots = sb("dots", [P, 2, HN])
        pt = ps("pt", [P, 2, P])
        pl = [[ps(f"pl{i}{d}") for d in range(2)] for i in range(2)]

        def tiles(eng, body, ahead=None):
            def one(t, par, more=True):
                body(t, par, (lambda: ahead(t + 1, 1 - par)) if ahead and more else lambda: None)
            if ahead:
                ahead(0, 0)
            with eng.Fori(0, NTA // 2 - 1) as i:
                for par in range(2):
                    one(2 * i + par, par)
            one(NTA - 2, 0)
            one(NTA - 1, 1, more=False)

        def sides_in(eng, t, par):
            eng.wait_ge((s.side_even, s.side_odd)[par], (t - par) * DMA + 2 * DMA)

        def self_in(eng, t, par):
            eng.wait_ge((s.self_even, s.self_odd)[par], (t - par) * (DMA // 2) + DMA)

        @block.sync
        def _(sp):
            for dst, src in ((mu_h, mu), (rowsb["kkr"], kk_w), (rowsb["kar"], ka), (rowsb["rkr"], rk)):
                sp.dma_start(dst[:], src.partition_broadcast(P)).then_inc(s.const, DMA)
            for d in range(2):
                sp.dma_start(b_rows[:, 0, d], w0[d].partition_broadcast(P)).then_inc(s.const, DMA)
                sp.dma_start(b_rows[:, 1, d], a0[d].partition_broadcast(P)).then_inc(s.const, DMA)
            sp.dma_start(lw[:, 0], w2.rearrange("d r n -> (d r) n")).then_inc(s.const, DMA)
            sp.dma_start(lw[:, 1], a2.rearrange("d r n -> (d r) n")).then_inc(s.const, DMA)
            sp.dma_start(edges[:], t_edges).then_inc(s.const, DMA)

            def load(i, par, which):
                for n in which:
                    off = (1, 0, 2)[n]
                    sp.dma_start(x[:, par, n], U2p[rows(i * (2 * P) + (par * P + off)), U_SHIFT:EVEN_IN]).then_inc(
                        (s.side_even, s.side_odd)[par] if n else (s.self_even, s.self_odd)[par], DMA)

            def store_rv(i, par):
                tile = rows(i * (2 * P) + par * P)
                sp.wait_ge(s.mixed, 2 * i + par + 1)
                sp.dma_start(PC[tile, 0:512], x[:, par, 0, 0:512]).then_inc((s.rv_even, s.rv_odd)[par], DMA)
                sp.dma_start(PC[tile, 512:1024], x[:, par, 0, 1024:1536]).then_inc((s.rv_even, s.rv_odd)[par], DMA)
            load(0, 0, (0, 1, 2))
            load(0, 1, (0, 1, 2))
            store_rv(0, 0)
            with sp.Fori(1, NTA // 2) as i:
                for par in range(2):
                    store_rv(i - (1 - par), 1 - par)
                    sp.wait_ge((s.rv_even, s.rv_odd)[par], i * (2 * DMA))
                    load(i, par, (1, 2))
                    sp.wait_ge(s.k_done, 2 * i + (par - 1))
                    load(i, par, (0,))
            store_rv(NTA // 2 - 1, 1)
            sp.wait_ge(s.rv_even, NTA // 2 * 2 * DMA)
            sp.wait_ge(s.rv_odd, NTA // 2 * 2 * DMA)

        @block.gpsimd
        def _(pool):
            pool.wait_ge(s.const, 11 * DMA)
            pool.tensor_scalar(mu_n[:], mu_h[:], -1.0, 1.0, ALU.mult, ALU.add)
            pool.drain()
            pool.tensor_scalar(mu_h[:], mu_h[:], 0.5, None, ALU.mult)
            pool.drain()
            pool.sem_inc(s.halves, 1)

            def own(t, par):
                self_in(pool, t, par)
                pool.tensor_tensor(x[:, par, 0], x[:, par, 0], mu_n[:], ALU.mult).then_inc(s.own, 1)

            def store(t, par, ahead):
                ahead()
                pool.wait_ge(s.k_done, t + 1)
                done = (s.stored_even, s.stored_odd)[par]
                pool.dma_start(PC[rows(t * P), 1024:1536], okk[:, par]).then_inc(done, DMA)
                pool.dma_start(PC[rows(t * P), 1536:], dots[:, par]).then_inc(done, DMA)
                pool.dma_start(PD[:, rows(t * P), :].rearrange("d p n -> p d n"), od[:, par].rearrange("p d a n -> p d (a n)")).then_inc(done, DMA)
            tiles(pool, store, own)
            pool.wait_ge(s.stored_even, NTA // 2 * STORES)
            pool.wait_ge(s.stored_odd, NTA // 2 * STORES)

        @block.tensor
        def _(pe):
            pe.wait_ge(s.const, 11 * DMA)
            with pe.Fori(0, NTA) as i:
                pe.wait_ge(s.tanh, i + 1)
                for n in range(2):
                    op = pe.transpose(pt[:, n, :], td[:, n, :], ident[:])
                op.then_inc(s.turned, 1)
                pe.wait_ge(s.tT, i + 1)
                pe.wait_ge(s.lora_b, i)
                for d in range(2):
                    base = d * 64
                    for n in range(2):
                        op = pe.matmul(pl[n][d][:], tT[base:base + 64, n, :], lw[base:base + 64, n, :], start=True, stop=True)
                op.then_inc(s.lora, 1)

        @block.scalar
        def _(act):
            act.wait_ge(s.const, 11 * DMA)

            def edge(t, par):
                sides_in(act, t, par)
                act.activation(x[:, par, 1], x[:, par, 1], ACT.Copy, scale=edges[:, 0, bass.ds(t, 1)]).then_inc(s.edged, 1)

            def body(t, par, ahead):
                act.wait_ge(s.mixed, t + 1)
                act.activation(td[:, 0, :], x[:, par, 0, 1536:1664], ACT.Tanh)
                act.activation(td[:, 1, :], x[:, par, 0, 1664:1792], ACT.Copy)
                act.drain()
                act.sem_inc(s.tanh, 1)
                act.wait_ge(s.turned, t + 1)
                act.activation(tT[:], pt[:], ACT.Copy).then_inc(s.tT, 1)
                ahead()
                act.wait_ge(s.norm_sq, t + 1)
                act.activation(ss[:], ss[:], ACT.Sqrt).then_inc(s.root, 1)
                act.wait_ge(s.lora_b, t + 1)
                act.activation(sg[:], sg[:], ACT.Sigmoid).then_inc(s.sig, 1)
            tiles(act, body, edge)

        @block.vector
        def _(dve):
            dve.wait_ge(s.const, 11 * DMA)
            dve.wait_ge(s.halves, 1)

            def mix(t, par):
                sides_in(dve, t, par)
                dve.wait_ge(s.edged, t + 1)
                dve.scalar_tensor_tensor(x[:, par, 1], x[:, par, 2], edges[:, 1, bass.ds(t, 1)], x[:, par, 1], ALU.mult, ALU.add)
                dve.drain()
                dve.tensor_tensor(x[:, par, 1], x[:, par, 1], mu_h[:], ALU.mult)
                dve.drain()
                dve.wait_ge(s.own, t + 1)
                dve.tensor_tensor(x[:, par, 0], x[:, par, 0], x[:, par, 1], ALU.add).then_inc(s.mixed, 1)

            def body(t, par, ahead):
                r, k = x[:, par, 0, 0:512], x[:, par, 0, 512:1024]
                kf = kk[:].rearrange("p h d -> p (h d)")
                dve.wait_ge(s.mixed, t + 1)
                dve.tensor_tensor(kf, k, rowsb["kkr"][:], ALU.mult)
                dve.drain()
                dve.tensor_tensor(sq[:], kk[:], kk[:], ALU.mult)
                dve.drain()
                dve.tensor_reduce(ss[:, :, 0], sq[:], AX_X, ALU.add).then_inc(s.norm_sq, 1)
                ahead()
                dve.wait_ge(s.root, t + 1)
                dve.tensor_scalar(ss[:], ss[:], 1e-12, None, ALU.max)
                dve.drain()
                dve.reciprocal(ss[:], ss[:])
                dve.drain()
                if not isinstance(t, int) or t >= 2:
                    dve.wait_ge((s.stored_even, s.stored_odd)[par], (t - par) * (STORES // 2))
                dve.tensor_tensor(okk[:, par].rearrange("p (h d) -> p h d", d=HD), kk[:], ss[:].broadcast_to([P, HN, HD]), ALU.mult)
                dve.wait_ge(s.lora, t + 1)
                for n in range(2):
                    for d in range(2):
                        dve.tensor_tensor(sg[:, n, d], pl[n][d][:], b_rows[:, n, d], ALU.add)
                dve.drain()
                dve.sem_inc(s.lora_b, 1)
                dve.tensor_tensor(sq[:].rearrange("p h d -> p (h d)"), r, rowsb["rkr"][:], ALU.mult)
                dve.wait_ge(s.sig, t + 1)
                dve.tensor_scalar(od[:, par, :, 0], sg[:, 0], -math.exp(-0.5), None, ALU.mult)
                for d in range(2):
                    dve.tensor_tensor(od[:, par, d, 2], okk[:, par], sg[:, 1, d], ALU.mult)
                dve.drain()
                for d in range(2):
                    dve.scalar_tensor_tensor(sg[:, 1, d], sg[:, 1, d], 1.0, rowsb["kar"][:], ALU.subtract, ALU.mult)
                dve.drain()
                for d in range(2):
                    dve.scalar_tensor_tensor(od[:, par, d, 1], sg[:, 1, d], 1.0, k, ALU.add, ALU.mult)
                dve.drain()
                dve.tensor_tensor(kf, od[:, par, 0, 1], od[:, par, 1, 1], ALU.add)
                dve.drain()
                dve.tensor_tensor(kk[:], kk[:], sq[:], ALU.mult)
                dve.drain()
                dve.tensor_reduce(dots[:, par], kk[:], AX_X, ALU.add).then_inc(s.k_done, 1)
                dve.drain()
            tiles(dve, body, mix)


def rwkv_tables():
    j, t = np.arange(P)[:, None], np.arange(P)[None, :]
    sums = np.zeros((2, P, 3, P), np.float32)
    ends = np.zeros((2, P, 2), np.float32)
    pairs = np.zeros((2, P, 4, P), np.uint32)
    level = np.zeros((2, P, 8, P), np.float32)
    for d in range(2):
        upto = (j <= t) if d == 0 else (j >= t)
        before = (j < t) if d == 0 else (j > t)
        mid = (j < 64) if d == 0 else (j >= 64)
        sums[d, :, 0] = upto.astype(np.float32) - mid
        sums[d, :, 1] = before.astype(np.float32) - mid
        sums[d, :, 2] = 1.0 - upto
        ends[d, :, 0], ends[d, :, 1] = 1.0, mid[:, 0]
        for n, m in enumerate((before, upto, before, upto)):
            pairs[d, :, n] = m
        for lv in range(7):
            b = 1 << lv
            same = (j // (2 * b)) == (t // (2 * b))
            late = ((j // b) % 2) == (1 - d)
            early = ((t // b) % 2) == d
            level[d, :, lv] = same & late & early
        level[d, :, 7] = level[d, :, 0].T
    return sums, ends, pairs, level


def rwkv_stage(nc, ident, PC, PD, t_sums, t_ends, t_pairs, t_level, RW):
    LV = 7
    UNITS = 2 * NTA
    PLAN = {("level", 0): "back_right", ("X", 1): "front_sums", ("T", 1): "back_u", ("X", 2): "front_late", ("T", 2): "back_out",
            ("X", 3): "front_turn0", ("T", 3): "front_turn1", ("X", 4): "front_pairs0", ("T", 4): "front_pairs1",
            ("X", 5): "front_pairs2", ("T", 5): "front_pairs3"}

    def wait(eng, sem, count):
        if not isinstance(count, int) or count > 0:
            eng.wait_ge(sem, count)

    def in_order(eng, part):
        def step(i, d, front=True, back=True):
            n = 2 * i + d
            after = (n + 1, i + d, 1 - d)
            before = (n - 1, i + d - 1, 1 - d)
            for lv in range(LV):
                for kind in ("X", "T") if lv else ("level",):
                    part(kind + str(lv), n, i, d)
                    what = PLAN.get((kind, lv), "none")
                    if front and what.startswith("front"):
                        part(what, *after)
                    if back and what.startswith("back"):
                        part(what, *before)
        for what in PLAN.values():
            if what.startswith("front"):
                part(what, 0, 0, 0)
        step(0, 0, back=False)
        step(0, 1)
        with eng.Fori(1, NTA - 1) as i:
            step(i, 0)
            step(i, 1)
        step(NTA - 1, 0)
        step(NTA - 1, 1, front=False)
        for what in PLAN.values():
            if what.startswith("back"):
                part(what, UNITS - 1, NTA - 1, 1)

    def tokens(i, d):
        return rows(i * P) if d == 0 else rows(((i * (NTA - 1) + (NTC - 1)) % NTA) * P)

    with stage(nc, "rwkv", "const", "init", "in_f", "in_b", "v_f", "v_b", "gsum", "exps", "late", "ew", "turned", "t_act", "amat", "a_out", "mc", "tt0",
               "x_mm", "x_out", "t_mm", "t_out", "r_mm", "r_out", "u_mm", "u_out", "o_mm", "o_out", "m_mm", "m_out", "stored_f", "stored_b") as (block, s, sb, ps):
        xr = sb("xr", [P, 2, 512])
        xk = sb("xk", [P, 2, 512])
        v = sb("v", [P, 2, 512])
        xd = sb("xd", [P, 2, 3, 512])
        sums = sb("sums", [P, 2, 3, P])
        ends = sb("ends", [P, 2, 2])
        pairs = sb("pairs", [P, 2, 512], U32)
        level = sb("level", [P, 2, 8, P])
        ex = sb("ex", [P, 4, 512])
        ecol = sb("ecol", [P, 4, 2])
        ew = sb("ew", [P, 4, 512])
        lat = sb("lat", [P, 2, 2, 512])
        arT = sb("arT", [P, 2, 4, 2, P])
        bT = sb("bT", [P, 4, P])
        kT = sb("kT", [P, 4, P])
        A = sb("A", [P, 2, HN, 4, P])
        T = sb("T", [P, HN, P])
        TT = sb("TT", [P, 2, HN, P])
        X = sb("X", [P, HN, P])
        M = sb("M", [P, 2, 4, P])
        Mc = sb("Mc", [P, 2, 4, P])
        R = sb("R", [P, 512])
        U = sb("U", [P, 512])
        O = sb("O", [P, 2, 512])
        idle = sb("idle", [P, HN])
        w = [ps(f"w{i}") for i in range(4)]
        f = [ps(f"f{i}") for i in range(2)]
        ru = ps("ru")
        om = ps("om")
        C = lambda bank, h: bank[:, (h % 4) * P:(h % 4 + 1) * P]
        by_block = lambda bank: bank[:].rearrange("p (b t) -> p b t", b=4)

        @block.sync
        def _(sp):
            sp.dma_start(sums[:], t_sums.rearrange("d p n t -> p d n t")).then_inc(s.const, DMA)
            sp.dma_start(ends[:], t_ends.rearrange("d p n -> p d n")).then_inc(s.const, DMA)
            sp.dma_start(pairs[:], t_pairs.rearrange("d p n t -> p d (n t)")).then_inc(s.const, DMA)
            sp.dma_start(level[:], t_level.rearrange("d p n t -> p d n t")).then_inc(s.const, DMA)

            def load(i, d):
                n = 2 * i + d
                tile = tokens(i, d)
                wait(sp, s.gsum, (n - 1) * 2)
                wait(sp, s.ew, n - 1)
                wait(sp, s.late, n - 1)
                done = (s.in_f, s.in_b)[d]
                sp.dma_start(xr[:, d], PC[tile, 0:512]).then_inc(done, DMA)
                sp.dma_start(xk[:, d], PC[tile, 1024:1536]).then_inc(done, DMA)
                sp.dma_start(xd[:, d].rearrange("p a n -> p (a n)"), PD[d, tile, :]).then_inc(done, DMA)
                wait(sp, s.m_mm, n - 1)
                wait(sp, s.o_mm, n - 1)
                sp.dma_start(v[:, d], PC[tile, 512:1024]).then_inc((s.v_f, s.v_b)[d], DMA)
            load(0, 0)
            load(0, 1)
            with sp.Fori(1, NTA) as i:
                load(i, 0)
                load(i, 1)

        @block.gpsimd
        def _(pool):
            pool.wait_ge(s.const, 4 * DMA)

            idb = ident[:].rearrange("p (a t) -> p a t", a=1).broadcast_to([P, 4, P])

            def part(what, n, i, d):
                if what == "level0":
                    wait(pool, s.u_mm, n - 1)
                    for q in range(2):
                        hs = slice(4 * q, 4 * q + 4)
                        pool.wait_ge(s.a_out, n * HN + 4 * q + 4)
                        pool.tensor_tensor(TT[:, d, hs, :], A[:, d, hs, 0, :], level[:, d, 7:8, :].broadcast_to([P, 4, P]), ALU.mult)
                        pool.drain()
                        pool.tensor_tensor(TT[:, d, hs, :], TT[:, d, hs, :], idb, ALU.add)
                        pool.drain()
                        pool.sem_inc(s.tt0, 1)
                if what == "front_late":
                    pool.wait_ge((s.in_f, s.in_b)[d], (i + 1) * (3 * DMA))
                    pool.wait_ge(s.exps, 2 * n + 2)
                    wait(pool, s.m_mm, n - 1)
                    pool.tensor_tensor(lat[:, d, 0], xd[:, d, 2], ex[:, 3], ALU.mult)
                    pool.tensor_tensor(lat[:, d, 1], xd[:, d, 1], ex[:, 3], ALU.mult)
                    pool.drain()
                    pool.sem_inc(s.late, 1)
                if what == "back_out":
                    pool.wait_ge(s.o_out, n + 1)
                    pool.dma_start(RW[d, tokens(i, d), :], O[:, d]).then_inc((s.stored_f, s.stored_b)[d], DMA)
            in_order(pool, part)
            pool.wait_ge(s.stored_f, NTA * DMA)
            pool.wait_ge(s.stored_b, NTA * DMA)

        @block.tensor
        def _(pe):
            pe.wait_ge(s.const, 4 * DMA)
            pe.wait_ge(s.init, 1)

            def part(what, n, i, d):
                if what == "front_sums":
                    pe.wait_ge((s.in_f, s.in_b)[d], (i + 1) * (3 * DMA))
                    wait(pe, s.a_out, n * HN)
                    pe.matmul(f[0][:], sums[:, d, 0, :], xd[:, d, 0, :], start=True, stop=True)
                    pe.matmul(f[1][:], sums[:, d, 1, :], xd[:, d, 0, :], start=True, stop=True).then_inc(s.gsum, 1)
                if what == "front_late":
                    pe.wait_ge(s.exps, 2 * n + 1)
                    pe.matmul(f[0][:], sums[:, d, 2, :], xd[:, d, 0, :], start=True, stop=True)
                    for b in range(4):
                        op = pe.matmul(f[1][:, 2 * b:2 * b + 2], xd[:, d, 0, b * P:(b + 1) * P], ends[:, d, :], start=True, stop=True)
                    op.then_inc(s.gsum, 1)
                if what.startswith("front_turn"):
                    first = 2 * int(what[-1])
                    if first == 0:
                        pe.wait_ge(s.ew, n + 1)
                        pe.wait_ge(s.exps, 2 * n + 2)
                    for q in range(2):
                        if first:
                            pe.wait_ge(s.t_act, 4 * n + q + 1)
                        for b in range(4):
                            op = pe.transpose(f[q][:, b * P:(b + 1) * P], ew[:, first + q, b * P:(b + 1) * P], ident[:])
                        op.then_inc(s.turned, 1)
                if what.startswith("front_pairs"):
                    first = 2 * int(what[-1])
                    if first == 0:
                        pe.wait_ge(s.t_act, 4 * n + 4)
                    else:
                        pe.wait_ge(s.a_out, n * HN + first)
                    for h in (first, first + 1):
                        base = (h % 2) * HD
                        rhs = arT[base:base + HD, d, h // 2].rearrange("p a t -> p (a t)")
                        pe.matmul(f[h % 2][:, 0:256], bT[base:base + HD, h // 2, :], rhs, start=True, stop=True)
                        pe.matmul(f[h % 2][:, 256:512], kT[base:base + HD, h // 2, :], rhs, start=True, stop=True).then_inc(s.amat, 1)
                if what == "level0":
                    pe.wait_ge(s.a_out, n * HN + HN)
                    wait(pe, s.t_out, n * (2 * LV))
                    for q in range(2):
                        for h in range(4 * q, 4 * q + 4):
                            op = pe.matmul(C(w[q], h), A[:, d, h, 0, :], ident[:], start=True, stop=True)
                        op.then_inc(s.x_mm, 1)
                if what[0] == "X":
                    lv = int(what[1])
                    for q in range(2):
                        pe.wait_ge(s.t_out, n * (2 * LV) + 2 * lv - 1 + q)
                        for h in range(4 * q, 4 * q + 4):
                            op = pe.matmul(C(w[q], h), A[:, d, h, 0, :], T[:, h, :], start=True, stop=True)
                        op.then_inc(s.x_mm, 1)
                if what[0] == "T":
                    lv = int(what[1])
                    for q in range(2):
                        if lv == 1:
                            pe.wait_ge(s.tt0, 2 * n + q + 1)
                        pe.wait_ge(s.x_out, n * (2 * LV) + 2 * lv + 1 + q)
                        for h in range(4 * q, 4 * q + 4):
                            if lv < LV - 1:
                                pe.matmul(C(w[q], h), TT[:, d, h, :], X[:, h, :], start=True, stop=True)
                            op = pe.matmul(C(w[2 + q], h), X[:, h, :], TT[:, d, h, :], start=True, stop=True)
                        op.then_inc(s.t_mm, 1)
                if what == "back_right":
                    pe.wait_ge(s.mc, n + 1)
                    pe.wait_ge((s.v_f, s.v_b)[d], (i + 1) * DMA)
                    wait(pe, s.o_out, n)
                    for b in range(4):
                        pe.matmul(ru[:, b * P:(b + 1) * P], arT[:, d, b, 0, :], Mc[:, d, b, :], start=True, stop=False)
                        for h in (2 * b, 2 * b + 1):
                            op = pe.matmul(ru[:, h * HD:(h + 1) * HD], A[:, d, h, 2, :], v[:, d, h * HD:(h + 1) * HD], start=False, stop=h % 2 == 1)
                    op.then_inc(s.r_mm, 1)
                if what == "back_u":
                    pe.wait_ge(s.t_out, n * (2 * LV) + 2 * LV)
                    pe.wait_ge(s.r_out, n + 1)
                    for h in range(HN):
                        op = pe.matmul(ru[:, h * HD:(h + 1) * HD], TT[:, d, h, :], R[:, h * HD:(h + 1) * HD], start=True, stop=True)
                    op.then_inc(s.u_mm, 1)
                if what == "back_out":
                    pe.wait_ge(s.u_out, n + 1)
                    pe.wait_ge(s.late, n + 1)
                    wait(pe, s.m_out, n)
                    for b in range(4):
                        pe.matmul(om[:, b * P:(b + 1) * P], lat[:, d, 0, b * P:(b + 1) * P], U[:, b * P:(b + 1) * P], start=True, stop=False)
                        op = pe.matmul(om[:, b * P:(b + 1) * P], lat[:, d, 1, b * P:(b + 1) * P], v[:, d, b * P:(b + 1) * P], start=False, stop=True)
                    op.then_inc(s.m_mm, 1)
                    for b in range(4):
                        pe.matmul(ru[:, b * P:(b + 1) * P], arT[:, d, b, 1, :], Mc[:, d, b, :], start=True, stop=False)
                        for h in (2 * b, 2 * b + 1):
                            pe.matmul(ru[:, h * HD:(h + 1) * HD], A[:, d, h, 1, :], U[:, h * HD:(h + 1) * HD], start=False, stop=False)
                            op = pe.matmul(ru[:, h * HD:(h + 1) * HD], A[:, d, h, 3, :], v[:, d, h * HD:(h + 1) * HD], start=False, stop=h % 2 == 1)
                    op.then_inc(s.o_mm, 1)
            in_order(pe, part)

        @block.scalar
        def _(act):
            def part(what, n, i, d):
                if what == "front_sums":
                    act.wait_ge(s.gsum, 2 * n + 1)
                    wait(act, s.ew, n)
                    wait(act, s.late, n)
                    act.activation(ex[:, 0], f[0][:], ACT.Exp)
                    act.activation(ex[:, 1], f[0][:], ACT.Exp, scale=-1.0)
                    act.activation(ex[:, 2], f[1][:], ACT.Exp)
                    act.drain()
                    act.sem_inc(s.exps, 1)
                if what == "front_late":
                    act.wait_ge(s.gsum, 2 * n + 2)
                    wait(act, s.mc, n)
                    act.activation(ex[:, 3], f[0][:], ACT.Exp)
                    act.activation(ecol[:], f[1][:, 0:8].rearrange("p (b n) -> p b n", n=2), ACT.Exp)
                    act.drain()
                    act.sem_inc(s.exps, 1)
                if what == "front_turn0":
                    wait(act, s.o_mm, n - 1)
                    for q in range(2):
                        act.wait_ge(s.turned, 4 * n + q + 1)
                        act.activation(arT[:, d, :, q, :], by_block(f[q]), ACT.Copy).then_inc(s.t_act, 1)
                if what == "front_turn1":
                    wait(act, s.amat, n * HN)
                    for q, dst in enumerate((bT, kT)):
                        act.wait_ge(s.turned, 4 * n + q + 3)
                        act.activation(dst[:], by_block(f[q]), ACT.Copy).then_inc(s.t_act, 1)
                if what == "back_right":
                    act.wait_ge(s.r_mm, n + 1)
                    act.activation(R[:], ru[:], ACT.Copy).then_inc(s.r_out, 1)
                if what == "back_u":
                    act.wait_ge(s.u_mm, n + 1)
                    act.activation(U[:], ru[:], ACT.Copy).then_inc(s.u_out, 1)
                if what == "back_out":
                    act.wait_ge(s.o_mm, n + 1)
                    wait(act, (s.stored_f, s.stored_b)[d], i * DMA)
                    act.activation(O[:, d], ru[:], ACT.Copy).then_inc(s.o_out, 1)
            in_order(act, part)

        @block.vector
        def _(dve):
            dve.memset(A[:], 0.0)
            dve.memset(M[:], 0.0)
            dve.drain()
            dve.sem_inc(s.init, 1)
            dve.wait_ge(s.const, 4 * DMA)
            by_head = lambda bank: bank[:].rearrange("p (h t) -> p h t", h=4)
            idb = ident[:].rearrange("p (a t) -> p a t", a=1).broadcast_to([P, 4, P])

            def part(what, n, i, d):
                if what == "front_late":
                    dve.wait_ge((s.in_f, s.in_b)[d], (i + 1) * (3 * DMA))
                    dve.wait_ge(s.exps, 2 * n + 2)
                    wait(dve, s.turned, 4 * n)
                    dve.scalar_tensor_tensor(ew[:, 0], xk[:, d], -1.0, ex[:, 2], ALU.mult, ALU.mult)
                    dve.tensor_tensor(ew[:, 1], xr[:, d], ex[:, 0], ALU.mult)
                    dve.tensor_tensor(ew[:, 2], xd[:, d, 2], ex[:, 1], ALU.mult)
                    dve.tensor_tensor(ew[:, 3], xd[:, d, 1], ex[:, 1], ALU.mult)
                    dve.drain()
                    dve.sem_inc(s.ew, 1)
                if what == "back_out":
                    dve.wait_ge(s.m_mm, n + 1)
                    for a in range(2):
                        e = slice(a * HD, (a + 1) * HD)
                        dve.tensor_tensor(M[e, d, :, e], M[e, d, :, e], by_block(om)[e, :, e], ALU.add)
                    dve.drain()
                    dve.sem_inc(s.m_out, 1)
                if what == "front_turn0":
                    wait(dve, s.o_mm, n - 1)
                    dve.tensor_tensor(Mc[:, d], M[:, d], ecol[:, :, 1:2].broadcast_to([P, 4, P]), ALU.mult)
                    dve.drain()
                    dve.tensor_tensor(M[:, d], M[:, d], ecol[:, :, 0:1].broadcast_to([P, 4, P]), ALU.mult)
                    dve.drain()
                    dve.sem_inc(s.mc, 1)
                if what.startswith("front_pairs"):
                    for h in range(2 * int(what[-1]), 2 * int(what[-1]) + 2):
                        dve.wait_ge(s.amat, n * HN + h + 1)
                        dve.memset(idle[:, h:h + 1], 0.0)
                        dve.copy_predicated(A[:, d, h].rearrange("p a t -> p (a t)"), pairs[:, d], f[h % 2][:]).then_inc(s.a_out, 1)
                if what == "level0":
                    for q in range(2):
                        hs = slice(4 * q, 4 * q + 4)
                        m0 = level[:, d, 0:1, :].broadcast_to([P, 4, P])
                        dve.wait_ge(s.x_mm, n * (2 * LV) + q + 1)
                        dve.tensor_tensor(T[:, hs, :], by_head(w[q]), m0, ALU.mult)
                        dve.drain()
                        dve.tensor_tensor(T[:, hs, :], T[:, hs, :], idb, ALU.add)
                        dve.drain()
                        dve.sem_inc(s.x_out, 1)
                        dve.sem_inc(s.t_out, 1)
                if what[0] == "X":
                    lv = int(what[1])
                    for q in range(2):
                        hs = slice(4 * q, 4 * q + 4)
                        dve.wait_ge(s.x_mm, n * (2 * LV) + 2 * lv + q + 1)
                        ml = level[:, d, lv:lv + 1, :].broadcast_to([P, 4, P])
                        dve.tensor_tensor(X[:, hs, :], by_head(w[q]), ml, ALU.mult).then_inc(s.x_out, 1)
                if what[0] == "T":
                    lv = int(what[1])
                    for q in range(2):
                        hs = slice(4 * q, 4 * q + 4)
                        dve.wait_ge(s.t_mm, n * (2 * LV - 2) + 2 * (lv - 1) + q + 1)
                        if lv < LV - 1:
                            dve.tensor_tensor(T[:, hs, :], by_head(w[q]), T[:, hs, :], ALU.add)
                        dve.tensor_tensor(TT[:, d, hs, :], by_head(w[2 + q]), TT[:, d, hs, :], ALU.add)
                        dve.drain()
                        dve.sem_inc(s.t_out, 1)
            in_order(dve, part)


def rwkv_out_stage(nc, RW, PC, U2, ln_w, ln_b, YB2):
    with stage(nc, "rwo", "const", "x_even", "x_odd", "bonus", "y_done", "center", "sq", "var", "std", "silu", "stored_even", "stored_odd") as (block, s, sb, ps):
        x = sb("x", [P, 2, 2, 512])
        v = sb("v", [P, 2, HN, HD])
        dot = sb("dot", [P, 2, HN, 1])
        z = sb("z", [P, 2, 512])
        w_r = sb("w_r", [P, 512])
        b_r = sb("b_r", [P, 512])
        sq = sb("sq", [P, HN, HD])
        mean = sb("mean", [P, HN, 1])
        var = sb("var", [P, HN, 1])
        y = sb("y", [P, 2, 512])
        arrived = lambda eng, i, par: eng.wait_ge((s.x_even, s.x_odd)[par], i * (5 * DMA) + 5 * DMA)

        @block.sync
        def _(sp):
            sp.dma_start(w_r[:], ln_w.partition_broadcast(P)).then_inc(s.const, DMA)
            sp.dma_start(b_r[:], ln_b.partition_broadcast(P)).then_inc(s.const, DMA)

            def load(i, par):
                t = rows(i * (2 * P) + par * P)
                done = (s.x_even, s.x_odd)[par]
                if not isinstance(i, int):
                    sp.wait_ge(s.y_done, 2 * i + (par - 1))
                for d in range(2):
                    sp.dma_start(x[:, par, d], RW[d, t, :]).then_inc(done, DMA)
                sp.dma_start(v[:, par].rearrange("p h d -> p (h d)"), PC[t, 512:1024]).then_inc(done, DMA)
                sp.dma_start(dot[:, par, :, 0], PC[t, 1536:1536 + HN]).then_inc(done, DMA)
                sp.dma_start(z[:, par], U2[t, U_WZ:U_SHIFT]).then_inc(done, DMA)
            load(0, 0)
            load(0, 1)
            with sp.Fori(1, NTA // 2) as i:
                load(i, 0)
                load(i, 1)

        @block.gpsimd
        def _(pool):
            pool.wait_ge(s.const, 2 * DMA)

            def bonus(i, par):
                arrived(pool, i, par)
                pool.tensor_tensor(v[:, par], v[:, par], dot[:, par].broadcast_to([P, HN, HD]), ALU.mult)
                pool.drain()
                vf = v[:, par].rearrange("p h d -> p (h d)")
                pool.tensor_tensor(vf, vf, b_r[:], ALU.add)
                pool.drain()
                pool.sem_inc(s.bonus, 1)

            def store(i, par):
                pool.wait_ge(s.y_done, 2 * i + par + 1)
                pool.dma_start(YB2[rows(i * (2 * P) + par * P), 512:1024], y[:, par]).then_inc((s.stored_even, s.stored_odd)[par], DMA)
            bonus(0, 0)
            with pool.Fori(0, NTA // 2 - 1) as i:
                bonus(i, 1)
                store(i, 0)
                bonus(i + 1, 0)
                store(i, 1)
            bonus(NTA // 2 - 1, 1)
            store(NTA // 2 - 1, 0)
            store(NTA // 2 - 1, 1)
            pool.wait_ge(s.stored_even, NTA // 2 * DMA)
            pool.wait_ge(s.stored_odd, NTA // 2 * DMA)

        @block.scalar
        def _(act):
            with act.Fori(0, NTA // 2) as i:
                for par in range(2):
                    arrived(act, i, par)
                    act.activation(z[:, par], z[:, par], ACT.Silu).then_inc(s.silu, 1)
                    act.wait_ge(s.center, 2 * i + par + 1)
                    act.activation(sq[:], x[:, par, 0].rearrange("p (h d) -> p h d", d=HD), ACT.Square).then_inc(s.sq, 1)
                    act.wait_ge(s.var, 2 * i + par + 1)
                    act.activation(var[:], var[:], ACT.Sqrt).then_inc(s.std, 1)

        @block.vector
        def _(dve):
            dve.wait_ge(s.const, 2 * DMA)
            with dve.Fori(0, NTA // 2) as i:
                for par in range(2):
                    n = 2 * i + par + 1
                    arrived(dve, i, par)
                    xf = x[:, par, 0]
                    h0 = xf.rearrange("p (h d) -> p h d", d=HD)
                    dve.tensor_tensor(xf, xf, x[:, par, 1], ALU.add)
                    dve.drain()
                    dve.tensor_reduce(mean[:, :, 0], h0, AX_X, ALU.add)
                    dve.drain()
                    dve.tensor_scalar(mean[:], mean[:], 1.0 / HD, None, ALU.mult)
                    dve.drain()
                    dve.tensor_tensor(h0, h0, mean[:].broadcast_to([P, HN, HD]), ALU.subtract).then_inc(s.center, 1)
                    dve.wait_ge(s.sq, n)
                    dve.tensor_reduce(var[:, :, 0], sq[:], AX_X, ALU.add)
                    dve.drain()
                    dve.tensor_scalar(var[:], var[:], 1.0 / HD, 64e-5, ALU.mult, ALU.add).then_inc(s.var, 1)
                    dve.wait_ge(s.std, n)
                    dve.reciprocal(var[:], var[:])
                    dve.drain()
                    dve.tensor_tensor(h0, h0, var[:].broadcast_to([P, HN, HD]), ALU.mult)
                    dve.drain()
                    dve.tensor_tensor(xf, xf, w_r[:], ALU.mult)
                    dve.drain()
                    dve.wait_ge(s.bonus, n)
                    dve.tensor_tensor(xf, xf, v[:, par].rearrange("p h d -> p (h d)"), ALU.add)
                    dve.drain()
                    dve.wait_ge(s.silu, n)
                    dve.wait_ge((s.stored_even, s.stored_odd)[par], i * DMA)
                    dve.tensor_tensor(y[:, par], xf, z[:, par], ALU.mult).then_inc(s.y_done, 1)


O_HY, O_HZ, O_NQ, O_NK, O_NV, O_NZ, ODD_IN = 0, 1536, 2048, 2560, 3072, 3584, 4096
HYW = 512
NFREQ = SEQ
HALF = NFREQ // 2
FCH = HALF // P
GRID_C, GRID_R = 64, 16
WIN_R, WIN_C = 8, 16


def hyena_tables():
    n = np.arange(SEQ, dtype=np.float64)
    t = np.linspace(0.0, 1.0, SEQ, dtype=np.float32)[:, None]
    bands = np.linspace(1e-4, 15, 16, dtype=np.float32)
    ang = (np.float32(2.0 * math.pi / SEQ) * np.arange(SEQ, dtype=np.float32)[:, None] * bands[None]).astype(np.float32)
    feats = np.concatenate([t, np.cos(ang), -np.sin(ang)], -1).astype(np.float32).T.copy()
    deltas = np.abs(np.linspace(math.log(1e-2) / 1.5, math.log(1e-2) / 0.3, HYW, dtype=np.float32))
    decay = np.exp(-t * deltas).astype(np.float32)
    th = math.pi * ((np.outer(n, 2 * np.arange(HALF) + 1)) % 4096) / 2048
    both = np.stack([np.cos(th), np.sin(th)], 1).astype(np.float32)
    both = both.reshape(NT // 2, P, 2, 2, FCH, P)
    fwd = both.transpose(4, 1, 2, 0, 3, 5).reshape(FCH, P, NT, 2, P)
    inv = both.transpose(0, 5, 2, 4, 3, 1)
    return feats, decay, np.ascontiguousarray(fwd), np.ascontiguousarray(inv)


def edges_of_sequence():
    before, behind = np.ones((P, NT), np.float32), np.ones((P, NT), np.float32)
    before[0, 0] = 0.0
    behind[P - 1, NT - 1] = 0.0
    return np.stack([before, behind], 1)


def short_conv_stage(nc, U3p, cw, cb, t_edges, VX):
    with stage(nc, "sc", "const", "x_even", "x_odd", "own", "y_done", "out_even", "out_odd") as (block, s, sb, ps):
        W = 3 * HYW
        x = sb("x", [P, 2, 3, W])
        y = sb("y", [P, 2, W])
        w = sb("w", [P, 4, W])
        edges = sb("edges", [P, 2, NT])

        @block.sync
        def _(sp):
            for n in range(3):
                sp.dma_start(w[:, n], cw[n].partition_broadcast(P)).then_inc(s.const, DMA)
            sp.dma_start(w[:, 3], cb.partition_broadcast(P)).then_inc(s.const, DMA)
            sp.dma_start(edges[:], t_edges).then_inc(s.const, DMA)
            def load(i, par):
                if not isinstance(i, int):
                    sp.wait_ge(s.y_done, 2 * i + (par - 1))
                for n in range(3):
                    sp.dma_start(x[:, par, n], U3p[rows(i * (2 * P) + (par * P + n)), 0:W]).then_inc((s.x_even, s.x_odd)[par], DMA)
            load(0, 0)
            load(0, 1)
            with sp.Fori(1, NT // 2) as i:
                load(i, 0)
                load(i, 1)

        @block.scalar
        def _(act):
            with act.Fori(0, NT // 2) as i:
                for par in range(2):
                    act.wait_ge(s.y_done, 2 * i + par + 1)
                    act.dma_start(VX[rows(i * (2 * P) + par * P), :], y[:, par]).then_inc((s.out_even, s.out_odd)[par], DMA)
            act.wait_ge(s.out_even, NT // 2 * DMA)
            act.wait_ge(s.out_odd, NT // 2 * DMA)

        @block.gpsimd
        def _(pool):
            pool.wait_ge(s.const, 5 * DMA)
            with pool.Fori(0, NT // 2) as i:
                for par in range(2):
                    pool.wait_ge((s.x_even, s.x_odd)[par], (i + 1) * (3 * DMA))
                    pool.tensor_tensor(x[:, par, 1], x[:, par, 1], w[:, 1], ALU.mult)
                    pool.drain()
                    pool.tensor_tensor(x[:, par, 1], x[:, par, 1], w[:, 3], ALU.add)
                    pool.drain()
                    pool.sem_inc(s.own, 1)

        @block.vector
        def _(dve):
            dve.wait_ge(s.const, 5 * DMA)
            with dve.Fori(0, NT // 2) as i:
                for par in range(2):
                    dve.wait_ge((s.x_even, s.x_odd)[par], (i + 1) * (3 * DMA))
                    a, b, c = (x[:, par, n] for n in range(3))
                    e0, e1 = (edges[:, n, bass.ds(i * 2 + par, 1)] for n in range(2))
                    dve.scalar_tensor_tensor(a, a, e0, w[:, 0], ALU.mult, ALU.mult)
                    dve.scalar_tensor_tensor(c, c, e1, w[:, 2], ALU.mult, ALU.mult)
                    dve.drain()
                    dve.tensor_tensor(a, a, c, ALU.add)
                    dve.drain()
                    dve.wait_ge(s.own, 2 * i + par + 1)
                    dve.wait_ge((s.out_even, s.out_odd)[par], i * DMA)
                    dve.tensor_tensor(y[:, par], a, b, ALU.add).then_inc(s.y_done, 1)


def filter_stage(nc, t_feats, t_decay, w1, b1, f1, w2, b2, f2, w3, FS):
    with stage(nc, "filt", "const", "h_mm", "arg", "sine", "w3_mm", "f_done", "stored") as (block, s, sb, ps):
        feats = sb("feats", [33, SEQ])
        w1s = sb("w1s", [33, 64])
        w2s = sb("w2s", [64, 64])
        w3s = sb("w3s", [64, 2048])
        cols = sb("cols", [64, 4])
        dec = sb("dec", [P, NT, HYW])
        ang = sb("ang", [64, SEQ])
        turns = sb("turns", [64, SEQ])
        arg = sb("arg", [64, SEQ])
        hid = sb("hid", [64, SEQ])
        f = sb("f", [P, 4, HYW])
        o = sb("o", [P, 4, HYW])
        first = sb("first", [P, 1])
        ph = ps("ph", [64, SEQ])
        pw = [ps(f"pw{i}") for i in range(4)]

        @block.sync
        def _(sp):
            sp.dma_start(feats[:], t_feats).then_inc(s.const, DMA)
            sp.dma_start(w1s[:], w1).then_inc(s.const, DMA)
            sp.dma_start(w2s[:], w2).then_inc(s.const, DMA)
            sp.dma_start(w3s[:], w3).then_inc(s.const, DMA)
            for n, v in enumerate((b1, f1, b2, f2)):
                sp.dma_start(cols[:, n:n + 1], v.rearrange("(p a) -> p a", a=1), allow_slow_non_contiguous=True).then_inc(s.const, DMA)
            sp.dma_start(dec[:], t_decay.rearrange("(t p) c -> p t c", p=P)).then_inc(s.const, DMA)
            with sp.Fori(0, NT) as i:
                sp.wait_ge(s.f_done, i + 1)
                for n in range(2):
                    sp.dma_start(FS[n, rows(i * P), :], o[:, 2 * n:2 * n + 2].rearrange("p a c -> p (a c)")).then_inc(s.stored, DMA)
            sp.wait_ge(s.stored, 2 * NT * DMA)

        @block.tensor
        def _(pe):
            pe.wait_ge(s.const, 9 * DMA)
            for layer, (w, src) in enumerate(((w1s, feats), (w2s, hid))):
                if layer:
                    pe.wait_ge(s.sine, 1)
                for hf in range(2):
                    op = pe.matmul(ph[:, hf * 512:(hf + 1) * 512], w[:], src[:, hf * 512:(hf + 1) * 512], start=True, stop=True)
                op.then_inc(s.h_mm, 1)
            pe.wait_ge(s.sine, 2)
            with pe.Fori(0, NT) as i:
                pe.wait_ge(s.arg, 2 + i + 1)
                for n in range(4):
                    op = pe.matmul(pw[n][:], ang[:, 0:P], w3s[:, n * 512:(n + 1) * 512], start=True, stop=True)
                op.then_inc(s.w3_mm, 1)

        @block.scalar
        def _(act):
            for layer in range(2):
                act.wait_ge(s.arg, layer + 1)
                act.activation(hid[:], arg[:], ACT.Sin).then_inc(s.sine, 1)

        @block.vector
        def _(dve):
            dve.memset(first[:], 1.0)
            dve.drain()
            dve.memset(first[0:1, :], 0.0)
            dve.wait_ge(s.const, 9 * DMA)
            for layer in range(2):
                dve.wait_ge(s.h_mm, layer + 1)
                b, fr = cols[:, 2 * layer:2 * layer + 1], cols[:, 2 * layer + 1:2 * layer + 2]
                dve.tensor_scalar(ang[:], ph[:], b, fr, ALU.add, ALU.mult)
                dve.drain()
                reduced_sine(dve, arg[:], ang[:], turns[:], 0.0)
                dve.sem_inc(s.arg, 1)
            dve.wait_ge(s.sine, 2)

            def place(i):
                dve.tensor_copy(ang[:, 0:P], hid[:, rows(i * P)])
                dve.drain()
                dve.sem_inc(s.arg, 1)

            def filters(i, more):
                dve.wait_ge(s.w3_mm, i + 1)
                for n in range(4):
                    dve.tensor_tensor(f[:, n], pw[n][:], dec[:, bass.ds(i, 1), :].rearrange("p a c -> p (a c)"), ALU.mult)
                dve.drain()
                if more:
                    place(i + 1)
                for n in (1, 3):
                    dve.tensor_scalar(f[:, n], f[:, n], first[:, 0:1], None, ALU.mult)
                dve.drain()
                dve.memset(first[:], 1.0)
                if not isinstance(i, int) or i:
                    dve.wait_ge(s.stored, i * (2 * DMA))
                for n in range(2):
                    dve.tensor_tensor(o[:, 2 * n], f[:, 2 * n], f[:, 2 * n + 1], ALU.add)
                    dve.tensor_tensor(o[:, 2 * n + 1], f[:, 2 * n], f[:, 2 * n + 1], ALU.subtract)
                dve.drain()
                dve.sem_inc(s.f_done, 1)
            place(0)
            filters(0, True)
            with dve.Fori(1, NT - 1) as i:
                filters(i, True)
            filters(NT - 1, False)


def spectrum_stage(nc, name, t_fwd, zin, out):
    with stage(nc, name, "z_in", "w_even", "w_odd", "mm", "odd_out", "sums_out", "stored_even", "stored_odd") as (block, s, sb, ps):
        z = sb("z", [P, 2, NT // 2, 2, HYW])
        w = sb("w", [P, 2, NT, 2, P])
        odd = sb("odd", [P, 2, 2, HYW])
        o = sb("o", [P, 2, 2, 2, HYW])
        acc = [[[ps(f"acc{i}{n}{r}") for r in range(2)] for n in range(2)] for i in range(2)]

        @block.sync
        def _(sp):
            for r in range(2):
                sp.dma_start(z[:, r], zin.rearrange("(t p r) (a c) -> r p t a c", p=P, r=2, a=2)[r]).then_inc(s.z_in, DMA)
            sp.dma_start(w[:, 0], t_fwd[0]).then_inc(s.w_even, DMA)
            sp.dma_start(w[:, 1], t_fwd[1]).then_inc(s.w_odd, DMA)
            for f in range(2, FCH):
                sp.wait_ge(s.mm, (f - 1) * 4)
                sp.dma_start(w[:, f % 2], t_fwd[f]).then_inc((s.w_even, s.w_odd)[f % 2], DMA)

        @block.tensor
        def _(pe):
            pe.wait_ge(s.z_in, 2 * DMA)
            with pe.Fori(0, FCH // 2) as i:
                for par in range(2):
                    pe.wait_ge((s.w_even, s.w_odd)[par], i * DMA + DMA)
                    pe.wait_ge(s.sums_out, 2 * i + par + 1)
                    for n in range(2):
                        for r in range(2):
                            for t in range(NT // 2):
                                op = pe.matmul(acc[par][n][r][:], w[:, par, r * (NT // 2) + t, n, :], z[:, r, t, n, :], start=t == 0, stop=t == NT // 2 - 1)
                            op.then_inc(s.mm, 1)

        @block.scalar
        def _(act):
            with act.Fori(0, FCH // 2) as i:
                for par in range(2):
                    for n in range(2):
                        act.wait_ge(s.mm, (2 * i + par) * 4 + (2 * n + 2))
                        act.wait_ge(s.sums_out, 2 * i + par + 1)
                        act.activation(odd[:, par, n], acc[par][n][1][:], ACT.Copy).then_inc(s.odd_out, 1)

        @block.vector
        def _(dve):
            dve.sem_inc(s.sums_out, 2)
            with dve.Fori(0, FCH // 2) as i:
                for par in range(2):
                    dve.wait_ge((s.stored_even, s.stored_odd)[par], i * DMA)
                    for n in range(2):
                        dve.wait_ge(s.odd_out, (2 * i + par) * 2 + (n + 1))
                        dve.tensor_tensor(o[:, par, n, 0], acc[par][n][0][:], odd[:, par, n], ALU.add)
                        dve.tensor_tensor(o[:, par, n, 1], acc[par][n][0][:], odd[:, par, n], ALU.subtract)
                    dve.drain()
                    dve.sem_inc(s.sums_out, 1)

        @block.gpsimd
        def _(pool):
            with pool.Fori(0, FCH // 2) as i:
                for par in range(2):
                    pool.wait_ge(s.sums_out, 2 * i + par + 3)
                    pool.dma_start(out[rows(i * (2 * P) + par * P), :], o[:, par].rearrange("p n a c -> p (n a c)")).then_inc((s.stored_even, s.stored_odd)[par], DMA)
            pool.wait_ge(s.stored_even, FCH // 2 * DMA)
            pool.wait_ge(s.stored_odd, FCH // 2 * DMA)


def conv_stage(nc, name, t_fwd, t_inv, zin, KS, gate, bias, ZO):
    with stage(nc, name, "z_in", "b_in", "f_even", "f_odd", "k_even", "k_odd", "fwd_mm", "odd_out", "read", "prod", "mixed", "i_even", "i_odd",
               "g_even", "g_odd", "inv_mm", "y_done", "stored_even", "stored_odd") as (block, s, sb, ps):
        z = sb("z", [P, 2, NT // 2, HYW])
        Y = sb("Y", [P, FCH, 2, 2, HYW])
        w = sb("w", [P, 2, NT, 2, P])
        ks = sb("ks", [P, 2, 2, 2, HYW])
        odd = sb("odd", [P, 2, HYW])
        zz = sb("zz", [P, 2, 2, HYW])
        prod = sb("prod", [P, 2, 2, 2, 2, HYW])
        g = sb("g", [P, 2, 2, HYW])
        b_row = sb("b_row", [P, HYW])
        tmp = sb("tmp", [P, 2, HYW])
        o = sb("o", [P, 2, 2, HYW])
        acc = [[[ps(f"acc{i}{n}{r}") for r in range(2)] for n in range(2)] for i in range(2)]
        yac = acc[0][0]

        @block.sync
        def _(sp):
            for r in range(2):
                sp.dma_start(z[:, r], zin.rearrange("(t p r) c -> r p t c", p=P, r=2)[r]).then_inc(s.z_in, DMA)
            sp.dma_start(b_row[:], bias.partition_broadcast(P)).then_inc(s.b_in, DMA)
            for f in range(FCH):
                if f >= 2:
                    sp.wait_ge(s.fwd_mm, (f - 1) * 2)
                sp.dma_start(w[:, f % 2], t_fwd[f]).then_inc((s.f_even, s.f_odd)[f % 2], DMA)
                if f >= 2:
                    sp.wait_ge(s.prod, f - 1)
                sp.dma_start(ks[:, f % 2].rearrange("p n a c -> p (n a c)"), KS[f * P:(f + 1) * P, :]).then_inc((s.k_even, s.k_odd)[f % 2], DMA)
            for t in range(NT // 2):
                if t < 2:
                    sp.wait_ge(s.fwd_mm, (FCH - 1 + t) * 2)
                else:
                    sp.wait_ge(s.inv_mm, (t - 1) * 2)
                    sp.wait_ge(s.y_done, (t - 1) * 2)
                sp.dma_start(w[:, t % 2].rearrange("p a b q -> p (a b q)"), t_inv[t].rearrange("p r f n t -> p (r f n t)")).then_inc((s.i_even, s.i_odd)[t % 2], DMA)
                sp.dma_start(g[:, t % 2], gate.rearrange("(t p r) c -> t p r c", p=P, r=2)[t]).then_inc((s.g_even, s.g_odd)[t % 2], DMA)

        @block.gpsimd
        def _(pool):
            for f in range(FCH):
                pool.wait_ge(s.prod, f + 1)
                a = prod[:, f % 2, 0]
                for n in range(2):
                    pool.tensor_tensor(Y[:, f, 0, n], a[:, 0, n], a[:, 1, n], ALU.add)
                    pool.tensor_tensor(Y[:, f, 1, n], a[:, 0, n], a[:, 1, n], ALU.subtract)
                pool.drain()
                pool.sem_inc(s.mixed, 1)
            for t in range(NT // 2):
                pool.wait_ge(s.y_done, 2 * t + 2)
                pool.dma_start(ZO.rearrange("(t p r) c -> t p r c", p=P, r=2)[t], o[:, t % 2]).then_inc((s.stored_even, s.stored_odd)[t % 2], DMA)
            pool.wait_ge(s.stored_even, NT // 4 * DMA)
            pool.wait_ge(s.stored_odd, NT // 4 * DMA)

        @block.tensor
        def _(pe):
            pe.wait_ge(s.z_in, 2 * DMA)
            for f in range(FCH):
                par = f % 2
                pe.wait_ge((s.f_even, s.f_odd)[par], (f // 2 + 1) * DMA)
                if f >= 2:
                    pe.wait_ge(s.read, f - 1)
                for n in range(2):
                    for r in range(2):
                        for t in range(NT // 2):
                            op = pe.matmul(acc[par][n][r][:], w[:, par, r * (NT // 2) + t, n, :], z[:, r, t, :], start=t == 0, stop=t == NT // 2 - 1)
                    op.then_inc(s.fwd_mm, 1)
            pe.wait_ge(s.read, FCH)
            for t in range(NT // 2):
                pe.wait_ge((s.i_even, s.i_odd)[t % 2], (t // 2 + 1) * DMA)
                for r in range(2):
                    if t:
                        pe.wait_ge(s.y_done, 2 * t - 1 + r)
                    for f in range(FCH):
                        if t == 0 and r == 0:
                            pe.wait_ge(s.mixed, f + 1)
                        for n in range(2):
                            op = pe.matmul(yac[r][:], w[:, t % 2, r * FCH + f, n, :], Y[:, f, r, n, :], start=n == 0 and f == 0, stop=n == 1 and f == FCH - 1)
                    op.then_inc(s.inv_mm, 1)

        @block.scalar
        def _(act):
            for f in range(FCH):
                for n in range(2):
                    act.wait_ge(s.fwd_mm, 2 * f + n + 1)
                    if f:
                        act.wait_ge(s.read, f)
                    act.activation(odd[:, n], acc[f % 2][n][1][:], ACT.Copy).then_inc(s.odd_out, 1)

        @block.vector
        def _(dve):
            for f in range(FCH):
                par = f % 2
                for n in range(2):
                    dve.wait_ge(s.odd_out, 2 * f + n + 1)
                    dve.tensor_tensor(zz[:, 0, n], acc[par][n][0][:], odd[:, n], ALU.add)
                    dve.tensor_tensor(zz[:, 1, n], acc[par][n][0][:], odd[:, n], ALU.subtract)
                dve.drain()
                dve.sem_inc(s.read, 1)
                dve.wait_ge((s.k_even, s.k_odd)[par], (f // 2 + 1) * DMA)
                if f >= 2:
                    dve.wait_ge(s.mixed, f - 1)
                for a in range(2):
                    (zc, zs), (kc, kz) = (zz[:, a, 0], zz[:, a, 1]), (ks[:, par, 0, a], ks[:, par, 1, a])
                    for q, n, u, v in ((0, 0, zc, kc), (1, 0, zs, kz), (0, 1, zc, kz), (1, 1, zs, kc)):
                        dve.tensor_tensor(prod[:, par, q, a, n], u, v, ALU.mult)
                dve.drain()
                first, second = prod[:, par, 0], prod[:, par, 1]
                dve.tensor_tensor(first[:, :, 0], first[:, :, 0], second[:, :, 0], ALU.subtract)
                dve.tensor_tensor(first[:, :, 1], first[:, :, 1], second[:, :, 1], ALU.add)
                dve.drain()
                dve.sem_inc(s.prod, 1)
            dve.wait_ge(s.b_in, DMA)
            for t in range(NT // 2):
                dve.wait_ge((s.g_even, s.g_odd)[t % 2], (t // 2 + 1) * DMA)
                if t >= 2:
                    dve.wait_ge((s.stored_even, s.stored_odd)[t % 2], DMA)
                for r in range(2):
                    dve.tensor_tensor(tmp[:, r], z[:, r, t, :], b_row[:], ALU.mult)
                dve.drain()
                for r in range(2):
                    dve.wait_ge(s.inv_mm, 2 * t + r + 1)
                    dve.scalar_tensor_tensor(tmp[:, r], yac[r][:], 1.0 / NFREQ, tmp[:, r], ALU.mult, ALU.add)
                    dve.drain()
                    dve.tensor_tensor(o[:, t % 2, r], tmp[:, r], g[:, t % 2, r], ALU.mult)
                    dve.drain()
                    dve.sem_inc(s.y_done, 1)


def na_tables():
    q, k = np.arange(GRID_C)[:, None], np.arange(GRID_C)[None, :]
    lo = np.clip(q - WIN_C // 2, 0, GRID_C - WIN_C)
    inside = (k >= lo) & (k < lo + WIN_C)
    hot = np.zeros((2 * WIN_C, GRID_C, GRID_C), np.float32)
    for o in range(2 * WIN_C - 1):
        hot[o] = inside & (k - q + WIN_C - 1 == o)
    hot[2 * WIN_C - 1] = np.where(inside, 0.0, NEG)
    return hot.reshape(2 * WIN_C, GRID_C * GRID_C)


def na_bias_stage(nc, ident, rpb, t_hot, BIAS):
    HR = HN * (2 * WIN_R - 1)
    NC_ = 2 * WIN_C - 1
    with stage(nc, "nab", "const", "init", "turned", "tab", "mm", "b_out", "stored") as (block, s, sb, ps):
        tab = sb("tab", [HR, 2 * WIN_C])
        tabT = sb("tabT", [2 * WIN_C, HR])
        hot = sb("hot", [2 * WIN_C, GRID_C * GRID_C])
        o = sb("o", [HR, GRID_C * GRID_C])
        pt = ps("pt")
        acc = ps("acc")

        @block.sync
        def _(sp):
            sp.wait_ge(s.init, 1)
            sp.dma_start(tab[:, 0:NC_], rpb.rearrange("h r c -> (h r) c")).then_inc(s.const, DMA)
            sp.dma_start(hot[:], t_hot).then_inc(s.const, DMA)
            sp.wait_ge(s.b_out, GRID_C * GRID_C // 512)
            sp.dma_start(BIAS, o[:]).then_inc(s.stored, DMA)
            sp.wait_ge(s.stored, DMA)

        @block.tensor
        def _(pe):
            pe.wait_ge(s.const, 2 * DMA)
            pe.transpose(pt[:2 * WIN_C, :HR], tab[:], ident[:HR, :HR]).then_inc(s.turned, 1)
            pe.wait_ge(s.tab, 1)
            for n in range(GRID_C * GRID_C // 512):
                if n:
                    pe.wait_ge(s.b_out, n)
                pe.matmul(acc[:HR, :], tabT[:], hot[:, n * 512:(n + 1) * 512], start=True, stop=True).then_inc(s.mm, 1)

        @block.vector
        def _(dve):
            dve.memset(tab[:], 1.0)
            dve.drain()
            dve.sem_inc(s.init, 1)
            dve.wait_ge(s.turned, 1)
            dve.tensor_copy(tabT[:], pt[:2 * WIN_C, :HR]).then_inc(s.tab, 1)
            for n in range(GRID_C * GRID_C // 512):
                dve.wait_ge(s.mm, n + 1)
                dve.tensor_copy(o[:, n * 512:(n + 1) * 512], acc[:HR, :]).then_inc(s.b_out, 1)


def na_stage(nc, ident, U3, KV3, BIAS, NA):
    NR = 2 * WIN_R - 1
    WK = WIN_R * GRID_C
    NK = WK + CTX
    NP_ = NK // P
    HP = HN // 2
    NU = HP * GRID_R
    with stage(nc, "na", "init", "k_in", "q_in", "v_in", "b_in", "turned", "qk_out", "q_bd", "s_mm", "s_done", "neg_max", "probs",
               "p_turned", "p_out", "pv", "y", "stored") as (block, s, sb, ps):
        kin = sb("kin", [P, NTA, 512])
        qin = sb("qin", [P, NT, 512])
        kT = sb("kT", [P, HP * ALL])
        qT = sb("qT", [P, HP * SEQ + GRID_C])
        vc = sb("vc", [P, NTC, 512])
        vl = sb("vl", [P, 2 * NT, 512])
        bias = sb("bias", [P, HP * NR, GRID_C])
        qbd = sb("qbd", [P, 2, P])
        sc = sb("sc", [P, 2, NK])
        mx = sb("mx", [P, 2])
        sm = sb("sm", [P, 4])
        pT = sb("pT", [P, 2, NP_, P])
        y = sb("y", [P, NU, HD])
        pS = [ps(f"pS{i}", [P, 1024]) for i in range(2)]
        pP = ps("pP", [P, 8, P])
        pV = ps("pV")

        def place(u):
            r = u % GRID_R
            start = (r - 4) * (r >= 4) - (r - 12) * (r >= 12)
            off = start - r + (WIN_R - 1)
            if not isinstance(u, int):
                start, off = start.with_bounds(min_val=0, max_val=GRID_R - WIN_R), off.with_bounds(min_val=0, max_val=WIN_R - 1)
            return r, start, off

        def tile_of(start):
            tile = (start % 2) * NT + start // 2
            return tile if isinstance(start, int) else tile.with_bounds(min_val=0, max_val=2 * NT - 5)

        def steps(eng, body):
            for u in range(2):
                body(u, u % 2, u)
            with eng.Fori(1, NU // 2) as i:
                for par in range(2):
                    body(2 * i + par, par, None)
            for u in range(NU, NU + 2):
                body(u, u % 2, u)

        def active(at, lag):
            return at is None or 0 <= at - lag < NU

        @block.sync
        def _(sp):
            sp.dma_start(kin[:, 0:NTC], KV3[:, 0:512].rearrange("(t p) c -> p t c", p=P)).then_inc(s.k_in, DMA)
            sp.dma_start(kin[:, NTC:], U3[:, O_NK:O_NV].rearrange("(t p) c -> p t c", p=P)).then_inc(s.k_in, DMA)
            sp.dma_start(qin[:], U3[:, O_NQ:O_NK].rearrange("(t p) c -> p t c", p=P)).then_inc(s.q_in, DMA)
            for a in range(2):
                for hp in range(HP):
                    r0 = (2 * hp + a) * NR
                    sp.dma_start(bias[a * GRID_C:(a + 1) * GRID_C, hp * NR:(hp + 1) * NR], BIAS[r0:r0 + NR, :].rearrange("r (q c) -> q r c", q=GRID_C)).then_inc(s.b_in, DMA)
            sp.dma_start(vc[:], KV3[:, 512:1024].rearrange("(t p) c -> p t c", p=P)).then_inc(s.v_in, DMA)
            sp.dma_start(vl[:, 0:NT], U3[:, O_NV:O_NZ].rearrange("(t p) c -> p t c", p=P)).then_inc(s.v_in, DMA)
            sp.dma_start(vl[:, NT:2 * NT - 1], U3[GRID_C:SEQ - GRID_C, O_NV:O_NZ].rearrange("(t p) c -> p t c", p=P)).then_inc(s.v_in, DMA)
            na_v = NA.rearrange("(r q) c -> q r c", q=GRID_C)
            for hp in range(HP):
                sp.wait_ge(s.y, (hp + 1) * GRID_R)
                for a in range(2):
                    h = 2 * hp + a
                    sp.dma_start(na_v[:, :, h * HD:(h + 1) * HD], y[a * GRID_C:(a + 1) * GRID_C, hp * GRID_R:(hp + 1) * GRID_R]).then_inc(s.stored, DMA)
            sp.wait_ge(s.stored, 2 * HP * DMA)

        @block.tensor
        def _(pe):
            pe.wait_ge(s.init, 1)
            pe.wait_ge(s.k_in, 2 * DMA)
            pe.wait_ge(s.q_in, DMA)
            n = 0
            for hp in range(HP):
                for src, lo, hi in ((kin, 0, 5), (kin, 5, NTA), (qin, 0, NT)):
                    if n >= 2:
                        pe.wait_ge(s.qk_out, n - 1)
                    for t in range(lo, hi):
                        op = pe.transpose(pS[n % 2][:, (t - lo) * P:(t - lo + 1) * P], src[:, t, hp * P:(hp + 1) * P], ident[:])
                    op.then_inc(s.turned, 1)
                    n += 1
            pe.wait_ge(s.qk_out, n)
            pe.wait_ge(s.v_in, 3 * DMA)

            def step(u, par, at):
                if active(at, 0):
                    _, start, _ = place(u)
                    pe.wait_ge(s.q_bd, u + 1)
                    if at is None:
                        pe.wait_ge(s.s_done, u - 1)
                    col = (u // GRID_R) * ALL
                    pe.matmul(pS[par][:, 0:WK], qbd[:, par], kT[:, bass.ds(col + start * GRID_C + CTX, WK)], start=True, stop=True)
                    pe.matmul(pS[par][:, WK:NK], qbd[:, par], kT[:, bass.ds(col, CTX)], start=True, stop=True).then_inc(s.s_mm, 1)
                if active(at, 1):
                    pe.wait_ge(s.probs, u)
                    if active(at, 2):
                        pe.wait_ge(s.p_out, u - 1)
                    for c in range(NP_):
                        op = pe.transpose(pP[:, c, :], sc[:, 1 - par, c * P:(c + 1) * P], ident[:])
                    op.then_inc(s.p_turned, 1)
                if active(at, 2):
                    v = u - 2
                    _, start, _ = place(v)
                    pe.wait_ge(s.p_out, v + 1)
                    if at != 2:
                        pe.wait_ge(s.y, v)
                    hp = v // GRID_R
                    tile = tile_of(start)
                    for c in range(WK // P):
                        pe.matmul(pV[:, 0:P], pT[:, par, c, :], vl[:].rearrange("p t c -> p (t c)")[:, bass.ds((tile + c) * 512 + hp * P, P)], start=c == 0, stop=False)
                    for c in range(NTC):
                        op = pe.matmul(pV[:, 0:P], pT[:, par, WK // P + c, :], vc[:].rearrange("p t c -> p (t c)")[:, bass.ds(hp * P + c * 512, P)], start=False, stop=c == NTC - 1)
                    op.then_inc(s.pv, 1)
            steps(pe, step)

        @block.scalar
        def _(act):
            n = 0
            for hp in range(HP):
                for lo, hi in ((0, 5), (5, NTA), (NTA, NTA + NT)):
                    act.wait_ge(s.turned, n + 1)
                    src = pS[n % 2][:, 0:(hi - lo) * P]
                    if lo < NTA:
                        op = act.activation(kT[:, hp * ALL + lo * P:hp * ALL + hi * P], src, ACT.Copy)
                    else:
                        op = act.activation(qT[:, hp * SEQ:(hp + 1) * SEQ], src, ACT.Copy, scale=HD ** -0.5)
                    op.then_inc(s.qk_out, 1)
                    n += 1

            def step(u, par, at):
                if active(at, 1):
                    act.wait_ge(s.p_turned, u)
                    if active(at, 3):
                        act.wait_ge(s.pv, u - 2)
                    act.activation(pT[:, 1 - par], pP[:, 0:NP_], ACT.Copy).then_inc(s.p_out, 1)
                if active(at, 0):
                    act.wait_ge(s.neg_max, u + 1)
                    act.activation(sc[:, par], sc[:, par], ACT.Exp, bias=mx[:, par:par + 1], accum_out=sm[:, 2 * par:2 * par + 1])
                    act.drain()
                    act.sem_inc(s.probs, 1)
            steps(act, step)

        @block.vector
        def _(dve):
            def spread(v, par):
                for a in range(2):
                    e = slice(a * HD, (a + 1) * HD)
                    dve.tensor_copy(qbd[e, par, e], qT[e, bass.ds(v * GRID_C, GRID_C)])
                dve.drain()
                dve.sem_inc(s.q_bd, 1)

            dve.memset(qbd[:], 0.0)
            dve.memset(qT[:, HP * SEQ:], 0.0)
            dve.drain()
            dve.sem_inc(s.init, 1)
            dve.wait_ge(s.qk_out, 3 * HP)
            spread(0, 0)
            dve.wait_ge(s.b_in, 2 * HP * DMA)

            def step(u, par, at):
                if active(at, 0):
                    _, _, off = place(u)
                    if at is None or u + 1 < NU:
                        if at != 0:
                            dve.wait_ge(s.s_mm, u)
                        spread(u + 1, 1 - par)
                    dve.wait_ge(s.s_mm, u + 1)
                    if at is None:
                        dve.wait_ge(s.p_turned, u - 1)
                    b = bias[:, bass.ds((u // GRID_R) * NR + off, WIN_R), :].rearrange("p a c -> p (a c)")
                    dve.tensor_tensor(sc[:, par, 0:WK], pS[par][:, 0:WK], b, ALU.add)
                    dve.tensor_copy(sc[:, par, WK:], pS[par][:, WK:NK])
                    dve.drain()
                    dve.sem_inc(s.s_done, 1)
                    dve.tensor_reduce(mx[:, par:par + 1], sc[:, par], AX_X, ALU.max, negate=True)
                    dve.drain()
                    dve.sem_inc(s.neg_max, 1)
                if active(at, 2):
                    v = u - 2
                    dve.wait_ge(s.pv, v + 1)
                    for a in range(2):
                        e = slice(a * HD, (a + 1) * HD)
                        dve.tensor_scalar(y[e, bass.ds(v, 1), :].rearrange("p a c -> p (a c)"), pV[e, a * HD:(a + 1) * HD], sm[e, 2 * par + 1:2 * par + 2], None, ALU.mult)
                    dve.drain()
                    dve.sem_inc(s.y, 1)
                if active(at, 1):
                    dve.wait_ge(s.probs, u)
                    dve.reciprocal(sm[:, 3 - 2 * par:4 - 2 * par], sm[:, 2 - 2 * par:3 - 2 * par])
                    dve.drain()
            steps(dve, step)


def tables():
    prefix, suffix, causal = gla_tables()
    mask, first, freq = swa_tables()
    rope, dist, q_pos, k_pos = retention_tables()
    sums, ends, pairs, level = rwkv_tables()
    feats, decay, fwd, inv = hyena_tables()
    return {
        "t_eye": np.eye(P, dtype=np.float32), "t_prefix": prefix, "t_suffix": suffix, "t_causal": causal,
        "t_mask": mask, "t_first": first, "t_freq": freq, "t_rope": rope, "t_dist": dist, "t_qpos": q_pos,
        "t_kpos": k_pos, "t_edges_all": rwkv_edges(), "t_sums": sums, "t_ends": ends, "t_pairs": pairs,
        "t_level": level, "t_edges_seq": edges_of_sequence(), "t_feats": feats, "t_decay": decay,
        "t_fwd": fwd, "t_inv": inv, "t_hot": na_tables(),
    }


def start_stage(nc, ident, t_eye, padded):
    with stage(nc, "start", "id_in", "zero", "pad_out") as (block, s, sb, ps):
        zero = sb("zero", [1, EVEN_IN])

        @block.vector
        def _(dve):
            dve.memset(zero[:], 0.0).then_inc(s.zero, 1)

        @block.sync
        def _(sp):
            sp.dma_start(ident[:], t_eye).then_inc(s.id_in, DMA)
            sp.wait_ge(s.zero, 1)
            for t in padded:
                for row in (0, t.shape[0] - 1):
                    sp.dma_start(t[row:row + 1, :], zero[:, :t.shape[1]]).then_inc(s.pad_out, DMA)
            sp.wait_ge(s.id_in, DMA)
            sp.wait_ge(s.pad_out, 2 * len(padded) * DMA)


@contextmanager
def split_pair(nc, name, tokens):
    with nc.sbuf_tensor(f"{name}_hi", [P, KC, tokens], F32R) as hi, nc.sbuf_tensor(f"{name}_lo", [P, KC, tokens], F32R) as lo:
        yield hi, lo


def program(nc, T):
    def scratch(name, *shape):
        return nc.dram_tensor(name, shape, F32, kind="Internal").ap()

    mod1 = scratch("mod1", 1, 6 * D)
    mod2 = scratch("mod2", 2, 2, 3 * D)
    P1 = scratch("P1", SEQ, T["w_in"].shape[2])
    YA, Y1, O1, X1, D1, X2 = (scratch(n, SEQ, D) for n in ("YA", "Y1", "O1", "X1", "D1", "X2"))
    U2p = scratch("U2p", ALL + 2, EVEN_IN)
    U2 = U2p[1:ALL + 1, :]
    YB2, O2 = scratch("YB2", ALL, D), scratch("O2", ALL, D)
    PC, PD = scratch("PC", ALL, 3 * 512 + HN), scratch("PD", 2, ALL, 3 * 512)
    RW = scratch("RW", 2, ALL, 512)
    H1 = scratch("H1", SEQ, D)
    U3p = scratch("U3p", SEQ + 2, ODD_IN)
    U3 = U3p[1:SEQ + 1, :]
    KV3 = scratch("KV3", CTX, 1024)
    VX = scratch("VX", SEQ, 3 * HYW)
    FS, KS = scratch("FS", 2, SEQ, 2 * HYW), scratch("KS", 2, HALF, 4 * HYW)
    Z1, Z2, NA = (scratch(n, SEQ, HYW) for n in ("Z1", "Z2", "NA"))
    BIAS = scratch("BIAS", HN * (2 * WIN_R - 1), GRID_C * GRID_C)
    O3 = scratch("O3", SEQ, D)

    x, ctx = T["x"][0], T["ctx_2"][0]
    part1 = lambda n: mod1[0, n * D:(n + 1) * D]
    part2 = lambda layer, who, n: mod2[layer, who, n * D:(n + 1) * D]

    with nc.sbuf_tensor("ident", [P, P], F32) as ident:
        start_stage(nc, ident, T["t_eye"], (U2p, U3p))
        ada_stage(nc, [([T["c"][0]], T["w_ada"][0], T["b_ada"][0], mod1)]
                  + [([T["c_2"][0], T["c_ctx_2"]], T["ada_w_2"][n], T["ada_b_2"][n], mod2[n]) for n in range(2)])

        with split_pair(nc, "h1", SEQ) as (hi, lo):
            with nc.sbuf_tensor("h1T", [P, KC, SEQ], F32) as hT:
                norm_stage(nc, "n1", ident, x, 0, NT, hT, 0, norm="ln", scale=part1(1), shift=part1(0))
                split_stage(nc, "h1s", hT, hi, lo, KC)
            gemm_stage(nc, "g_in", hi, lo, KC, NT, T["w_in"][0], P1)
        gla_stage(nc, ident, P1, T["gla_w_lr"][0], T["gla_b_lr"][0], T["gla_norm_g"][0], T["t_prefix"], T["t_suffix"], T["t_causal"], YA)
        swa_stage(nc, ident, P1, T["positions"][0], T["swa_sinks"][0], T["t_mask"], T["t_first"], T["t_freq"], YA, Y1)
        with split_pair(nc, "y1", SEQ) as (hi, lo):
            turn_stage(nc, "turn1", ident, [Y1], NT, hi, lo)
            gemm_stage(nc, "g_o", hi, lo, KC, NT, T["w_o"][0], O1)
        with nc.sbuf_tensor("fT", [P, FC, SEQ], F32) as fT:
            with split_pair(nc, "h2", SEQ) as (hi, lo):
                hT = fT[:, 0:KC, :]
                norm_stage(nc, "n2", ident, x, 0, NT, hT, 0, norm="ln", scale=part1(4), shift=part1(3), res=O1, gate=part1(2),
                           alpha=ALPHA, affine=(T["ln1_g"][0], T["ln1_b"][0]), keep=X1)
                split_stage(nc, "h2s", hT, hi, lo, KC)
                ffn_up_stage(nc, ident, hi, lo, T["w_up"][0], T["conv_w"][0], T["conv_b"][0], fT)
            gemm_stage(nc, "g_down", fT, None, FC, NT, T["w_down"][0], D1, width=256)

        with split_pair(nc, "h3", ALL) as (hi, lo):
          with nc.sbuf_tensor("h3T", [P, KC, ALL], F32) as hT:
            norm_stage(nc, "n3", ident, X1, 0, NT, hT, CTX, norm="rms", scale=part2(0, 0, 1), shift=part2(0, 0, 0), weight=T["norm_w_2"][0],
                       res=D1, gate=part1(5), alpha=ALPHA, affine=(T["ln2_g"][0], T["ln2_b"][0]), keep=X2)
            norm_stage(nc, "n3c", ident, ctx, 0, NTC, hT, 0, norm="rms", scale=part2(0, 1, 1), shift=part2(0, 1, 0), weight=T["norm_w_2"][0])
            split_stage(nc, "h3s", hT, hi, lo, KC)
          gemm_stage(nc, "g_even", hi, lo, KC, NTA, T["even_w_in_2"][0], U2, width=384)
        retention_stage(nc, ident, U2, T["ret_decay_2"][0], T["t_rope"], T["t_dist"], T["t_qpos"], T["t_kpos"], YB2)
        rwkv_prep_stage(nc, ident, U2p, T["rw_mu_2"][0], T["rw_w0_2"][0], T["rw_w2_2"][0], T["rw_a0_2"][0], T["rw_a2_2"][0], T["rw_kk_2"][0],
                        T["rw_ka_2"][0], T["rw_rk_2"][0].rearrange("h d -> (h d)"), T["t_edges_all"], PC, PD)
        rwkv_stage(nc, ident, PC, PD, T["t_sums"], T["t_ends"], T["t_pairs"], T["t_level"], RW)
        rwkv_out_stage(nc, RW, PC, U2, T["rw_ln_w_2"][0], T["rw_ln_b_2"][0], YB2)
        with split_pair(nc, "y2", ALL) as (hi, lo):
            turn_stage(nc, "turn2", ident, [YB2], NTA, hi, lo)
            gemm_stage(nc, "g_eout", hi, lo, KC, NTA, T["even_w_out_2"][0], O2, width=384)

        with split_pair(nc, "h4", ALL) as (hi, lo):
          with nc.sbuf_tensor("h4T", [P, KC, ALL], F32) as hT:
            norm_stage(nc, "n4", ident, X2, 0, NT, hT, CTX, norm="rms", scale=part2(1, 0, 1), shift=part2(1, 0, 0), weight=T["norm_w_2"][1],
                       res=O2, res_row0=CTX, gate=part2(0, 0, 2), keep=H1)
            norm_stage(nc, "n4c", ident, ctx, 0, NTC, hT, 0, norm="rms", scale=part2(1, 1, 1), shift=part2(1, 1, 0), weight=T["norm_w_2"][1],
                       res=O2, gate=part2(0, 1, 2))
            split_stage(nc, "h4s", hT, hi, lo, KC)
          gemm_stage(nc, "g_odd", hi[:, :, CTX:], lo[:, :, CTX:], KC, NT, T["odd_w_in_2"][0], U3, width=384)
          gemm_stage(nc, "g_ckv", hi[:, :, 0:CTX], lo[:, :, 0:CTX], KC, NTC, T["odd_w_in_2"][0][:, O_NK:O_NZ], KV3, width=384)
        short_conv_stage(nc, U3p, T["hy_conv_w_2"][0], T["hy_conv_b_2"][0], T["t_edges_seq"], VX)
        filter_stage(nc, T["t_feats"], T["t_decay"], T["hy_w1_2"][0], T["hy_b1_2"][0], T["hy_f1_2"][0], T["hy_w2_2"][0], T["hy_b2_2"][0],
                     T["hy_f2_2"][0], T["hy_w3_2"][0], FS)
        for order, (zin, zout) in enumerate(((VX[:, 0:HYW], Z1), (Z1, Z2))):
            spectrum_stage(nc, f"spec{order}", T["t_fwd"], FS[order], KS[order])
            conv_stage(nc, f"conv{order}", T["t_fwd"], T["t_inv"], zin, KS[order], VX[:, (order + 1) * HYW:(order + 2) * HYW], T["hy_bias_2"][0, order], zout)
        na_bias_stage(nc, ident, T["na_rpb_2"][0], T["t_hot"], BIAS)
        na_stage(nc, ident, U3, KV3, BIAS, NA)
        with split_pair(nc, "y3", SEQ) as (hi, lo):
            turn_stage(nc, "turn3", ident, [Z2, NA], NT, hi, lo, gates=[U3[:, O_HZ:O_NQ], U3[:, O_NZ:ODD_IN]])
            gemm_stage(nc, "g_oout", hi, lo, KC, NT, T["odd_w_out_2"][0], O3)
        norm_stage(nc, "n5", ident, H1, 0, NT, None, 0, norm="rms", res=O3, gate=part2(1, 0, 2), final=T["final_norm_w_2"], keep=T["out"][0])


def kernel(**inputs):
    import concourse.bacc as bacc
    from concourse.bass_utils import run_bass_kernel_spmd

    nc = bacc.Bacc("TRN2", target_bir_lowering=False, num_devices=1)
    arrays, T = {}, {}
    for name, a in list(inputs.items()) + list(tables().items()):
        a = np.ascontiguousarray(a)
        arrays[f"in_{name}"] = a
        T[name] = nc.dram_tensor(f"in_{name}", a.shape, mybir.dt.from_np(a.dtype), kind="ExternalInput").ap()
    T["out"] = nc.dram_tensor("out_y", (1, SEQ, D), F32, kind="ExternalOutput").ap()
    program(nc, T)
    r = run_bass_kernel_spmd(nc, [arrays], core_ids=[0])
    return r.results[0]["out_y"]
```
